# Optimizing a Trainium2 kernel written in Bass

```python
import math
import jax
import jax.numpy as jnp
from jax import lax
import numpy as np
import jax, jax.numpy as jnp

D_MODEL = 1024
BATCH = 1
SEQ = 512
DEPTH = 1

CTX_LEN = 256
GRID_W = 64
EPS = 1e-6

ATT_HEADS = 8
ATT_KV_HEADS = 2
ATT_GROUP = ATT_HEADS // ATT_KV_HEADS
HEAD_DIM = 128
ROPE_PAIRS_PER_AXIS = HEAD_DIM // 4
ROPE_THETA = 10000.0
Q_BLOCK = 128

GLA_HEADS = 4
GLA_DK = 64
GLA_DV = 128
GLA_RANK = 16
GLA_TAU = 16.0
GLA_CHUNK = 64

HY_WIDTH = 512
HY_ORDER = 2
HY_BANDS = 16
HY_EMB = 1 + 2 * HY_BANDS
HY_FFN = 64
HY_DECAY_SLOW = -math.log(1e-2) / 1.5
HY_DECAY_FAST = -math.log(1e-2) / 0.3

N_EXPERTS = 16
N_GROUPS = 4
EXPERTS_PER_GROUP = N_EXPERTS // N_GROUPS
TOP_K = 2
D_EXPERT = 512

N_BRANCH = 3
ATT_Q_W = ATT_HEADS * HEAD_DIM
ATT_KV_W = ATT_KV_HEADS * HEAD_DIM
GLA_K_W = GLA_HEADS * GLA_DK
GLA_V_W = GLA_HEADS * GLA_DV
KV_SPLITS = (ATT_KV_W, ATT_KV_W, GLA_K_W, GLA_V_W, 2 * GLA_RANK)
REST_SPLITS = (ATT_Q_W, GLA_K_W, GLA_V_W, 3 * HY_WIDTH, N_BRANCH * D_MODEL)
N_KV_COLS = sum(KV_SPLITS)
N_IN = N_KV_COLS + sum(REST_SPLITS)


def rms_norm(x, g):
    xf = x.astype(jnp.float32)
    y = xf * lax.rsqrt(jnp.mean(xf * xf, axis=-1, keepdims=True) + EPS)
    return (y * g.astype(jnp.float32)).astype(x.dtype)

def split_cols(t, sizes):
    cuts = [int(v) for v in np.cumsum(sizes)[:-1]]
    return jnp.split(t, cuts, axis=-1)

def modulate(h, shift, scale):
    return h * (1 + scale[..., None, :]) + shift[..., None, :]

def to_heads(t, n_heads):
    b, n, w = t.shape
    return t.reshape(b, n, n_heads, w // n_heads).transpose(0, 2, 1, 3)

def q_heads(t):
    b, n, _ = t.shape
    return t.reshape(b, n, ATT_KV_HEADS, ATT_GROUP, HEAD_DIM).transpose(0, 2, 3, 1, 4)

def tflip(t):
    return jnp.flip(t, axis=2)

def axial_rope_tables(n_tokens):
    rows = n_tokens // GRID_W
    row = jnp.broadcast_to(jnp.arange(rows)[:, None], (rows, GRID_W)).reshape(-1).astype(jnp.float32)
    col = jnp.broadcast_to(jnp.arange(GRID_W)[None, :], (rows, GRID_W)).reshape(-1).astype(jnp.float32)
    inv_freq = ROPE_THETA ** (-jnp.arange(ROPE_PAIRS_PER_AXIS, dtype=jnp.float32) / ROPE_PAIRS_PER_AXIS)
    ang = jnp.concatenate([row[:, None] * inv_freq, col[:, None] * inv_freq], axis=-1)
    return jnp.cos(ang), jnp.sin(ang)

def apply_rope(x, cos, sin):
    xf = x.astype(jnp.float32)
    x1, x2 = xf[..., 0::2], xf[..., 1::2]
    out = jnp.stack([x1 * cos - x2 * sin, x1 * sin + x2 * cos], axis=-1)
    return out.reshape(x.shape).astype(x.dtype)

def gqa_latent(q, k, v):
    b, hkv, g, s, hd = q.shape
    nb = s // Q_BLOCK
    qb = jnp.moveaxis(q.reshape(b, hkv, g, nb, Q_BLOCK, hd), 3, 0)
    scale = HEAD_DIM ** -0.5

    def one_block(qblk):
        sc = jnp.einsum('bkgqd,bknd->bkgqn', qblk, k).astype(jnp.float32) * scale
        p = jax.nn.softmax(sc, axis=-1).astype(v.dtype)
        return jnp.einsum('bkgqn,bknd->bkgqd', p, v)

    o = lax.map(one_block, qb)
    return o.transpose(1, 0, 4, 2, 3, 5).reshape(b, s, hkv * g * hd)

def gqa_context(q, k, v):
    b, hkv, g, n, hd = q.shape
    sc = jnp.einsum('bkgqd,bknd->bkgqn', q, k).astype(jnp.float32) * HEAD_DIM ** -0.5
    p = jax.nn.softmax(sc, axis=-1).astype(v.dtype)
    o = jnp.einsum('bkgqn,bknd->bkgqd', p, v)
    return o.transpose(0, 3, 1, 2, 4).reshape(b, n, hkv * g * hd)

def gla_q(t):
    return to_heads(t, GLA_HEADS).astype(jnp.float32) * GLA_DK ** -0.5

def gla_log_decay(a_low, w_a2, b_a):
    z = (a_low @ w_a2 + b_a).astype(jnp.float32)
    return to_heads(jax.nn.log_sigmoid(z) / GLA_TAU, GLA_HEADS)

def gla_chunked(q, k, v, log_a, s0):
    b, h, n_tok, dk = q.shape
    dv = v.shape[-1]
    n = n_tok // GLA_CHUNK

    def rs(t):
        return t.reshape(b, h, n, GLA_CHUNK, t.shape[-1])

    q, k, v, log_a = rs(q), rs(k), rs(v), rs(log_a)
    cum = jnp.cumsum(log_a, axis=3)
    cum_last = cum[:, :, :, -1:, :]
    q_dec = q * jnp.exp(cum)
    k_inv = k * jnp.exp(-cum)
    k_to_end = k * jnp.exp(cum_last - cum)
    mask = jnp.tril(jnp.ones((GLA_CHUNK, GLA_CHUNK), dtype=bool))
    att = jnp.where(mask, jnp.einsum('bhnqd,bhnsd->bhnqs', q_dec, k_inv), 0.0)
    o_intra = jnp.einsum('bhnqs,bhnsv->bhnqv', att, v)
    chunk_state = jnp.einsum('bhnsd,bhnsv->bhndv', k_to_end, v)
    chunk_decay = jnp.exp(cum_last[:, :, :, 0, :])

    def step(state, xs):
        dec, cs = xs
        return dec[..., None] * state + cs, state

    s_final, s_prev = lax.scan(step, s0, (jnp.moveaxis(chunk_decay, 2, 0), jnp.moveaxis(chunk_state, 2, 0)))
    s_prev = jnp.moveaxis(s_prev, 0, 2)
    o_inter = jnp.einsum('bhnqd,bhndv->bhnqv', q_dec, s_prev)
    return (o_intra + o_inter).reshape(b, h, n_tok, dv), s_final

def gla_final_state(k, v, log_a):
    cum = jnp.cumsum(log_a, axis=2)
    w = jnp.exp(cum[:, :, -1:, :] - cum)
    return jnp.einsum('bhld,bhlv->bhdv', k * w, v)

def gla_bidir(q, k, v, la_f, la_b, s0_f, s0_b):
    o_f, s_f = gla_chunked(q, k, v, la_f, s0_f)
    o_b, s_b = gla_chunked(tflip(q), tflip(k), tflip(v), tflip(la_b), s0_b)
    return o_f + tflip(o_b), s_f, s_b

def gla_output(o, og, norm_g):
    b, h, n, dv = o.shape
    on = rms_norm(o, norm_g).transpose(0, 2, 1, 3).reshape(b, n, h * dv)
    return (on * jax.nn.silu(og.astype(jnp.float32))).astype(og.dtype)

def hyena_filters(n, P):
    f32 = jnp.float32
    t = jnp.arange(n, dtype=f32)
    t_norm = t / n
    bands = jnp.linspace(1e-4, HY_BANDS - 1, HY_BANDS, dtype=f32)
    phase = (2 * math.pi / n) * t[:, None] * bands[None, :]
    z = jnp.concatenate([t_norm[:, None], jnp.cos(phase), -jnp.sin(phase)], axis=-1)
    freq = P['hy_sin_freq'].astype(f32)
    hid = jnp.sin(freq * (z @ P['hy_pos_w1'].astype(f32) + P['hy_pos_b1'].astype(f32)))
    hid = jnp.sin(freq * (hid @ P['hy_pos_w2'].astype(f32) + P['hy_pos_b2'].astype(f32)))
    filt = (hid @ P['hy_pos_w3'].astype(f32)).reshape(n, HY_ORDER, 2, HY_WIDTH)
    filt = filt * jnp.exp(-t_norm[:, None, None, None] * jnp.abs(P['hy_decay'].astype(f32)))
    fwd, bwd = filt[:, :, 0], filt[:, :, 1]
    taps = jnp.concatenate([fwd, jnp.zeros_like(fwd[:1]), jnp.flip(bwd[1:], axis=0)], axis=0)
    taps = taps / (jnp.sum(jnp.abs(taps), axis=0, keepdims=True) + EPS)
    return jnp.fft.rfft(taps, axis=0)

def short_conv(u, w, b):
    up = jnp.pad(u, ((0, 0), (1, 1), (0, 0)))
    return up[:, :-2] * w[0] + up[:, 1:-1] * w[1] + up[:, 2:] * w[2] + b

def hyena_mix(u, P):
    n = u.shape[1]
    filt = hyena_filters(n, P)
    uc = short_conv(u, P['hy_conv_w'], P['hy_conv_b']).astype(jnp.float32)
    x1, x2, z = jnp.split(uc, 3, axis=-1)
    skip = P['hy_skip'].astype(jnp.float32)
    for o, gate in enumerate((x1, x2)):
        zf = jnp.fft.rfft(z, n=2 * n, axis=1)
        conv = jnp.fft.irfft(zf * filt[None, :, o], n=2 * n, axis=1)[:, :n]
        z = gate * (conv + skip[o] * z)
    return z.astype(u.dtype)

def merge_branches(y_hy, y_gla, y_att, br_g, P):
    g_hy, g_gla, g_att = jnp.split(br_g, N_BRANCH, axis=-1)
    m = (jax.nn.sigmoid(g_hy) * (y_hy @ P['w_br_hy'])
         + jax.nn.sigmoid(g_gla) * (y_gla @ P['w_br_gla'])
         + jax.nn.sigmoid(g_att) * (y_att @ P['w_br_att']))
    return m @ P['w_out']

def token_mixer(h, hc, P, last):
    f32 = jnp.float32
    b, s, _ = h.shape
    cos, sin = axial_rope_tables(s)
    proj = h @ P['w_in']
    a_k, a_v, g_k, g_v, g_a = split_cols(proj[..., :N_KV_COLS], KV_SPLITS)
    a_q, g_q, g_og, hy_u, br_g = split_cols(proj[..., N_KV_COLS:], REST_SPLITS)
    cproj = hc @ (P['w_in'][:, :N_KV_COLS] if last else P['w_in'])
    c_ak, c_av, c_gk, c_gv, c_ga = split_cols(cproj[..., :N_KV_COLS], KV_SPLITS)

    k_ctx = rms_norm(to_heads(c_ak, ATT_KV_HEADS), P['k_norm_g'])
    v_ctx = to_heads(c_av, ATT_KV_HEADS)
    k_lat = apply_rope(rms_norm(to_heads(a_k, ATT_KV_HEADS), P['k_norm_g']), cos, sin)
    q_lat = apply_rope(rms_norm(q_heads(a_q), P['q_norm_g']), cos, sin)
    keys = jnp.concatenate([k_lat, k_ctx], axis=2)
    vals = jnp.concatenate([to_heads(a_v, ATT_KV_HEADS), v_ctx], axis=2)
    y_att = gqa_latent(q_lat, keys, vals)

    c_k = to_heads(c_gk, GLA_HEADS).astype(f32)
    c_v = to_heads(c_gv, GLA_HEADS).astype(f32)
    c_la_f = gla_log_decay(c_ga[..., :GLA_RANK], P['gla_wa2'][0], P['gla_ba'][0])
    c_la_b = gla_log_decay(c_ga[..., GLA_RANK:], P['gla_wa2'][1], P['gla_ba'][1])
    if last:
        s_f = gla_final_state(c_k, c_v, c_la_f)
        s_b = gla_final_state(tflip(c_k), tflip(c_v), tflip(c_la_b))
    else:
        c_aq, c_gq, c_og, c_hy, c_brg = split_cols(cproj[..., N_KV_COLS:], REST_SPLITS)
        s0 = jnp.zeros((b, GLA_HEADS, GLA_DK, GLA_DV), f32)
        c_o, s_f, s_b = gla_bidir(gla_q(c_gq), c_k, c_v, c_la_f, c_la_b, s0, s0)
    la_f = gla_log_decay(g_a[..., :GLA_RANK], P['gla_wa2'][0], P['gla_ba'][0])
    la_b = gla_log_decay(g_a[..., GLA_RANK:], P['gla_wa2'][1], P['gla_ba'][1])
    o_lat, _, _ = gla_bidir(gla_q(g_q), to_heads(g_k, GLA_HEADS).astype(f32),
                            to_heads(g_v, GLA_HEADS).astype(f32), la_f, la_b, s_f, s_b)
    y_gla = gla_output(o_lat, g_og, P['gla_norm_g'])

    y_hy = hyena_mix(hy_u, P)

    out = merge_branches(y_hy, y_gla, y_att, br_g, P)
    if last:
        return out, None
    yc_att = gqa_context(rms_norm(q_heads(c_aq), P['q_norm_g']), k_ctx, v_ctx)
    yc_gla = gla_output(c_o, c_og, P['gla_norm_g'])
    yc_hy = hyena_mix(c_hy, P)
    return out, merge_branches(yc_hy, yc_gla, yc_att, c_brg, P)

def grouped_moe(h, router_w, router_b, w_gate, w_up, w_down):
    f32 = jnp.float32
    shape = h.shape
    ht = h.reshape(-1, shape[-1])
    scores = jax.nn.sigmoid((ht @ router_w).astype(f32))
    sel = scores + router_b.astype(f32)
    group_score = lax.top_k(sel.reshape(-1, N_GROUPS, EXPERTS_PER_GROUP), TOP_K)[0].sum(-1)
    group = jnp.argmax(group_score, axis=-1)
    in_group = (jnp.arange(N_EXPERTS) // EXPERTS_PER_GROUP)[None, :] == group[:, None]
    _, idx = lax.top_k(jnp.where(in_group, sel, -jnp.inf), TOP_K)
    w = jnp.take_along_axis(scores, idx, axis=-1)
    w = w / jnp.sum(w, axis=-1, keepdims=True)
    gates = jnp.sum(jax.nn.one_hot(idx, N_EXPERTS, dtype=f32) * w[..., None], axis=1).astype(h.dtype)
    out = jnp.zeros_like(ht)
    for e in range(N_EXPERTS):
        hid = jax.nn.silu(ht @ w_gate[e]) * (ht @ w_up[e])
        out = out + gates[:, e:e + 1] * (hid @ w_down[e])
    return out.reshape(shape)

def first_inputs(seed: int = 0) -> dict:
    key = jax.random.key(seed)
    keys = iter(jax.random.split(key, 48))

    def nrm(shape, scale):
        return jax.random.normal(next(keys), shape, jnp.float32) * scale

    D = D_MODEL
    decay_base = jnp.linspace(HY_DECAY_SLOW, HY_DECAY_FAST, HY_WIDTH, dtype=jnp.float32)
    return {
        'x': nrm((BATCH, SEQ, D), 1.0),
        'c': nrm((BATCH, D), 1.0),
        'ctx': nrm((BATCH, CTX_LEN, D), 1.0),
        'c_ctx': nrm((D,), 1.0),
        'w_mod': nrm((DEPTH, D, 6 * D), 0.5 * D ** -0.5),
        'b_mod': nrm((DEPTH, 6 * D), 0.02),
        'norm1_g': 1.0 + nrm((DEPTH, D), 0.05),
        'norm2_g': 1.0 + nrm((DEPTH, D), 0.05),
        'w_in': nrm((DEPTH, D, N_IN), D ** -0.5),
        'q_norm_g': 1.0 + nrm((DEPTH, HEAD_DIM), 0.05),
        'k_norm_g': 1.0 + nrm((DEPTH, HEAD_DIM), 0.05),
        'gla_wa2': nrm((DEPTH, 2, GLA_RANK, GLA_K_W), GLA_RANK ** -0.5),
        'gla_ba': nrm((DEPTH, 2, GLA_K_W), 0.02),
        'gla_norm_g': 1.0 + nrm((DEPTH, GLA_DV), 0.05),
        'hy_conv_w': nrm((DEPTH, 3, 3 * HY_WIDTH), 3 ** -0.5),
        'hy_conv_b': nrm((DEPTH, 3 * HY_WIDTH), 0.02),
        'hy_pos_w1': nrm((DEPTH, HY_EMB, HY_FFN), HY_EMB ** -0.5),
        'hy_pos_b1': nrm((DEPTH, HY_FFN), 0.02),
        'hy_sin_freq': 1.0 + nrm((DEPTH, HY_FFN), 0.05),
        'hy_pos_w2': nrm((DEPTH, HY_FFN, HY_FFN), HY_FFN ** -0.5),
        'hy_pos_b2': nrm((DEPTH, HY_FFN), 0.02),
        'hy_pos_w3': nrm((DEPTH, HY_FFN, HY_ORDER * 2 * HY_WIDTH), HY_FFN ** -0.5),
        'hy_decay': decay_base * (1.0 + nrm((DEPTH, HY_ORDER, 2, HY_WIDTH), 0.05)),
        'hy_skip': nrm((DEPTH, HY_ORDER, HY_WIDTH), 1.0),
        'w_br_hy': nrm((DEPTH, HY_WIDTH, D), HY_WIDTH ** -0.5),
        'w_br_gla': nrm((DEPTH, GLA_V_W, D), GLA_V_W ** -0.5),
        'w_br_att': nrm((DEPTH, ATT_Q_W, D), ATT_Q_W ** -0.5),
        'w_out': nrm((DEPTH, D, D), D ** -0.5),
        'router_w': nrm((D, N_EXPERTS), D ** -0.5),
        'router_b': nrm((N_EXPERTS,), 0.01),
        'moe_w_gate': nrm((DEPTH, N_EXPERTS, D, D_EXPERT), D ** -0.5),
        'moe_w_up': nrm((DEPTH, N_EXPERTS, D, D_EXPERT), D ** -0.5),
        'moe_w_down': nrm((DEPTH, N_EXPERTS, D_EXPERT, D), D_EXPERT ** -0.5),
    }

def first_block(x, c, ctx, c_ctx, w_mod, b_mod, norm1_g, norm2_g, w_in, q_norm_g, k_norm_g,
              gla_wa2, gla_ba, gla_norm_g, hy_conv_w, hy_conv_b, hy_pos_w1, hy_pos_b1,
              hy_sin_freq, hy_pos_w2, hy_pos_b2, hy_pos_w3, hy_decay, hy_skip,
              w_br_hy, w_br_gla, w_br_att, w_out, router_w, router_b,
              moe_w_gate, moe_w_up, moe_w_down):
    xc = ctx
    sc = jax.nn.silu(c)
    scc = jax.nn.silu(c_ctx)
    for l in range(DEPTH):
        last = l == DEPTH - 1
        P = {
            'w_in': w_in[l], 'q_norm_g': q_norm_g[l], 'k_norm_g': k_norm_g[l],
            'gla_wa2': gla_wa2[l], 'gla_ba': gla_ba[l], 'gla_norm_g': gla_norm_g[l],
            'hy_conv_w': hy_conv_w[l], 'hy_conv_b': hy_conv_b[l],
            'hy_pos_w1': hy_pos_w1[l], 'hy_pos_b1': hy_pos_b1[l], 'hy_sin_freq': hy_sin_freq[l],
            'hy_pos_w2': hy_pos_w2[l], 'hy_pos_b2': hy_pos_b2[l], 'hy_pos_w3': hy_pos_w3[l],
            'hy_decay': hy_decay[l], 'hy_skip': hy_skip[l],
            'w_br_hy': w_br_hy[l], 'w_br_gla': w_br_gla[l], 'w_br_att': w_br_att[l], 'w_out': w_out[l],
        }
        shift1, scale1, gate1, shift2, scale2, gate2 = jnp.split(sc @ w_mod[l] + b_mod[l], 6, axis=-1)
        n_cmod = 2 if last else 6
        cmods = jnp.split(scc @ w_mod[l][:, :n_cmod * D_MODEL] + b_mod[l][:n_cmod * D_MODEL], n_cmod, axis=-1)

        h = modulate(rms_norm(x, norm1_g[l]), shift1, scale1)
        hc = modulate(rms_norm(xc, norm1_g[l]), cmods[0], cmods[1])
        y, yc = token_mixer(h, hc, P, last)
        x = x + gate1[:, None, :] * y
        h = modulate(rms_norm(x, norm2_g[l]), shift2, scale2)
        x = x + gate2[:, None, :] * grouped_moe(h, router_w, router_b, moe_w_gate[l], moe_w_up[l], moe_w_down[l])
        if not last:
            xc = xc + cmods[2] * yc
            hc = modulate(rms_norm(xc, norm2_g[l]), cmods[3], cmods[4])
            xc = xc + cmods[5] * grouped_moe(hc, router_w, router_b, moe_w_gate[l], moe_w_up[l], moe_w_down[l])
    return x


N_MEM = 256
MEM_HEADS = 4
MEM_HEAD_DIM = 128
MEM_WIDTH = MEM_HEADS * MEM_HEAD_DIM
D_RNN = 3 * D_MODEL // 4
LRU_BLOCK = 64
N_LRU_BLOCKS = D_RNN // LRU_BLOCK
CONV_WIDTH = 4
LRU_C = 8.0
DIL_GROUPS = ((128, 1), (512, 4), (2048, 16))
N_DIL_GROUPS = len(DIL_GROUPS)
HEADS_PER_GROUP = 4
DIL_HEAD_DIM = 64
N_DIL_HEADS = N_DIL_GROUPS * HEADS_PER_GROUP
DIL_QKV_WIDTH = 3 * N_DIL_HEADS * DIL_HEAD_DIM
DIL_OUT_WIDTH = HEADS_PER_GROUP * DIL_HEAD_DIM
NUM_BUCKETS = 32
MAX_DISTANCE = 2048
N_BRANCHES = 3
D_FF = 4 * D_MODEL
NEG = -1e30

SPLITS = (D_RNN, 2 * D_RNN, 2 * D_RNN + DIL_QKV_WIDTH, 2 * D_RNN + DIL_QKV_WIDTH + MEM_WIDTH)
D_IN = 2 * D_RNN + DIL_QKV_WIDTH + MEM_WIDTH + N_BRANCHES * D_MODEL


def _rmsnorm(x, g):
    x32 = x.astype(jnp.float32)
    y = x32 * lax.rsqrt(jnp.mean(x32 * x32, axis=-1, keepdims=True) + EPS)
    return (y * g.astype(jnp.float32)).astype(x.dtype)

def _t5_bucket(dist):
    max_exact = NUM_BUCKETS // 2
    df = jnp.maximum(dist, 1).astype(jnp.float32)
    large = max_exact + (jnp.log(df / max_exact) / math.log(MAX_DISTANCE / max_exact)
                         * (NUM_BUCKETS - max_exact)).astype(jnp.int32)
    large = jnp.minimum(large, NUM_BUCKETS - 1)
    return jnp.where(dist < max_exact, dist, large)

def _rg_lru(xc, w_a, b_a, w_x, b_x, lam):
    B, S, C = xc.shape
    xb = xc.reshape(B, S, N_LRU_BLOCKS, LRU_BLOCK)
    r = jax.nn.sigmoid((jnp.einsum('bshi,hij->bshj', xb, w_a).reshape(B, S, C) + b_a).astype(jnp.float32))
    i = jax.nn.sigmoid((jnp.einsum('bshi,hij->bshj', xb, w_x).reshape(B, S, C) + b_x).astype(jnp.float32))
    log_a = -LRU_C * r * jax.nn.softplus(-lam.astype(jnp.float32))
    a = jnp.exp(log_a)
    mult = jnp.sqrt(-jnp.expm1(2.0 * log_a))
    b = mult * (i * xc.astype(jnp.float32))

    def combine(left, right):
        a1, b1 = left
        a2, b2 = right
        return a1 * a2, a2 * b1 + b2

    _, h = lax.associative_scan(combine, (a, b), axis=1)
    return h

def _dilated_group(q, k, v, table_g, dilation, span):
    B, S, H, Dh = q.shape
    L = S // dilation
    nb = -(-L // span)
    Lp = nb * span

    def to_blocks(t):
        t = t.reshape(B, L, dilation, H, Dh).transpose(0, 2, 3, 1, 4)
        t = jnp.pad(t, ((0, 0), (0, 0), (0, 0), (0, Lp - L), (0, 0)))
        return t.reshape(B, dilation, H, nb, span, Dh)

    def with_prev(t):
        prev = jnp.pad(t, ((0, 0), (0, 0), (0, 0), (1, 0), (0, 0), (0, 0)))[:, :, :, :-1]
        return jnp.concatenate([prev, t], axis=-2)

    qb = to_blocks(q)
    kk = with_prev(to_blocks(k))
    vv = with_prev(to_blocks(v))

    qi = jnp.arange(span)[:, None]
    kj = jnp.arange(2 * span)[None, :]
    off = qi + span - kj
    valid = (off >= 0) & (off <= span)
    mask = valid[None] & ((jnp.arange(nb)[:, None, None] > 0) | (kj >= span)[None])
    bucket = _t5_bucket(jnp.maximum(off, 0) * dilation)
    bias = jnp.transpose(table_g.astype(jnp.float32)[bucket], (2, 0, 1))

    s = jnp.einsum('brhnqc,brhnkc->brhnqk', qb, kk) * (DIL_HEAD_DIM ** -0.5) + bias[None, None, :, None]
    s = jnp.where(mask[None, None, None], s, NEG)
    m = jnp.max(s, axis=-1, keepdims=True)
    p = jnp.exp(s - m)
    den = jnp.sum(p, axis=-1)
    o = jnp.einsum('brhnqk,brhnkc->brhnqc', p, vv) / den[..., None]
    lse = m[..., 0] + jnp.log(den)

    o = o.reshape(B, dilation, H, Lp, Dh)[:, :, :, :L].transpose(0, 3, 1, 2, 4).reshape(B, S, H, Dh)
    lse = lse.reshape(B, dilation, H, Lp)[:, :, :, :L].transpose(0, 3, 1, 2).reshape(B, S, H)
    return o, lse

def second_inputs(seed: int = 0) -> dict:
    key = jax.random.key(seed)
    ks = jax.random.split(key, 24)
    f32 = jnp.float32

    def nrm(k, shape, fan_in):
        return jax.random.normal(k, shape, f32) * (fan_in ** -0.5)

    def gain(k, n):
        return 1.0 + 0.05 * jax.random.normal(k, (n,), f32)

    u = jax.random.uniform(ks[11], (D_RNN,), f32, 0.9, 0.999)
    sig = u ** (1.0 / LRU_C)
    lam = jnp.log(sig) - jnp.log1p(-sig)
    return {
        "x": jax.random.normal(ks[0], (BATCH, SEQ, D_MODEL), f32),
        "mem": jax.random.normal(ks[1], (BATCH, N_MEM, D_MODEL), f32),
        "g_mix": gain(ks[2], D_MODEL),
        "w_in": nrm(ks[3], (D_MODEL, D_IN), D_MODEL),
        "b_gate": 0.01 * jax.random.normal(ks[4], (N_BRANCHES * D_MODEL,), f32),
        "conv_w": nrm(ks[5], (CONV_WIDTH, D_RNN), CONV_WIDTH),
        "conv_b": 0.01 * jax.random.normal(ks[6], (D_RNN,), f32),
        "w_rg_a": nrm(ks[7], (N_LRU_BLOCKS, LRU_BLOCK, LRU_BLOCK), LRU_BLOCK),
        "b_rg_a": 0.01 * jax.random.normal(ks[8], (D_RNN,), f32),
        "w_rg_x": nrm(ks[9], (N_LRU_BLOCKS, LRU_BLOCK, LRU_BLOCK), LRU_BLOCK),
        "b_rg_x": 0.01 * jax.random.normal(ks[10], (D_RNN,), f32),
        "lru_lambda": lam,
        "w_lru_out": nrm(ks[12], (D_RNN, D_MODEL), D_RNN),
        "rel_bias": 0.1 * jax.random.normal(ks[13], (NUM_BUCKETS, N_DIL_HEADS), f32),
        "w_dil_out": nrm(ks[14], (DIL_OUT_WIDTH, D_MODEL), DIL_OUT_WIDTH),
        "g_mem": gain(ks[15], D_MODEL),
        "w_mem_kv": nrm(ks[16], (D_MODEL, 2 * MEM_WIDTH), D_MODEL),
        "w_mem_out": nrm(ks[17], (MEM_WIDTH, D_MODEL), MEM_WIDTH),
        "w_out": nrm(ks[18], (D_MODEL, D_MODEL), D_MODEL),
        "g_mlp": gain(ks[19], D_MODEL),
        "w_mlp_in": nrm(ks[20], (D_MODEL, D_FF), D_MODEL),
        "w_mlp_out": nrm(ks[21], (D_FF, D_MODEL), D_FF),
        "g_final": gain(ks[22], D_MODEL),
    }

def second_block(x, mem, g_mix, w_in, b_gate, conv_w, conv_b, w_rg_a, b_rg_a, w_rg_x, b_rg_x,
              lru_lambda, w_lru_out, rel_bias, w_dil_out, g_mem, w_mem_kv, w_mem_out, w_out,
              g_mlp, w_mlp_in, w_mlp_out, g_final):
    B, S, D = x.shape
    dt = x.dtype
    f32 = jnp.float32
    mem_n = _rmsnorm(mem, g_mem)

    for _ in range(DEPTH):
        h = _rmsnorm(x, g_mix)
        proj = h @ w_in
        x_lru, gate_lru, qkv, q_mem, gates = jnp.split(proj, SPLITS, axis=-1)

        xc = lax.conv_general_dilated(x_lru, conv_w[:, None, :].astype(x_lru.dtype), window_strides=(1,),
                                      padding=[(CONV_WIDTH - 1, 0)], dimension_numbers=('NWC', 'WIO', 'NWC'),
                                      feature_group_count=D_RNN) + conv_b
        hl = _rg_lru(xc, w_rg_a, b_rg_a, w_rg_x, b_rg_x, lru_lambda)
        y_lru = (jax.nn.gelu(gate_lru.astype(f32)) * hl).astype(dt) @ w_lru_out

        qkv = qkv.astype(f32).reshape(B, S, 3, N_DIL_GROUPS, HEADS_PER_GROUP, DIL_HEAD_DIM)
        outs, lses = [], []
        for g, (window, dil) in enumerate(DIL_GROUPS):
            o_g, lse_g = _dilated_group(qkv[:, :, 0, g], qkv[:, :, 1, g], qkv[:, :, 2, g],
                                        rel_bias[:, g * HEADS_PER_GROUP:(g + 1) * HEADS_PER_GROUP],
                                        dil, window // dil)
            outs.append(o_g)
            lses.append(lse_g)
        alpha = jax.nn.softmax(jnp.stack(lses, axis=0), axis=0)
        o_dil = jnp.sum(alpha[..., None] * jnp.stack(outs, axis=0), axis=0)
        y_dil = o_dil.reshape(B, S, DIL_OUT_WIDTH).astype(dt) @ w_dil_out

        kv = (mem_n @ w_mem_kv).astype(f32).reshape(B, N_MEM, 2, MEM_HEADS, MEM_HEAD_DIM)
        qm = q_mem.astype(f32).reshape(B, S, MEM_HEADS, MEM_HEAD_DIM)
        sm = jnp.einsum('bqhc,bkhc->bhqk', qm, kv[:, :, 0]) * (MEM_HEAD_DIM ** -0.5)
        pm = jax.nn.softmax(sm, axis=-1)
        om = jnp.einsum('bhqk,bkhc->bqhc', pm, kv[:, :, 1]).reshape(B, S, MEM_WIDTH)
        y_mem = om.astype(dt) @ w_mem_out

        gt = jax.nn.sigmoid((gates + b_gate).astype(f32)).reshape(B, S, N_BRANCHES, D)
        merged = (gt[:, :, 0] * y_lru.astype(f32) + gt[:, :, 1] * y_dil.astype(f32)
                  + gt[:, :, 2] * y_mem.astype(f32)).astype(dt)
        x = x + merged @ w_out

        hm = _rmsnorm(x, g_mlp)
        x = x + jnp.square(jax.nn.relu(hm @ w_mlp_in)) @ w_mlp_out

    return _rmsnorm(x, g_final)


def setup_inputs(seed=0):
    out = dict(first_inputs(seed))
    for name, value in second_inputs(seed + 1).items():
        if name != "x":
            out[name + "_2"] = value
    return out


def reference(
    x, c, ctx, c_ctx, w_mod, b_mod, norm1_g, norm2_g, w_in, q_norm_g, k_norm_g, gla_wa2, gla_ba,
    gla_norm_g, hy_conv_w, hy_conv_b, hy_pos_w1, hy_pos_b1, hy_sin_freq, hy_pos_w2, hy_pos_b2,
    hy_pos_w3, hy_decay, hy_skip, w_br_hy, w_br_gla, w_br_att, w_out, router_w, router_b,
    moe_w_gate, moe_w_up, moe_w_down, mem_2, g_mix_2, w_in_2, b_gate_2, conv_w_2, conv_b_2,
    w_rg_a_2, b_rg_a_2, w_rg_x_2, b_rg_x_2, lru_lambda_2, w_lru_out_2, rel_bias_2, w_dil_out_2,
    g_mem_2, w_mem_kv_2, w_mem_out_2, w_out_2, g_mlp_2, w_mlp_in_2, w_mlp_out_2, g_final_2,
):
    x = first_block(
        x, c, ctx, c_ctx, w_mod, b_mod, norm1_g, norm2_g, w_in, q_norm_g, k_norm_g, gla_wa2,
        gla_ba, gla_norm_g, hy_conv_w, hy_conv_b, hy_pos_w1, hy_pos_b1, hy_sin_freq, hy_pos_w2,
        hy_pos_b2, hy_pos_w3, hy_decay, hy_skip, w_br_hy, w_br_gla, w_br_att, w_out, router_w,
        router_b, moe_w_gate, moe_w_up, moe_w_down,
    )
    return second_block(
        x, mem_2, g_mix_2, w_in_2, b_gate_2, conv_w_2, conv_b_2, w_rg_a_2, b_rg_a_2, w_rg_x_2,
        b_rg_x_2, lru_lambda_2, w_lru_out_2, rel_bias_2, w_dil_out_2, g_mem_2, w_mem_kv_2,
        w_mem_out_2, w_out_2, g_mlp_2, w_mlp_in_2, w_mlp_out_2, g_final_2,
    )


_drawn_inputs = setup_inputs


def setup_inputs(seed=0):
    import zlib

    import numpy as np

    out = dict(_drawn_inputs(seed))
    spreads = {}
    factors = {'ctx': 2.738,
     'q_norm_g': 6.952,
     'k_norm_g': 6.95,
     'gla_ba': 8.0,
     'gla_norm_g': 3.5,
     'hy_conv_b': 3.591,
     'hy_pos_b1': 7.25,
     'hy_sin_freq': 6.853,
     'hy_pos_b2': 8.0,
     'hy_decay': 3.036,
     'g_mix_2': 3.203,
     'b_gate_2': 25.126,
     'conv_b_2': 3.497,
     'b_rg_a_2': 57.53,
     'b_rg_x_2': 54.757,
     'rel_bias_2': 8.0,
     'g_mem_2': 8.0,
     'g_mlp_2': 4.635}
    for name, (base, spread) in spreads.items():
        noise = np.random.default_rng([zlib.crc32(name.encode()), seed]).standard_normal(out[name].shape)
        drawn = base * np.exp(spread * noise) if base else spread * noise
        out[name] = jnp.asarray(drawn.astype(out[name].dtype))
    for name, factor in factors.items():
        out[name] = (out[name] * factor).astype(out[name].dtype)
    return out
```

```python
from contextlib import ExitStack

import numpy as np

import concourse.bass as bass
from concourse import mybir
from concourse.alu_op_type import AluOpType as ALU

F32 = mybir.dt.float32
ACT = mybir.ActivationFunctionType
AX = mybir.AxisListType

P = 128
D = 1024
KD = D // P
S = 512
NCTX = 256
ST = S // P
CT = NCTX // P
EPS = 1e-6
HALF = 512
RING = 6
NSIG = 20

VECS = [("c", 8), ("c_ctx", 8), ("b_mod", 48), ("norm1_g", 8), ("norm2_g", 8), ("q_norm_g", 1), ("k_norm_g", 1),
        ("gla_ba", 4), ("hy_conv_w", 36), ("hy_conv_b", 12),
        ("g_mix_2", 8), ("b_gate_2", 24), ("conv_w_2", 24), ("conv_b_2", 6), ("b_rg_a_2", 6), ("b_rg_x_2", 6),
        ("lru_lambda_2", 6), ("g_mem_2", 8), ("g_mlp_2", 8), ("g_final_2", 8)]
VEC_AT = {}
NVEC = 0
for _name, _n in VECS:
    VEC_AT[_name] = NVEC
    NVEC += _n

C_KV, C_GK, C_GV, C_GA = 0, 512, 768, 1280
C_Q, C_GQ, C_OG, C_HY, C_BR = 1312, 2336, 2592, 3104, 4640
C2_X, C2_G, C2_QKV, C2_QM, C2_BR = 0, 768, 1536, 3840, 4352
NEG = -1e30
NEXP = 16


class Ring:

    def __init__(self, nc, ctx):
        self.slots = [ctx.enter_context(nc.sbuf_tensor(f"weights{i}", [P, 4 * HALF], F32)) for i in range(RING)]
        self.arrived = [ctx.enter_context(nc.semaphore(f"arrived{i}")) for i in range(RING)]
        self.used = ctx.enter_context(nc.semaphore("used"))
        self.plan = []
        self.issued = 0

    def add(self, name, ap):
        self.plan.append((name, ap))

    def add_matrix(self, name, w, c0, c1):
        rows = w.shape[0]
        for a in range(c0, c1, HALF):
            b = min(a + HALF, c1)
            for r in range(0, rows, HALF):
                q = min(HALF, rows - r)
                self.add(name, w[r:r + q, a:b].rearrange("(t p) c -> p t c", p=P))

    def first(self, name):
        return [n for n, _ in self.plan].index(name)

    def view(self, n):
        _, ap = self.plan[n]
        t, c = ap.shape[1], ap.shape[2]
        return self.slots[n % RING][:, 0:t * c].rearrange("p (t c) -> p t c", c=c)

    def arrival(self, n):
        return 16 * (n // RING + 1)

    def issue_until(self, sp, n):
        for k in range(self.issued, min(n, len(self.plan))):
            if k >= RING:
                sp.wait_ge(self.used, k - RING + 1)
            sp.dma_start(self.view(k), self.plan[k][1]).then_inc(self.arrived[k % RING], 16)
        self.issued = max(self.issued, min(n, len(self.plan)))


class Core:

    def __init__(self, nc, ctx, T):
        self.nc, self.T = nc, T
        self.ring = Ring(nc, ctx)
        self.arena = ctx.enter_context(nc.sbuf_tensor("arena", [P, ARENA], F32))
        self.vecs = ctx.enter_context(nc.sbuf_tensor("vec_cols", [P, NVEC], F32))
        self.ident = ctx.enter_context(nc.sbuf_tensor("ident", [P, P], F32))
        self.ones = ctx.enter_context(nc.sbuf_tensor("ones", [P, P], F32))
        self.mods = ctx.enter_context(nc.sbuf_tensor("mods", [P, 96], F32))
        self.psum = [ctx.enter_context(nc.psum_tensor(f"bank{i}", [P, 512], F32)) for i in range(0)]
        self.ps = ctx.enter_context(nc.psum_tensor("ps", [P, 8, 512], F32))
        self.banks = [[ctx.enter_context(nc.semaphore(f"sig{b}_{i}")) for i in range(NSIG)] for b in range(2)]
        self.loaded = ctx.enter_context(nc.semaphore("loaded"))
        self.load_base = 0
        self.stage = 0

    def loads(self, k):
        return self.load_base + 16 * k

    def signals(self, n):
        self.stage += 1
        self.idle = self.banks[(self.stage + 1) % 2]
        return self.banks[self.stage % 2][:n]

    def start(self, eng):
        if self.stage > 1:
            lo = min(s.num for s in self.idle)
            eng.sem_clear(range(lo, lo + NSIG))

    def at(self, kb, *dims):
        n = int(np.prod(dims))
        o = int(kb * 256)
        assert o + n <= ARENA, (kb, dims)
        v = self.arena[:, o:o + n]
        if len(dims) == 2:
            v = v.rearrange("p (a b) -> p a b", b=dims[1])
        if len(dims) == 3:
            v = v.rearrange("p (a b c) -> p a b c", b=dims[1], c=dims[2])
        return v

    def vec(self, name, t=0):
        o = VEC_AT[name] + t
        return self.vecs[:, o:o + 1]


ARENA = 152 * 256


def accumulate(pe, out, pairs):
    for n, (l, r) in enumerate(pairs):
        last = pe.matmul(out, l, r, start=(n == 0), stop=(n == len(pairs) - 1))
    return last


def project(K, pe, n, col, m, x, tokens, out):
    for k in range(KD):
        w = K.ring.view(n + k // 4)
        ins = pe.matmul(out, w[:, k % 4, col:col + m], x[:, k, tokens], start=(k == 0), stop=(k == KD - 1))
    return ins


def arrived(K, pe, n, count=2):
    for k in range(n, n + count):
        pe.wait_ge(K.ring.arrived[k % RING], K.ring.arrival(k))


def release(K, pe, count=2):
    pe.matmul(K.ps[:, 7, 511:512], K.ones[:, :], K.ones[:, 0:1], start=True, stop=True).then_inc(K.ring.used, count)


def load_stage(K):
    T = K.T
    (loaded, made) = K.signals(2)
    with K.nc.Block() as block:
        @block.sync
        def _(sp):
            sp.dma_start(K.vecs[:, :], T["vecs"]).then_inc(loaded, 16)
            K.ring.issue_until(sp, RING)
            sp.dma_start(K.ident[:, :], T["k_ident"]).then_inc(loaded, 16)
            sp.dma_start(K.xT, T["xT"].rearrange("(t p) n -> p t n", p=P)).then_inc(loaded, 16)
            sp.dma_start(K.at(40, 8, NCTX), T["ctxT"].rearrange("(t p) n -> p t n", p=P)).then_inc(loaded, 16)
            sp.wait_ge(loaded, 64)

        @block.vector
        def _(dve):
            dve.memset(K.ones[:, :], 1.0).then_inc(made, 1)
            dve.wait_ge(made, 1)


def mod_stage(K):
    r, T = K.ring, K.T
    act_ready, cols_done, modded = K.signals(3)
    n0 = r.first("mod")
    sc = K.sc
    cols = K.ps[:, 0, 0:96]
    w = T["w_mod"].rearrange("(h t p) c -> h p t c", h=2, p=P)
    with K.nc.Block() as block:
        @block.sync
        def _(sp):
            K.start(sp)
            with sp.Fori(1, 4) as i:
                for s in range(RING):
                    sp.wait_ge(r.used, i * RING + (n0 + s + 1 - RING))
                    sp.dma_start(r.slots[s][:, :].rearrange("p (t c) -> p t c", c=HALF),
                                 w[s % 2][:, :, bass.ds(i * 3 * HALF + (s // 2) * HALF, HALF)])\
                        .then_inc(r.arrived[s], 16)
            r.issued = n0 + 24
            r.issue_until(sp, n0 + 24 + RING)

        @block.scalar
        def _(act):
            act.activation(sc[:, :, 0], K.vecs[:, VEC_AT["c"]:VEC_AT["c"] + 8], ACT.Silu).then_inc(act_ready, 1)
            act.activation(sc[:, :, 1], K.vecs[:, VEC_AT["c_ctx"]:VEC_AT["c_ctx"] + 8], ACT.Silu)\
                .then_inc(act_ready, 1)

        @block.tensor
        def _(pe):
            pe.wait_ge(act_ready, 2)
            with pe.Fori(0, 4) as i:
                for g in range(3):
                    for h in range(2):
                        pe.wait_ge(r.arrived[2 * g + h], i * 16 + 16)
                    for c in range(4):
                        out = K.ps[:, 0, bass.ds((i * 3 + g) * 8 + 2 * c, 2)]
                        for k in range(KD):
                            wk = r.slots[2 * g + k // 4][:, (k % 4) * HALF + c * P:(k % 4) * HALF + (c + 1) * P]
                            ins = pe.matmul(out, wk, sc[:, k, :], start=(k == 0), stop=(k == KD - 1))
                            if c == 3 and k in (3, KD - 1):
                                ins.then_inc(r.used, 1)

        @block.vector
        def _(dve):
            dve.wait_ge(r.used, n0 + 24)
            m = K.mods[:, :].rearrange("p (j b) -> p j b", b=2)
            pv = cols.rearrange("p (j b) -> p j b", b=2)
            bm = K.vecs[:, VEC_AT["b_mod"]:VEC_AT["b_mod"] + 48]
            for b in range(2):
                dve.tensor_tensor(m[:, :, b], pv[:, :, b], bm, ALU.add).then_inc(modded, 1)
            dve.wait_ge(modded, 2)
            g1 = K.vecs[:, VEC_AT["norm1_g"]:VEC_AT["norm1_g"] + 8]
            g2 = K.vecs[:, VEC_AT["norm2_g"]:VEC_AT["norm2_g"] + 8]
            dve.scalar_tensor_tensor(K.gain1, m[:, 8:16, 0], 1.0, g1, ALU.add, ALU.mult).then_inc(modded, 1)
            dve.scalar_tensor_tensor(K.gain1c, m[:, 8:16, 1], 1.0, g1, ALU.add, ALU.mult).then_inc(modded, 1)
            dve.scalar_tensor_tensor(K.gain2, m[:, 32:40, 0], 1.0, g2, ALU.add, ALU.mult).then_inc(modded, 1)
            dve.wait_ge(modded, 5)


def mod_col(K, part, t, b=0):
    o = 2 * (part * KD + t) + b
    return K.mods[:, o:o + 1]


def norm_stage(K, items, tmp):
    sq_done, sum_done, mean_done, rec_done, rstd_done, scaled, shifted, sq_used = K.signals(8)
    sq = K.at(tmp, 4, S)
    rec, rstd = K.at(tmp + 8, S), K.at(tmp + 10, S)
    with K.nc.Block() as block:
        @block.sync
        def _(sp):
            K.start(sp)

        @block.scalar
        def _(act):
            for j, (x, n, out, gain, shift) in enumerate(items):
                for t in range(KD):
                    a = j * KD + t
                    if a >= 4:
                        act.wait_ge(sq_used, a - 3)
                    act.activation(sq[:, a % 4, 0:n], x[:, t, :], ACT.Square).then_inc(sq_done, 1)
                act.wait_ge(rec_done, j + 1)
                act.activation(rstd[:, 0:n], rec[:, 0:n], ACT.Sqrt).then_inc(rstd_done, 1)
                if shift is not None:
                    for t in range(KD):
                        act.wait_ge(scaled, j * KD + t + 1)
                        act.activation(out[:, t, :], out[:, t, :], ACT.Identity, bias=shift(t)).then_inc(shifted, 1)
            if shift is not None:
                act.wait_ge(shifted, 1)

        @block.tensor
        def _(pe):
            for j, (x, n, out, gain, shift) in enumerate(items):
                if j >= 1:
                    pe.wait_ge(mean_done, j)
                for t in range(KD):
                    a = j * KD + t
                    pe.wait_ge(sq_done, a + 1)
                    pe.matmul(K.ps[:, 0, 0:n], K.ones[:, :], sq[:, a % 4, 0:n], start=(t == 0), stop=(t == KD - 1))\
                        .then_inc(sq_used, 1)

        @block.vector
        def _(dve):
            for j, (x, n, out, gain, shift) in enumerate(items):
                dve.wait_ge(sq_used, (j + 1) * KD)
                if j >= 1:
                    dve.wait_ge(scaled, j * KD)
                dve.tensor_scalar(rec[:, 0:n], K.ps[:, 0, 0:n], 1.0 / D, EPS, ALU.mult, ALU.add).then_inc(mean_done, 1)
                dve.wait_ge(mean_done, j + 1)
                dve.reciprocal(rec[:, 0:n], rec[:, 0:n]).then_inc(rec_done, 1)
                dve.wait_ge(rstd_done, j + 1)
                for t in range(KD):
                    dve.scalar_tensor_tensor(out[:, t, :], x[:, t, :], gain(t), rstd[:, 0:n], ALU.mult, ALU.mult)\
                        .then_inc(scaled, 1)
            dve.wait_ge(scaled, len(items) * KD)


def qk_stage(K):
    r, T = K.ring, K.T
    (raw_done, sq_done, ss_done, mean_done, rec_done, rstd_done, qn_done, swap_done, t1_done, t2_done, out_done,
     v_done, v_copied) = K.signals(13)
    sq, rec, rstd, qn, t1, t2 = (K.at(100 + 4 * i, 2, S) for i in range(6))
    cos, sin, swap = K.at(124, S), K.at(126, S), K.at(128, P)
    n0 = r.first("kv")
    items = []
    for h in range(2):
        items.append((n0, h * P, K.hT, S, "k_norm_g", True, K.kT[:, h, 0:S]))
        items.append((n0, h * P, K.hcT, NCTX, "k_norm_g", False, K.kT[:, h, S:S + NCTX]))
    for h in range(8):
        items.append((n0 + 2 + 2 * (h // 4), (h % 4) * P, K.hT, S, "q_norm_g", True, K.qT[:, h, :]))
    NI = len(items)
    rope_no = [sum(1 for it in items[:j] if it[5]) for j in range(NI + 1)]
    with K.nc.Block() as block:
        @block.gpsimd
        def _(pool):
            pool.dma_start(cos, T["k_cos"]).then_inc(K.loaded, 16)
            pool.dma_start(sin, T["k_sin"]).then_inc(K.loaded, 16)
            pool.dma_start(swap, T["k_swap"]).then_inc(K.loaded, 16)

        @block.sync
        def _(sp):
            K.start(sp)
            r.issue_until(sp, n0 + 6 + RING)

        @block.tensor
        def _(pe):
            def raw(j):
                n, col, x, ntok, *_ = items[j]
                if j == 0 or items[j - 1][0] != n:
                    arrived(K, pe, n)
                if j >= 3:
                    pe.wait_ge(qn_done, j - 2)
                project(K, pe, n, col, P, x, slice(0, ntok), K.ps[:, j % 3, 0:ntok]).then_inc(raw_done, 1)
                if n != n0 and col == 3 * P:
                    release(K, pe)

            def values():
                for t in range(ST + CT):
                    x, o = (K.hT, t * P) if t < ST else (K.hcT, (t - ST) * P)
                    if t >= 2:
                        pe.wait_ge(v_copied, t - 1)
                    accumulate(pe, K.ps[:, 5 + t % 2, 0:256],
                               [(x[:, k, o:o + P], r.view(n0 + k // 4)[:, k % 4, 256:512]) for k in range(KD)])\
                        .then_inc(v_done, 1)
                release(K, pe)

            def square_sum(j):
                ntok = items[j][3]
                pe.wait_ge(sq_done, j + 1)
                if j >= 1:
                    pe.wait_ge(mean_done, j)
                pe.matmul(K.ps[:, 3, 0:ntok], K.ones[:, :], sq[:, j % 2, 0:ntok], start=True, stop=True)\
                    .then_inc(ss_done, 1)

            def swapped(j):
                if items[j][5]:
                    pe.wait_ge(qn_done, j + 1)
                    if rope_no[j] >= 1:
                        pe.wait_ge(t2_done, rope_no[j])
                    else:
                        pe.wait_ge(K.loaded, K.loads(3))
                    pe.matmul(K.ps[:, 4, :], swap, qn[:, j % 2, :], start=True, stop=True).then_inc(swap_done, 1)

            for j in range(NI + 2):
                if j < NI:
                    raw(j)
                if j == 3:
                    values()
                if 1 <= j <= NI:
                    square_sum(j - 1)
                if j >= 2:
                    swapped(j - 2)

        @block.scalar
        def _(act):
            def copy_v(t):
                act.wait_ge(v_done, t + 1)
                act.activation(K.v[:, t, :], K.ps[:, 5 + t % 2, 0:256], ACT.Copy).then_inc(v_copied, 1)

            for j in range(NI + 1):
                if j < NI:
                    ntok = items[j][3]
                    act.wait_ge(raw_done, j + 1)
                    if j >= 2:
                        act.wait_ge(ss_done, j - 1)
                    act.activation(sq[:, j % 2, 0:ntok], K.ps[:, j % 3, 0:ntok], ACT.Square).then_inc(sq_done, 1)
                if j == 3:
                    for t in range(ST + CT):
                        copy_v(t)
                if j >= 1:
                    ntok = items[j - 1][3]
                    act.wait_ge(rec_done, j)
                    if j >= 3:
                        act.wait_ge(qn_done, j - 2)
                    act.activation(rstd[:, (j - 1) % 2, 0:ntok], rec[:, (j - 1) % 2, 0:ntok], ACT.Sqrt)\
                        .then_inc(rstd_done, 1)

        @block.vector
        def _(dve):
            def invert(j):
                ntok = items[j][3]
                m = rec[:, j % 2, 0:ntok]
                dve.wait_ge(ss_done, j + 1)
                if j >= 2:
                    dve.wait_ge(rstd_done, j - 1)
                dve.tensor_scalar(m, K.ps[:, 3, 0:ntok], 1.0 / P, EPS, ALU.mult, ALU.add).then_inc(mean_done, 1)
                dve.wait_ge(mean_done, j + 1)
                dve.reciprocal(m, m).then_inc(rec_done, 1)

            def finish(j):
                _, _, _, ntok, gain, rotary, dest = items[j]
                out = qn[:, j % 2, :] if rotary else dest
                dve.wait_ge(rstd_done, j + 1)
                if j >= 2:
                    dve.wait_ge(swap_done, rope_no[j - 1])
                dve.scalar_tensor_tensor(out, K.ps[:, j % 3, 0:ntok], K.vec(gain), rstd[:, j % 2, 0:ntok],
                                         ALU.mult, ALU.mult).then_inc(qn_done, 1)
                if rotary:
                    q = rope_no[j]
                    dve.wait_ge(qn_done, j + 1)
                    dve.wait_ge(K.loaded, K.loads(3))
                    dve.tensor_tensor(t1[:, q % 2, :], qn[:, j % 2, :], cos, ALU.mult).then_inc(t1_done, 1)
                    dve.wait_ge(swap_done, q + 1)
                    dve.tensor_tensor(t2[:, q % 2, :], K.ps[:, 4, :], sin, ALU.mult).then_inc(t2_done, 1)
                    dve.wait_ge(t1_done, q + 1)
                    dve.wait_ge(t2_done, q + 1)
                    dve.tensor_tensor(dest, t1[:, q % 2, :], t2[:, q % 2, :], ALU.add).then_inc(out_done, 1)

            for j in range(NI + 1):
                if j < NI:
                    invert(j)
                if j >= 1:
                    finish(j - 1)
            dve.wait_ge(out_done, rope_no[NI])
    K.load_base = K.loads(3)


def items_stage(K, items, banks=(0, 1, 2, 3), loads=(), issue=None):
    r = K.ring
    mm_done, act_out, dve_out = K.signals(3)
    count = {"act": 0, "dve": 0}
    emptied = []
    for it in items:
        count[it["eng"]] += 1
        emptied.append((act_out if it["eng"] == "act" else dve_out, count[it["eng"]]))
    last = {e: max([n for n, it in enumerate(items) if it["eng"] == e], default=None) for e in count}
    NB = len(banks)
    with K.nc.Block() as block:
        @block.gpsimd
        def _(pool):
            for dst, src in loads:
                pool.dma_start(dst, src).then_inc(K.loaded, 16)
            if loads:
                pool.wait_ge(K.loaded, K.loads(len(loads)))

        @block.sync
        def _(sp):
            K.start(sp)
            if issue is not None:
                r.issue_until(sp, issue + RING)

        @block.tensor
        def _(pe):
            if loads:
                pe.wait_ge(K.loaded, K.loads(len(loads)))
            for j, it in enumerate(items):
                for n in it.get("first", ()):
                    arrived(K, pe, n, 1)
                if it.get("after"):
                    for e in ("act", "dve"):
                        v = sum(1 for x in items[:it["after"]] if x["eng"] == e)
                        if v:
                            pe.wait_ge(act_out if e == "act" else dve_out, v)
                if j >= NB:
                    pe.wait_ge(*emptied[j - NB])
                it["mm"](pe, K.ps[:, banks[j % NB], :]).then_inc(mm_done, 1)
                if it.get("rel"):
                    release(K, pe, it["rel"])

        def emptier(e, eng, sem):
            if loads:
                eng.wait_ge(K.loaded, K.loads(len(loads)))
            for j, it in enumerate(items):
                if it["eng"] == e:
                    eng.wait_ge(mm_done, j + 1)
                    it["out"](eng, K.ps[:, banks[j % NB], :]).then_inc(sem, 1)

        @block.scalar
        def _(act):
            emptier("act", act, act_out)

        @block.vector
        def _(dve):
            emptier("dve", dve, dve_out)
    K.load_base = K.loads(len(loads))


def channel_item(K, n, col, m, x, ntok, dest, eng="act", func=ACT.Copy, first=(), rel=0, pairs=None, **kw):
    def mm(pe, bank):
        if pairs is not None:
            return accumulate(pe, bank[0:m, 0:ntok], pairs)
        return project(K, pe, n, col, m, x, slice(0, ntok), bank[0:m, 0:ntok])

    def out(e, bank):
        if eng == "act":
            return e.activation(dest, bank[0:m, 0:ntok], func, **kw)
        return e.tensor_copy(dest, bank[0:m, 0:ntok])
    return {"first": first, "mm": mm, "rel": rel, "eng": eng, "out": out}


def token_item(K, n, c0, c1, x, tok, dest, eng="act", func=ACT.Copy, first=(), rel=0, **kw):
    def mm(pe, bank):
        return accumulate(pe, bank[:, 0:c1 - c0],
                          [(x[:, k, tok], K.ring.view(n + k // 4)[:, k % 4, c0:c1]) for k in range(KD)])

    def out(e, bank):
        if eng == "act":
            return e.activation(dest, bank[:, 0:c1 - c0], func, **kw)
        return e.tensor_copy(dest, bank[:, 0:c1 - c0])
    return {"first": first, "mm": mm, "rel": rel, "eng": eng, "out": out}


def gla_project_stage(K):
    r = K.ring
    n = r.first("gk")
    items = []
    for t in range(2):
        items.append(channel_item(K, n, t * P, P, K.hT, S, K.gk[:, t, 0:S], first=(n, n + 1) if t == 0 else ()))
        items.append(channel_item(K, n, t * P, P, K.hcT, NCTX, K.gk[:, t, S:S + NCTX], eng="dve",
                                  rel=2 if t == 1 else 0))
    n += 2
    for t in range(6):
        x, o = (K.hT, t * P) if t < ST else (K.hcT, (t - ST) * P)
        items.append(token_item(K, n, 0, 512, x, slice(o, o + P), K.gv[:, t, :], eng=("act", "dve")[t % 2],
                                first=(n, n + 1) if t == 0 else (), rel=2 if t == 5 else 0))
    n += 2
    for d in range(2):
        items.append(channel_item(K, n, 16 * d, 16, K.hT, S, K.ga[0:16, d, 0:S], first=(n, n + 1) if d == 0 else ()))
        items.append(channel_item(K, n, 16 * d, 16, K.hcT, NCTX, K.ga[0:16, d, S:S + NCTX], eng="dve",
                                  rel=2 if d == 1 else 0))
    n += 2
    for t in range(2):
        items.append(channel_item(K, n, t * P, P, K.hT, S, K.gq[:, t, :], func=ACT.Copy, scale=0.125,
                                  first=(n, n + 1) if t == 0 else (), rel=2 if t == 1 else 0))
    n += 2
    for t in range(ST):
        items.append(token_item(K, n, 0, 512, K.hT, slice(t * P, t * P + P), K.og[:, t, :], func=ACT.Silu,
                                first=(n, n + 1) if t == 0 else (), rel=2 if t == 3 else 0))
    items_stage(K, items, issue=n + 2)


def gla_decay_stage(K):
    T = K.T
    L = S + NCTX
    chain, z_done, kend_done, turned, copied = K.signals(5)
    A, B, C = K.at(40, L), K.at(43, L), K.at(46, L)
    E, F = K.at(49, L), K.at(52, L)
    X = K.at(146, L)
    wa2, mask = K.at(149, 2, 256)[0:16], K.at(128, L)
    STEPS = 13
    kd = [0]

    with K.nc.Block() as block:
        @block.gpsimd
        def _(pool):
            pool.dma_start(wa2, T["gla_wa2"].rearrange("d r c -> r d c")).then_inc(K.loaded, 16)
            pool.dma_start(mask, T["k_scan"]).then_inc(K.loaded, 16)

        @block.sync
        def _(sp):
            K.start(sp)

        def z_of(u):
            return K.ps[:, 2 * (u % 2):2 * (u % 2) + 2, :].rearrange("p b n -> p (b n)")[:, 0:L]

        def turn(pe, u):
            pe.wait_ge(chain, (u + 1) * STEPS)
            if u >= 1:
                pe.wait_ge(copied, u)
            for t in range(6):
                ins = pe.transpose(K.ps[:, 4 + t // 4, (t % 4) * P:(t % 4 + 1) * P], X[:, t * P:(t + 1) * P],
                                   K.ident[:, :])
            ins.then_inc(turned, 1)

        @block.tensor
        def _(pe):
            pe.wait_ge(K.loaded, K.loads(2))
            for u in range(4):
                d, p = u // 2, u % 2
                w = wa2[:, d, p * P:(p + 1) * P]
                if u >= 2:
                    pe.wait_ge(chain, (u - 2) * STEPS + 4)
                pe.matmul(K.ps[:, 2 * (u % 2), :], w, K.ga[0:16, d, 0:S], start=True, stop=True)
                pe.matmul(K.ps[:, 2 * (u % 2) + 1, 0:NCTX], w, K.ga[0:16, d, S:L], start=True, stop=True)\
                    .then_inc(z_done, 1)
                if u >= 1:
                    turn(pe, u - 1)
            turn(pe, 3)

        @block.scalar
        def _(act):
            def step(u, j, out, in_, func, **kw):
                act.wait_ge(chain, u * STEPS + j)
                act.activation(out, in_, func, **kw).then_inc(chain, 1)

            for u in range(4):
                d, p = u // 2, u % 2
                act.wait_ge(z_done, u + 1)
                step(u, 0, A, z_of(u), ACT.Abs, bias=K.vec("gla_ba", u))
                step(u, 1, A, A, ACT.Exp, scale=-1.0)
                step(u, 2, A, A, ACT.Ln, bias=1.0)
                step(u, 7, A[:, 0:S], E[:, 0:S], ACT.Exp, scale=1 / 16)
                step(u, 8, B[:, 0:S], E[:, 0:S], ACT.Exp, scale=-1 / 16)
                step(u, 9, F, F, ACT.Exp, scale=1 / 16)
                act.wait_ge(turned, u + 1)
                for t in range(2):
                    n = 4 if t == 0 else 2
                    ins = act.activation(K.kend[:, 4 * t:4 * t + n, u, :],
                                         K.ps[:, 4 + t, 0:n * P].rearrange("p (t c) -> p t c", c=P), ACT.Copy)
                ins.then_inc(copied, 1)

        @block.vector
        def _(dve):
            def step(u, j, f):
                dve.wait_ge(chain, u * STEPS + j)
                f().then_inc(chain, 1)

            dve.wait_ge(K.loaded, K.loads(2))
            for u in range(4):
                d, p = u // 2, u % 2
                step(u, 3, lambda: dve.tensor_scalar(B, z_of(u), K.vec("gla_ba", u), 0.0, ALU.add, ALU.min))
                step(u, 4, lambda: dve.tensor_tensor(C, B, A, ALU.subtract))
                step(u, 5, lambda: dve.tensor_tensor_scan(E, mask, C, 0.0, ALU.mult, ALU.add))
                dve.wait_ge(chain, u * STEPS + 6)
                dve.tensor_copy(K.tot[:, u, 0:8], E[:, 0:S].rearrange("p (c t) -> p c t", t=64)[:, :, 63])\
                    .then_inc(kend_done, 1)
                dve.tensor_copy(K.tot[:, u, 8:9], E[:, L - 1:L]).then_inc(kend_done, 1)
                n = kd[0] = kd[0] + 2
                dve.wait_ge(kend_done, n)
                tl, tc = K.tot[:, u, 0:8].unsqueeze(2).broadcast_to([P, 8, 64]), K.tot[:, u, 8:9].broadcast_to([P, NCTX])
                if d == 1:
                    dve.tensor_tensor(E, C, E, ALU.subtract).then_inc(kend_done, 1)
                    dve.wait_ge(kend_done, n + 1)
                    dve.tensor_tensor(c64(E), c64(E), tl, ALU.add).then_inc(kend_done, 1)
                    dve.tensor_tensor(E[:, S:L], E[:, S:L], tc, ALU.add).then_inc(kend_done, 1)
                    dve.wait_ge(kend_done, n + 3)
                    kd[0] = n + 3
                dve.tensor_tensor(c64(F), tl, c64(E), ALU.subtract).then_inc(kend_done, 1)
                kd[0] += 1
                dve.wait_ge(kend_done, kd[0])
                step(u, 6, lambda: dve.tensor_tensor(F[:, S:L], tc, E[:, S:L], ALU.subtract))
                step(u, 10, lambda: dve.tensor_tensor(K.qdec[:, u, :], K.gq[:, p, :], A[:, 0:S], ALU.mult))
                step(u, 11, lambda: dve.tensor_tensor(K.kinv[:, u, :], K.gk[:, p, 0:S], B[:, 0:S], ALU.mult))
                if u >= 1:
                    dve.wait_ge(turned, u)
                step(u, 12, lambda: dve.tensor_tensor(X, K.gk[:, p, :], F, ALU.mult))

        @block.scalar
        def _(act):
            act.wait_ge(chain, 4 * STEPS)
            act.activation(K.tot[:, :, :], K.tot[:, :, :], ACT.Exp, scale=1 / 16).then_inc(copied, 1)
            act.wait_ge(copied, 5)
    K.load_base = K.loads(2)


def c64(v):
    return v[:, 0:S].rearrange("p (c t) -> p c t", t=64)


def gla_chunk_stage(K):
    T = K.T
    (cs_done, st_done, att_done, masked, o_done, sq_done, mean_done, rec_done, rstd_done, y_done, turned,
     copied, init_done) = K.signals(13)
    NC = S // 64
    masks = K.at(40, 2, P)
    gain = K.at(41, P)
    att = K.at(42, 2, 2, P)
    ysq = K.at(44, 2, P)
    o_sb = K.at(45, 2, 512)
    stats = K.at(49, 3, 16)
    states = K.states
    with K.nc.Block() as block:
        @block.gpsimd
        def _(pool):
            pool.dma_start(masks, T["k_causal"].rearrange("d s q -> s d q")).then_inc(K.loaded, 16)
            pool.dma_start(gain, T["gla_norm_g"].broadcast_to([P, P])).then_inc(K.loaded, 16)

        @block.sync
        def _(sp):
            K.start(sp)

        def order(d, c):
            return c if d == 0 else NC - 1 - c

        @block.tensor
        def _(pe):
            for u in range(4):
                d, p = u // 2, u % 2
                b = 3 * (u % 2)
                if u >= 2:
                    pe.wait_ge(st_done, (u - 1) * NC)
                for h in range(2):
                    rows = slice(64 * h, 64 * h + 64)
                    hv = slice((2 * p + h) * P, (2 * p + h + 1) * P)
                    accumulate(pe, K.ps[rows, b + 2, 0:P],
                               [(K.kend[:, 4 + t, u, rows], K.gv[:, 4 + t, hv]) for t in range(2)])
                    for c in range(NC):
                        toks = slice(64 * (c % 2), 64 * (c % 2) + 64)
                        ins = pe.matmul(K.ps[rows, b + c % 2, (c // 2) * P:(c // 2 + 1) * P],
                                        K.kend[toks, c // 2, u, rows], K.gv[toks, c // 2, hv], start=True, stop=True)
                ins.then_inc(cs_done, 1)

            def scores(a):
                t, h = a // 4, a % 4
                rows, toks = slice(64 * (h % 2), 64 * (h % 2) + 64), slice(t * P, (t + 1) * P)
                if a >= 2:
                    pe.wait_ge(masked, a - 1)
                else:
                    pe.wait_ge(st_done, 4 * NC)
                for d in range(2):
                    u = 2 * d + h // 2
                    ins = pe.matmul(K.ps[:, a % 2, d * P:(d + 1) * P], K.kinv[rows, u, toks], K.qdec[rows, u, toks],
                                    start=True, stop=True)
                ins.then_inc(att_done, 1)

            def outputs(a):
                t, h = a // 4, a % 4
                rows, toks = slice(64 * (h % 2), 64 * (h % 2) + 64), slice(t * P, (t + 1) * P)
                hv = slice(h * P, (h + 1) * P)
                pe.wait_ge(masked, a + 1)
                if a >= 2:
                    pe.wait_ge(y_done, a - 1)
                out = K.ps[:, 2 + a % 2, 0:P]
                for d in range(2):
                    pe.matmul(out, att[:, a % 2, d, :], K.gv[:, t, hv], start=(d == 0), stop=False)
                for d in range(2):
                    u = 2 * d + h // 2
                    for j in range(2):
                        c = 2 * t + j
                        before = c if d == 0 else NC - 1 - c
                        ins = pe.matmul(K.ps[64 * j:64 * j + 64, 2 + a % 2, 0:P], K.qdec[rows, u, 64 * c:64 * c + 64],
                                        states[rows, u, before, :], start=False, stop=(d == 1))
                ins.then_inc(o_done, 1)

            for a in range(17):
                if a < 16:
                    scores(a)
                if a >= 1:
                    outputs(a - 1)
            for a in range(16):
                t, h = a // 4, a % 4
                if h == 0:
                    pe.wait_ge(y_done, a + 4)
                    if t >= 2:
                        pe.wait_ge(copied, t - 1)
                ins = pe.transpose(K.ps[:, 4 + t % 2, h * P:(h + 1) * P], K.og[:, t, h * P:(h + 1) * P], K.ident[:, :])
                if h == 3:
                    ins.then_inc(turned, 1)

        @block.scalar
        def _(act):
            for a in range(16):
                act.wait_ge(o_done, a + 1)
                act.activation(ysq[:, a % 2, :], K.ps[:, 2 + a % 2, 0:P], ACT.Square, accum_out=stats[:, 0, a:a + 1])\
                    .then_inc(sq_done, 1)
                act.wait_ge(rec_done, a + 1)
                act.activation(stats[:, 2, a:a + 1], stats[:, 1, a:a + 1], ACT.Sqrt).then_inc(rstd_done, 1)
            for t in range(ST):
                act.wait_ge(turned, t + 1)
                act.activation(K.yglaT[:, :, t * P:(t + 1) * P],
                               K.ps[:, 4 + t % 2, :].rearrange("p (h c) -> p h c", c=P), ACT.Copy).then_inc(copied, 1)
            act.wait_ge(copied, ST)

        @block.vector
        def _(dve):
            for u in range(4):
                d = u // 2
                b = 3 * (u % 2)
                dve.wait_ge(cs_done, u + 1)
                dve.tensor_copy(states[:, u, 0, :], K.ps[:, b + 2, 0:P]).then_inc(init_done, 1)
                dve.wait_ge(init_done, u + 1)
                for s in range(NC):
                    c = order(d, s)
                    if s < NC - 1:
                        dve.scalar_tensor_tensor(states[:, u, s + 1, :], states[:, u, s, :], K.tot[:, u, c:c + 1],
                                                 K.ps[:, b + c % 2, (c // 2) * P:(c // 2 + 1) * P], ALU.mult, ALU.add)\
                            .then_inc(st_done, 1)
                        dve.wait_ge(st_done, u * NC + s + 1)
                    else:
                        dve.tensor_copy(stats[:, 0, 0:1], K.tot[:, u, 0:1]).then_inc(st_done, 1)
            dve.wait_ge(K.loaded, K.loads(2))

            def mask(a):
                dve.wait_ge(att_done, a + 1)
                if a >= 2:
                    dve.wait_ge(o_done, a - 1)
                dve.tensor_tensor(att[:, a % 2, :, :], K.ps[:, a % 2, 0:2 * P].rearrange("p (d q) -> p d q", q=P),
                                  masks, ALU.mult).then_inc(masked, 1)

            mask(0)
            for a in range(16):
                t, h = a // 4, a % 4
                if a + 1 < 16:
                    mask(a + 1)
                dve.wait_ge(sq_done, a + 1)
                dve.tensor_scalar(stats[:, 1, a:a + 1], stats[:, 0, a:a + 1], 1.0 / P, EPS, ALU.mult, ALU.add)\
                    .then_inc(mean_done, 1)
                dve.wait_ge(mean_done, 2 * a + 1)
                dve.reciprocal(stats[:, 1, a:a + 1], stats[:, 1, a:a + 1]).then_inc(rec_done, 1)
                dve.wait_ge(rstd_done, a + 1)
                o = o_sb[:, a % 2, 0:P]
                dve.scalar_tensor_tensor(o, K.ps[:, 2 + a % 2, 0:P], stats[:, 2, a:a + 1], gain, ALU.mult, ALU.mult)\
                    .then_inc(mean_done, 1)
                dve.wait_ge(mean_done, 2 * a + 2)
                og = K.og[:, t, h * P:(h + 1) * P]
                dve.tensor_tensor(og, o, og, ALU.mult).then_inc(y_done, 1)
    K.load_base = K.loads(2)


def attention_stage(K, heads, nk, scores, values, dest, scale, tmp):
    s_done, max_done, bias_done, exp_done, rec_done, normed, turned, copied, o_done, o_copied = K.signals(10)
    NB, NJ = heads * ST, nk // P
    Pb = K.at(tmp, 2, nk)
    PT = K.at(tmp + 2 * nk / 256, 2, NJ, S)
    st = K.at(tmp + 2 * nk / 256 + 2 * NJ * 2, 4, NB)
    with K.nc.Block() as block:
        @block.sync
        def _(sp):
            K.start(sp)

        def sbank(a):
            return K.ps[:, 2 * (a % 2):2 * (a % 2) + 2, :].rearrange("p b n -> p (b n)")[:, 0:nk]

        def tbank():
            return K.ps[:, 4:6, :].rearrange("p b n -> p (b n)")[:, 0:nk].rearrange("p (j q) -> p j q", q=P)

        @block.tensor
        def _(pe):
            for a in range(NB + 1):
                if a < NB:
                    if a >= 2:
                        pe.wait_ge(exp_done, a - 1)
                    for cols, l, r in scores(a // ST, a % ST):
                        ins = pe.matmul(sbank(a)[:, cols], l, r, start=True, stop=True)
                    ins.then_inc(s_done, 1)
                if a >= 1:
                    b = a - 1
                    pe.wait_ge(normed, b + 1)
                    if b >= 1:
                        pe.wait_ge(copied, b)
                    for j in range(NJ):
                        ins = pe.transpose(tbank()[:, j, :], Pb[:, b % 2, j * P:(j + 1) * P], K.ident[:, :])
                    ins.then_inc(turned, 1)
                    if b % ST == ST - 1:
                        h = b // ST
                        pe.wait_ge(copied, b + 1)
                        if h >= 1:
                            pe.wait_ge(o_copied, h)
                        accumulate(pe, K.ps[:, 6, :], [(values(h, j), PT[:, h % 2, j, :]) for j in range(NJ)])\
                            .then_inc(o_done, 1)

        @block.scalar
        def _(act):
            for a in range(NB + 1):
                if a < NB:
                    act.wait_ge(bias_done, a + 1)
                    if a >= 2:
                        act.wait_ge(turned, a - 1)
                    act.activation(Pb[:, a % 2, :], sbank(a), ACT.Exp, bias=st[:, 1, a:a + 1], scale=scale,
                                   accum_out=st[:, 2, a:a + 1]).then_inc(exp_done, 1)
                if a >= 1 and (a - 1) % ST == ST - 1:
                    h = (a - 1) // ST
                    act.wait_ge(o_done, h + 1)
                    act.activation(dest(h), K.ps[:, 6, :], ACT.Copy).then_inc(o_copied, 1)
            act.wait_ge(o_copied, heads)

        @block.vector
        def _(dve):
            def bias(a):
                dve.wait_ge(s_done, a + 1)
                dve.tensor_reduce(st[:, 0, a:a + 1], sbank(a), AX.X, ALU.max).then_inc(max_done, 1)
                dve.wait_ge(max_done, a + 1)
                dve.tensor_scalar(st[:, 1, a:a + 1], st[:, 0, a:a + 1], -scale, None, ALU.mult).then_inc(bias_done, 1)

            bias(0)
            for a in range(NB):
                if a + 1 < NB:
                    bias(a + 1)
                dve.wait_ge(exp_done, a + 1)
                dve.reciprocal(st[:, 3, a:a + 1], st[:, 2, a:a + 1]).then_inc(rec_done, 1)
                dve.wait_ge(rec_done, a + 1)
                dve.tensor_scalar(Pb[:, a % 2, :], Pb[:, a % 2, :], st[:, 3, a:a + 1], None, ALU.mult)\
                    .then_inc(normed, 1)
                dve.wait_ge(turned, a + 1)
                h = a // ST
                if h >= 2:
                    dve.wait_ge(o_done, h - 1)
                dve.tensor_copy(PT[:, h % 2, :, (a % ST) * P:(a % ST + 1) * P], tbank()).then_inc(copied, 1)


def latent_attention_stage(K):
    def scores(h, i):
        q = K.qT[:, h, i * P:(i + 1) * P]
        return [(slice(0, S), q, K.kT[:, h // 4, 0:S]), (slice(S, S + NCTX), q, K.kT[:, h // 4, S:S + NCTX])]

    attention_stage(K, 8, S + NCTX, scores, lambda h, j: K.v[:, j, (h // 4) * P:(h // 4 + 1) * P],
                    lambda h: K.yattT[:, h, :], P ** -0.5, 100)


TWO_PI = 2.0 * np.pi
ROUND = 1.5 * 2.0 ** 23
PI_HI = 6.28125
PI_LO = TWO_PI - PI_HI
SIN_MAX = 3.1415925


def hyena_project_stage(K):
    r = K.ring
    mm_done, mid_done, left_done, conv_done, turned, copied = K.signals(6)
    n0 = r.first("hy")
    NT = 12
    ys = K.at(96, 4, S)
    turn_no = [t if t < 4 else t - 4 for t in range(NT)]

    def y_of(t):
        return K.x2T[:, t - 4, :] if 4 <= t < 8 else ys[:, turn_no[t] % 4, :]

    with K.nc.Block() as block:
        @block.sync
        def _(sp):
            K.start(sp)
            r.issue_until(sp, n0 + 6 + RING)

        @block.tensor
        def _(pe):
            def turn(t):
                if 4 <= t < 8:
                    return
                q = turn_no[t]
                pe.wait_ge(conv_done, t + 1)
                if q >= 2:
                    pe.wait_ge(copied, q - 1)
                for tt in range(ST):
                    ins = pe.transpose(K.ps[:, 4 + q % 2, tt * P:(tt + 1) * P], y_of(t)[:, tt * P:(tt + 1) * P],
                                       K.ident[:, :])
                ins.then_inc(turned, 1)

            for t in range(NT):
                n = n0 + 2 * (t // 4)
                if t % 4 == 0:
                    arrived(K, pe, n)
                if t >= 4:
                    pe.wait_ge(conv_done, t - 3)
                project(K, pe, n, (t % 4) * P, P, K.hT, slice(0, S), K.ps[:, t % 4, :]).then_inc(mm_done, 1)
                if t % 4 == 3:
                    release(K, pe)
                if t >= 2:
                    turn(t - 2)
            turn(NT - 2)
            turn(NT - 1)

        @block.scalar
        def _(act):
            def copy(t):
                if 4 <= t < 8:
                    return
                q = turn_no[t]
                dest = K.x1 if t < 4 else K.z
                act.wait_ge(turned, q + 1)
                act.activation(dest[:, :, (t % 4) * P:(t % 4 + 1) * P],
                               K.ps[:, 4 + q % 2, :].rearrange("p (t c) -> p t c", c=P), ACT.Copy).then_inc(copied, 1)

            for t in range(NT):
                act.wait_ge(mm_done, t + 1)
                q = turn_no[t]
                if not 4 <= t < 8 and q >= 4:
                    act.wait_ge(turned, q - 3)
                act.activation(y_of(t), K.ps[:, t % 4, :], ACT.Identity, bias=K.vec("hy_conv_b", t),
                               scale=K.vec("hy_conv_w", NT + t)).then_inc(mid_done, 1)
                if t >= 3:
                    copy(t - 3)
            for t in range(NT - 3, NT):
                copy(t)
            act.wait_ge(copied, 8)

        @block.vector
        def _(dve):
            for t in range(NT):
                y, u = y_of(t), K.ps[:, t % 4, :]
                dve.wait_ge(mid_done, t + 1)
                dve.scalar_tensor_tensor(y[:, 1:S], u[:, 0:S - 1], K.vec("hy_conv_w", t), y[:, 1:S], ALU.mult, ALU.add)\
                    .then_inc(left_done, 1)
                dve.wait_ge(left_done, t + 1)
                dve.scalar_tensor_tensor(y[:, 0:S - 1], u[:, 1:S], K.vec("hy_conv_w", 2 * NT + t), y[:, 0:S - 1],
                                         ALU.mult, ALU.add).then_inc(conv_done, 1)


def hyena_hidden_stage(K):
    T = K.T
    mm_done, chain, sin_done = K.signals(3)
    F = 64
    pos, w1, w2, cols = K.at(96, S)[0:33], K.at(98, F)[0:33], K.at(98.25, F)[0:F], K.at(98.5, 3)[0:F]
    a, b, c, h1 = (K.at(100 + 2 * i, S)[0:F] for i in range(4))
    with K.nc.Block() as block:
        @block.gpsimd
        def _(pool):
            for dst, src in ((pos, T["k_pos"]), (w1, T["hy_pos_w1"]), (w2, T["hy_pos_w2"]), (cols, T["hy_cols"])):
                pool.dma_start(dst, src).then_inc(K.loaded, 16)

        @block.sync
        def _(sp):
            K.start(sp)

        @block.tensor
        def _(pe):
            pe.wait_ge(K.loaded, K.loads(4))
            pe.matmul(K.ps[0:F, 0, :], w1, pos, start=True, stop=True).then_inc(mm_done, 1)
            pe.wait_ge(sin_done, 1)
            pe.matmul(K.ps[0:F, 1, :], w2, h1, start=True, stop=True).then_inc(mm_done, 1)

        @block.vector
        def _(dve):
            dve.wait_ge(K.loaded, K.loads(4))
            for layer in range(2):
                n = 6 * layer
                dve.wait_ge(mm_done, layer + 1)
                if layer:
                    dve.wait_ge(sin_done, 1)
                dve.tensor_scalar(a, K.ps[0:F, layer, :], cols[:, layer:layer + 1], cols[:, 2:3], ALU.add, ALU.mult)\
                    .then_inc(chain, 1)
                dve.wait_ge(chain, n + 1)
                dve.tensor_scalar(b, a, 1.0 / TWO_PI, ROUND, ALU.mult, ALU.add).then_inc(chain, 1)
                dve.wait_ge(chain, n + 2)
                dve.tensor_scalar(b, b, ROUND, None, ALU.subtract).then_inc(chain, 1)
                dve.wait_ge(chain, n + 3)
                dve.scalar_tensor_tensor(c, b, -PI_HI, a, ALU.mult, ALU.add).then_inc(chain, 1)
                dve.wait_ge(chain, n + 4)
                dve.scalar_tensor_tensor(c, b, -PI_LO, c, ALU.mult, ALU.add).then_inc(chain, 1)
                dve.wait_ge(chain, n + 5)
                dve.tensor_scalar(c, c, SIN_MAX, -SIN_MAX, ALU.min, ALU.max).then_inc(chain, 1)

        @block.scalar
        def _(act):
            for layer, out in enumerate((h1, K.hid)):
                act.wait_ge(chain, 6 * layer + 6)
                act.activation(out, c, ACT.Sin).then_inc(sin_done, 1)
            act.wait_ge(sin_done, 2)
    K.load_base = K.loads(4)


def hyena_filter_stage(K, o):
    r, T = K.ring, K.T
    (dec_done, filt_done, win_done, g_done, abs_done, sum_done, chain, ft_done, ft_out, abs_dec) = K.signals(10)
    n0 = r.first(f"dft{o}")
    nC, nS, nE = n0, n0 + 1, n0 + 2
    g = K.at(96, 8, S)
    total = K.at(112, 4, S)
    absb, win, dec, inv = K.at(112, 2, S), K.at(124, 2, S), K.at(120, 2, S), K.at(144, S)
    w3, row, skip, cols = K.at(148, 1024)[0:64], K.at(72 + 64, 1024)[0:1], K.at(140, S)[0:1], K.at(142, 5)
    with K.nc.Block() as block:
        @block.gpsimd
        def _(pool):
            for dst, src in ((w3, T["hy_pos_w3"][:, o * 1024:(o + 1) * 1024]),
                             (row, T["hy_decay"][:, o * 1024:(o + 1) * 1024]),
                             (skip, T["hy_skip"][:, o * S:(o + 1) * S]), (cols, T["k_time"])):
                pool.dma_start(dst, src).then_inc(K.loaded, 16)

        @block.sync
        def _(sp):
            K.start(sp)

        @block.tensor
        def _(pe):
            pe.wait_ge(K.loaded, K.loads(4))
            for d in range(2):
                pe.matmul(K.ps[:, 5 + d, :], K.ones[0:1, :], row[:, d * S:(d + 1) * S], start=True, stop=True)\
                    .then_inc(dec_done, 1)
            for e in range(9):
                if e < 8:
                    if e >= 2:
                        pe.wait_ge(g_done, e - 1)
                    pe.matmul(K.ps[:, e % 2, :], K.hid[:, (e % 4) * P:(e % 4 + 1) * P],
                              w3[:, (e // 4) * S:(e // 4 + 1) * S], start=True, stop=True).then_inc(filt_done, 1)
                if e >= 1:
                    pe.wait_ge(abs_done, e)
                    pe.matmul(K.ps[:, 2, :], K.ones[:, :], absb[:, (e - 1) % 2, :], start=(e == 1), stop=(e == 8))\
                        .then_inc(sum_done, 1)
            pe.wait_ge(chain, 19)
            arrived(K, pe, n0, 3)
            C, Sm, Ed = r.view(nC), r.view(nS), r.view(nE)
            for j in range(9):
                m = j % 4
                if j >= 2:
                    pe.wait_ge(ft_out, j - 1)
                if j < 4:
                    pairs = [(C[:, t, m * P:(m + 1) * P], total[:, t, :]) for t in range(4)]
                elif j < 8:
                    pairs = [((Ed[:, t, P:2 * P] if m == 0 else Sm[:, t, m * P:(m + 1) * P]), g[:, t, :])
                             for t in range(4)]
                else:
                    pairs = [(Ed[:, t, 0:P], total[:, t, :]) for t in range(4)]
                accumulate(pe, K.ps[:, 3 + j % 2, :], pairs).then_inc(ft_done, 1)

        @block.scalar
        def _(act):
            for d in range(2):
                act.wait_ge(dec_done, d + 1)
                act.activation(dec[:, d, :], K.ps[:, 5 + d, :], ACT.Abs).then_inc(abs_dec, 1)
            act.wait_ge(K.loaded, K.loads(4))
            for e in range(9):
                if e < 8:
                    act.wait_ge(abs_dec, e // 4 + 1)
                    if e >= 2:
                        act.wait_ge(g_done, e - 1)
                    act.activation(win[:, e % 2, :], dec[:, e // 4, :], ACT.Exp, scale=cols[:, e % 4:e % 4 + 1])\
                        .then_inc(win_done, 1)
                if e >= 1:
                    act.wait_ge(g_done, e)
                    if e >= 3:
                        act.wait_ge(sum_done, e - 2)
                    act.activation(absb[:, (e - 1) % 2, :], g[:, e - 1, :], ACT.Abs).then_inc(abs_done, 1)
            for j in range(9):
                dest = K.Rf[:, j, :] if j < 4 else K.If[:, j - 4, :] if j < 8 else K.edge
                act.wait_ge(ft_done, j + 1)
                act.activation(dest, K.ps[:, 3 + j % 2, :], ACT.Copy).then_inc(ft_out, 1)
            act.wait_ge(ft_out, 9)

        @block.vector
        def _(dve):
            dve.wait_ge(K.loaded, K.loads(4))
            for e in range(8):
                dve.wait_ge(filt_done, e + 1)
                dve.wait_ge(win_done, e + 1)
                if e == 4:
                    dve.scalar_tensor_tensor(g[:, e, :], K.ps[:, e % 2, :], cols[:, 4:5], win[:, e % 2, :],
                                             ALU.mult, ALU.mult).then_inc(g_done, 1)
                else:
                    dve.tensor_tensor(g[:, e, :], K.ps[:, e % 2, :], win[:, e % 2, :], ALU.mult).then_inc(g_done, 1)
            dve.wait_ge(sum_done, 8)
            dve.tensor_scalar(inv, K.ps[:, 2, :], EPS, None, ALU.add).then_inc(chain, 1)
            dve.wait_ge(chain, 1)
            dve.reciprocal(inv, inv).then_inc(chain, 1)
            dve.wait_ge(chain, 2)
            for e in range(8):
                dve.tensor_tensor(g[:, e, :], g[:, e, :], inv, ALU.mult).then_inc(chain, 1)
            dve.wait_ge(chain, 10)
            dve.tensor_tensor(g[0:1, 0, :], g[0:1, 0, :], skip, ALU.add).then_inc(chain, 1)
            dve.wait_ge(chain, 11)
            for t in range(4):
                dve.tensor_tensor(total[:, t, :], g[:, t, :], g[:, 4 + t, :], ALU.add).then_inc(chain, 1)
                dve.wait_ge(chain, 12 + 2 * t)
                dve.tensor_tensor(g[:, t, :], g[:, t, :], g[:, 4 + t, :], ALU.subtract).then_inc(chain, 1)
    K.load_base = K.loads(4)


def hyena_conv_stage(K, o):
    r = K.ring
    ft_done, p1, p2, p3, p4, prod, inv_done, out_done = K.signals(8)
    n0 = r.first(f"dft{o}")
    nC, nS, nCi, nSi = n0, n0 + 1, n0 + 3, n0 + 4
    Pre, Pim = K.at(96, 4, S), K.at(104, 4, S)
    tmp = K.at(112, 4, S)
    with K.nc.Block() as block:
        @block.sync
        def _(sp):
            K.start(sp)
            r.issue_until(sp, n0 + 5 + RING)

        @block.tensor
        def _(pe):
            C, Sm = r.view(nC), r.view(nS)
            for m in range(4):
                if m >= 2:
                    pe.wait_ge(p4, m - 1)
                b = 2 * (m % 2)
                accumulate(pe, K.ps[:, b, :], [(C[:, t, m * P:(m + 1) * P], K.z[:, t, :]) for t in range(4)])
                accumulate(pe, K.ps[:, b + 1, :], [(Sm[:, t, m * P:(m + 1) * P], K.z[:, t, :]) for t in range(4)])\
                    .then_inc(ft_done, 1)
            release(K, pe, 3)
            arrived(K, pe, nCi)
            Ci, Si = r.view(nCi), r.view(nSi)
            pe.wait_ge(prod, 8)
            for m in range(4):
                if m >= 2:
                    pe.wait_ge(out_done, m - 1)
                if o == 0:
                    pairs = [(w[:, k, m * P:(m + 1) * P], x[:, k, :]) for w, x in ((Ci, Pre), (Si, Pim))
                             for k in range(4)]
                else:
                    pairs = [(x[:, k, m * P:(m + 1) * P], w[:, k, :]) for w, x in ((Ci, Pre), (Si, Pim))
                             for k in range(4)]
                accumulate(pe, K.ps[:, 4 + m % 2, :], pairs).then_inc(inv_done, 1)
            release(K, pe, 2)

        @block.vector
        def _(dve):
            for m in range(4):
                zr, zi = K.ps[:, 2 * (m % 2), :], K.ps[:, 2 * (m % 2) + 1, :]
                dve.wait_ge(ft_done, m + 1)
                if m >= 1:
                    dve.wait_ge(prod, 2 * m)
                dve.tensor_tensor(tmp[:, 0, :], zr, K.Rf[:, m, :], ALU.mult).then_inc(p1, 1)
                dve.tensor_tensor(tmp[:, 1, :], zi, K.If[:, m, :], ALU.mult).then_inc(p2, 1)
                dve.tensor_tensor(tmp[:, 2, :], zr, K.If[:, m, :], ALU.mult).then_inc(p3, 1)
                dve.tensor_tensor(tmp[:, 3, :], zi, K.edge if m == 0 else K.Rf[:, m, :], ALU.mult).then_inc(p4, 1)
                dve.wait_ge(p1, m + 1)
                dve.wait_ge(p2, m + 1)
                dve.tensor_tensor(Pre[:, m, :], tmp[:, 0, :], tmp[:, 1, :], ALU.subtract).then_inc(prod, 1)
                dve.wait_ge(p3, m + 1)
                dve.wait_ge(p4, m + 1)
                dve.tensor_tensor(Pim[:, m, :], tmp[:, 2, :], tmp[:, 3, :], ALU.add).then_inc(prod, 1)
            for m in range(4):
                gate, dest = (K.x1, K.z) if o == 0 else (K.x2T, K.yhyT)
                dve.wait_ge(inv_done, m + 1)
                dve.tensor_tensor(dest[:, m, :], K.ps[:, 4 + m % 2, :], gate[:, m, :], ALU.mult).then_inc(out_done, 1)
            dve.wait_ge(out_done, 4)


def merge_stage(K, name, x, branches, mT, bias=None, tmp=96):
    r = K.ring
    gate_done, y_done, sig_done, prod_done, sum_done = K.signals(5)
    n0 = r.first(name)
    sizes = [2 + -(-kt // 4) for _, kt in branches]
    sig, tm = K.at(tmp, 2, S), K.at(tmp + 4, 2, S)
    items = []
    n = n0
    for half in range(2):
        for b in range(3):
            for c in range(4):
                items.append((half, b, c, n))
            n += sizes[b]
    with K.nc.Block() as block:
        @block.sync
        def _(sp):
            K.start(sp)
            r.issue_until(sp, n + RING)

        @block.tensor
        def _(pe):
            for i, (half, b, c, n) in enumerate(items):
                y, kt = branches[b]
                if c == 0:
                    arrived(K, pe, n, sizes[b])
                if i >= 2:
                    pe.wait_ge(sig_done, i - 1)
                project(K, pe, n, c * P, P, x, slice(0, S), K.ps[:, i % 2, :]).then_inc(gate_done, 1)
                if i >= 2:
                    pe.wait_ge(prod_done, i - 1)
                accumulate(pe, K.ps[:, 2 + i % 2, :],
                           [(r.view(n + 2 + k // 4)[:, k % 4, c * P:(c + 1) * P], y[:, k, :]) for k in range(kt)])\
                    .then_inc(y_done, 1)
                if c == 3:
                    release(K, pe, sizes[b])

        @block.scalar
        def _(act):
            for i, (half, b, c, n) in enumerate(items):
                act.wait_ge(gate_done, i + 1)
                if i >= 2:
                    act.wait_ge(prod_done, i - 1)
                kw = {} if bias is None else {"bias": K.vec(bias, b * KD + half * 4 + c)}
                act.activation(sig[:, i % 2, :], K.ps[:, i % 2, :], ACT.Sigmoid, **kw).then_inc(sig_done, 1)

        @block.vector
        def _(dve):
            sums = 0
            for i, (half, b, c, n) in enumerate(items):
                m = mT[:, half * 4 + c, :]
                dve.wait_ge(sig_done, i + 1)
                dve.wait_ge(y_done, i + 1)
                if b and i >= 6:
                    dve.wait_ge(sum_done, sums - 1)
                dve.tensor_tensor(tm[:, i % 2, :] if b else m, K.ps[:, 2 + i % 2, :], sig[:, i % 2, :], ALU.mult)\
                    .then_inc(prod_done, 1)
                if b:
                    dve.wait_ge(prod_done, i + 1)
                    if b == 2:
                        dve.wait_ge(sum_done, sums - 3)
                    dve.tensor_tensor(m, m, tm[:, i % 2, :], ALU.add).then_inc(sum_done, 1)
                    sums += 1
            dve.wait_ge(sum_done, sums)


def residual_stage(K, name, mT, gate):
    n = K.ring.first(name)
    items = []
    for t in range(KD):
        nn = n + 2 * (t // 4)

        def out(e, bank, t=t):
            x = K.xT[:, t, :]
            if gate is None:
                return e.tensor_tensor(x, bank, x, ALU.add)
            return e.scalar_tensor_tensor(x, bank, gate(t), x, ALU.mult, ALU.add)
        items.append({"first": (nn, nn + 1) if t % 4 == 0 else (), "rel": 2 if t % 4 == 3 else 0, "eng": "dve",
                      "mm": lambda pe, bank, t=t, nn=nn: project(K, pe, nn, (t % 4) * P, P, mT, slice(0, S), bank),
                      "out": out})
    items_stage(K, items, issue=n + 4)


def router_stage(K):
    T = K.T
    s_done, sig_done, chain, turned, copied, stored = K.signals(6)
    rw, rb = K.at(96, KD, NEXP), K.at(97, NEXP)
    sc, sel, gates = K.at(98, 64), K.at(98.25, 64), K.at(98.5, 64)
    hi, lo, top, gs = (K.at(99 + 0.25 * i, 4 * 4 * 2) for i in range(4))
    rank, lose, gt, tmp = K.at(100, 64), K.at(100.25, 16), K.at(100.5, 16), K.at(100.75, 64)
    gT = K.at(102, S)[0:NEXP]

    def e4(v):
        return v.rearrange("p (g e) -> p g e", e=4)

    with K.nc.Block() as block:
        @block.gpsimd
        def _(pool):
            pool.dma_start(rw, T["router_w"].rearrange("(t p) e -> p t e", p=P)).then_inc(K.loaded, 16)
            pool.dma_start(rb, T["router_b"].broadcast_to([P, NEXP])).then_inc(K.loaded, 16)

        @block.sync
        def _(sp):
            K.start(sp)
            sp.wait_ge(copied, 1)
            sp.dma_start(K.gate_rows, gT).then_inc(stored, 16)
            sp.wait_ge(stored, 16)

        @block.tensor
        def _(pe):
            pe.wait_ge(K.loaded, K.loads(2))
            for t in range(ST):
                ins = accumulate(pe, K.ps[:, 0, t * NEXP:(t + 1) * NEXP],
                                 [(K.hT[:, k, t * P:(t + 1) * P], rw[:, k, :]) for k in range(KD)])
            ins.then_inc(s_done, 1)
            pe.wait_ge(turned, 1)
            for t in range(ST):
                ins = pe.transpose(K.ps[0:NEXP, 1, t * P:(t + 1) * P], gates[:, t * NEXP:(t + 1) * NEXP], K.ident[:, :])
            ins.then_inc(s_done, 1)

        @block.scalar
        def _(act):
            act.wait_ge(s_done, 1)
            act.activation(sc, K.ps[:, 0, 0:64], ACT.Sigmoid).then_inc(sig_done, 1)
            act.wait_ge(s_done, 2)
            act.activation(gT, K.ps[0:NEXP, 1, :], ACT.Copy).then_inc(copied, 1)

        @block.vector
        def _(dve):
            n = [0]

            def then(ins):
                n[0] += 1
                ins.then_inc(chain, 1)
                dve.wait_ge(chain, n[0])

            def tt(out, a, b, op):
                then(dve.tensor_tensor(out, a, b, op))

            dve.wait_ge(K.loaded, K.loads(2))
            dve.wait_ge(sig_done, 1)
            tt(sel.rearrange("p (t e) -> p t e", e=NEXP), sc.rearrange("p (t e) -> p t e", e=NEXP),
               rb.unsqueeze(1).broadcast_to([P, ST, NEXP]), ALU.add)
            s4 = e4(sel)
            pair = sel.rearrange("p (g h e) -> p g h e", h=2, e=2)
            h2, l2 = hi.rearrange("p (g h) -> p g h", h=2), lo.rearrange("p (g h) -> p g h", h=2)
            tt(h2, pair[:, :, :, 0], pair[:, :, :, 1], ALU.max)
            tt(l2, pair[:, :, :, 0], pair[:, :, :, 1], ALU.min)
            t1, t2 = top[:, 0:16], top[:, 16:32]
            tt(t1, h2[:, :, 0], h2[:, :, 1], ALU.min)
            tt(t2, l2[:, :, 0], l2[:, :, 1], ALU.max)
            tt(t2, t1, t2, ALU.max)
            tt(t1, h2[:, :, 0], h2[:, :, 1], ALU.max)
            g = gs[:, 0:16]
            tt(g, t1, t2, ALU.add)
            then(dve.memset(lose, 0.0))
            then(dve.memset(rank, 0.0))
            gg, ll, r4 = g.rearrange("p (t g) -> p t g", g=4), lose.rearrange("p (t g) -> p t g", g=4), e4(rank)
            gt4 = gt[:, 0:4]
            for i in range(4):
                for j in range(i + 1, 4):
                    tt(gt4, gg[:, :, j], gg[:, :, i], ALU.is_gt)
                    tt(ll[:, :, i], ll[:, :, i], gt4, ALU.add)
                    then(dve.scalar_tensor_tensor(ll[:, :, j], ll[:, :, j], 1.0, gt4, ALU.add, ALU.subtract))
                    tt(gt, s4[:, :, j], s4[:, :, i], ALU.is_gt)
                    tt(r4[:, :, i], r4[:, :, i], gt, ALU.add)
                    then(dve.scalar_tensor_tensor(r4[:, :, j], r4[:, :, j], 1.0, gt, ALU.add, ALU.subtract))
            then(dve.tensor_scalar(lose, lose, 0.5, None, ALU.is_lt))
            then(dve.scalar_tensor_tensor(tmp, rank, 1.5, sc, ALU.is_lt, ALU.mult))
            tt(e4(gates), e4(tmp), lose.unsqueeze(2).broadcast_to([P, 16, 4]), ALU.mult)
            g16 = gates.rearrange("p (t e) -> p t e", e=NEXP)
            then(dve.tensor_reduce(gt4, g16, AX.X, ALU.add))
            then(dve.reciprocal(gt4, gt4))
            n[0] += 1
            dve.tensor_tensor(g16, g16, gt4.unsqueeze(2).broadcast_to([P, ST, NEXP]), ALU.mult).then_inc(chain, 1)
            dve.wait_ge(chain, n[0])
            dve.tensor_copy(tmp, gates).then_inc(turned, 1)
    K.load_base = K.loads(2)


def moe_stage(K):
    r, T = K.ring, K.T
    gu_done, silu_done, up_done, hid_done, down_done, acc_done, zeroed = K.signals(7)
    n0 = r.first("moe")
    base = n0 // RING
    o0 = n0 % RING
    FT = 4
    silu, prod = K.at(88, 2, S), K.at(92, 2, S)
    hid, row = K.at(96, FT, S), K.at(104, S)
    acc = K.acc
    wg, wu, wd = T["moe_w_gate"], T["moe_w_up"], T["moe_w_down"]

    def slot(s):
        return r.slots[(o0 + s) % RING][:, :].rearrange("p (t c) -> p t c", c=HALF)

    def source(e, s):
        h = slice((s % 2) * HALF, (s % 2 + 1) * HALF)
        return ((wg, wg, wu, wu)[s][bass.ds(e, 1), h, :] if s < 4 else wd[bass.ds(e, 1), :, h])

    with K.nc.Block() as block:
        @block.sync
        def _(sp):
            K.start(sp)
            with sp.Fori(1, NEXP) as e:
                for s in range(RING):
                    sp.wait_ge(r.used, e * RING + (n0 + s + 1 - RING))
                    sp.dma_start(slot(s), source(e, s).rearrange("o (t p) c -> p (o t) c", p=P))\
                        .then_inc(r.arrived[(o0 + s) % RING], 16)
            r.issued = n0 + NEXP * RING
            r.issue_until(sp, n0 + NEXP * RING + RING)

        @block.gpsimd
        def _(pool):
            pool.dma_start(row, K.gate_rows[0:1, :].broadcast_to([P, S])).then_inc(K.loaded, 16)
            with pool.Fori(1, NEXP) as e:
                pool.wait_ge(hid_done, e * FT)
                pool.dma_start(row, K.gate_rows[bass.ds(e, 1), :].broadcast_to([P, S])).then_inc(K.loaded, 16)

        def arrive(pe, e, s):
            n = o0 + s
            pe.wait_ge(r.arrived[n % RING], e * 16 + 16 * (base + n // RING + 1))

        @block.tensor
        def _(pe):
            pe.wait_ge(zeroed, 1)
            with pe.Fori(0, NEXP) as e:
                for s in range(4):
                    arrive(pe, e, s)
                for f in range(FT):
                    pe.wait_ge(up_done, e * FT + f + 1)
                    for m in range(2):
                        for k in range(KD):
                            w = slot(2 * m + k // 4)[:, k % 4, f * P:(f + 1) * P]
                            ins = pe.matmul(K.ps[:, 2 * m + f % 2, :], w, K.hT[:, k, :], start=(k == 0),
                                            stop=(k == KD - 1))
                    ins.then_inc(gu_done, 1)
                release(K, pe, 4)
                for s in range(4, 6):
                    arrive(pe, e, s)
                for t in range(KD):
                    pe.wait_ge(acc_done, e * KD + t + 1)
                    if t == 0:
                        pe.wait_ge(hid_done, e * FT + FT)
                    accumulate(pe, K.ps[:, 4 + t % 2, :],
                               [(slot(4 + t // 4)[:, k, (t % 4) * P:(t % 4 + 1) * P], hid[:, k, :])
                                for k in range(FT)]).then_inc(down_done, 1)
                release(K, pe, 2)

        @block.scalar
        def _(act):
            with act.Fori(0, NEXP) as e:
                for f in range(FT):
                    act.wait_ge(gu_done, e * FT + f + 1)
                    act.wait_ge(up_done, e * FT + f + 1)
                    act.activation(silu[:, f % 2, :], K.ps[:, f % 2, :], ACT.Silu).then_inc(silu_done, 1)

        @block.vector
        def _(dve):
            for b in range(2):
                dve.memset(prod[:, b, 0:1], 0.0).then_inc(up_done, 1)
                dve.memset(prod[:, b, 1:2], 0.0).then_inc(acc_done, 1)
            dve.memset(acc, 0.0).then_inc(zeroed, 1)
            dve.wait_ge(zeroed, 1)
            dve.wait_ge(up_done, 2)
            dve.wait_ge(acc_done, 2)
            with dve.Fori(0, NEXP) as e:
                dve.wait_ge(K.loaded, e * 16 + K.loads(1))
                for f in range(FT):
                    dve.wait_ge(silu_done, e * FT + f + 1)
                    dve.tensor_tensor(prod[:, f % 2, :], K.ps[:, 2 + f % 2, :], silu[:, f % 2, :], ALU.mult)\
                        .then_inc(up_done, 1)
                    dve.wait_ge(up_done, e * FT + f + 3)
                    dve.tensor_tensor(hid[:, f, :], prod[:, f % 2, :], row, ALU.mult).then_inc(hid_done, 1)
                for t in range(KD):
                    dve.wait_ge(down_done, e * KD + t + 1)
                    dve.tensor_tensor(acc[:, t, :], K.ps[:, 4 + t % 2, :], acc[:, t, :], ALU.add).then_inc(acc_done, 1)
            dve.wait_ge(acc_done, NEXP * KD + 2)
            dve.wait_ge(hid_done, NEXP * FT)
            for t in range(KD):
                dve.scalar_tensor_tensor(K.xT[:, t, :], acc[:, t, :], mod_col(K, 5, t), K.xT[:, t, :], ALU.mult,
                                         ALU.add).then_inc(zeroed, 1)
            dve.wait_ge(zeroed, 1 + KD)
    K.load_base = K.loads(NEXP)


def lru_weights_stage(K):
    T = K.T
    zeroed, chain, exp_done, stored = K.signals(4)
    LT = 6
    lam = K.vecs[:, VEC_AT["lru_lambda_2"]:VEC_AT["lru_lambda_2"] + LT]
    e, w, s, p, y = (K.at(150 + 0.25 * i, LT) for i in range(5))
    with K.nc.Block() as block:
        @block.sync
        def _(sp):
            K.start(sp)
            sp.wait_ge(zeroed, 1)
            for m, name in enumerate(("w_rg_a_2", "w_rg_x_2")):
                for h in range(2):
                    blocks = T[name].rearrange("(t h) i j -> h i t j", h=2)[h]
                    sp.dma_start(K.rg[64 * h:64 * h + 64, m, :, 64 * h:64 * h + 64], blocks).then_inc(stored, 16)
            sp.wait_ge(stored, 64)

        @block.scalar
        def _(act):
            act.wait_ge(chain, 1)
            act.activation(e, e, ACT.Exp).then_inc(exp_done, 1)

        @block.vector
        def _(dve):
            dve.memset(K.rg, 0.0).then_inc(zeroed, 1)
            n = [0]

            def then(ins):
                n[0] += 1
                ins.then_inc(chain, 1)
                dve.wait_ge(chain, n[0])

            then(dve.scalar_tensor_tensor(e, lam, -1.0, lam, ALU.mult, ALU.min))
            then(dve.tensor_scalar(y, lam, -1.0, 0.0, ALU.mult, ALU.max))
            dve.wait_ge(exp_done, 1)
            then(dve.tensor_scalar(w, e, 2.0, None, ALU.add))
            then(dve.reciprocal(w, w))
            then(dve.tensor_tensor(w, w, e, ALU.mult))
            then(dve.tensor_tensor(s, w, w, ALU.mult))
            then(dve.tensor_scalar(p, s, 1.0 / 15, 1.0 / 13, ALU.mult, ALU.add))
            for d in (11, 9, 7, 5, 3, 1):
                then(dve.tensor_tensor(p, p, s, ALU.mult))
                then(dve.tensor_scalar(p, p, 1.0 / d, None, ALU.add))
            then(dve.tensor_tensor(p, p, w, ALU.mult))
            then(dve.scalar_tensor_tensor(p, p, 2.0, y, ALU.mult, ALU.add))
            then(dve.tensor_scalar(K.lru_rate, p, -8.0, None, ALU.mult))


def lru_stage(K):
    r = K.ring
    (x_done, mid_done, conv_done, rg_done, sig_done, exp_done, tanh_done, chain, sqrt_done, g_done, gelu_done,
     y_done, h_chain) = K.signals(13)
    n0 = r.first("lru")
    LT = 6
    xc, rr, ii, aa, th, bb, ge = (K.at(56 + 4 * j, 2, S) for j in range(7))
    with K.nc.Block() as block:
        @block.sync
        def _(sp):
            K.start(sp)
            r.issue_until(sp, n0 + 8 + RING)

        @block.tensor
        def _(pe):
            for t in range(LT + 1):
                if t < LT:
                    n = n0 + 4 * (t // 4)
                    if t % 4 == 0:
                        arrived(K, pe, n, 4)
                    if t >= 2:
                        pe.wait_ge(conv_done, 3 * (t - 1))
                    project(K, pe, n, (t % 4) * P, P, K.hT, slice(0, S), K.ps[:, t % 2, :]).then_inc(x_done, 1)
                    if t >= 2:
                        pe.wait_ge(gelu_done, t - 1)
                    project(K, pe, n + 2, (t % 4) * P, P, K.hT, slice(0, S), K.ps[:, 4 + t % 2, :]).then_inc(g_done, 1)
                    if t in (3, LT - 1):
                        release(K, pe, 4)
                if t >= 1:
                    u = t - 1
                    pe.wait_ge(conv_done, 3 * (u + 1))
                    if u >= 1:
                        pe.wait_ge(sig_done, 2 * u)
                    for m in range(2):
                        pe.matmul(K.ps[:, 2 + m, :], K.rg[:, m, u, :], xc[:, u % 2, :], start=True, stop=True)\
                            .then_inc(rg_done, 1)

        @block.scalar
        def _(act):
            for t in range(LT + 1):
                if t < LT:
                    act.wait_ge(x_done, t + 1)
                    if t >= 2:
                        act.wait_ge(y_done, t - 1)
                    act.activation(xc[:, t % 2, :], K.ps[:, t % 2, :], ACT.Identity, bias=K.vec("conv_b_2", t),
                                   scale=K.vec("conv_w_2", 3 * LT + t)).then_inc(mid_done, 1)
                if t >= 1:
                    u = t - 1
                    b = u % 2
                    act.wait_ge(rg_done, 2 * t)
                    act.activation(rr[:, b, :], K.ps[:, 2, :], ACT.Sigmoid, bias=K.vec("b_rg_a_2", u))\
                        .then_inc(sig_done, 1)
                    act.activation(ii[:, b, :], K.ps[:, 3, :], ACT.Sigmoid, bias=K.vec("b_rg_x_2", u))\
                        .then_inc(sig_done, 1)
                    act.wait_ge(sig_done, 2 * u + 1)
                    act.activation(th[:, b, :], rr[:, b, :], ACT.Tanh, scale=K.lru_rate[:, u:u + 1])\
                        .then_inc(tanh_done, 1)
                    act.activation(aa[:, b, :], rr[:, b, :], ACT.Exp, scale=K.lru_rate[:, u:u + 1])\
                        .then_inc(exp_done, 1)
                    act.wait_ge(g_done, u + 1)
                    act.activation(ge[:, b, :], K.ps[:, 4 + b, :], ACT.Gelu_apprx_tanh).then_inc(gelu_done, 1)
                    act.wait_ge(chain, 4 * u + 3)
                    act.activation(bb[:, b, :], bb[:, b, :], ACT.Sqrt).then_inc(sqrt_done, 1)

        @block.vector
        def _(dve):
            for t in range(LT + 1):
                if t < LT:
                    x, u = xc[:, t % 2, :], K.ps[:, t % 2, :]
                    dve.wait_ge(mid_done, t + 1)
                    for k in range(1, 4):
                        dve.scalar_tensor_tensor(x[:, k:S], u[:, 0:S - k], K.vec("conv_w_2", (3 - k) * LT + t),
                                                 x[:, k:S], ALU.mult, ALU.add).then_inc(conv_done, 1)
                        dve.wait_ge(conv_done, 3 * t + k)
                if t >= 1:
                    u = t - 1
                    b = u % 2
                    dve.wait_ge(tanh_done, u + 1)
                    dve.tensor_scalar(bb[:, b, :], th[:, b, :], -1.0, 1.0, ALU.mult, ALU.add).then_inc(chain, 1)
                    dve.wait_ge(chain, 4 * u + 1)
                    dve.reciprocal(bb[:, b, :], bb[:, b, :]).then_inc(chain, 1)
                    dve.wait_ge(chain, 4 * u + 2)
                    dve.scalar_tensor_tensor(bb[:, b, :], th[:, b, :], -2.0, bb[:, b, :], ALU.mult, ALU.mult)\
                        .then_inc(chain, 1)
                    dve.wait_ge(sig_done, 2 * u + 2)
                    dve.tensor_tensor(ii[:, b, :], ii[:, b, :], xc[:, b, :], ALU.mult).then_inc(chain, 1)
                    dve.wait_ge(chain, 4 * u + 4)
                    dve.wait_ge(sqrt_done, u + 1)
                    dve.wait_ge(exp_done, u + 1)
                    dve.wait_ge(gelu_done, u + 1)
                    dve.tensor_tensor(bb[:, b, :], bb[:, b, :], ii[:, b, :], ALU.mult).then_inc(h_chain, 1)
                    dve.wait_ge(h_chain, 2 * u + 1)
                    dve.tensor_tensor_scan(th[:, b, :], aa[:, b, :], bb[:, b, :], 0.0, ALU.mult, ALU.add)\
                        .then_inc(h_chain, 1)
                    dve.wait_ge(h_chain, 2 * u + 2)
                    dve.tensor_tensor(K.ylruT[:, u, :], th[:, b, :], ge[:, b, :], ALU.mult).then_inc(y_done, 1)
            dve.wait_ge(y_done, LT)


def memory_project_stage(K):
    n = K.ring.first("mem")
    items = [channel_item(K, n, t * P, P, K.memT, NCTX, K.kmT[:, t, :], eng=("act", "dve")[t % 2],
                          first=(n, n + 1) if t == 0 else (), rel=2 if t == 3 else 0) for t in range(4)]
    n += 2
    items += [token_item(K, n, 0, 512, K.memT, slice(t * P, t * P + P), K.vm[:, t, :], eng=("act", "dve")[t],
                         first=(n, n + 1) if t == 0 else (), rel=2 if t == 1 else 0) for t in range(2)]
    items_stage(K, items, issue=n + 2)


def group_tokens(v, g, j):
    return v[:, j * P:(j + 1) * P] if g == 0 else v.rearrange("p (l r) -> p r l", r=4)[:, j, :]


def dilated_project_stage(K):
    n0 = K.ring.first("qkv")
    items = []
    for c in range(12):
        n = n0 + 2 * (c // 4)
        dest = K.qd[:, c, :] if c < 6 else K.kd[:, c - 6, :]
        items.append(channel_item(K, n, (c % 4) * P, P, K.hT, S, dest, eng="act" if c < 6 else "dve",
                                  first=(n, n + 1) if c % 4 == 0 else (), rel=2 if c % 4 == 3 else 0,
                                  **({"scale": 0.125} if c < 6 else {})))
    for g in range(3):
        n = n0 + 6 + 2 * (g // 2)
        for j in range(4):
            c0 = 256 * (g % 2)

            def mm(pe, bank, g=g, j=j, n=n, c0=c0):
                return accumulate(pe, bank[:, 0:256],
                                  [(group_tokens(K.hT[:, k, :], g, j), K.ring.view(n + k // 4)[:, k % 4, c0:c0 + 256])
                                   for k in range(KD)])
            dest = K.vd[:, g * 4 + j, :]
            items.append({"first": (n, n + 1) if (g != 1 and j == 0) else (), "mm": mm,
                          "rel": 2 if (g > 0 and j == 3) else 0, "eng": "act" if j % 2 else "dve",
                          "out": (lambda e, bank, dest=dest: e.activation(dest, bank[:, 0:256], ACT.Copy)) if j % 2 else
                                 (lambda e, bank, dest=dest: e.tensor_copy(dest, bank[:, 0:256]))})
    n = K.ring.first("qm")
    for c in range(4):
        items.append(channel_item(K, n, c * P, P, K.hT, S, K.qm[:, c, :], eng=("act", "dve")[c % 2],
                                  first=(n, n + 1) if c == 0 else (), rel=2 if c == 3 else 0))
    items_stage(K, items, issue=n + 2)


NU = 384


def bias_stage(K):
    T = K.T
    mm_done, added, stored, read = K.signals(4)
    table, hot, neg, u = K.at(116, 12)[0:32], K.at(117, 3, NU)[0:32], K.at(122, 3, NU)[0:4], K.at(127, 3, NU)[0:4]
    rows = K.bias_rows
    with K.nc.Block() as block:
        @block.gpsimd
        def _(pool):
            for dst, src in ((table, T["rel_bias_2"]), (hot, T["k_bucket"]), (neg, T["k_neg"]),
                             (K.flip, T["k_flip"]), (K.pick, T["k_pick"])):
                pool.dma_start(dst, src).then_inc(K.loaded, 16)
            pool.wait_ge(K.loaded, K.loads(5))

        @block.sync
        def _(sp):
            K.start(sp)
            sp.wait_ge(added, 3)
            sp.dma_start(rows.rearrange("g h n -> h g n"), u).then_inc(stored, 16)
            sp.wait_ge(stored, 16)
            n = 0
            for h in range(4):
                for dst, off, c in ((K.hank0, 0, 256), (K.hank1, 4 * NU + P, P), (K.hank2, 8 * NU + P, P)):
                    sp.dma_start(dst[:, h, :], bass.AP(rows.tensor, off + h * NU, [[1, P], [1, c]]))\
                        .then_inc(read, 16)
                    n += 16
            sp.wait_ge(read, n)

        @block.tensor
        def _(pe):
            pe.wait_ge(K.loaded, K.loads(5))
            for g in range(3):
                pe.matmul(K.ps[0:4, g, 0:NU], table[:, 4 * g:4 * g + 4], hot[:, g, :], start=True, stop=True)\
                    .then_inc(mm_done, 1)

        @block.vector
        def _(dve):
            dve.wait_ge(K.loaded, K.loads(5))
            for g in range(3):
                dve.wait_ge(mm_done, g + 1)
                dve.tensor_tensor(u[:, g, :], K.ps[0:4, g, 0:NU], neg[:, g, :], ALU.add).then_inc(added, 1)
    K.load_base = K.loads(5)


def dilated_attention_stage(K):
    (s_done, max_done, neg_done, exp_done, turned, copied, o_done, o_copied, st_turned, st_copied, chain, e_done,
     bc_done, part, summed) = K.signals(15)
    units = [(g, j, h) for g in range(3) for j in range(4) for h in range(4)]
    NUNIT = len(units)
    Pb, PT = K.at(116, 2, 256), K.at(118, 2, 2, P)
    stats = K.at(120, 3, NUNIT)
    num = K.at(121, 6, S)
    mrow, drow = K.at(133, 3, S)[0:4], K.at(139, 3, S)[0:4]
    m, tmp = K.at(145, S)[0:4], K.at(116, 2, S)

    def keys(g, j):
        return ([j - 1, j] if j else [0]) if g == 0 else [j]

    def hank(g, j, h):
        return (K.hank0[:, h, 0:256] if j else K.hank0[:, h, P:256]) if g == 0 else (K.hank1, K.hank2)[g - 1][:, h, :]

    def key_view(g, j, rows, c):
        v = K.kd[rows, c, :]
        return v[:, (j - 1) * P:(j + 1) * P] if g == 0 and j else group_tokens(v, g, j)

    def spread(v, g, j):
        return group_tokens(v, g, j)

    with K.nc.Block() as block:
        @block.sync
        def _(sp):
            K.start(sp)

        @block.tensor
        def _(pe):
            def scores(b):
                g, j, h = units[b]
                c, rows = g * 2 + h // 2, slice(64 * (h % 2), 64 * (h % 2) + 64)
                nk = P * len(keys(g, j))
                if b >= 2:
                    pe.wait_ge(exp_done, b - 1)
                out = K.ps[:, b % 2, 0:nk]
                pe.matmul(out, K.flip, hank(g, j, h), start=True, stop=False)
                pe.matmul(out, group_tokens(K.qd[rows, c, :], g, j), key_view(g, j, rows, c), start=False, stop=True)\
                    .then_inc(s_done, 1)

            def values(b):
                g, j, h = units[b]
                pe.wait_ge(exp_done, b + 1)
                if b >= 2:
                    pe.wait_ge(copied, b - 1)
                ks = keys(g, j)
                for i in range(len(ks)):
                    ins = pe.transpose(K.ps[:, 2 + b % 2, i * P:(i + 1) * P], Pb[:, b % 2, i * P:(i + 1) * P],
                                       K.ident[:, :])
                ins.then_inc(turned, 1)
                if h == 3:
                    q = b // 4
                    if q >= 1:
                        pe.wait_ge(st_copied, 2 * q)
                    for i in (0, 2):
                        ins = pe.transpose(K.ps[0:4, 6, (i // 2) * P:(i // 2 + 1) * P], stats[:, i, b - 3:b + 1],
                                           K.ident[:, :])
                    ins.then_inc(st_turned, 1)
                if h == 0 and b >= 8:
                    pe.wait_ge(o_copied, b // 4 - 1)
                pe.wait_ge(copied, b + 1)
                out = K.ps[64 * (h % 2):64 * (h % 2) + 64, 4 + (b // 4) % 2, (h // 2) * P:(h // 2 + 1) * P]
                accumulate(pe, out, [(K.vd[:, g * 4 + kt, 64 * h:64 * h + 64], PT[:, b % 2, i, :])
                                     for i, kt in enumerate(ks)]).then_inc(o_done, 1)

            for b in range(NUNIT + 1):
                if b < NUNIT:
                    scores(b)
                if b >= 1:
                    values(b - 1)
            pe.wait_ge(chain, 11)
            for i in range(6):
                if i >= 2:
                    pe.wait_ge(part, i - 1)
                pe.matmul(K.ps[:, i % 2, :], K.pick[:, (i % 2) * P:(i % 2 + 1) * P], drow[:, i // 2, :], start=True,
                          stop=True).then_inc(bc_done, 1)

        @block.scalar
        def _(act):
            def empty(b):
                g, j, h = units[b]
                if h == 3:
                    q = b // 4
                    act.wait_ge(st_turned, q + 1)
                    for dst, c in ((mrow, 0), (drow, 1)):
                        act.activation(spread(dst[:, g, :], g, j), K.ps[0:4, 6, c * P:(c + 1) * P],
                                       ACT.Copy).then_inc(st_copied, 1)
                    act.wait_ge(o_done, b + 1)
                    for pr in range(2):
                        ins = act.activation(spread(num[:, 2 * g + pr, :], g, j),
                                             K.ps[:, 4 + q % 2, pr * P:(pr + 1) * P], ACT.Copy)
                    ins.then_inc(o_copied, 1)

            for b in range(NUNIT + 1):
                if b < NUNIT:
                    g, j, h = units[b]
                    nk = P * len(keys(g, j))
                    act.wait_ge(neg_done, b + 1)
                    if b >= 2:
                        act.wait_ge(turned, b - 1)
                    act.activation(Pb[:, b % 2, 0:nk], K.ps[:, b % 2, 0:nk], ACT.Exp, bias=stats[:, 1, b:b + 1],
                                   accum_out=stats[:, 2, b:b + 1]).then_inc(exp_done, 1)
                if b >= 1:
                    empty(b - 1)
            for g in range(3):
                act.wait_ge(chain, 2 + g + 1)
                act.activation(mrow[:, g, :], mrow[:, g, :], ACT.Exp).then_inc(e_done, 1)

        @block.vector
        def _(dve):
            def maximum(b):
                g, j, h = units[b]
                dve.wait_ge(s_done, b + 1)
                dve.tensor_reduce(stats[:, 0, b:b + 1], K.ps[:, b % 2, 0:P * len(keys(g, j))], AX.X, ALU.max)\
                    .then_inc(max_done, 1)
                dve.wait_ge(max_done, b + 1)
                dve.tensor_scalar(stats[:, 1, b:b + 1], stats[:, 0, b:b + 1], -1.0, None, ALU.mult)\
                    .then_inc(neg_done, 1)

            maximum(0)
            for b in range(NUNIT):
                if b + 1 < NUNIT:
                    maximum(b + 1)
                g, j, h = units[b]
                n = len(keys(g, j))
                dve.wait_ge(turned, b + 1)
                if b >= 2:
                    dve.wait_ge(o_done, b - 1)
                dve.tensor_copy(PT[:, b % 2, 0:n, :], K.ps[:, 2 + b % 2, 0:n * P].rearrange("p (i q) -> p i q", q=P))\
                    .then_inc(copied, 1)
            dve.wait_ge(st_copied, 24)
            dve.tensor_tensor(m, mrow[:, 0, :], mrow[:, 1, :], ALU.max).then_inc(chain, 1)
            dve.wait_ge(chain, 1)
            dve.tensor_tensor(m, m, mrow[:, 2, :], ALU.max).then_inc(chain, 1)
            dve.wait_ge(chain, 2)
            for g in range(3):
                dve.tensor_tensor(mrow[:, g, :], mrow[:, g, :], m, ALU.subtract).then_inc(chain, 1)
            t0 = tmp[0:4, 0, :]
            for g in range(3):
                dve.wait_ge(e_done, g + 1)
                dve.wait_ge(chain, 5 if g == 0 else 5 + g)
                if g == 0:
                    dve.tensor_tensor(m, drow[:, 0, :], mrow[:, 0, :], ALU.mult).then_inc(chain, 1)
                else:
                    dve.tensor_tensor(drow[:, g, :], drow[:, g, :], mrow[:, g, :], ALU.mult).then_inc(chain, 1)
            dve.wait_ge(chain, 8)
            dve.tensor_tensor(t0, drow[:, 1, :], drow[:, 2, :], ALU.add).then_inc(summed, 1)
            dve.wait_ge(summed, 1)
            dve.tensor_tensor(m, m, t0, ALU.add).then_inc(summed, 1)
            dve.wait_ge(summed, 2)
            dve.reciprocal(m, m).then_inc(summed, 1)
            dve.wait_ge(summed, 3)
            for g in range(3):
                dve.tensor_tensor(drow[:, g, :], mrow[:, g, :], m, ALU.mult).then_inc(chain, 1)
            dve.wait_ge(o_copied, 12)
            for i in range(6):
                g, pr = i // 2, i % 2
                dve.wait_ge(bc_done, i + 1)
                dest = K.odT[:, pr, :]
                dve.tensor_tensor(dest if g == 0 else tmp[:, pr, :], K.ps[:, i % 2, :], num[:, i, :], ALU.mult)\
                    .then_inc(part, 1)
                dve.wait_ge(part, i + 1)
                if g:
                    dve.tensor_tensor(dest, dest, tmp[:, pr, :], ALU.add).then_inc(summed, 1)
                    dve.wait_ge(summed, 3 + i - 1)


def memory_attention_stage(K):
    attention_stage(K, 4, NCTX, lambda h, i: [(slice(0, NCTX), K.qm[:, h, i * P:(i + 1) * P], K.kmT[:, h, :])],
                    lambda h, j: K.vm[:, j, h * P:(h + 1) * P], lambda h: K.omT[:, h, :], P ** -0.5, 116)


def mlp_stage(K):
    r, T = K.ring, K.T
    h_done, relu_done, hid_done, down_done, acc_done, began = K.signals(6)
    n0 = r.first("mlp")
    UNITS, CH, FT = 8, 4, 4
    BODY = 3
    LOOPS = UNITS // BODY
    relu, hid = K.at(40, 2, S), K.at(48, FT, S)
    win, wout = T["w_mlp_in_2"], T["w_mlp_out_2"]

    def view(n):
        return r.slots[n % RING][:, :].rearrange("p (t c) -> p t c", c=HALF)

    with K.nc.Block() as block:
        @block.sync
        def _(sp):
            K.start(sp)
            with sp.Fori(0, LOOPS) as i:
                for k in range(BODY * CH):
                    c = k + RING
                    u, s = i * BODY + c // CH, c % CH
                    sp.wait_ge(r.used, i * (BODY * CH) + (n0 + c - RING + 1))
                    src = (win[s * HALF:(s + 1) * HALF, bass.ds(u * HALF, HALF)] if s < 2 else
                           wout[bass.ds(u * HALF, HALF), (s - 2) * HALF:(s - 1) * HALF])
                    sp.dma_start(view(n0 + c), src.rearrange("(t p) c -> p t c", p=P))\
                        .then_inc(r.arrived[(n0 + c) % RING], 16)
            r.issued = n0 + RING + LOOPS * BODY * CH
            r.issue_until(sp, n0 + UNITS * CH + RING)

        @block.tensor
        def _(pe):
            def unit(u, v, i):
                def arrive(s):
                    n = n0 + v * CH + s
                    pe.wait_ge(r.arrived[n % RING], i * 32 + r.arrival(n))
                for s in range(2):
                    arrive(s)
                for f in range(FT):
                    pe.wait_ge(hid_done, u * FT + f + 1)
                    for k in range(KD):
                        ins = pe.matmul(K.ps[:, f % 2, :], view(n0 + v * CH + k // 4)[:, k % 4, f * P:(f + 1) * P],
                                        K.hT[:, k, :], start=(k == 0), stop=(k == KD - 1))
                    ins.then_inc(h_done, 1)
                release(K, pe, 2)
                for s in range(2, 4):
                    arrive(s)
                for t in range(KD):
                    pe.wait_ge(acc_done, u * KD + t + 1)
                    if t == 0:
                        pe.wait_ge(hid_done, u * FT + FT + 2)
                    accumulate(pe, K.ps[:, 4 + t % 2, :],
                               [(view(n0 + v * CH + 2 + t // 4)[:, k, (t % 4) * P:(t % 4 + 1) * P], hid[:, k, :])
                                for k in range(FT)]).then_inc(down_done, 1)
                release(K, pe, 2)

            pe.wait_ge(began, 1)
            with pe.Fori(0, LOOPS) as i:
                for v in range(BODY):
                    unit(i * BODY + v, v, i)
            for v in range(LOOPS * BODY, UNITS):
                unit(v, v, 0)

        @block.scalar
        def _(act):
            with act.Fori(0, UNITS) as u:
                for f in range(FT):
                    act.wait_ge(h_done, u * FT + f + 1)
                    act.wait_ge(hid_done, u * FT + f + 1)
                    act.activation(relu[:, f % 2, :], K.ps[:, f % 2, :], ACT.Relu).then_inc(relu_done, 1)

        @block.vector
        def _(dve):
            for b in range(2):
                dve.memset(hid[:, b, 0:1], 0.0).then_inc(hid_done, 1)
                dve.memset(hid[:, b, 1:2], 0.0).then_inc(acc_done, 1)
            dve.wait_ge(hid_done, 2)
            dve.wait_ge(acc_done, 2)
            dve.memset(hid[:, 0, 2:3], 0.0).then_inc(began, 1)
            dve.wait_ge(began, 1)
            with dve.Fori(0, UNITS) as u:
                for f in range(FT):
                    dve.wait_ge(relu_done, u * FT + f + 1)
                    dve.tensor_tensor(hid[:, f, :], K.ps[:, f % 2, :], relu[:, f % 2, :], ALU.mult)\
                        .then_inc(hid_done, 1)
                for t in range(KD):
                    dve.wait_ge(down_done, u * KD + t + 1)
                    dve.tensor_tensor(K.xT[:, t, :], K.ps[:, 4 + t % 2, :], K.xT[:, t, :], ALU.add)\
                        .then_inc(acc_done, 1)
            dve.wait_ge(acc_done, UNITS * KD + 2)


def store_stage(K):
    (stored,) = K.signals(1)
    with K.nc.Block() as block:
        @block.sync
        def _(sp):
            K.start(sp)
            sp.dma_start(K.out.rearrange("(t p) n -> p t n", p=P), K.hT).then_inc(stored, 16)
            sp.wait_ge(stored, 16)


def load_memory_stage(K):
    (came,) = K.signals(1)
    with K.nc.Block() as block:
        @block.sync
        def _(sp):
            K.start(sp)
            sp.dma_start(K.memT, K.T["memT"].rearrange("(t p) n -> p t n", p=P)).then_inc(came, 16)
            sp.wait_ge(came, 16)


def host_constants():
    f32 = np.float32
    out = {"k_ident": np.eye(P, dtype=f32)}
    pos = np.arange(S)
    inv = f32(10000.0) ** (-np.arange(32, dtype=f32) / f32(32))
    ang = np.concatenate([(pos // 64).astype(f32)[:, None] * inv, (pos % 64).astype(f32)[:, None] * inv], axis=1)
    out["k_cos"] = np.repeat(np.cos(ang.astype(f32)), 2, axis=1).T.astype(f32)
    out["k_sin"] = np.repeat(np.sin(ang.astype(f32)), 2, axis=1).T.astype(f32)
    swap = np.zeros((P, P), f32)
    for i in range(0, P, 2):
        swap[i + 1, i] = -1.0
        swap[i, i + 1] = 1.0
    out["k_swap"] = swap
    scan = np.ones((P, S + NCTX), f32)
    scan[:, 0:S:64] = 0.0
    scan[:, S] = 0.0
    out["k_scan"] = scan
    t = np.arange(S, dtype=f32)
    tn = (t / f32(S)).astype(f32)
    bands = np.linspace(1e-4, 15, 16, dtype=f32)
    phase = (f32(2 * np.pi / S) * t[:, None] * bands[None, :]).astype(f32)
    out["k_pos"] = np.concatenate([tn[:, None], np.cos(phase), -np.sin(phase)], axis=1).T.astype(f32)
    first = np.ones(P, f32)
    first[0] = 0.0
    out["k_time"] = np.concatenate([-tn.reshape(ST, P).T, first[:, None]], axis=1)
    nn = 2 * S
    ang2 = 2 * np.pi * ((np.arange(S)[:, None] * np.arange(S)[None, :]) % nn) / nn
    alt = 1.0 - 2.0 * (np.arange(S) % 2)
    cosm, sinm = np.cos(ang2), -np.sin(ang2)
    out["k_dft_cos"] = cosm.astype(f32)
    s1 = sinm.copy()
    s1[:, 0] = alt
    out["k_dft_sin"] = s1.astype(f32)
    c1 = cosm[:, 0:P].copy()
    c1[:, 0] = alt
    out["k_dft_edge"] = np.concatenate([c1, sinm[:, 0:P]], axis=1).astype(f32)
    ic, isn = 2.0 * cosm / nn, 2.0 * sinm / nn
    ic[0] = 1.0 / nn
    isn[0] = alt / nn
    out["k_idft_cos"] = ic.astype(f32)
    out["k_idft_sin"] = isn.astype(f32)
    hot, neg = np.zeros((32, 3, NU), f32), np.zeros((4, 3, NU), f32)
    for g, (dil, each) in enumerate(((1, 1), (4, 1), (4, 4))):
        for j in range(NU):
            off = 255 - j
            if not (0 <= off <= P and off % each == 0):
                neg[:, g, j] = NEG
                continue
            dist = off * dil
            b = dist
            if dist >= 16:
                large = f32(np.log(f32(dist) / f32(16))) / f32(np.log(128.0)) * f32(16)
                b = min(16 + int(large), 31)
            hot[b, g, j] = 1.0
    out["k_bucket"], out["k_neg"] = hot, neg
    out["k_flip"] = np.eye(P, dtype=f32)[::-1]
    pick = np.zeros((4, 256), f32)
    for h in range(4):
        pick[h, (h // 2) * P + 64 * (h % 2):(h // 2) * P + 64 * (h % 2) + 64] = 1.0
    out["k_pick"] = pick
    a = np.arange(P)
    same = (a[:, None] // 64) == (a[None, :] // 64)
    out["k_causal"] = np.stack([same & (a[:, None] <= a[None, :]), same & (a[:, None] >= a[None, :])]).astype(f32)
    return out


WEIGHTS = ["w_mod", "w_in", "gla_wa2", "hy_pos_w1", "hy_pos_w2", "hy_pos_w3", "w_br_hy", "w_br_gla", "w_br_att",
           "w_out", "router_w", "moe_w_gate", "moe_w_up", "moe_w_down", "w_in_2", "w_rg_a_2", "w_rg_x_2",
           "w_lru_out_2", "rel_bias_2", "w_dil_out_2", "w_mem_kv_2", "w_mem_out_2", "w_out_2", "w_mlp_in_2",
           "w_mlp_out_2"]
ROWS = ["gla_norm_g", "hy_decay", "hy_skip", "router_b"]


def layout(inputs):
    out = {k: np.ascontiguousarray(v) for k, v in host_constants().items()}
    for name in WEIGHTS:
        a = np.asarray(inputs[name])
        out[name] = np.ascontiguousarray(a[0] if a.shape[0] == 1 else a)
    for name in ROWS:
        out[name] = np.ascontiguousarray(np.asarray(inputs[name]).reshape(1, -1))
    out["xT"] = np.ascontiguousarray(np.asarray(inputs["x"])[0].T)
    out["ctxT"] = np.ascontiguousarray(np.asarray(inputs["ctx"])[0].T)
    out["memT"] = np.ascontiguousarray(np.asarray(inputs["mem_2"])[0].T)
    out["hy_cols"] = np.ascontiguousarray(
        np.stack([np.asarray(inputs[n]).reshape(-1) for n in ("hy_pos_b1", "hy_pos_b2", "hy_sin_freq")], axis=1))
    out["vecs"] = np.ascontiguousarray(
        np.concatenate([np.asarray(inputs[n]).reshape(-1, P).T for n, _ in VECS], axis=1))
    return out


def build(nc, T, out, upto=99, debug=None):
    with ExitStack() as ctx:
        K = Core(nc, ctx, T)
        K.out = out
        K.sc = ctx.enter_context(nc.sbuf_tensor("silu_c", [P, KD, 2], F32))
        g = ctx.enter_context(nc.sbuf_tensor("gains", [P, 24], F32))
        K.gain1, K.gain1c, K.gain2 = g[:, 0:8], g[:, 8:16], g[:, 16:24]
        K.xT, K.hT, K.hcT = K.at(0, KD, S), K.at(16, KD, S), K.at(32, KD, NCTX)
        K.tot = ctx.enter_context(nc.sbuf_tensor("chunk_decay", [P, 4, 9], F32))
        K.gate_rows = nc.dram_tensor("gate_rows", (NEXP, S), F32).ap()
        plan_block1(K)
        K.bias_rows = nc.dram_tensor("bias_rows", (3, 4, NU), F32).ap()
        plan_block2(K)
        stages = block1_stages(K) + block2_stages(K)
        for n, st in enumerate(stages[:upto]):
            st()
            if debug and n == upto - 1:
                dump(K, debug)


def dump(K, debug):
    (done,) = K.signals(1)
    with K.nc.Block() as block:
        @block.sync
        def _(sp):
            K.start(sp)
            n = 0
            for ap, src in debug(K):
                sp.dma_start(ap, src).then_inc(done, 16)
                n += 16
            sp.wait_ge(done, n)


def plan_block1(K):
    r, T = K.ring, K.T
    w = T["w_mod"].rearrange("(h t p) c -> h p t c", h=2, p=P)
    for g in range(12):
        for h in range(2):
            r.add("mod", w[h][:, :, g * HALF:(g + 1) * HALF])
    w = T["w_in"]
    r.add_matrix("gk", w, C_GK, C_GK + 256)
    r.add_matrix("gv", w, C_GV, C_GV + 512)
    r.add_matrix("ga", w, C_GA, C_GA + 32)
    r.add_matrix("gq", w, C_GQ, C_GQ + 256)
    r.add_matrix("og", w, C_OG, C_OG + 512)
    r.add_matrix("kv", w, C_KV, C_KV + 512)
    r.add_matrix("q", w, C_Q, C_Q + 1024)
    r.add_matrix("hy", w, C_HY, C_HY + 1536)
    for o in range(2):
        for m in ("k_dft_cos", "k_dft_sin", "k_dft_edge", "k_idft_cos", "k_idft_sin"):
            r.add_matrix(f"dft{o}", T[m], 0, T[m].shape[1])
    for half in range(2):
        for b, y in enumerate(("w_br_hy", "w_br_gla", "w_br_att")):
            a = half * HALF
            r.add_matrix("merge1", w, C_BR + b * D + a, C_BR + b * D + a + HALF)
            r.add_matrix("merge1", T[y], a, a + HALF)
    r.add_matrix("out1", T["w_out"], 0, D)
    for e in range(NEXP):
        for m in ("moe_w_gate", "moe_w_up", "moe_w_down"):
            r.add_matrix("moe", T[m][e], 0, T[m].shape[2])


def plan_block2(K):
    r, T = K.ring, K.T
    w = T["w_in_2"]
    r.add_matrix("mem", T["w_mem_kv_2"], 0, D)
    r.add_matrix("lru", w, C2_X, C2_X + 512)
    r.add_matrix("lru", w, C2_G, C2_G + 512)
    r.add_matrix("lru", w, C2_X + 512, C2_X + 768)
    r.add_matrix("lru", w, C2_G + 512, C2_G + 768)
    r.add_matrix("qkv", w, C2_QKV, C2_QKV + 2304)
    r.add_matrix("qm", w, C2_QM, C2_QM + 512)
    for half in range(2):
        for b, y in enumerate(("w_lru_out_2", "w_dil_out_2", "w_mem_out_2")):
            a = half * HALF
            r.add_matrix("merge2", w, C2_BR + b * D + a, C2_BR + b * D + a + HALF)
            r.add_matrix("merge2", T[y], a, a + HALF)
    r.add_matrix("out2", T["w_out_2"], 0, D)
    for u in range(8):
        r.add_matrix("mlp", T["w_mlp_in_2"], u * HALF, (u + 1) * HALF)
        r.add_matrix("mlp", T["w_mlp_out_2"][u * HALF:(u + 1) * HALF, :], 0, D)


def gain_of(K, name):
    return lambda t: K.vec(name, t)


def block2_stages(K):
    K.ylruT, K.odT, K.omT = K.at(32, 6, S), K.at(44, 2, S), K.at(48, 4, S)
    K.rg = K.at(92, 2, 6, P)
    K.qd, K.kd, K.vd, K.qm = K.at(56, 6, S), K.at(68, 6, S), K.at(80, 12, 256), K.at(92, 4, S)
    K.kmT, K.vm = K.at(100, 4, NCTX), K.at(104, 2, 512)
    K.hank0, K.hank1, K.hank2 = K.at(108, 4, 256), K.at(112, 4, P), K.at(114, 4, P)
    K.memT = K.at(56, KD, NCTX)
    K.lru_rate, K.flip, K.pick = K.at(151.5, 6), K.at(151, P), K.at(150, 256)[0:4]
    m2 = K.at(56, KD, S)
    return [
        lambda: load_memory_stage(K),
        lambda: norm_stage(K, [(K.memT, NCTX, K.memT, gain_of(K, "g_mem_2"), None),
                               (K.xT, S, K.hT, gain_of(K, "g_mix_2"), None)], 72),
        lambda: memory_project_stage(K),
        lambda: lru_weights_stage(K),
        lambda: lru_stage(K),
        lambda: dilated_project_stage(K),
        lambda: bias_stage(K),
        lambda: dilated_attention_stage(K),
        lambda: memory_attention_stage(K),
        lambda: merge_stage(K, "merge2", K.hT, [(K.ylruT, 6), (K.odT, 2), (K.omT, 4)], m2, "b_gate_2"),
        lambda: residual_stage(K, "out2", m2, None),
        lambda: norm_stage(K, [(K.xT, S, K.hT, gain_of(K, "g_mlp_2"), None)], 72),
        lambda: mlp_stage(K),
        lambda: norm_stage(K, [(K.xT, S, K.hT, gain_of(K, "g_final_2"), None)], 72),
        lambda: store_stage(K),
    ]


def block1_stages(K):
    K.yattT, K.yglaT = K.at(40, 8, S), K.at(56, 4, S)
    K.gv, K.gq, K.gk, K.ga, K.og = K.at(64, 6, 512), K.at(76, 2, S), K.at(80, 2, 768), K.at(86, 2, 768), K.at(92, 4, 512)
    K.qdec, K.kinv, K.kend, K.states = K.at(100, 4, S), K.at(108, 4, S), K.at(116, 6, 4, P), K.at(128, 4, 9, P)
    K.kT, K.v, K.qT = K.at(72, 2, S + NCTX), K.at(78, 6, 256), K.at(84, 8, S)
    K.yhyT, K.x2T, K.x1, K.z = (K.at(64 + 8 * i, 4, S) for i in range(4))
    K.Rf, K.If, K.edge, K.hid = K.at(128, 4, S), K.at(136, 4, S), K.at(144, S), K.at(146, S)[0:64]
    K.mT, K.acc = K.at(72, 8, S), K.at(40, 8, S)
    return [
        lambda: load_stage(K),
        lambda: mod_stage(K),
        lambda: norm_stage(K, [
            (K.xT, S, K.hT, lambda t: K.gain1[:, t:t + 1], lambda t: mod_col(K, 0, t)),
            (K.at(40, KD, NCTX), NCTX, K.hcT, lambda t: K.gain1c[:, t:t + 1], lambda t: mod_col(K, 0, t, 1))], 72),
        lambda: gla_project_stage(K),
        lambda: gla_decay_stage(K),
        lambda: gla_chunk_stage(K),
        lambda: qk_stage(K),
        lambda: latent_attention_stage(K),
        lambda: hyena_project_stage(K),
        lambda: hyena_hidden_stage(K),
        lambda: hyena_filter_stage(K, 0),
        lambda: hyena_conv_stage(K, 0),
        lambda: hyena_filter_stage(K, 1),
        lambda: hyena_conv_stage(K, 1),
        lambda: merge_stage(K, "merge1", K.hT, [(K.yhyT, 4), (K.yglaT, 4), (K.yattT, 8)], K.mT),
        lambda: residual_stage(K, "out1", K.mT, lambda t: mod_col(K, 2, t)),
        lambda: norm_stage(K, [(K.xT, S, K.hT, lambda t: K.gain2[:, t:t + 1], lambda t: mod_col(K, 3, t))], 72),
        lambda: router_stage(K),
        lambda: moe_stage(K),
    ]


def kernel(**inputs):
    import concourse.bacc as bacc
    from concourse.bass_utils import run_bass_kernel_spmd

    nc = bacc.Bacc("TRN2", target_bir_lowering=False, num_devices=1)
    arrays = layout(inputs)
    T = {k: nc.dram_tensor(k, v.shape, mybir.dt.from_np(v.dtype), kind="ExternalInput").ap() for k, v in arrays.items()}
    out = nc.dram_tensor("out", (D, S), F32, kind="ExternalOutput").ap()
    build(nc, T, out)
    r = run_bass_kernel_spmd(nc, [arrays], core_ids=[0])
    return np.ascontiguousarray(np.asarray(r.results[0]["out"]).T).reshape(1, S, D)
```

```python
from contextlib import ExitStack, contextmanager

import numpy as np

import concourse.bass as bass
from concourse import mybir
from concourse.alu_op_type import AluOpType as ALU

F32 = mybir.dt.float32
F32R = mybir.dt.float32r
ACT = mybir.ActivationFunctionType
AX = mybir.AxisListType

P = 128
D = 1024
KD = D // P
S = 512
NCTX = 256
ST = S // P
CT = NCTX // P
EPS = 1e-6
HALF = 512
RING = 6
NSIG = 20

VECS = [("c", 8), ("c_ctx", 8), ("b_mod", 48), ("norm1_g", 8), ("norm2_g", 8), ("q_norm_g", 1), ("k_norm_g", 1),
        ("gla_ba", 4), ("hy_conv_w", 36), ("hy_conv_b", 12),
        ("g_mix_2", 8), ("b_gate_2", 24), ("conv_w_2", 24), ("conv_b_2", 6), ("b_rg_a_2", 6), ("b_rg_x_2", 6),
        ("lru_lambda_2", 6), ("g_mem_2", 8), ("g_mlp_2", 8), ("g_final_2", 8)]
VEC_AT = {}
NVEC = 0
for _name, _n in VECS:
    VEC_AT[_name] = NVEC
    NVEC += _n

C_KV, C_GK, C_GV, C_GA = 0, 512, 768, 1280
C_Q, C_GQ, C_OG, C_HY, C_BR = 1312, 2336, 2592, 3104, 4640
C2_X, C2_G, C2_QKV, C2_QM, C2_BR = 0, 768, 1536, 3840, 4352
NEG = -1e30
ARENA_KB = 152
NEXP = 16
GE = 4
SLOTS = P


class Ring:

    def __init__(self, nc, ctx):
        self.slots = [ctx.enter_context(nc.sbuf_tensor(f"weights{i}", [P, 4 * HALF], F32)) for i in range(RING)]
        self.arrived = [ctx.enter_context(nc.semaphore(f"arrived{i}")) for i in range(RING)]
        self.used = ctx.enter_context(nc.semaphore("used"))
        self.plan = []
        self.issued = 0

    def add(self, name, ap):
        self.plan.append((name, ap))

    def add_matrix(self, name, w, c0, c1):
        rows = w.shape[0]
        for a in range(c0, c1, HALF):
            b = min(a + HALF, c1)
            for r in range(0, rows, HALF):
                q = min(HALF, rows - r)
                self.add(name, w[r:r + q, a:b].rearrange("(t p) c -> p t c", p=P))

    def first(self, name):
        return [n for n, _ in self.plan].index(name)

    def view(self, n):
        _, ap = self.plan[n]
        t, c = ap.shape[1], ap.shape[2]
        return self.slots[n % RING][:, 0:t * c].rearrange("p (t c) -> p t c", c=c)

    def arrival(self, n):
        return 16 * (n // RING + 1)

    def issue_until(self, sp, n):
        for k in range(self.issued, min(n, len(self.plan))):
            if k >= RING:
                sp.wait_ge(self.used, k - RING + 1)
            sp.dma_start(self.view(k), self.plan[k][1]).then_inc(self.arrived[k % RING], 16)
        self.issued = max(self.issued, min(n, len(self.plan)))


class Core:

    def __init__(self, nc, ctx, T):
        self.nc, self.T = nc, T
        self.ring = Ring(nc, ctx)
        self.base = ctx.enter_context(nc.sbuf_tensor("x_and_h", [P, 32 * 256], F32))
        self.phases = 0
        self.vecs = ctx.enter_context(nc.sbuf_tensor("vec_cols", [P, NVEC], F32))
        self.ident = ctx.enter_context(nc.sbuf_tensor("ident", [P, P], F32))
        self.ones = ctx.enter_context(nc.sbuf_tensor("ones", [P, P], F32))
        self.mods = ctx.enter_context(nc.sbuf_tensor("mods", [P, 96], F32))
        self.ps = ctx.enter_context(nc.psum_tensor("ps", [P, 8, 512], F32))
        self.banks = [[ctx.enter_context(nc.semaphore(f"sig{b}_{i}")) for i in range(NSIG)] for b in range(2)]
        self.loaded = ctx.enter_context(nc.semaphore("loaded"))
        self.load_base = 0
        self.stage = 0

    def loads(self, k):
        return self.load_base + 16 * k

    def signals(self, n):
        self.stage += 1
        self.idle = self.banks[(self.stage + 1) % 2]
        return self.banks[self.stage % 2][:n]

    def start(self, eng):
        if self.stage > 1:
            lo = min(s.num for s in self.idle)
            eng.sem_clear(range(lo, lo + NSIG))

    @contextmanager
    def phase(self, rounded_kb=0):
        self.phases += 1
        with ExitStack() as ctx:
            if rounded_kb:
                self.rounded = ctx.enter_context(
                    self.nc.sbuf_tensor(f"rounded{self.phases}", [P, rounded_kb * 256], F32R))
            self.low = 32 + rounded_kb
            self.arena = ctx.enter_context(
                self.nc.sbuf_tensor(f"arena{self.phases}", [P, (ARENA_KB - self.low) * 256], F32))
            yield

    @staticmethod
    def shaped(v, dims):
        if len(dims) == 2:
            v = v.rearrange("p (a b) -> p a b", b=dims[1])
        if len(dims) == 3:
            v = v.rearrange("p (a b c) -> p a b c", b=dims[1], c=dims[2])
        return v

    def at(self, kb, *dims):
        n = int(np.prod(dims))
        mem, size, low = (self.base, 32, 0) if kb < 32 else (self.arena, ARENA_KB - self.low, self.low)
        o = int((kb - low) * 256)
        assert 0 <= o and o + n <= size * 256, (kb, dims)
        return self.shaped(mem[:, o:o + n], dims)

    def rounded_at(self, kb, *dims):
        n, o = int(np.prod(dims)), int((kb - 32) * 256)
        assert 0 <= o and o + n <= (self.low - 32) * 256, (kb, dims)
        return self.shaped(self.rounded[:, o:o + n], dims)

    def vec(self, name, t=0):
        o = VEC_AT[name] + t
        return self.vecs[:, o:o + 1]




def accumulate(pe, out, pairs):
    for n, (l, r) in enumerate(pairs):
        last = pe.matmul(out, l, r, start=(n == 0), stop=(n == len(pairs) - 1))
    return last


def project(K, pe, n, col, m, x, tokens, out):
    for k in range(KD):
        w = K.ring.view(n + k // 4)
        ins = pe.matmul(out, w[:, k % 4, col:col + m], x[:, k, tokens], start=(k == 0), stop=(k == KD - 1))
    return ins


def arrived(K, pe, n, count=2):
    for k in range(n, n + count):
        pe.wait_ge(K.ring.arrived[k % RING], K.ring.arrival(k))


def release(K, pe, count=2):
    pe.matmul(K.ps[:, 7, 511:512], K.ones[:, :], K.ones[:, 0:1], start=True, stop=True).then_inc(K.ring.used, count)


def mod_stage(K):
    r, T = K.ring, K.T
    act_ready, rows_copied, turned, modded, loaded, ident_in, inputs_in = K.signals(7)
    n0 = r.first("mod")
    GROUPS, BODY = 12, 3
    sc, rows = K.sc, K.at(64, BODY, HALF)[0:2]
    cols = K.ps[:, 0, 0:96]
    w = T["w_mod"].rearrange("(h t p) c -> h p t c", h=2, p=P)
    with K.nc.Block() as block:
        @block.sync
        def _(sp):
            sp.dma_start(K.vecs[:, :], T["vecs"]).then_inc(loaded, 16)
            r.issue_until(sp, RING)
            sp.dma_start(K.ident[:, :], T["k_ident"]).then_inc(ident_in, 16)
            with sp.Fori(1, GROUPS // BODY) as i:
                for s in range(RING):
                    sp.wait_ge(r.used, i * RING + (n0 + s + 1 - RING))
                    sp.dma_start(r.slots[s][:, :].rearrange("p (t c) -> p t c", c=HALF),
                                 w[s % 2][:, :, bass.ds(i * BODY * HALF + (s // 2) * HALF, HALF)])\
                        .then_inc(r.arrived[s], 16)
            r.issued = n0 + 2 * GROUPS
            sp.dma_start(K.xT, T["xT"].rearrange("(t p) n -> p t n", p=P)).then_inc(inputs_in, 16)
            sp.dma_start(K.at(40, 8, NCTX), T["ctxT"].rearrange("(t p) n -> p t n", p=P)).then_inc(inputs_in, 16)
            r.issue_until(sp, n0 + 2 * GROUPS + RING)
            sp.wait_ge(inputs_in, 32)

        @block.scalar
        def _(act):
            act.wait_ge(loaded, 16)
            act.activation(sc[:, :, 0], K.vecs[:, VEC_AT["c"]:VEC_AT["c"] + 8], ACT.Silu).then_inc(act_ready, 1)
            act.activation(sc[:, :, 1], K.vecs[:, VEC_AT["c_ctx"]:VEC_AT["c_ctx"] + 8], ACT.Silu)\
                .then_inc(act_ready, 1)
            with act.Fori(0, GROUPS // BODY) as i:
                for g in range(BODY):
                    act.wait_ge(r.used, i * RING + (n0 + 2 * g + 2))
                    act.activation(rows[:, g, :], K.ps[0:2, 1 + g, :], ACT.Copy).then_inc(rows_copied, 1)

        @block.tensor
        def _(pe):
            pe.wait_ge(act_ready, 2)
            pe.wait_ge(ident_in, 16)
            with pe.Fori(0, GROUPS // BODY) as i:
                def turn(g):
                    pe.wait_ge(rows_copied, i * BODY + g + 1)
                    for c in range(4):
                        ins = pe.matmul(K.ps[:, 0, bass.ds((i * BODY + g) * 8 + 2 * c, 2)],
                                        rows[:, g, c * P:(c + 1) * P], K.ident[0:2, 0:2], start=True, stop=True)
                    ins.then_inc(turned, 1)

                for g in range(BODY):
                    for k in range(KD):
                        if k % 4 == 0:
                            pe.wait_ge(r.arrived[2 * g + k // 4], i * 16 + 16)
                        ins = pe.matmul(K.ps[0:2, 1 + g, :], sc[:, k, :],
                                        r.slots[2 * g + k // 4][:, (k % 4) * HALF:(k % 4 + 1) * HALF],
                                        start=(k == 0), stop=(k == KD - 1))
                        if k % 4 == 3:
                            ins.then_inc(r.used, 1)
                    if g == 1:
                        turn(0)
                turn(1)
                turn(2)

        @block.vector
        def _(dve):
            dve.memset(K.ones[:, :], 1.0).then_inc(modded, 1)
            dve.wait_ge(modded, 1)
            dve.wait_ge(loaded, 16)
            dve.wait_ge(turned, GROUPS)
            m = K.mods[:, :].rearrange("p (j b) -> p j b", b=2)
            pv = cols.rearrange("p (j b) -> p j b", b=2)
            bm = K.vecs[:, VEC_AT["b_mod"]:VEC_AT["b_mod"] + 48]
            for b in range(2):
                dve.tensor_tensor(m[:, :, b], pv[:, :, b], bm, ALU.add).then_inc(modded, 1)
            dve.wait_ge(modded, 3)
            g1 = K.vecs[:, VEC_AT["norm1_g"]:VEC_AT["norm1_g"] + 8]
            g2 = K.vecs[:, VEC_AT["norm2_g"]:VEC_AT["norm2_g"] + 8]
            dve.scalar_tensor_tensor(K.gain1, m[:, 8:16, 0], 1.0, g1, ALU.add, ALU.mult).then_inc(modded, 1)
            dve.scalar_tensor_tensor(K.gain1c, m[:, 8:16, 1], 1.0, g1, ALU.add, ALU.mult).then_inc(modded, 1)
            dve.scalar_tensor_tensor(K.gain2, m[:, 32:40, 0], 1.0, g2, ALU.add, ALU.mult).then_inc(modded, 1)
            dve.wait_ge(modded, 6)


def mod_col(K, part, t, b=0):
    o = 2 * (part * KD + t) + b
    return K.mods[:, o:o + 1]


def norm_stage(K, items, tmp):
    sq_done, sum_done, mean_done, rec_done, rstd_done, scaled, shifted, sq_used = K.signals(8)
    sq = K.at(tmp, 4, S)
    rec, rstd = K.at(tmp + 8, S), K.at(tmp + 10, S)
    with K.nc.Block() as block:
        @block.sync
        def _(sp):
            K.start(sp)

        @block.scalar
        def _(act):
            for j, (x, n, out, gain, shift) in enumerate(items):
                for t in range(KD):
                    a = j * KD + t
                    if a >= 4:
                        act.wait_ge(sq_used, a - 3)
                    act.activation(sq[:, a % 4, 0:n], x[:, t, :], ACT.Square).then_inc(sq_done, 1)
                act.wait_ge(rec_done, j + 1)
                act.activation(rstd[:, 0:n], rec[:, 0:n], ACT.Sqrt).then_inc(rstd_done, 1)
                if shift is not None:
                    for t in range(KD):
                        act.wait_ge(scaled, j * KD + t + 1)
                        act.activation(out[:, t, :], out[:, t, :], ACT.Identity, bias=shift(t)).then_inc(shifted, 1)
            if shift is not None:
                act.wait_ge(shifted, 1)

        @block.tensor
        def _(pe):
            for j, (x, n, out, gain, shift) in enumerate(items):
                if j >= 1:
                    pe.wait_ge(mean_done, j)
                for t in range(KD):
                    a = j * KD + t
                    pe.wait_ge(sq_done, a + 1)
                    pe.matmul(K.ps[:, 0, 0:n], K.ones[:, :], sq[:, a % 4, 0:n], start=(t == 0), stop=(t == KD - 1))\
                        .then_inc(sq_used, 1)

        @block.vector
        def _(dve):
            for j, (x, n, out, gain, shift) in enumerate(items):
                dve.wait_ge(sq_used, (j + 1) * KD)
                if j >= 1:
                    dve.wait_ge(scaled, j * KD)
                dve.tensor_scalar(rec[:, 0:n], K.ps[:, 0, 0:n], 1.0 / D, EPS, ALU.mult, ALU.add).then_inc(mean_done, 1)
                dve.wait_ge(mean_done, j + 1)
                dve.reciprocal(rec[:, 0:n], rec[:, 0:n]).then_inc(rec_done, 1)
                dve.wait_ge(rstd_done, j + 1)
                for t in range(KD):
                    dve.scalar_tensor_tensor(out[:, t, :], x[:, t, :], gain(t), rstd[:, 0:n], ALU.mult, ALU.mult)\
                        .then_inc(scaled, 1)
            dve.wait_ge(scaled, len(items) * KD)


def qk_stage(K):
    r, T = K.ring, K.T
    (raw_done, sq_done, ss_done, mean_done, rec_done, rstd_done, qn_done, swap_done, t1_done, t2_done, out_done,
     v_done, v_copied) = K.signals(13)
    sq, rec, rstd, qn, t1, t2 = (K.at(100 + 4 * i, 2, S) for i in range(6))
    cos, sin, swap = K.at(124, S), K.at(126, S), K.at(128, P)
    n0 = r.first("kv")
    items = []
    for h in range(2):
        items.append((n0, h * P, K.hT, S, "k_norm_g", True, K.kT[:, h, 0:S]))
        items.append((n0, h * P, K.hcT, NCTX, "k_norm_g", False, K.kT[:, h, S:S + NCTX]))
    for h in range(8):
        items.append((n0 + 2 + 2 * (h // 4), (h % 4) * P, K.hT, S, "q_norm_g", True, K.qT[:, h, :]))
    NI = len(items)
    rope_no = [sum(1 for it in items[:j] if it[5]) for j in range(NI + 1)]
    with K.nc.Block() as block:
        @block.gpsimd
        def _(pool):
            pool.dma_start(cos, T["k_cos"]).then_inc(K.loaded, 16)
            pool.dma_start(sin, T["k_sin"]).then_inc(K.loaded, 16)
            pool.dma_start(swap, T["k_swap"]).then_inc(K.loaded, 16)

        @block.sync
        def _(sp):
            K.start(sp)
            r.issue_until(sp, n0 + 6 + RING)

        @block.tensor
        def _(pe):
            def raw(j):
                n, col, x, ntok, *_ = items[j]
                if j == 0 or items[j - 1][0] != n:
                    arrived(K, pe, n)
                if j >= 3:
                    pe.wait_ge(qn_done, j - 2)
                project(K, pe, n, col, P, x, slice(0, ntok), K.ps[:, j % 3, 0:ntok]).then_inc(raw_done, 1)
                if n != n0 and col == 3 * P:
                    release(K, pe)

            def values():
                for t in range(ST + CT):
                    x, o = (K.hT, t * P) if t < ST else (K.hcT, (t - ST) * P)
                    if t >= 2:
                        pe.wait_ge(v_copied, t - 1)
                    accumulate(pe, K.ps[:, 5 + t % 2, 0:256],
                               [(x[:, k, o:o + P], r.view(n0 + k // 4)[:, k % 4, 256:512]) for k in range(KD)])\
                        .then_inc(v_done, 1)
                release(K, pe)

            def square_sum(j):
                ntok = items[j][3]
                pe.wait_ge(sq_done, j + 1)
                if j >= 1:
                    pe.wait_ge(mean_done, j)
                pe.matmul(K.ps[:, 3, 0:ntok], K.ones[:, :], sq[:, j % 2, 0:ntok], start=True, stop=True)\
                    .then_inc(ss_done, 1)

            def swapped(j):
                if items[j][5]:
                    pe.wait_ge(qn_done, j + 1)
                    if rope_no[j] >= 1:
                        pe.wait_ge(t2_done, rope_no[j])
                    else:
                        pe.wait_ge(K.loaded, K.loads(3))
                    pe.matmul(K.ps[:, 4, :], swap, qn[:, j % 2, :], start=True, stop=True).then_inc(swap_done, 1)

            for j in range(NI + 2):
                if j < NI:
                    raw(j)
                if j == 3:
                    values()
                if 1 <= j <= NI:
                    square_sum(j - 1)
                if j >= 2:
                    swapped(j - 2)

        @block.scalar
        def _(act):
            def copy_v(t):
                act.wait_ge(v_done, t + 1)
                act.activation(K.v[:, t, :], K.ps[:, 5 + t % 2, 0:256], ACT.Copy).then_inc(v_copied, 1)

            for j in range(NI + 1):
                if j < NI:
                    ntok = items[j][3]
                    act.wait_ge(raw_done, j + 1)
                    if j >= 2:
                        act.wait_ge(ss_done, j - 1)
                    act.activation(sq[:, j % 2, 0:ntok], K.ps[:, j % 3, 0:ntok], ACT.Square).then_inc(sq_done, 1)
                if j == 3:
                    for t in range(ST + CT):
                        copy_v(t)
                if j >= 1:
                    ntok = items[j - 1][3]
                    act.wait_ge(rec_done, j)
                    if j >= 3:
                        act.wait_ge(qn_done, j - 2)
                    act.activation(rstd[:, (j - 1) % 2, 0:ntok], rec[:, (j - 1) % 2, 0:ntok], ACT.Sqrt)\
                        .then_inc(rstd_done, 1)

        @block.vector
        def _(dve):
            def invert(j):
                ntok = items[j][3]
                m = rec[:, j % 2, 0:ntok]
                dve.wait_ge(ss_done, j + 1)
                if j >= 2:
                    dve.wait_ge(rstd_done, j - 1)
                dve.tensor_scalar(m, K.ps[:, 3, 0:ntok], 1.0 / P, EPS, ALU.mult, ALU.add).then_inc(mean_done, 1)
                dve.wait_ge(mean_done, j + 1)
                dve.reciprocal(m, m).then_inc(rec_done, 1)

            def norm(j):
                _, _, _, ntok, gain, rotary, dest = items[j]
                out = qn[:, j % 2, :] if rotary else dest
                dve.wait_ge(rstd_done, j + 1)
                if j >= 2:
                    dve.wait_ge(swap_done, rope_no[j - 1])
                dve.scalar_tensor_tensor(out, K.ps[:, j % 3, 0:ntok], K.vec(gain), rstd[:, j % 2, 0:ntok],
                                         ALU.mult, ALU.mult).then_inc(qn_done, 1)

            def rotate(j):
                rotary, dest = items[j][5:7]
                if rotary:
                    q = rope_no[j]
                    dve.wait_ge(qn_done, j + 1)
                    dve.wait_ge(K.loaded, K.loads(3))
                    dve.tensor_tensor(t1[:, q % 2, :], qn[:, j % 2, :], cos, ALU.mult).then_inc(t1_done, 1)
                    dve.wait_ge(swap_done, q + 1)
                    dve.tensor_tensor(t2[:, q % 2, :], K.ps[:, 4, :], sin, ALU.mult).then_inc(t2_done, 1)
                    dve.wait_ge(t1_done, q + 1)
                    dve.wait_ge(t2_done, q + 1)
                    dve.tensor_tensor(dest, t1[:, q % 2, :], t2[:, q % 2, :], ALU.add).then_inc(out_done, 1)

            for j in range(NI + 1):
                if j < NI:
                    invert(j)
                    norm(j)
                if j >= 1:
                    rotate(j - 1)
            dve.wait_ge(out_done, rope_no[NI])
    K.load_base = K.loads(3)


def items_stage(K, items, banks=(0, 1, 2, 3), loads=(), issue=None):
    r = K.ring
    mm_done, act_out, dve_out = K.signals(3)
    count = {"act": 0, "dve": 0}
    emptied = []
    for it in items:
        count[it["eng"]] += 1
        emptied.append((act_out if it["eng"] == "act" else dve_out, count[it["eng"]]))
    last = {e: max([n for n, it in enumerate(items) if it["eng"] == e], default=None) for e in count}
    NB = len(banks)
    with K.nc.Block() as block:
        @block.gpsimd
        def _(pool):
            for dst, src in loads:
                pool.dma_start(dst, src).then_inc(K.loaded, 16)
            if loads:
                pool.wait_ge(K.loaded, K.loads(len(loads)))

        @block.sync
        def _(sp):
            K.start(sp)
            if issue is not None:
                r.issue_until(sp, issue + RING)

        @block.tensor
        def _(pe):
            if loads:
                pe.wait_ge(K.loaded, K.loads(len(loads)))
            for j, it in enumerate(items):
                for n in it.get("first", ()):
                    arrived(K, pe, n, 1)
                if it.get("after"):
                    for e in ("act", "dve"):
                        v = sum(1 for x in items[:it["after"]] if x["eng"] == e)
                        if v:
                            pe.wait_ge(act_out if e == "act" else dve_out, v)
                if j >= NB:
                    pe.wait_ge(*emptied[j - NB])
                it["mm"](pe, K.ps[:, banks[j % NB], :]).then_inc(mm_done, 1)
                if it.get("rel"):
                    release(K, pe, it["rel"])

        def emptier(e, eng, sem):
            if loads:
                eng.wait_ge(K.loaded, K.loads(len(loads)))
            for j, it in enumerate(items):
                if it["eng"] == e:
                    eng.wait_ge(mm_done, j + 1)
                    it["out"](eng, K.ps[:, banks[j % NB], :]).then_inc(sem, 1)

        @block.scalar
        def _(act):
            emptier("act", act, act_out)

        @block.vector
        def _(dve):
            emptier("dve", dve, dve_out)
    K.load_base = K.loads(len(loads))


def channel_item(K, n, col, m, x, ntok, dest, eng="act", func=ACT.Copy, first=(), rel=0, pairs=None, **kw):
    def mm(pe, bank):
        if pairs is not None:
            return accumulate(pe, bank[0:m, 0:ntok], pairs)
        return project(K, pe, n, col, m, x, slice(0, ntok), bank[0:m, 0:ntok])

    def out(e, bank):
        if eng == "act":
            return e.activation(dest, bank[0:m, 0:ntok], func, **kw)
        return e.tensor_copy(dest, bank[0:m, 0:ntok])
    return {"first": first, "mm": mm, "rel": rel, "eng": eng, "out": out}


def token_item(K, n, c0, c1, x, tok, dest, eng="act", func=ACT.Copy, first=(), rel=0, **kw):
    def mm(pe, bank):
        return accumulate(pe, bank[:, 0:c1 - c0],
                          [(x[:, k, tok], K.ring.view(n + k // 4)[:, k % 4, c0:c1]) for k in range(KD)])

    def out(e, bank):
        if eng == "act":
            return e.activation(dest, bank[:, 0:c1 - c0], func, **kw)
        return e.tensor_copy(dest, bank[:, 0:c1 - c0])
    return {"first": first, "mm": mm, "rel": rel, "eng": eng, "out": out}


def gla_project_stage(K):
    r = K.ring
    n = r.first("gk")
    items = []
    for t in range(2):
        items.append(channel_item(K, n, t * P, P, K.hT, S, K.gk[:, t, 0:S], first=(n, n + 1) if t == 0 else ()))
        items.append(channel_item(K, n, t * P, P, K.hcT, NCTX, K.gk[:, t, S:S + NCTX], eng="dve",
                                  rel=2 if t == 1 else 0))
    n += 2
    for t in range(6):
        x, o = (K.hT, t * P) if t < ST else (K.hcT, (t - ST) * P)
        items.append(token_item(K, n, 0, 512, x, slice(o, o + P), K.gv[:, t, :], eng=("act", "dve")[t % 2],
                                first=(n, n + 1) if t == 0 else (), rel=2 if t == 5 else 0))
    n += 2
    for d in range(2):
        items.append(channel_item(K, n, 16 * d, 16, K.hT, S, K.ga[0:16, d, 0:S], first=(n, n + 1) if d == 0 else ()))
        items.append(channel_item(K, n, 16 * d, 16, K.hcT, NCTX, K.ga[0:16, d, S:S + NCTX], eng="dve",
                                  rel=2 if d == 1 else 0))
    n += 2
    for t in range(2):
        items.append(channel_item(K, n, t * P, P, K.hT, S, K.gq[:, t, :], func=ACT.Copy, scale=0.125,
                                  first=(n, n + 1) if t == 0 else (), rel=2 if t == 1 else 0))
    n += 2
    for t in range(ST):
        items.append(token_item(K, n, 0, 512, K.hT, slice(t * P, t * P + P), K.og[:, t, :], func=ACT.Silu,
                                first=(n, n + 1) if t == 0 else (), rel=2 if t == 3 else 0))
    items_stage(K, items, issue=n + 2)


def gla_decay_stage(K):
    T = K.T
    L = S + NCTX
    *chains, z_done, kend_done, turned, copied = K.signals(6)
    scratch = [[K.at(kb + 3 * i, L) for i in range(5)] + [K.at(x, L)] for kb, x in ((40, 146), (131, 56))]
    wa2, mask = K.at(149, 2, 256)[0:16], K.at(128, L)
    STEPS = 13
    kd = [0]

    with K.nc.Block() as block:
        @block.gpsimd
        def _(pool):
            pool.dma_start(wa2, T["gla_wa2"].rearrange("d r c -> r d c")).then_inc(K.loaded, 16)
            pool.dma_start(mask, T["k_scan"]).then_inc(K.loaded, 16)

        @block.sync
        def _(sp):
            K.start(sp)

        def z_of(u):
            return K.ps[:, 2 * (u % 2):2 * (u % 2) + 2, :].rearrange("p b n -> p (b n)")[:, 0:L]

        def turn(pe, u):
            X = scratch[u % 2][5]
            pe.wait_ge(chains[u % 2], (u // 2 + 1) * STEPS)
            if u >= 1:
                pe.wait_ge(copied, u)
            for t in range(6):
                ins = pe.transpose(K.ps[:, 4 + t // 4, (t % 4) * P:(t % 4 + 1) * P], X[:, t * P:(t + 1) * P],
                                   K.ident[:, :])
            ins.then_inc(turned, 1)

        @block.tensor
        def _(pe):
            pe.wait_ge(K.loaded, K.loads(2))
            for u in range(4):
                d, p = u // 2, u % 2
                w = wa2[:, d, p * P:(p + 1) * P]
                if u >= 2:
                    pe.wait_ge(chains[u % 2], 4)
                pe.matmul(K.ps[:, 2 * (u % 2), :], w, K.ga[0:16, d, 0:S], start=True, stop=True)
                pe.matmul(K.ps[:, 2 * (u % 2) + 1, 0:NCTX], w, K.ga[0:16, d, S:L], start=True, stop=True)\
                    .then_inc(z_done, 1)
                if u == 3:
                    turn(pe, 0)
                    turn(pe, 1)
            turn(pe, 2)
            turn(pe, 3)

        @block.scalar
        def _(act):
            def step(u, j, out, in_, func, **kw):
                act.wait_ge(chains[u % 2], u // 2 * STEPS + j)
                act.activation(out, in_, func, **kw).then_inc(chains[u % 2], 1)

            A, B, C, E, F, X = zip(*scratch)
            for pair in (0, 2):
                both = (pair, pair + 1)
                act.wait_ge(z_done, pair + 2)
                for u in both:
                    step(u, 0, A[u % 2], z_of(u), ACT.Abs, bias=K.vec("gla_ba", u))
                for u in both:
                    step(u, 1, A[u % 2], A[u % 2], ACT.Exp, scale=-1.0)
                for u in both:
                    step(u, 2, A[u % 2], A[u % 2], ACT.Ln, bias=1.0)
                for u in both:
                    step(u, 7, A[u % 2][:, 0:S], E[u % 2][:, 0:S], ACT.Exp, scale=1 / 16)
                    step(u, 8, B[u % 2][:, 0:S], E[u % 2][:, 0:S], ACT.Exp, scale=-1 / 16)
                    step(u, 9, F[u % 2], F[u % 2], ACT.Exp, scale=1 / 16)
                for u in both:
                    act.wait_ge(turned, u + 1)
                    for t in range(2):
                        n = 4 if t == 0 else 2
                        ins = act.activation(K.kend[:, 4 * t:4 * t + n, u, :],
                                             K.ps[:, 4 + t, 0:n * P].rearrange("p (t c) -> p t c", c=P), ACT.Copy)
                    ins.then_inc(copied, 1)

        @block.vector
        def _(dve):
            def step(u, j, f):
                dve.wait_ge(chains[u % 2], u // 2 * STEPS + j)
                f().then_inc(chains[u % 2], 1)

            def sums(u):
                d, (A, B, C, E, F, X) = u // 2, scratch[u % 2]
                step(u, 3, lambda: dve.tensor_scalar(B, z_of(u), K.vec("gla_ba", u), 0.0, ALU.add, ALU.min))
                step(u, 4, lambda: dve.tensor_tensor(C, B, A, ALU.subtract))
                step(u, 5, lambda: dve.tensor_tensor_scan(E, mask, C, 0.0, ALU.mult, ALU.add))
                dve.wait_ge(chains[u % 2], u // 2 * STEPS + 6)
                dve.tensor_copy(K.tot[:, u, 0:8], E[:, 0:S].rearrange("p (c t) -> p c t", t=64)[:, :, 63])\
                    .then_inc(kend_done, 1)
                dve.tensor_copy(K.tot[:, u, 8:9], E[:, L - 1:L]).then_inc(kend_done, 1)
                n = kd[0] = kd[0] + 2
                dve.wait_ge(kend_done, n)
                tl, tc = K.tot[:, u, 0:8].unsqueeze(2).broadcast_to([P, 8, 64]), K.tot[:, u, 8:9].broadcast_to([P, NCTX])
                if d == 1:
                    dve.tensor_tensor(E, C, E, ALU.subtract).then_inc(kend_done, 1)
                    dve.wait_ge(kend_done, n + 1)
                    dve.tensor_tensor(c64(E), c64(E), tl, ALU.add).then_inc(kend_done, 1)
                    dve.tensor_tensor(E[:, S:L], E[:, S:L], tc, ALU.add).then_inc(kend_done, 1)
                    dve.wait_ge(kend_done, n + 3)
                    kd[0] = n + 3
                dve.tensor_tensor(c64(F), tl, c64(E), ALU.subtract).then_inc(kend_done, 1)
                kd[0] += 1
                dve.wait_ge(kend_done, kd[0])
                step(u, 6, lambda: dve.tensor_tensor(F[:, S:L], tc, E[:, S:L], ALU.subtract))

            def scale(u):
                p, (A, B, C, E, F, X) = u % 2, scratch[u % 2]
                step(u, 10, lambda: dve.tensor_tensor(K.qdec[:, u, :], K.gq[:, p, :], A[:, 0:S], ALU.mult))
                step(u, 11, lambda: dve.tensor_tensor(K.kinv[:, u, :], K.gk[:, p, 0:S], B[:, 0:S], ALU.mult))
                if u >= 2:
                    dve.wait_ge(turned, u - 1)
                step(u, 12, lambda: dve.tensor_tensor(X, K.gk[:, p, :], F, ALU.mult))

            dve.wait_ge(K.loaded, K.loads(2))
            for pair in (0, 2):
                for stage in (sums, scale):
                    for u in (pair, pair + 1):
                        stage(u)

        @block.scalar
        def _(act):
            for c in chains:
                act.wait_ge(c, 2 * STEPS)
            act.activation(K.tot[:, :, :], K.tot[:, :, :], ACT.Exp, scale=1 / 16).then_inc(copied, 1)
            act.wait_ge(copied, 5)
    K.load_base = K.loads(2)


def c64(v):
    return v[:, 0:S].rearrange("p (c t) -> p c t", t=64)


def gla_chunk_stage(K):
    T = K.T
    (cs_done, st_done, att_done, masked, o_done, sq_done, mean_done, rec_done, rstd_done, y_done, turned,
     copied, init_done) = K.signals(13)
    NC = S // 64
    masks = K.at(40, 2, P)
    gain = K.at(41, P)
    att = K.at(42, 2, 2, P)
    ysq = K.at(44, 2, P)
    o_sb = K.at(45, 2, 512)
    stats = K.at(49, 3, 16)
    states = K.states
    with K.nc.Block() as block:
        @block.gpsimd
        def _(pool):
            pool.dma_start(masks, T["k_causal"].rearrange("d s q -> s d q")).then_inc(K.loaded, 16)
            pool.dma_start(gain, T["gla_norm_g"].broadcast_to([P, P])).then_inc(K.loaded, 16)

        @block.sync
        def _(sp):
            K.start(sp)

        def order(d, c):
            return c if d == 0 else NC - 1 - c

        @block.tensor
        def _(pe):
            for u in range(4):
                d, p = u // 2, u % 2
                b = 3 * (u % 2)
                if u >= 2:
                    pe.wait_ge(st_done, (u - 1) * NC)
                for h in range(2):
                    rows = slice(64 * h, 64 * h + 64)
                    hv = slice((2 * p + h) * P, (2 * p + h + 1) * P)
                    accumulate(pe, K.ps[rows, b + 2, 0:P],
                               [(K.kend[:, 4 + t, u, rows], K.gv[:, 4 + t, hv]) for t in range(2)])
                    for c in range(NC):
                        toks = slice(64 * (c % 2), 64 * (c % 2) + 64)
                        ins = pe.matmul(K.ps[rows, b + c % 2, (c // 2) * P:(c // 2 + 1) * P],
                                        K.kend[toks, c // 2, u, rows], K.gv[toks, c // 2, hv], start=True, stop=True)
                ins.then_inc(cs_done, 1)

            def scores(a):
                t, h = a // 4, a % 4
                rows, toks = slice(64 * (h % 2), 64 * (h % 2) + 64), slice(t * P, (t + 1) * P)
                if a >= 2:
                    pe.wait_ge(masked, a - 1)
                else:
                    pe.wait_ge(st_done, 4 * NC)
                for d in range(2):
                    u = 2 * d + h // 2
                    ins = pe.matmul(K.ps[:, a % 2, d * P:(d + 1) * P], K.kinv[rows, u, toks], K.qdec[rows, u, toks],
                                    start=True, stop=True)
                ins.then_inc(att_done, 1)

            def outputs(a):
                t, h = a // 4, a % 4
                rows, toks = slice(64 * (h % 2), 64 * (h % 2) + 64), slice(t * P, (t + 1) * P)
                hv = slice(h * P, (h + 1) * P)
                pe.wait_ge(masked, a + 1)
                if a >= 2:
                    pe.wait_ge(y_done, a - 1)
                out = K.ps[:, 2 + a % 2, 0:P]
                for d in range(2):
                    pe.matmul(out, att[:, a % 2, d, :], K.gv[:, t, hv], start=(d == 0), stop=False)
                for d in range(2):
                    u = 2 * d + h // 2
                    for j in range(2):
                        c = 2 * t + j
                        before = c if d == 0 else NC - 1 - c
                        ins = pe.matmul(K.ps[64 * j:64 * j + 64, 2 + a % 2, 0:P], K.qdec[rows, u, 64 * c:64 * c + 64],
                                        states[rows, u, before, :], start=False, stop=(d == 1))
                ins.then_inc(o_done, 1)

            for a in range(17):
                if a < 16:
                    scores(a)
                if a >= 1:
                    outputs(a - 1)
            for a in range(16):
                t, h = a // 4, a % 4
                if h == 0:
                    pe.wait_ge(y_done, a + 4)
                    if t >= 2:
                        pe.wait_ge(copied, t - 1)
                ins = pe.transpose(K.ps[:, 4 + t % 2, h * P:(h + 1) * P], K.og[:, t, h * P:(h + 1) * P], K.ident[:, :])
                if h == 3:
                    ins.then_inc(turned, 1)

        @block.scalar
        def _(act):
            for a in range(16):
                act.wait_ge(o_done, a + 1)
                act.activation(ysq[:, a % 2, :], K.ps[:, 2 + a % 2, 0:P], ACT.Square, accum_out=stats[:, 0, a:a + 1])\
                    .then_inc(sq_done, 1)
                act.wait_ge(rec_done, a + 1)
                act.activation(stats[:, 2, a:a + 1], stats[:, 1, a:a + 1], ACT.Sqrt).then_inc(rstd_done, 1)
            for t in range(ST):
                act.wait_ge(turned, t + 1)
                act.activation(K.yglaT[:, :, t * P:(t + 1) * P],
                               K.ps[:, 4 + t % 2, :].rearrange("p (h c) -> p h c", c=P), ACT.Copy).then_inc(copied, 1)
            act.wait_ge(copied, ST)

        @block.vector
        def _(dve):
            for u in range(4):
                d = u // 2
                b = 3 * (u % 2)
                dve.wait_ge(cs_done, u + 1)
                dve.tensor_copy(states[:, u, 0, :], K.ps[:, b + 2, 0:P]).then_inc(init_done, 1)
                dve.wait_ge(init_done, u + 1)
                for s in range(NC):
                    c = order(d, s)
                    if s < NC - 1:
                        dve.scalar_tensor_tensor(states[:, u, s + 1, :], states[:, u, s, :], K.tot[:, u, c:c + 1],
                                                 K.ps[:, b + c % 2, (c // 2) * P:(c // 2 + 1) * P], ALU.mult, ALU.add)\
                            .then_inc(st_done, 1)
                        dve.wait_ge(st_done, u * NC + s + 1)
                    else:
                        dve.tensor_copy(stats[:, 0, 0:1], K.tot[:, u, 0:1]).then_inc(st_done, 1)
            dve.wait_ge(K.loaded, K.loads(2))

            def mask(a):
                dve.wait_ge(att_done, a + 1)
                if a >= 2:
                    dve.wait_ge(o_done, a - 1)
                dve.tensor_tensor(att[:, a % 2, :, :], K.ps[:, a % 2, 0:2 * P].rearrange("p (d q) -> p d q", q=P),
                                  masks, ALU.mult).then_inc(masked, 1)

            mask(0)
            for a in range(16):
                t, h = a // 4, a % 4
                if a + 1 < 16:
                    mask(a + 1)
                dve.wait_ge(sq_done, a + 1)
                dve.tensor_scalar(stats[:, 1, a:a + 1], stats[:, 0, a:a + 1], 1.0 / P, EPS, ALU.mult, ALU.add)\
                    .then_inc(mean_done, 1)
                dve.wait_ge(mean_done, 2 * a + 1)
                dve.reciprocal(stats[:, 1, a:a + 1], stats[:, 1, a:a + 1]).then_inc(rec_done, 1)
                dve.wait_ge(rstd_done, a + 1)
                o = o_sb[:, a % 2, 0:P]
                dve.scalar_tensor_tensor(o, K.ps[:, 2 + a % 2, 0:P], stats[:, 2, a:a + 1], gain, ALU.mult, ALU.mult)\
                    .then_inc(mean_done, 1)
                dve.wait_ge(mean_done, 2 * a + 2)
                og = K.og[:, t, h * P:(h + 1) * P]
                dve.tensor_tensor(og, o, og, ALU.mult).then_inc(y_done, 1)
    K.load_base = K.loads(2)


def attention_stage(K, heads, nk, scores, values, dest, scale, tmp):
    s_done, max_done, bias_done, exp_done, rec_done, normed, turned, copied, o_done, o_copied = K.signals(10)
    NB, NJ = heads * ST, nk // P
    Pb = K.at(tmp, 3, nk)
    PT = K.at(tmp + 3 * nk / 256, 2, NJ, S)
    st = K.at(tmp + 3 * nk / 256 + 2 * NJ * 2, 4, NB)
    with K.nc.Block() as block:
        @block.sync
        def _(sp):
            K.start(sp)

        def sbank(a):
            return K.ps[:, 2 * (a % 2):2 * (a % 2) + 2, :].rearrange("p b n -> p (b n)")[:, 0:nk]

        def tbank():
            return K.ps[:, 4:6, :].rearrange("p b n -> p (b n)")[:, 0:nk].rearrange("p (j q) -> p j q", q=P)

        @block.tensor
        def _(pe):
            for a in range(NB + 3):
                if a < NB:
                    if a >= 2:
                        pe.wait_ge(exp_done, a - 1)
                    for cols, l, r in scores(a // ST, a % ST):
                        ins = pe.matmul(sbank(a)[:, cols], l, r, start=True, stop=True)
                    ins.then_inc(s_done, 1)
                b = a - 2
                if 0 <= b < NB:
                    pe.wait_ge(normed, b + 1)
                    if b >= 1:
                        pe.wait_ge(copied, b)
                    for j in range(NJ):
                        ins = pe.transpose(tbank()[:, j, :], Pb[:, b % 3, j * P:(j + 1) * P], K.ident[:, :])
                    ins.then_inc(turned, 1)
                b = a - 3
                if b >= 0 and b % ST == ST - 1:
                    h = b // ST
                    pe.wait_ge(copied, b + 1)
                    if h >= 1:
                        pe.wait_ge(o_copied, h)
                    accumulate(pe, K.ps[:, 6, :], [(values(h, j), PT[:, h % 2, j, :]) for j in range(NJ)])\
                        .then_inc(o_done, 1)

        @block.scalar
        def _(act):
            for a in range(NB + 3):
                if a < NB:
                    act.wait_ge(bias_done, a + 1)
                    if a >= 3:
                        act.wait_ge(turned, a - 2)
                    act.activation(Pb[:, a % 3, :], sbank(a), ACT.Exp, bias=st[:, 1, a:a + 1], scale=scale,
                                   accum_out=st[:, 2, a:a + 1]).then_inc(exp_done, 1)
                b = a - 3
                if b >= 0 and b % ST == ST - 1:
                    h = b // ST
                    act.wait_ge(o_done, h + 1)
                    act.activation(dest(h), K.ps[:, 6, :], ACT.Copy).then_inc(o_copied, 1)
            act.wait_ge(o_copied, heads)

        @block.vector
        def _(dve):
            for a in range(NB + 2):
                if a < NB:
                    dve.wait_ge(s_done, a + 1)
                    dve.tensor_reduce(st[:, 0, a:a + 1], sbank(a), AX.X, ALU.max).then_inc(max_done, 1)
                    dve.wait_ge(max_done, a + 1)
                    dve.tensor_scalar(st[:, 1, a:a + 1], st[:, 0, a:a + 1], -scale, None, ALU.mult)\
                        .then_inc(bias_done, 1)
                b = a - 1
                if 0 <= b < NB:
                    dve.wait_ge(exp_done, b + 1)
                    dve.reciprocal(st[:, 3, b:b + 1], st[:, 2, b:b + 1]).then_inc(rec_done, 1)
                    dve.wait_ge(rec_done, b + 1)
                    dve.tensor_scalar(Pb[:, b % 3, :], Pb[:, b % 3, :], st[:, 3, b:b + 1], None, ALU.mult)\
                        .then_inc(normed, 1)
                b = a - 2
                if b >= 0:
                    dve.wait_ge(turned, b + 1)
                    h = b // ST
                    if h >= 2:
                        dve.wait_ge(o_done, h - 1)
                    dve.tensor_copy(PT[:, h % 2, :, (b % ST) * P:(b % ST + 1) * P], tbank()).then_inc(copied, 1)


def latent_attention_stage(K):
    def scores(h, i):
        q = K.qT[:, h, i * P:(i + 1) * P]
        return [(slice(0, S), q, K.kT[:, h // 4, 0:S]), (slice(S, S + NCTX), q, K.kT[:, h // 4, S:S + NCTX])]

    attention_stage(K, 8, S + NCTX, scores, lambda h, j: K.v[:, j, (h // 4) * P:(h // 4 + 1) * P],
                    lambda h: K.yattT[:, h, :], P ** -0.5, 100)


TWO_PI = 2.0 * np.pi
ROUND = 1.5 * 2.0 ** 23
PI_HI = 6.28125
PI_LO = TWO_PI - PI_HI
SIN_MAX = 3.1415925


def hyena_project_stage(K):
    r = K.ring
    mm_done, mid_done, left_done, conv_done, turned, copied = K.signals(6)
    n0 = r.first("hy")
    NT = 12
    ys = K.at(96, 4, S)
    turn_no = [t if t < 4 else t - 4 for t in range(NT)]

    def y_of(t):
        return K.x2T[:, t - 4, :] if 4 <= t < 8 else ys[:, turn_no[t] % 4, :]

    with K.nc.Block() as block:
        @block.sync
        def _(sp):
            K.start(sp)
            r.issue_until(sp, n0 + 6 + RING)

        @block.tensor
        def _(pe):
            def turn(t):
                if 4 <= t < 8:
                    return
                q = turn_no[t]
                pe.wait_ge(conv_done, t + 1)
                if q >= 2:
                    pe.wait_ge(copied, q - 1)
                for tt in range(ST):
                    ins = pe.transpose(K.ps[:, 4 + q % 2, tt * P:(tt + 1) * P], y_of(t)[:, tt * P:(tt + 1) * P],
                                       K.ident[:, :])
                ins.then_inc(turned, 1)

            for t in range(NT):
                n = n0 + 2 * (t // 4)
                if t % 4 == 0:
                    arrived(K, pe, n)
                if t >= 4:
                    pe.wait_ge(conv_done, t - 3)
                project(K, pe, n, (t % 4) * P, P, K.hT, slice(0, S), K.ps[:, t % 4, :]).then_inc(mm_done, 1)
                if t % 4 == 3:
                    release(K, pe)
                if t >= 2:
                    turn(t - 2)
            turn(NT - 2)
            turn(NT - 1)

        @block.scalar
        def _(act):
            def copy(t):
                if 4 <= t < 8:
                    return
                q = turn_no[t]
                dest = K.x1 if t < 4 else K.z
                act.wait_ge(turned, q + 1)
                act.activation(dest[:, :, (t % 4) * P:(t % 4 + 1) * P],
                               K.ps[:, 4 + q % 2, :].rearrange("p (t c) -> p t c", c=P), ACT.Copy).then_inc(copied, 1)

            for t in range(NT):
                act.wait_ge(mm_done, t + 1)
                q = turn_no[t]
                if not 4 <= t < 8 and q >= 4:
                    act.wait_ge(turned, q - 3)
                act.activation(y_of(t), K.ps[:, t % 4, :], ACT.Identity, bias=K.vec("hy_conv_b", t),
                               scale=K.vec("hy_conv_w", NT + t)).then_inc(mid_done, 1)
                if t >= 3:
                    copy(t - 3)
            for t in range(NT - 3, NT):
                copy(t)
            act.wait_ge(copied, 8)

        @block.vector
        def _(dve):
            for t in range(NT):
                y, u = y_of(t), K.ps[:, t % 4, :]
                dve.wait_ge(mid_done, t + 1)
                dve.scalar_tensor_tensor(y[:, 1:S], u[:, 0:S - 1], K.vec("hy_conv_w", t), y[:, 1:S], ALU.mult, ALU.add)\
                    .then_inc(left_done, 1)
                dve.wait_ge(left_done, t + 1)
                dve.scalar_tensor_tensor(y[:, 0:S - 1], u[:, 1:S], K.vec("hy_conv_w", 2 * NT + t), y[:, 0:S - 1],
                                         ALU.mult, ALU.add).then_inc(conv_done, 1)


def hyena_hidden_stage(K):
    T = K.T
    mm_done, chain, sin_done = K.signals(3)
    F = 64
    pos, w1, w2, cols = K.at(96, S)[0:33], K.at(98, F)[0:33], K.at(98.25, F)[0:F], K.at(98.5, 3)[0:F]
    a, b, c, h1 = (K.at(100 + 2 * i, S)[0:F] for i in range(4))
    with K.nc.Block() as block:
        @block.gpsimd
        def _(pool):
            for dst, src in ((pos, T["k_pos"]), (w1, T["hy_pos_w1"]), (w2, T["hy_pos_w2"]), (cols, T["hy_cols"])):
                pool.dma_start(dst, src).then_inc(K.loaded, 16)

        @block.sync
        def _(sp):
            K.start(sp)

        @block.tensor
        def _(pe):
            pe.wait_ge(K.loaded, K.loads(4))
            pe.matmul(K.ps[0:F, 0, :], w1, pos, start=True, stop=True).then_inc(mm_done, 1)
            pe.wait_ge(sin_done, 1)
            pe.matmul(K.ps[0:F, 1, :], w2, h1, start=True, stop=True).then_inc(mm_done, 1)

        @block.vector
        def _(dve):
            dve.wait_ge(K.loaded, K.loads(4))
            for layer in range(2):
                n = 6 * layer
                dve.wait_ge(mm_done, layer + 1)
                if layer:
                    dve.wait_ge(sin_done, 1)
                dve.tensor_scalar(a, K.ps[0:F, layer, :], cols[:, layer:layer + 1], cols[:, 2:3], ALU.add, ALU.mult)\
                    .then_inc(chain, 1)
                dve.wait_ge(chain, n + 1)
                dve.tensor_scalar(b, a, 1.0 / TWO_PI, ROUND, ALU.mult, ALU.add).then_inc(chain, 1)
                dve.wait_ge(chain, n + 2)
                dve.tensor_scalar(b, b, ROUND, None, ALU.subtract).then_inc(chain, 1)
                dve.wait_ge(chain, n + 3)
                dve.scalar_tensor_tensor(c, b, -PI_HI, a, ALU.mult, ALU.add).then_inc(chain, 1)
                dve.wait_ge(chain, n + 4)
                dve.scalar_tensor_tensor(c, b, -PI_LO, c, ALU.mult, ALU.add).then_inc(chain, 1)
                dve.wait_ge(chain, n + 5)
                dve.tensor_scalar(c, c, SIN_MAX, -SIN_MAX, ALU.min, ALU.max).then_inc(chain, 1)

        @block.scalar
        def _(act):
            for layer, out in enumerate((h1, K.hid)):
                act.wait_ge(chain, 6 * layer + 6)
                act.activation(out, c, ACT.Sin).then_inc(sin_done, 1)
            act.wait_ge(sin_done, 2)
    K.load_base = K.loads(4)


def hyena_filter_stage(K, o):
    r, T = K.ring, K.T
    (dec_done, filt_done, win_done, g_done, abs_done, sum_done, chain, ft_done, ft_out, abs_dec) = K.signals(10)
    n0 = r.first(f"dft{o}")
    nC, nS, nE = n0, n0 + 1, n0 + 2
    g = K.at(96, 8, S)
    total = K.at(112, 4, S)
    absb, win, dec, inv = K.at(112, 2, S), K.at(124, 2, S), K.at(120, 2, S), K.at(144, S)
    w3, row, skip, cols = K.at(148, 1024)[0:64], K.at(72 + 64, 1024)[0:1], K.at(140, S)[0:1], K.at(142, 5)
    with K.nc.Block() as block:
        @block.gpsimd
        def _(pool):
            for dst, src in ((w3, T["hy_pos_w3"][:, o * 1024:(o + 1) * 1024]),
                             (row, T["hy_decay"][:, o * 1024:(o + 1) * 1024]),
                             (skip, T["hy_skip"][:, o * S:(o + 1) * S]), (cols, T["k_time"])):
                pool.dma_start(dst, src).then_inc(K.loaded, 16)

        @block.sync
        def _(sp):
            K.start(sp)

        @block.tensor
        def _(pe):
            pe.wait_ge(K.loaded, K.loads(4))
            for d in range(2):
                pe.matmul(K.ps[:, 5 + d, :], K.ones[0:1, :], row[:, d * S:(d + 1) * S], start=True, stop=True)\
                    .then_inc(dec_done, 1)
            for e in range(9):
                if e < 8:
                    if e >= 2:
                        pe.wait_ge(g_done, e - 1)
                    pe.matmul(K.ps[:, e % 2, :], K.hid[:, (e % 4) * P:(e % 4 + 1) * P],
                              w3[:, (e // 4) * S:(e // 4 + 1) * S], start=True, stop=True).then_inc(filt_done, 1)
                if e >= 1:
                    pe.wait_ge(abs_done, e)
                    pe.matmul(K.ps[:, 2, :], K.ones[:, :], absb[:, (e - 1) % 2, :], start=(e == 1), stop=(e == 8))\
                        .then_inc(sum_done, 1)
            pe.wait_ge(chain, 19)
            arrived(K, pe, n0, 3)
            C, Sm, Ed = r.view(nC), r.view(nS), r.view(nE)
            for j in range(9):
                m = j % 4
                if j >= 2:
                    pe.wait_ge(ft_out, j - 1)
                if j < 4:
                    pairs = [(C[:, t, m * P:(m + 1) * P], total[:, t, :]) for t in range(4)]
                elif j < 8:
                    pairs = [((Ed[:, t, P:2 * P] if m == 0 else Sm[:, t, m * P:(m + 1) * P]), g[:, t, :])
                             for t in range(4)]
                else:
                    pairs = [(Ed[:, t, 0:P], total[:, t, :]) for t in range(4)]
                accumulate(pe, K.ps[:, 3 + j % 2, :], pairs).then_inc(ft_done, 1)

        @block.scalar
        def _(act):
            for d in range(2):
                act.wait_ge(dec_done, d + 1)
                act.activation(dec[:, d, :], K.ps[:, 5 + d, :], ACT.Abs).then_inc(abs_dec, 1)
            act.wait_ge(K.loaded, K.loads(4))
            for e in range(9):
                if e < 8:
                    act.wait_ge(abs_dec, e // 4 + 1)
                    if e >= 2:
                        act.wait_ge(g_done, e - 1)
                    act.activation(win[:, e % 2, :], dec[:, e // 4, :], ACT.Exp, scale=cols[:, e % 4:e % 4 + 1])\
                        .then_inc(win_done, 1)
                if e >= 1:
                    act.wait_ge(g_done, e)
                    if e >= 3:
                        act.wait_ge(sum_done, e - 2)
                    act.activation(absb[:, (e - 1) % 2, :], g[:, e - 1, :], ACT.Abs).then_inc(abs_done, 1)
            for j in range(9):
                dest = K.Rf[:, j, :] if j < 4 else K.If[:, j - 4, :] if j < 8 else K.edge
                act.wait_ge(ft_done, j + 1)
                act.activation(dest, K.ps[:, 3 + j % 2, :], ACT.Copy).then_inc(ft_out, 1)
            act.wait_ge(ft_out, 9)

        @block.vector
        def _(dve):
            dve.wait_ge(K.loaded, K.loads(4))
            for e in range(8):
                dve.wait_ge(filt_done, e + 1)
                dve.wait_ge(win_done, e + 1)
                if e == 4:
                    dve.scalar_tensor_tensor(g[:, e, :], K.ps[:, e % 2, :], cols[:, 4:5], win[:, e % 2, :],
                                             ALU.mult, ALU.mult).then_inc(g_done, 1)
                else:
                    dve.tensor_tensor(g[:, e, :], K.ps[:, e % 2, :], win[:, e % 2, :], ALU.mult).then_inc(g_done, 1)
            dve.wait_ge(sum_done, 8)
            dve.tensor_scalar(inv, K.ps[:, 2, :], EPS, None, ALU.add).then_inc(chain, 1)
            dve.wait_ge(chain, 1)
            dve.reciprocal(inv, inv).then_inc(chain, 1)
            dve.wait_ge(chain, 2)
            for e in range(8):
                dve.tensor_tensor(g[:, e, :], g[:, e, :], inv, ALU.mult).then_inc(chain, 1)
            dve.wait_ge(chain, 10)
            dve.tensor_tensor(g[0:1, 0, :], g[0:1, 0, :], skip, ALU.add).then_inc(chain, 1)
            dve.wait_ge(chain, 11)
            for t in range(4):
                dve.tensor_tensor(total[:, t, :], g[:, t, :], g[:, 4 + t, :], ALU.add).then_inc(chain, 1)
                dve.wait_ge(chain, 12 + 2 * t)
                dve.tensor_tensor(g[:, t, :], g[:, t, :], g[:, 4 + t, :], ALU.subtract).then_inc(chain, 1)
    K.load_base = K.loads(4)


def hyena_conv_stage(K, o):
    r = K.ring
    ft_done, p1, p2, p3, p4, prod, inv_done, out_done = K.signals(8)
    n0 = r.first(f"dft{o}")
    nC, nS, nCi, nSi = n0, n0 + 1, n0 + 3, n0 + 4
    Pre, Pim = K.at(96, 4, S), K.at(104, 4, S)
    tmp = K.at(112, 4, S)
    with K.nc.Block() as block:
        @block.sync
        def _(sp):
            K.start(sp)
            r.issue_until(sp, n0 + 5 + RING)

        @block.tensor
        def _(pe):
            C, Sm = r.view(nC), r.view(nS)
            for m in range(4):
                if m >= 2:
                    pe.wait_ge(p4, m - 1)
                b = 2 * (m % 2)
                accumulate(pe, K.ps[:, b, :], [(C[:, t, m * P:(m + 1) * P], K.z[:, t, :]) for t in range(4)])
                accumulate(pe, K.ps[:, b + 1, :], [(Sm[:, t, m * P:(m + 1) * P], K.z[:, t, :]) for t in range(4)])\
                    .then_inc(ft_done, 1)
            release(K, pe, 3)
            arrived(K, pe, nCi)
            Ci, Si = r.view(nCi), r.view(nSi)
            pe.wait_ge(prod, 8)
            for m in range(4):
                if m >= 2:
                    pe.wait_ge(out_done, m - 1)
                if o == 0:
                    pairs = [(w[:, k, m * P:(m + 1) * P], x[:, k, :]) for w, x in ((Ci, Pre), (Si, Pim))
                             for k in range(4)]
                else:
                    pairs = [(x[:, k, m * P:(m + 1) * P], w[:, k, :]) for w, x in ((Ci, Pre), (Si, Pim))
                             for k in range(4)]
                accumulate(pe, K.ps[:, 4 + m % 2, :], pairs).then_inc(inv_done, 1)
            release(K, pe, 2)

        @block.vector
        def _(dve):
            for m in range(4):
                zr, zi = K.ps[:, 2 * (m % 2), :], K.ps[:, 2 * (m % 2) + 1, :]
                dve.wait_ge(ft_done, m + 1)
                if m >= 1:
                    dve.wait_ge(prod, 2 * m)
                dve.tensor_tensor(tmp[:, 0, :], zr, K.Rf[:, m, :], ALU.mult).then_inc(p1, 1)
                dve.tensor_tensor(tmp[:, 1, :], zi, K.If[:, m, :], ALU.mult).then_inc(p2, 1)
                dve.tensor_tensor(tmp[:, 2, :], zr, K.If[:, m, :], ALU.mult).then_inc(p3, 1)
                dve.tensor_tensor(tmp[:, 3, :], zi, K.edge if m == 0 else K.Rf[:, m, :], ALU.mult).then_inc(p4, 1)
                dve.wait_ge(p1, m + 1)
                dve.wait_ge(p2, m + 1)
                dve.tensor_tensor(Pre[:, m, :], tmp[:, 0, :], tmp[:, 1, :], ALU.subtract).then_inc(prod, 1)
                dve.wait_ge(p3, m + 1)
                dve.wait_ge(p4, m + 1)
                dve.tensor_tensor(Pim[:, m, :], tmp[:, 2, :], tmp[:, 3, :], ALU.add).then_inc(prod, 1)
            for m in range(4):
                gate, dest = (K.x1, K.z) if o == 0 else (K.x2T, K.yhyT)
                dve.wait_ge(inv_done, m + 1)
                dve.tensor_tensor(dest[:, m, :], K.ps[:, 4 + m % 2, :], gate[:, m, :], ALU.mult).then_inc(out_done, 1)
            dve.wait_ge(out_done, 4)


def merge_stage(K, name, x, branches, mT, bias=None, tmp=96):
    r = K.ring
    gate_done, y_done, sig_done, prod_done, sum_done = K.signals(5)
    n0 = r.first(name)
    sizes = [2 + -(-kt // 4) for _, kt in branches]
    sig, tm = K.at(tmp, 2, S), K.at(tmp + 4, 2, S)
    items = []
    n = n0
    for half in range(2):
        for b in range(3):
            for c in range(4):
                items.append((half, b, c, n))
            n += sizes[b]
    with K.nc.Block() as block:
        @block.sync
        def _(sp):
            K.start(sp)
            r.issue_until(sp, n + RING)

        @block.tensor
        def _(pe):
            for i, (half, b, c, n) in enumerate(items):
                y, kt = branches[b]
                if c == 0:
                    arrived(K, pe, n, sizes[b])
                if i >= 2:
                    pe.wait_ge(sig_done, i - 1)
                project(K, pe, n, c * P, P, x, slice(0, S), K.ps[:, i % 2, :]).then_inc(gate_done, 1)
                if i >= 2:
                    pe.wait_ge(prod_done, i - 1)
                accumulate(pe, K.ps[:, 2 + i % 2, :],
                           [(r.view(n + 2 + k // 4)[:, k % 4, c * P:(c + 1) * P], y[:, k, :]) for k in range(kt)])\
                    .then_inc(y_done, 1)
                if c == 3:
                    release(K, pe, sizes[b])

        @block.scalar
        def _(act):
            for i, (half, b, c, n) in enumerate(items):
                act.wait_ge(gate_done, i + 1)
                if i >= 2:
                    act.wait_ge(prod_done, i - 1)
                kw = {} if bias is None else {"bias": K.vec(bias, b * KD + half * 4 + c)}
                act.activation(sig[:, i % 2, :], K.ps[:, i % 2, :], ACT.Sigmoid, **kw).then_inc(sig_done, 1)

        @block.vector
        def _(dve):
            sums = 0
            for i, (half, b, c, n) in enumerate(items):
                m = mT[:, half * 4 + c, :]
                dve.wait_ge(sig_done, i + 1)
                dve.wait_ge(y_done, i + 1)
                if b and i >= 6:
                    dve.wait_ge(sum_done, sums - 1)
                dve.tensor_tensor(tm[:, i % 2, :] if b else m, K.ps[:, 2 + i % 2, :], sig[:, i % 2, :], ALU.mult)\
                    .then_inc(prod_done, 1)
                if b:
                    dve.wait_ge(prod_done, i + 1)
                    if b == 2:
                        dve.wait_ge(sum_done, sums - 3)
                    dve.tensor_tensor(m, m, tm[:, i % 2, :], ALU.add).then_inc(sum_done, 1)
                    sums += 1
            dve.wait_ge(sum_done, sums)


def residual_stage(K, name, mT, gate):
    n = K.ring.first(name)
    items = []
    for t in range(KD):
        nn = n + 2 * (t // 4)

        def out(e, bank, t=t):
            x = K.xT[:, t, :]
            if gate is None:
                return e.tensor_tensor(x, bank, x, ALU.add)
            return e.scalar_tensor_tensor(x, bank, gate(t), x, ALU.mult, ALU.add)
        items.append({"first": (nn, nn + 1) if t % 4 == 0 else (), "rel": 2 if t % 4 == 3 else 0, "eng": "dve",
                      "mm": lambda pe, bank, t=t, nn=nn: project(K, pe, nn, (t % 4) * P, P, mT, slice(0, S), bank),
                      "out": out})
    items_stage(K, items, issue=n + 4)


def router_stage(K):
    T = K.T
    s_done, sig_done, chain, masked, copied, stored, place_done, over_done, turned, hi_done, lo_done, placed, \
        full_done = K.signals(13)
    full = K.at(112, 2 * ST, 512)
    rw, rb = K.at(128, KD, NEXP), K.at(129, NEXP)
    sc, sel, mask = K.at(130, 64), K.at(130.25, 64), K.at(130.5, 64)
    hi, lo, top, gs = (K.at(131 + 0.25 * i, 4 * 4 * 2) for i in range(4))
    rank, lose, gt, over = K.at(132, 64), K.at(132.25, 16), K.at(132.5, 16), K.at(132.75, 64)
    flags, frank, eq, listed = (K.at(133 + 0.25 * i, 16)[0:1] for i in range(4))
    match = K.at(137, NEXP, NEXP)[0:1]
    oT = K.at(135, S)[0:NEXP]
    gates, upto, slot_no = K.gates, K.at(140, P), K.slot_no

    def e4(v):
        return v.rearrange("p (g e) -> p g e", e=4)

    with K.nc.Block() as block:
        @block.gpsimd
        def _(pool):
            pool.dma_start(rw, T["router_w"].rearrange("(t p) e -> p t e", p=P)).then_inc(K.loaded, 16)
            pool.dma_start(rb, T["router_b"].broadcast_to([P, NEXP])).then_inc(K.loaded, 16)
            pool.dma_start(upto, T["k_upto"]).then_inc(K.loaded, 16)
            pool.dma_start(slot_no, T["k_slot_no"]).then_inc(K.loaded, 16)
            for j in range(2 * ST):
                pool.wait_ge(hi_done, j + 1)
                pool.wait_ge(full_done, j + 1)
                pool.tensor_tensor(K.h_lo[:, j // 2, (j % 2) * 512:(j % 2 + 1) * 512], full[:, j, :],
                                   K.h_hi[:, j // 2, (j % 2) * 512:(j % 2 + 1) * 512].bitcast(F32), ALU.subtract)\
                    .then_inc(lo_done, 1)

        @block.sync
        def _(sp):
            K.start(sp)
            sp.wait_ge(copied, 1)
            sp.dma_start(K.gate_rows, oT).then_inc(stored, 16)
            sp.wait_ge(stored, 16)

        @block.tensor
        def _(pe):
            pe.wait_ge(K.loaded, K.loads(4))
            for t in range(ST):
                ins = accumulate(pe, K.ps[:, 0, t * NEXP:(t + 1) * NEXP],
                                 [(K.hT[:, k, t * P:(t + 1) * P], rw[:, k, :]) for k in range(KD)])
            ins.then_inc(s_done, 1)
            for j in range(2 * ST):
                t, half = j // 2, j % 2
                if j >= 4:
                    pe.wait_ge(full_done, j - 3)
                for c in range(4):
                    ins = pe.transpose(K.ps[:, 2 + j % 4, c * P:(c + 1) * P],
                                       K.hT[:, half * 4 + c, t * P:(t + 1) * P], K.ident[:, :])
                ins.then_inc(turned, 1)
            pe.wait_ge(masked, 1)
            for t in range(ST):
                accumulate(pe, K.ps[:, 1, t * NEXP:(t + 1) * NEXP],
                           [(upto, mask[:, t * NEXP:(t + 1) * NEXP])] +
                           [(K.ones[:, :], mask[:, b * NEXP:(b + 1) * NEXP]) for b in range(t)])
            accumulate(pe, K.ps[:, 1, 64:64 + NEXP],
                       [(K.ones[:, :], mask[:, b * NEXP:(b + 1) * NEXP]) for b in range(ST)]).then_inc(place_done, 1)
            pe.wait_ge(over_done, 1)
            for t in range(ST):
                ins = pe.transpose(K.ps[0:NEXP, 6, t * P:(t + 1) * P], over[:, t * NEXP:(t + 1) * NEXP], K.ident[:, :])
            ins.then_inc(s_done, 1)

        @block.scalar
        def _(act):
            act.wait_ge(s_done, 1)
            act.activation(sc, K.ps[:, 0, 0:64], ACT.Sigmoid).then_inc(sig_done, 1)
            for j in range(2 * ST):
                act.wait_ge(turned, j + 1)
                act.activation(K.h_hi[:, j // 2, (j % 2) * 512:(j % 2 + 1) * 512], K.ps[:, 2 + j % 4, :], ACT.Copy)\
                    .then_inc(hi_done, 1)
                act.activation(full[:, j, :], K.ps[:, 2 + j % 4, :], ACT.Copy).then_inc(full_done, 1)
            act.wait_ge(s_done, 2)
            act.activation(oT, K.ps[0:NEXP, 6, :], ACT.Copy).then_inc(copied, 1)

        @block.vector
        def _(dve):
            n = [0]

            def then(ins):
                n[0] += 1
                ins.then_inc(chain, 1)
                dve.wait_ge(chain, n[0])

            def tt(out, a, b, op):
                then(dve.tensor_tensor(out, a, b, op))

            dve.wait_ge(K.loaded, K.loads(4))
            dve.wait_ge(sig_done, 1)
            tt(sel.rearrange("p (t e) -> p t e", e=NEXP), sc.rearrange("p (t e) -> p t e", e=NEXP),
               rb.unsqueeze(1).broadcast_to([P, ST, NEXP]), ALU.add)
            s4 = e4(sel)
            pair = sel.rearrange("p (g h e) -> p g h e", h=2, e=2)
            h2, l2 = hi.rearrange("p (g h) -> p g h", h=2), lo.rearrange("p (g h) -> p g h", h=2)
            tt(h2, pair[:, :, :, 0], pair[:, :, :, 1], ALU.max)
            tt(l2, pair[:, :, :, 0], pair[:, :, :, 1], ALU.min)
            t1, t2 = top[:, 0:16], top[:, 16:32]
            tt(t1, h2[:, :, 0], h2[:, :, 1], ALU.min)
            tt(t2, l2[:, :, 0], l2[:, :, 1], ALU.max)
            tt(t2, t1, t2, ALU.max)
            tt(t1, h2[:, :, 0], h2[:, :, 1], ALU.max)
            g = gs[:, 0:16]
            tt(g, t1, t2, ALU.add)
            then(dve.memset(lose, 0.0))
            then(dve.memset(rank, 0.0))
            then(dve.memset(K.place[:, 64:64 + GE], 0.0))
            gg, ll, r4 = g.rearrange("p (t g) -> p t g", g=4), lose.rearrange("p (t g) -> p t g", g=4), e4(rank)
            gt4 = gt[:, 0:4]
            for i in range(4):
                for j in range(i + 1, 4):
                    tt(gt4, gg[:, :, j], gg[:, :, i], ALU.is_gt)
                    tt(ll[:, :, i], ll[:, :, i], gt4, ALU.add)
                    then(dve.scalar_tensor_tensor(ll[:, :, j], ll[:, :, j], 1.0, gt4, ALU.add, ALU.subtract))
                    tt(gt, s4[:, :, j], s4[:, :, i], ALU.is_gt)
                    tt(r4[:, :, i], r4[:, :, i], gt, ALU.add)
                    then(dve.scalar_tensor_tensor(r4[:, :, j], r4[:, :, j], 1.0, gt, ALU.add, ALU.subtract))
            then(dve.tensor_scalar(lose, lose, 0.5, None, ALU.is_lt))
            n[0] += 1
            dve.scalar_tensor_tensor(e4(mask), e4(rank), 1.5, lose.unsqueeze(2).broadcast_to([P, 16, 4]), ALU.is_lt,
                                     ALU.mult).then_inc(chain, 1)
            dve.wait_ge(chain, n[0])
            dve.memset(flags, 0.0).then_inc(masked, 1)
            tt(gates, mask, sc, ALU.mult)
            g16 = gates.rearrange("p (t e) -> p t e", e=NEXP)
            then(dve.tensor_reduce(gt4, g16, AX.X, ALU.add))
            then(dve.reciprocal(gt4, gt4))
            tt(g16, g16, gt4.unsqueeze(2).broadcast_to([P, ST, NEXP]), ALU.mult)
            dve.wait_ge(place_done, 1)
            tt(K.place[:, 0:64], K.ps[:, 1, 0:64], mask, ALU.mult)
            dve.scalar_tensor_tensor(over, K.place[:, 0:64], SLOTS + 0.5, gates, ALU.is_gt, ALU.mult).then_inc(over_done, 1)
            dve.wait_ge(masked, 1)
            then(dve.tensor_scalar(flags, K.ps[0:1, 1, 64:64 + NEXP], SLOTS + 0.5, None, ALU.is_gt))
            then(dve.tensor_tensor_scan(frank, K.ones[0:1, 0:NEXP], flags, 0.0, ALU.mult, ALU.add))
            dve.tensor_copy(K.over_list[0:1, NEXP:NEXP + 1], frank[:, NEXP - 1:NEXP]).then_inc(placed, 1)
            tt(eq, frank, flags, ALU.mult)
            no = slot_no[0:1, 0:NEXP]
            tt(match, eq.unsqueeze(1).broadcast_to([1, NEXP, NEXP]), no.unsqueeze(2).broadcast_to([1, NEXP, NEXP]),
               ALU.is_equal)
            tt(match, match, no.unsqueeze(1).broadcast_to([1, NEXP, NEXP]), ALU.mult)
            then(dve.tensor_reduce(listed, match, AX.X, ALU.add))
            then(dve.tensor_scalar(listed, listed, -1.0, 0.0, ALU.add, ALU.max))
            dve.tensor_copy(K.over_list[0:1, 0:NEXP], listed).then_inc(placed, 1)
            dve.wait_ge(placed, 2)
            dve.wait_ge(over_done, 1)
    K.load_base = K.loads(4)


def moe_stage(K):
    r, T = K.ring, K.T
    (sel_done, sel_free, gat_done, gat_copied, gate_done, up_done, silu_done, slot_gates, slot_gates_in, hid_done,
     turn_done, turn_copied, back_done, back_copied, y_done, hi_done, lo_done, scat_done, x_added) = K.signals(19)
    n0 = r.first("moe")
    GROUPS, CH = NEXP // GE, 6 * GE
    hg, sel_r, back = K.at(112, KD, S), K.rounded_at(64, ST, GE, SLOTS), K.rounded_at(72, GE, S)
    y_hi, y_lo = K.rounded_at(80, GE, D), K.rounded_at(96, GE, D)
    silu, hid, hidT, gcol = K.at(128, 512), K.at(130, 512), K.at(132, 512), K.at(134, GE)
    gates = K.gates.rearrange("p (t e) -> p t e", e=NEXP)
    sel = sel_r.bitcast(F32)

    def view(c):
        return r.slots[(n0 + c) % RING][:, :].rearrange("p (t c) -> p t c", c=HALF)

    order = moe_order()
    at = {key: c for c, key in enumerate(order)}

    def source(g, c):
        j, m, h = order[c]
        s = slice(h * HALF, (h + 1) * HALF)
        w = T[("moe_w_gate", "moe_w_up", "moe_w_down")[m]]
        return w[bass.ds(g * GE + j, 1), :, s] if m == 2 else w[bass.ds(g * GE + j, 1), s, :]

    with K.nc.Block() as block:
        @block.sync
        def _(sp):
            K.start(sp)
            with sp.Fori(0, GROUPS - 1) as g:
                for k in range(CH):
                    c = k + RING
                    sp.wait_ge(r.used, g * CH + (n0 + c - RING + 1))
                    sp.dma_start(view(c), source(g + c // CH, c % CH).rearrange("o (t p) c -> p (o t) c", p=P))\
                        .then_inc(r.arrived[(n0 + c) % RING], 16)
            r.issued = n0 + RING + (GROUPS - 1) * CH
            r.issue_until(sp, n0 + GROUPS * CH + RING)

        @block.tensor
        def _(pe):
            def arrive(g, c):
                pe.wait_ge(r.arrived[(n0 + c) % RING], g * (16 * CH // RING) + r.arrival(n0 + c))

            def hidden(g, j):
                for m, done in ((0, gate_done), (1, up_done)):
                    for h in range(2):
                        arrive(g, at[j, m, h])
                    if m == 0 and j == 0:
                        pe.wait_ge(gat_copied, g * KD + KD)
                    for k in range(KD):
                        ins = pe.matmul(K.ps[:, m, :], hg[:, k, j * P:(j + 1) * P], view(at[j, m, k // 4])[:, k % 4, :],
                                        start=(k == 0), stop=(k == KD - 1))
                    ins.then_inc(done, 1)
                    release(K, pe, 2)

            def down(g, j):
                pe.wait_ge(turn_copied, g * GE + j + 1)
                for h in range(2):
                    arrive(g, at[j, 2, h])
                    pe.wait_ge(lo_done, g * (2 * GE) + 2 * j + h + 1)
                    for k in range(4):
                        ins = pe.matmul(K.ps[:, 3 + h, :], hidT[:, k * P:(k + 1) * P], view(at[j, 2, h])[:, k, :],
                                        start=(k == 0), stop=(k == 3))
                    ins.then_inc(y_done, 1)
                release(K, pe, 2)

            with pe.Fori(0, GROUPS) as g:
                pe.wait_ge(sel_done, g * ST + ST)
                for c in range(KD):
                    if c < 2:
                        pe.wait_ge(x_added, g * KD + 1)
                    else:
                        pe.wait_ge(gat_copied, g * KD + c - 1)
                    accumulate(pe, K.ps[:, 5 + c % 2, :],
                               [(part[:, t, c * P:(c + 1) * P], sel_r[:, t, :, :])
                                for t in range(ST) for part in (K.h_hi, K.h_lo)]).then_inc(gat_done, 1)
                for j in range(GE):
                    ins = accumulate(pe, K.ps[:, 2, j:j + 1],
                                     [(sel[:, t, j, :], gates[:, t, bass.ds(g * GE + j, 1)]) for t in range(ST)])
                ins.then_inc(slot_gates, 1)
                for j in range(GE):
                    hidden(g, j)
                    if j == 0:
                        for i in range(GE):
                            if i >= 2:
                                pe.wait_ge(back_copied, g * GE + i - 1)
                            for t in range(ST):
                                ins = pe.transpose(K.ps[:, 5 + i % 2, t * P:(t + 1) * P], sel[:, t, i, :],
                                                   K.ident[:, :])
                            ins.then_inc(back_done, 1)
                        pe.transpose(K.ps[:, 7, 0:P], sel[:, 0, 0, :], K.ident[:, :]).then_inc(sel_free, 1)
                    else:
                        down(g, j - 1)
                    pe.wait_ge(hid_done, g * GE + j + 1)
                    for k in range(4):
                        ins = pe.transpose(K.ps[:, 2, k * P:(k + 1) * P], hid[:, k * P:(k + 1) * P], K.ident[:, :])
                    ins.then_inc(turn_done, 1)
                down(g, GE - 1)
                pe.wait_ge(back_copied, g * GE + GE)
                pe.wait_ge(lo_done, g * (2 * GE) + 2 * GE + 2)
                for c in range(KD):
                    if c >= 2:
                        pe.wait_ge(x_added, g * KD + c)
                    accumulate(pe, K.ps[:, 5 + c % 2, :],
                               [(part[:, j, c * P:(c + 1) * P], back[:, j, :])
                                for j in range(GE) for part in (y_hi, y_lo)]).then_inc(scat_done, 1)

        @block.scalar
        def _(act):
            with act.Fori(0, GROUPS) as g:
                act.wait_ge(x_added, g * KD + 1)
                for c in range(KD):
                    act.wait_ge(gat_done, g * KD + c + 1)
                    act.activation(hg[:, c, :], K.ps[:, 5 + c % 2, :], ACT.Copy).then_inc(gat_copied, 1)

                def split(j):
                    for h in range(2):
                        act.wait_ge(y_done, g * (2 * GE) + 2 * j + h + 1)
                        act.activation(y_hi[:, j, h * 512:(h + 1) * 512], K.ps[:, 3 + h, :], ACT.Copy)\
                            .then_inc(hi_done, 1)

                for j in range(GE):
                    act.wait_ge(gate_done, g * GE + j + 1)
                    act.activation(silu, K.ps[:, 0, :], ACT.Silu).then_inc(silu_done, 1)
                    if j == 0:
                        for i in range(GE):
                            act.wait_ge(back_done, g * GE + i + 1)
                            act.activation(back[:, i, :], K.ps[:, 5 + i % 2, :], ACT.Copy).then_inc(back_copied, 1)
                    else:
                        split(j - 1)
                    act.wait_ge(turn_done, g * GE + j + 1)
                    act.activation(hidT, K.ps[:, 2, :], ACT.Copy).then_inc(turn_copied, 1)
                split(GE - 1)

        @block.vector
        def _(dve):
            dve.memset(silu[:, 0:1], 0.0).then_inc(lo_done, 1)
            dve.memset(silu[:, 1:2], 0.0).then_inc(lo_done, 1)
            dve.wait_ge(lo_done, 2)
            dve.memset(silu[:, 2:3], 0.0).then_inc(x_added, 1)

            def select(g):
                for t in range(ST):
                    dve.tensor_tensor(sel_r[:, t, :, :], K.slot_no.unsqueeze(1).broadcast_to([P, GE, SLOTS]),
                                      K.place[:, bass.ds(g * GE + t * NEXP, GE)].unsqueeze(2)
                                      .broadcast_to([P, GE, SLOTS]), ALU.is_equal).then_inc(sel_done, 1)

            select(0)
            with dve.Fori(0, GROUPS) as g:
                def split(j):
                    for h in range(2):
                        s = slice(h * 512, (h + 1) * 512)
                        dve.wait_ge(hi_done, g * (2 * GE) + 2 * j + h + 1)
                        dve.tensor_tensor(y_lo[:, j, s], K.ps[:, 3 + h, :], y_hi[:, j, s].bitcast(F32), ALU.subtract)\
                            .then_inc(lo_done, 1)

                dve.wait_ge(slot_gates, g + 1)
                dve.tensor_copy(gcol, K.ps[:, 2, 0:GE]).then_inc(slot_gates_in, 1)
                dve.wait_ge(slot_gates_in, g + 1)
                for j in range(GE):
                    dve.wait_ge(up_done, g * GE + j + 1)
                    dve.wait_ge(silu_done, g * GE + j + 1)
                    if j >= 1:
                        dve.wait_ge(turn_done, g * GE + j)
                    dve.scalar_tensor_tensor(hid, K.ps[:, 1, :], gcol[:, j:j + 1], silu, ALU.mult, ALU.mult)\
                        .then_inc(hid_done, 1)
                    if j >= 1:
                        split(j - 1)
                    if j == 2:
                        dve.wait_ge(sel_free, g + 1)
                        select(g + 1)
                split(GE - 1)
                for c in range(KD):
                    dve.wait_ge(scat_done, g * KD + c + 1)
                    dve.scalar_tensor_tensor(K.xT[:, c, :], K.ps[:, 5 + c % 2, :], mod_col(K, 5, c), K.xT[:, c, :],
                                             ALU.mult, ALU.add).then_inc(x_added, 1)
            dve.wait_ge(x_added, GROUPS * KD + 1)
            dve.wait_ge(sel_done, (GROUPS + 1) * ST)


def moe_order():
    out = []
    for j in range(GE):
        out += [(j, m, h) for m in range(2) for h in range(2)]
        if j >= 1:
            out += [(j - 1, 2, h) for h in range(2)]
    return out + [(GE - 1, 2, h) for h in range(2)]


def moe_overflow_stage(K):
    T = K.T
    came, freed, gu_done, silu_done, up_done, hid_done, down_done, x_added = K.signals(8)
    FT = 4
    w = K.at(32, 6, 2048)
    silu, prod, hid, row = K.at(80, 2, S), K.at(84, 2, S), K.at(88, FT, S), K.at(96, S)
    wg, wu, wd = T["moe_w_gate"], T["moe_w_up"], T["moe_w_down"]
    LOADS = 7

    def part(s):
        return w[:, s, :].rearrange("p (t c) -> p t c", c=HALF)

    def experts(eng, body):
        count = eng.value_load(K.over_list[0:1, NEXP:NEXP + 1], min_val=0, max_val=NEXP)
        with eng.If(count > 0):
            with eng.Fori(0, count) as i:
                body(i)

    with K.nc.Block() as block:
        @block.sync
        def _(sp):
            K.start(sp)

            def body(i):
                e = sp.value_load(K.over_list[0:1, bass.ds(i, 1)], min_val=0, max_val=NEXP - 1)
                sp.wait_ge(freed, i + 1)
                for s in range(6):
                    h = slice((s % 2) * HALF, (s % 2 + 1) * HALF)
                    src = (wg, wg, wu, wu)[s][bass.ds(e, 1), h, :] if s < 4 else wd[bass.ds(e, 1), :, h]
                    sp.dma_start(part(s), src.rearrange("o (t p) c -> p (o t) c", p=P)).then_inc(came, 16)
                sp.dma_start(row, K.gate_rows[bass.ds(e, 1), :].broadcast_to([P, S])).then_inc(came, 16)
            experts(sp, body)

        @block.tensor
        def _(pe):
            def body(i):
                pe.wait_ge(came, i * (16 * LOADS) + 16 * LOADS)
                for f in range(FT):
                    pe.wait_ge(up_done, i * FT + f + 1)
                    for m in range(2):
                        for k in range(KD):
                            ins = pe.matmul(K.ps[:, 2 * m + f % 2, :], part(2 * m + k // 4)[:, k % 4, f * P:(f + 1) * P],
                                            K.hT[:, k, :], start=(k == 0), stop=(k == KD - 1))
                    ins.then_inc(gu_done, 1)
                pe.wait_ge(hid_done, i * FT + FT)
                for t in range(KD):
                    pe.wait_ge(x_added, i * KD + t + 1)
                    accumulate(pe, K.ps[:, 4 + t % 2, :],
                               [(part(4 + t // 4)[:, k, (t % 4) * P:(t % 4 + 1) * P], hid[:, k, :])
                                for k in range(FT)]).then_inc(down_done, 1)
            experts(pe, body)

        @block.scalar
        def _(act):
            def body(i):
                for f in range(FT):
                    act.wait_ge(gu_done, i * FT + f + 1)
                    act.wait_ge(up_done, i * FT + f + 1)
                    act.activation(silu[:, f % 2, :], K.ps[:, f % 2, :], ACT.Silu).then_inc(silu_done, 1)
            experts(act, body)

        @block.vector
        def _(dve):
            for b in range(2):
                dve.memset(prod[:, b, 0:1], 0.0).then_inc(up_done, 1)
                dve.memset(prod[:, b, 1:2], 0.0).then_inc(x_added, 1)
            dve.wait_ge(up_done, 2)
            dve.wait_ge(x_added, 2)
            dve.memset(prod[:, 0, 2:3], 0.0).then_inc(freed, 1)
            dve.wait_ge(freed, 1)

            def body(i):
                for f in range(FT):
                    dve.wait_ge(silu_done, i * FT + f + 1)
                    dve.tensor_tensor(prod[:, f % 2, :], K.ps[:, 2 + f % 2, :], silu[:, f % 2, :], ALU.mult)\
                        .then_inc(up_done, 1)
                    dve.wait_ge(up_done, i * FT + f + 3)
                    dve.tensor_tensor(hid[:, f, :], prod[:, f % 2, :], row, ALU.mult).then_inc(hid_done, 1)
                for t in range(KD):
                    dve.wait_ge(down_done, i * KD + t + 1)
                    dve.scalar_tensor_tensor(K.xT[:, t, :], K.ps[:, 4 + t % 2, :], mod_col(K, 5, t), K.xT[:, t, :],
                                             ALU.mult, ALU.add).then_inc(x_added, 1)
                dve.wait_ge(x_added, i * KD + KD + 2)
                dve.memset(prod[:, 0, 2:3], 0.0).then_inc(freed, 1)
            experts(dve, body)


def lru_weights_stage(K):
    T = K.T
    zeroed, chain, exp_done, stored = K.signals(4)
    LT = 6
    lam = K.vecs[:, VEC_AT["lru_lambda_2"]:VEC_AT["lru_lambda_2"] + LT]
    e, w, s, p, y = (K.at(150 + 0.25 * i, LT) for i in range(5))
    with K.nc.Block() as block:
        @block.sync
        def _(sp):
            K.start(sp)
            sp.wait_ge(zeroed, 1)
            for m, name in enumerate(("w_rg_a_2", "w_rg_x_2")):
                for h in range(2):
                    blocks = T[name].rearrange("(t h) i j -> h i t j", h=2)[h]
                    sp.dma_start(K.rg[64 * h:64 * h + 64, m, :, 64 * h:64 * h + 64], blocks).then_inc(stored, 16)
            sp.wait_ge(stored, 64)

        @block.scalar
        def _(act):
            act.wait_ge(chain, 1)
            act.activation(e, e, ACT.Exp).then_inc(exp_done, 1)

        @block.vector
        def _(dve):
            dve.memset(K.rg, 0.0).then_inc(zeroed, 1)
            n = [0]

            def then(ins):
                n[0] += 1
                ins.then_inc(chain, 1)
                dve.wait_ge(chain, n[0])

            then(dve.scalar_tensor_tensor(e, lam, -1.0, lam, ALU.mult, ALU.min))
            then(dve.tensor_scalar(y, lam, -1.0, 0.0, ALU.mult, ALU.max))
            dve.wait_ge(exp_done, 1)
            then(dve.tensor_scalar(w, e, 2.0, None, ALU.add))
            then(dve.reciprocal(w, w))
            then(dve.tensor_tensor(w, w, e, ALU.mult))
            then(dve.tensor_tensor(s, w, w, ALU.mult))
            then(dve.tensor_scalar(p, s, 1.0 / 15, 1.0 / 13, ALU.mult, ALU.add))
            for d in (11, 9, 7, 5, 3, 1):
                then(dve.tensor_tensor(p, p, s, ALU.mult))
                then(dve.tensor_scalar(p, p, 1.0 / d, None, ALU.add))
            then(dve.tensor_tensor(p, p, w, ALU.mult))
            then(dve.scalar_tensor_tensor(p, p, 2.0, y, ALU.mult, ALU.add))
            then(dve.tensor_scalar(K.lru_rate, p, -8.0, None, ALU.mult))


def lru_stage(K):
    r = K.ring
    (x_done, mid_done, conv_done, rg_done, sig_done, exp_done, tanh_done, chain, sqrt_done, g_done, gelu_done,
     y_done, h_chain) = K.signals(13)
    n0 = r.first("lru")
    LT = 6
    xc, rr, ii, aa, th, bb, ge = (K.at(56 + 4 * j, 2, S) for j in range(7))
    with K.nc.Block() as block:
        @block.sync
        def _(sp):
            K.start(sp)
            r.issue_until(sp, n0 + 8 + RING)

        @block.tensor
        def _(pe):
            for t in range(LT + 1):
                if t < LT:
                    n = n0 + 4 * (t // 4)
                    if t % 4 == 0:
                        arrived(K, pe, n, 4)
                    if t >= 2:
                        pe.wait_ge(conv_done, 3 * (t - 1))
                    project(K, pe, n, (t % 4) * P, P, K.hT, slice(0, S), K.ps[:, t % 2, :]).then_inc(x_done, 1)
                    if t >= 2:
                        pe.wait_ge(gelu_done, t - 1)
                    project(K, pe, n + 2, (t % 4) * P, P, K.hT, slice(0, S), K.ps[:, 4 + t % 2, :]).then_inc(g_done, 1)
                    if t in (3, LT - 1):
                        release(K, pe, 4)
                if t >= 1:
                    u = t - 1
                    pe.wait_ge(conv_done, 3 * (u + 1))
                    if u >= 1:
                        pe.wait_ge(sig_done, 2 * u)
                    for m in range(2):
                        pe.matmul(K.ps[:, 2 + m, :], K.rg[:, m, u, :], xc[:, u % 2, :], start=True, stop=True)\
                            .then_inc(rg_done, 1)

        @block.scalar
        def _(act):
            for t in range(LT + 1):
                if t < LT:
                    act.wait_ge(x_done, t + 1)
                    if t >= 2:
                        act.wait_ge(y_done, t - 1)
                    act.activation(xc[:, t % 2, :], K.ps[:, t % 2, :], ACT.Identity, bias=K.vec("conv_b_2", t),
                                   scale=K.vec("conv_w_2", 3 * LT + t)).then_inc(mid_done, 1)
                if t >= 1:
                    u = t - 1
                    b = u % 2
                    act.wait_ge(rg_done, 2 * t)
                    act.activation(rr[:, b, :], K.ps[:, 2, :], ACT.Sigmoid, bias=K.vec("b_rg_a_2", u))\
                        .then_inc(sig_done, 1)
                    act.activation(ii[:, b, :], K.ps[:, 3, :], ACT.Sigmoid, bias=K.vec("b_rg_x_2", u))\
                        .then_inc(sig_done, 1)
                    act.wait_ge(sig_done, 2 * u + 1)
                    act.activation(th[:, b, :], rr[:, b, :], ACT.Tanh, scale=K.lru_rate[:, u:u + 1])\
                        .then_inc(tanh_done, 1)
                    act.activation(aa[:, b, :], rr[:, b, :], ACT.Exp, scale=K.lru_rate[:, u:u + 1])\
                        .then_inc(exp_done, 1)
                    act.wait_ge(g_done, u + 1)
                    act.activation(ge[:, b, :], K.ps[:, 4 + b, :], ACT.Gelu_apprx_tanh).then_inc(gelu_done, 1)
                    act.wait_ge(chain, 4 * u + 3)
                    act.activation(bb[:, b, :], bb[:, b, :], ACT.Sqrt).then_inc(sqrt_done, 1)

        @block.vector
        def _(dve):
            for t in range(LT + 1):
                if t < LT:
                    x, u = xc[:, t % 2, :], K.ps[:, t % 2, :]
                    dve.wait_ge(mid_done, t + 1)
                    for k in range(1, 4):
                        dve.scalar_tensor_tensor(x[:, k:S], u[:, 0:S - k], K.vec("conv_w_2", (3 - k) * LT + t),
                                                 x[:, k:S], ALU.mult, ALU.add).then_inc(conv_done, 1)
                        dve.wait_ge(conv_done, 3 * t + k)
                if t >= 1:
                    u = t - 1
                    b = u % 2
                    dve.wait_ge(tanh_done, u + 1)
                    dve.tensor_scalar(bb[:, b, :], th[:, b, :], -1.0, 1.0, ALU.mult, ALU.add).then_inc(chain, 1)
                    dve.wait_ge(chain, 4 * u + 1)
                    dve.reciprocal(bb[:, b, :], bb[:, b, :]).then_inc(chain, 1)
                    dve.wait_ge(chain, 4 * u + 2)
                    dve.scalar_tensor_tensor(bb[:, b, :], th[:, b, :], -2.0, bb[:, b, :], ALU.mult, ALU.mult)\
                        .then_inc(chain, 1)
                    dve.wait_ge(sig_done, 2 * u + 2)
                    dve.tensor_tensor(ii[:, b, :], ii[:, b, :], xc[:, b, :], ALU.mult).then_inc(chain, 1)
                    dve.wait_ge(chain, 4 * u + 4)
                    dve.wait_ge(sqrt_done, u + 1)
                    dve.wait_ge(exp_done, u + 1)
                    dve.wait_ge(gelu_done, u + 1)
                    dve.tensor_tensor(bb[:, b, :], bb[:, b, :], ii[:, b, :], ALU.mult).then_inc(h_chain, 1)
                    dve.wait_ge(h_chain, 2 * u + 1)
                    dve.tensor_tensor_scan(th[:, b, :], aa[:, b, :], bb[:, b, :], 0.0, ALU.mult, ALU.add)\
                        .then_inc(h_chain, 1)
                    dve.wait_ge(h_chain, 2 * u + 2)
                    dve.tensor_tensor(K.ylruT[:, u, :], th[:, b, :], ge[:, b, :], ALU.mult).then_inc(y_done, 1)
            dve.wait_ge(y_done, LT)


def memory_project_stage(K):
    n = K.ring.first("mem")
    items = [channel_item(K, n, t * P, P, K.memT, NCTX, K.kmT[:, t, :], eng=("act", "dve")[t % 2],
                          first=(n, n + 1) if t == 0 else (), rel=2 if t == 3 else 0) for t in range(4)]
    n += 2
    items += [token_item(K, n, 0, 512, K.memT, slice(t * P, t * P + P), K.vm[:, t, :], eng=("act", "dve")[t],
                         first=(n, n + 1) if t == 0 else (), rel=2 if t == 1 else 0) for t in range(2)]
    items_stage(K, items, issue=n + 2)


def group_tokens(v, g, j):
    return v[:, j * P:(j + 1) * P] if g == 0 else v.rearrange("p (l r) -> p r l", r=4)[:, j, :]


def dilated_project_stage(K):
    n0 = K.ring.first("qkv")
    items = []
    for c in range(12):
        n = n0 + 2 * (c // 4)
        dest = K.qd[:, c, :] if c < 6 else K.kd[:, c - 6, :]
        items.append(channel_item(K, n, (c % 4) * P, P, K.hT, S, dest, eng="act" if c < 6 else "dve",
                                  first=(n, n + 1) if c % 4 == 0 else (), rel=2 if c % 4 == 3 else 0,
                                  **({"scale": 0.125} if c < 6 else {})))
    for g in range(3):
        n = n0 + 6 + 2 * (g // 2)
        for j in range(4):
            c0 = 256 * (g % 2)

            def mm(pe, bank, g=g, j=j, n=n, c0=c0):
                return accumulate(pe, bank[:, 0:256],
                                  [(group_tokens(K.hT[:, k, :], g, j), K.ring.view(n + k // 4)[:, k % 4, c0:c0 + 256])
                                   for k in range(KD)])
            dest = K.vd[:, g * 4 + j, :]
            items.append({"first": (n, n + 1) if (g != 1 and j == 0) else (), "mm": mm,
                          "rel": 2 if (g > 0 and j == 3) else 0, "eng": "act" if j % 2 else "dve",
                          "out": (lambda e, bank, dest=dest: e.activation(dest, bank[:, 0:256], ACT.Copy)) if j % 2 else
                                 (lambda e, bank, dest=dest: e.tensor_copy(dest, bank[:, 0:256]))})
    n = K.ring.first("qm")
    for c in range(4):
        items.append(channel_item(K, n, c * P, P, K.hT, S, K.qm[:, c, :], eng=("act", "dve")[c % 2],
                                  first=(n, n + 1) if c == 0 else (), rel=2 if c == 3 else 0))
    items_stage(K, items, issue=n + 2)


NU = 384


def bias_stage(K):
    T = K.T
    mm_done, added, stored, read = K.signals(4)
    table, hot, neg, u = K.at(116, 12)[0:32], K.at(117, 3, NU)[0:32], K.at(122, 3, NU)[0:4], K.at(127, 3, NU)[0:4]
    rows = K.bias_rows
    with K.nc.Block() as block:
        @block.gpsimd
        def _(pool):
            for dst, src in ((table, T["rel_bias_2"]), (hot, T["k_bucket"]), (neg, T["k_neg"]),
                             (K.flip, T["k_flip"]), (K.pick, T["k_pick"])):
                pool.dma_start(dst, src).then_inc(K.loaded, 16)
            pool.wait_ge(K.loaded, K.loads(5))

        @block.sync
        def _(sp):
            K.start(sp)
            sp.wait_ge(added, 3)
            sp.dma_start(rows.rearrange("g h n -> h g n"), u).then_inc(stored, 16)
            sp.wait_ge(stored, 16)
            n = 0
            for h in range(4):
                for dst, off, c in ((K.hank0, 0, 256), (K.hank1, 4 * NU + P, P), (K.hank2, 8 * NU + P, P)):
                    sp.dma_start(dst[:, h, :], bass.AP(rows.tensor, off + h * NU, [[1, P], [1, c]]))\
                        .then_inc(read, 16)
                    n += 16
            sp.wait_ge(read, n)

        @block.tensor
        def _(pe):
            pe.wait_ge(K.loaded, K.loads(5))
            for g in range(3):
                pe.matmul(K.ps[0:4, g, 0:NU], table[:, 4 * g:4 * g + 4], hot[:, g, :], start=True, stop=True)\
                    .then_inc(mm_done, 1)

        @block.vector
        def _(dve):
            dve.wait_ge(K.loaded, K.loads(5))
            for g in range(3):
                dve.wait_ge(mm_done, g + 1)
                dve.tensor_tensor(u[:, g, :], K.ps[0:4, g, 0:NU], neg[:, g, :], ALU.add).then_inc(added, 1)
    K.load_base = K.loads(5)


def dilated_attention_stage(K):
    (s_done, max_done, neg_done, exp_done, turned, copied, o_done, o_copied, st_turned, st_copied, chain, e_done,
     bc_done, part, summed) = K.signals(15)
    units = [(g, j, h) for g in range(3) for j in range(4) for h in range(4)]
    NUNIT = len(units)
    Pb, PT = K.at(116, 3, 256), K.at(119, 2, 2, P)
    stats = K.at(121, 3, NUNIT)
    num = K.at(122, 6, S)
    mrow, drow = K.at(134, 3, S)[0:4], K.at(140, 3, S)[0:4]
    m, tmp = K.at(146, S)[0:4], K.at(116, 2, S)

    def keys(g, j):
        return ([j - 1, j] if j else [0]) if g == 0 else [j]

    def hank(g, j, h):
        return (K.hank0[:, h, 0:256] if j else K.hank0[:, h, P:256]) if g == 0 else (K.hank1, K.hank2)[g - 1][:, h, :]

    def key_view(g, j, rows, c):
        v = K.kd[rows, c, :]
        return v[:, (j - 1) * P:(j + 1) * P] if g == 0 and j else group_tokens(v, g, j)

    def spread(v, g, j):
        return group_tokens(v, g, j)

    with K.nc.Block() as block:
        @block.sync
        def _(sp):
            K.start(sp)

        @block.tensor
        def _(pe):
            def scores(b):
                g, j, h = units[b]
                c, rows = g * 2 + h // 2, slice(64 * (h % 2), 64 * (h % 2) + 64)
                nk = P * len(keys(g, j))
                if b >= 2:
                    pe.wait_ge(exp_done, b - 1)
                out = K.ps[:, b % 2, 0:nk]
                pe.matmul(out, K.flip, hank(g, j, h), start=True, stop=False)
                pe.matmul(out, group_tokens(K.qd[rows, c, :], g, j), key_view(g, j, rows, c), start=False, stop=True)\
                    .then_inc(s_done, 1)

            def turn(b):
                g, j, h = units[b]
                pe.wait_ge(exp_done, b + 1)
                if b >= 2:
                    pe.wait_ge(copied, b - 1)
                ks = keys(g, j)
                for i in range(len(ks)):
                    ins = pe.transpose(K.ps[:, 2 + b % 2, i * P:(i + 1) * P], Pb[:, b % 3, i * P:(i + 1) * P],
                                       K.ident[:, :])
                ins.then_inc(turned, 1)

            def values(b):
                g, j, h = units[b]
                ks = keys(g, j)
                if h == 3:
                    q = b // 4
                    if q >= 1:
                        pe.wait_ge(st_copied, 2 * q)
                    for i in (0, 2):
                        ins = pe.transpose(K.ps[0:4, 6, (i // 2) * P:(i // 2 + 1) * P], stats[:, i, b - 3:b + 1],
                                           K.ident[:, :])
                    ins.then_inc(st_turned, 1)
                if h == 0 and b >= 8:
                    pe.wait_ge(o_copied, b // 4 - 1)
                pe.wait_ge(copied, b + 1)
                out = K.ps[64 * (h % 2):64 * (h % 2) + 64, 4 + (b // 4) % 2, (h // 2) * P:(h // 2 + 1) * P]
                accumulate(pe, out, [(K.vd[:, g * 4 + kt, 64 * h:64 * h + 64], PT[:, b % 2, i, :])
                                     for i, kt in enumerate(ks)]).then_inc(o_done, 1)

            for a in range(NUNIT + 3):
                if a < NUNIT:
                    scores(a)
                if 0 <= a - 2 < NUNIT:
                    turn(a - 2)
                if a >= 3:
                    values(a - 3)
            pe.wait_ge(chain, 11)
            for i in range(6):
                if i >= 2:
                    pe.wait_ge(part, i - 1)
                pe.matmul(K.ps[:, i % 2, :], K.pick[:, (i % 2) * P:(i % 2 + 1) * P], drow[:, i // 2, :], start=True,
                          stop=True).then_inc(bc_done, 1)

        @block.scalar
        def _(act):
            def empty(b):
                g, j, h = units[b]
                if h == 3:
                    q = b // 4
                    act.wait_ge(st_turned, q + 1)
                    for dst, c in ((mrow, 0), (drow, 1)):
                        act.activation(spread(dst[:, g, :], g, j), K.ps[0:4, 6, c * P:(c + 1) * P],
                                       ACT.Copy).then_inc(st_copied, 1)
                    act.wait_ge(o_done, b + 1)
                    for pr in range(2):
                        ins = act.activation(spread(num[:, 2 * g + pr, :], g, j),
                                             K.ps[:, 4 + q % 2, pr * P:(pr + 1) * P], ACT.Copy)
                    ins.then_inc(o_copied, 1)

            for b in range(NUNIT + 3):
                if b < NUNIT:
                    g, j, h = units[b]
                    nk = P * len(keys(g, j))
                    act.wait_ge(neg_done, b + 1)
                    if b >= 3:
                        act.wait_ge(turned, b - 2)
                    act.activation(Pb[:, b % 3, 0:nk], K.ps[:, b % 2, 0:nk], ACT.Exp, bias=stats[:, 1, b:b + 1],
                                   accum_out=stats[:, 2, b:b + 1]).then_inc(exp_done, 1)
                if b >= 3:
                    empty(b - 3)
            for g in range(3):
                act.wait_ge(chain, 2 + g + 1)
                act.activation(mrow[:, g, :], mrow[:, g, :], ACT.Exp).then_inc(e_done, 1)

        @block.vector
        def _(dve):
            def maximum(b):
                g, j, h = units[b]
                dve.wait_ge(s_done, b + 1)
                dve.tensor_reduce(stats[:, 0, b:b + 1], K.ps[:, b % 2, 0:P * len(keys(g, j))], AX.X, ALU.max)\
                    .then_inc(max_done, 1)
                dve.wait_ge(max_done, b + 1)
                dve.tensor_scalar(stats[:, 1, b:b + 1], stats[:, 0, b:b + 1], -1.0, None, ALU.mult)\
                    .then_inc(neg_done, 1)

            for a in range(NUNIT + 2):
                if a < NUNIT:
                    maximum(a)
                if a < 2:
                    continue
                b = a - 2
                g, j, h = units[b]
                n = len(keys(g, j))
                dve.wait_ge(turned, b + 1)
                if b >= 2:
                    dve.wait_ge(o_done, b - 1)
                dve.tensor_copy(PT[:, b % 2, 0:n, :], K.ps[:, 2 + b % 2, 0:n * P].rearrange("p (i q) -> p i q", q=P))\
                    .then_inc(copied, 1)
            dve.wait_ge(st_copied, 24)
            dve.tensor_tensor(m, mrow[:, 0, :], mrow[:, 1, :], ALU.max).then_inc(chain, 1)
            dve.wait_ge(chain, 1)
            dve.tensor_tensor(m, m, mrow[:, 2, :], ALU.max).then_inc(chain, 1)
            dve.wait_ge(chain, 2)
            for g in range(3):
                dve.tensor_tensor(mrow[:, g, :], mrow[:, g, :], m, ALU.subtract).then_inc(chain, 1)
            t0 = tmp[0:4, 0, :]
            for g in range(3):
                dve.wait_ge(e_done, g + 1)
                dve.wait_ge(chain, 5 if g == 0 else 5 + g)
                if g == 0:
                    dve.tensor_tensor(m, drow[:, 0, :], mrow[:, 0, :], ALU.mult).then_inc(chain, 1)
                else:
                    dve.tensor_tensor(drow[:, g, :], drow[:, g, :], mrow[:, g, :], ALU.mult).then_inc(chain, 1)
            dve.wait_ge(chain, 8)
            dve.tensor_tensor(t0, drow[:, 1, :], drow[:, 2, :], ALU.add).then_inc(summed, 1)
            dve.wait_ge(summed, 1)
            dve.tensor_tensor(m, m, t0, ALU.add).then_inc(summed, 1)
            dve.wait_ge(summed, 2)
            dve.reciprocal(m, m).then_inc(summed, 1)
            dve.wait_ge(summed, 3)
            for g in range(3):
                dve.tensor_tensor(drow[:, g, :], mrow[:, g, :], m, ALU.mult).then_inc(chain, 1)
            dve.wait_ge(o_copied, 12)
            for i in range(6):
                g, pr = i // 2, i % 2
                dve.wait_ge(bc_done, i + 1)
                dest = K.odT[:, pr, :]
                dve.tensor_tensor(dest if g == 0 else tmp[:, pr, :], K.ps[:, i % 2, :], num[:, i, :], ALU.mult)\
                    .then_inc(part, 1)
                dve.wait_ge(part, i + 1)
                if g:
                    dve.tensor_tensor(dest, dest, tmp[:, pr, :], ALU.add).then_inc(summed, 1)
                    dve.wait_ge(summed, 3 + i - 1)


def memory_attention_stage(K):
    attention_stage(K, 4, NCTX, lambda h, i: [(slice(0, NCTX), K.qm[:, h, i * P:(i + 1) * P], K.kmT[:, h, :])],
                    lambda h, j: K.vm[:, j, h * P:(h + 1) * P], lambda h: K.omT[:, h, :], P ** -0.5, 116)


def split_products(pe, out, triples, before=None):
    for n, (w_hi, w_lo, x_hi, x_lo) in enumerate(triples):
        if before:
            before(n)
        pe.matmul(out, w_hi, x_hi, start=(n == 0), stop=False)
        pe.matmul(out, w_hi, x_lo, start=False, stop=False)
        last = pe.matmul(out, w_lo, x_hi, start=False, stop=(n == len(triples) - 1))
    return last


def mlp_stage(K):
    r, T = K.ring, K.T
    (h_hi_done, h_lo_done, w_hi_done, spent, up_done, relu_done, prod_done, hid_hi_done, hid_done, down_done,
     x_added) = K.signals(11)
    n0 = r.first("mlp")
    UNITS, CH, FT = 8, 4, 4
    BODY = 3
    LOOPS = UNITS // BODY
    BC = BODY * CH
    h_hi, h_lo = K.rounded_at(32, KD, S), K.rounded_at(48, KD, S)
    hid_hi, hid_lo = K.rounded_at(64, FT, S), K.rounded_at(72, FT, S)
    relu, prod = K.at(144, 2, S), K.at(148, 2, S)
    win, wout = T["w_mlp_in_2"], T["w_mlp_out_2"]

    def raw(c):
        return r.slots[(n0 + c) % RING]

    def part(c, lo):
        return K.rounded_at(80 + 16 * (c % CH) + 8 * lo, 4, HALF)

    def flat(v):
        return v.rearrange("p t c -> p (t c)")

    with K.nc.Block() as block:
        @block.sync
        def _(sp):
            K.start(sp)
            with sp.Fori(0, LOOPS) as i:
                for k in range(BC):
                    c = k + RING
                    u, s = i * BODY + c // CH, c % CH
                    sp.wait_ge(r.used, i * BC + (n0 + c - RING + 1))
                    src = (win[s * HALF:(s + 1) * HALF, bass.ds(u * HALF, HALF)] if s < 2 else
                           wout[bass.ds(u * HALF, HALF), (s - 2) * HALF:(s - 1) * HALF])
                    sp.dma_start(raw(c).rearrange("p (t c) -> p t c", c=HALF), src.rearrange("(t p) c -> p t c", p=P))\
                        .then_inc(r.arrived[(n0 + c) % RING], 16)
            r.issued = n0 + RING + LOOPS * BC
            r.issue_until(sp, n0 + UNITS * CH + RING)

        @block.gpsimd
        def _(pool):
            def rest(c, i):
                pool.wait_ge(w_hi_done, i * BC + c + 1)
                pool.tensor_tensor(flat(part(c, 1)), raw(c)[:, :], flat(part(c, 0)).bitcast(F32), ALU.subtract)\
                    .then_inc(r.used, 1)

            with pool.Fori(0, LOOPS) as i:
                for c in range(BC):
                    rest(c, i)
            for c in range(LOOPS * BC, UNITS * CH):
                rest(c, 0)

        @block.tensor
        def _(pe):
            def unit(v, i):
                u = i * BODY + v
                for f in range(FT):
                    pe.wait_ge(prod_done, u * FT + f + 1)
                    if f == 0:
                        pe.wait_ge(r.used, i * BC + (n0 + v * CH + 2))
                    ins = split_products(pe, K.ps[:, f % 2, :],
                                         [(part(k // 4, 0)[:, k % 4, f * P:(f + 1) * P],
                                           part(k // 4, 1)[:, k % 4, f * P:(f + 1) * P], h_hi[:, k, :], h_lo[:, k, :])
                                          for k in range(KD)])
                    ins.then_inc(up_done, 1)
                spend(2)
                for t in range(KD):
                    pe.wait_ge(x_added, u * KD + t + 1)
                    if t % 4 == 0:
                        pe.wait_ge(r.used, i * BC + (n0 + v * CH + 3 + t // 4))
                    c = 2 + t // 4
                    cols = slice((t % 4) * P, (t % 4 + 1) * P)
                    split_products(pe, K.ps[:, 4 + t % 2, :],
                                   [(part(c, 0)[:, k, cols], part(c, 1)[:, k, cols], hid_hi[:, k, :], hid_lo[:, k, :])
                                    for k in range(FT)],
                                   before=(lambda k: pe.wait_ge(hid_done, u * FT + k + 1)) if t == 0 else None)\
                        .then_inc(down_done, 1)
                    if t % 4 == 3:
                        spend(1)

            def spend(count):
                pe.matmul(K.ps[:, 7, 511:512], K.ones[:, :], K.ones[:, 0:1], start=True, stop=True)\
                    .then_inc(spent, count)

            pe.wait_ge(h_lo_done, KD)
            with pe.Fori(0, LOOPS) as i:
                for v in range(BODY):
                    unit(v, i)
            for v in range(LOOPS * BODY, UNITS):
                unit(v, 0)

        @block.scalar
        def _(act):
            def high(c, i):
                n = n0 + c
                act.wait_ge(r.arrived[n % RING], i * 32 + r.arrival(n))
                if c >= CH:
                    act.wait_ge(spent, i * BC + c - CH + 1)
                act.activation(flat(part(c, 0)), raw(c)[:, :], ACT.Copy).then_inc(w_hi_done, 1)

            def unit(v, i):
                u = i * BODY + v
                for f in range(FT):
                    act.wait_ge(up_done, u * FT + f + 1)
                    act.wait_ge(prod_done, u * FT + f + 1)
                    act.activation(relu[:, f % 2, :], K.ps[:, f % 2, :], ACT.Relu).then_inc(relu_done, 1)

            for k in range(KD):
                act.activation(h_hi[:, k, :], K.hT[:, k, :], ACT.Copy).then_inc(h_hi_done, 1)
            for c in range(CH):
                high(c, 0)
            with act.Fori(0, LOOPS) as i:
                for v in range(BODY):
                    unit(v, i)
                    for s in range(CH):
                        high((v + 1) * CH + s, i)
            for v in range(LOOPS * BODY, UNITS):
                unit(v, 0)
                if v + 1 < UNITS:
                    for s in range(CH):
                        high((v + 1) * CH + s, 0)

        @block.vector
        def _(dve):
            for k in range(KD):
                dve.wait_ge(h_hi_done, k + 1)
                dve.tensor_tensor(h_lo[:, k, :], K.hT[:, k, :], h_hi[:, k, :].bitcast(F32), ALU.subtract)\
                    .then_inc(h_lo_done, 1)
            for b in range(2):
                dve.memset(prod[:, b, 0:1], 0.0).then_inc(prod_done, 1)
                dve.memset(prod[:, b, 1:2], 0.0).then_inc(x_added, 1)
            dve.wait_ge(prod_done, 2)
            dve.wait_ge(x_added, 2)
            with dve.Fori(0, UNITS) as u:
                for f in range(FT):
                    m = prod[:, f % 2, :]
                    dve.wait_ge(relu_done, u * FT + f + 1)
                    dve.tensor_tensor(m, K.ps[:, f % 2, :], relu[:, f % 2, :], ALU.mult).then_inc(prod_done, 1)
                    dve.wait_ge(prod_done, u * FT + f + 3)
                    dve.tensor_copy(hid_hi[:, f, :], m).then_inc(hid_hi_done, 1)
                    dve.wait_ge(hid_hi_done, u * FT + f + 1)
                    dve.tensor_tensor(hid_lo[:, f, :], m, hid_hi[:, f, :].bitcast(F32), ALU.subtract)\
                        .then_inc(hid_done, 1)
                for t in range(KD):
                    dve.wait_ge(down_done, u * KD + t + 1)
                    dve.tensor_tensor(K.xT[:, t, :], K.ps[:, 4 + t % 2, :], K.xT[:, t, :], ALU.add)\
                        .then_inc(x_added, 1)
            dve.wait_ge(x_added, UNITS * KD + 2)


def store_stage(K):
    (stored,) = K.signals(1)
    with K.nc.Block() as block:
        @block.sync
        def _(sp):
            K.start(sp)
            sp.dma_start(K.out.rearrange("(t p) n -> p t n", p=P), K.hT).then_inc(stored, 16)
            sp.wait_ge(stored, 16)


def load_memory_stage(K):
    (came,) = K.signals(1)
    with K.nc.Block() as block:
        @block.sync
        def _(sp):
            K.start(sp)
            sp.dma_start(K.memT, K.T["memT"].rearrange("(t p) n -> p t n", p=P)).then_inc(came, 16)
            sp.wait_ge(came, 16)


def host_constants():
    f32 = np.float32
    out = {"k_ident": np.eye(P, dtype=f32)}
    pos = np.arange(S)
    inv = f32(10000.0) ** (-np.arange(32, dtype=f32) / f32(32))
    ang = np.concatenate([(pos // 64).astype(f32)[:, None] * inv, (pos % 64).astype(f32)[:, None] * inv], axis=1)
    out["k_cos"] = np.repeat(np.cos(ang.astype(f32)), 2, axis=1).T.astype(f32)
    out["k_sin"] = np.repeat(np.sin(ang.astype(f32)), 2, axis=1).T.astype(f32)
    swap = np.zeros((P, P), f32)
    for i in range(0, P, 2):
        swap[i + 1, i] = -1.0
        swap[i, i + 1] = 1.0
    out["k_swap"] = swap
    scan = np.ones((P, S + NCTX), f32)
    scan[:, 0:S:64] = 0.0
    scan[:, S] = 0.0
    out["k_scan"] = scan
    t = np.arange(S, dtype=f32)
    tn = (t / f32(S)).astype(f32)
    bands = np.linspace(1e-4, 15, 16, dtype=f32)
    phase = (f32(2 * np.pi / S) * t[:, None] * bands[None, :]).astype(f32)
    out["k_pos"] = np.concatenate([tn[:, None], np.cos(phase), -np.sin(phase)], axis=1).T.astype(f32)
    first = np.ones(P, f32)
    first[0] = 0.0
    out["k_time"] = np.concatenate([-tn.reshape(ST, P).T, first[:, None]], axis=1)
    nn = 2 * S
    ang2 = 2 * np.pi * ((np.arange(S)[:, None] * np.arange(S)[None, :]) % nn) / nn
    alt = 1.0 - 2.0 * (np.arange(S) % 2)
    cosm, sinm = np.cos(ang2), -np.sin(ang2)
    out["k_dft_cos"] = cosm.astype(f32)
    s1 = sinm.copy()
    s1[:, 0] = alt
    out["k_dft_sin"] = s1.astype(f32)
    c1 = cosm[:, 0:P].copy()
    c1[:, 0] = alt
    out["k_dft_edge"] = np.concatenate([c1, sinm[:, 0:P]], axis=1).astype(f32)
    ic, isn = 2.0 * cosm / nn, 2.0 * sinm / nn
    ic[0] = 1.0 / nn
    isn[0] = alt / nn
    out["k_idft_cos"] = ic.astype(f32)
    out["k_idft_sin"] = isn.astype(f32)
    hot, neg = np.zeros((32, 3, NU), f32), np.zeros((4, 3, NU), f32)
    for g, (dil, each) in enumerate(((1, 1), (4, 1), (4, 4))):
        for j in range(NU):
            off = 255 - j
            if not (0 <= off <= P and off % each == 0):
                neg[:, g, j] = NEG
                continue
            dist = off * dil
            b = dist
            if dist >= 16:
                large = f32(np.log(f32(dist) / f32(16))) / f32(np.log(128.0)) * f32(16)
                b = min(16 + int(large), 31)
            hot[b, g, j] = 1.0
    out["k_bucket"], out["k_neg"] = hot, neg
    out["k_flip"] = np.eye(P, dtype=f32)[::-1]
    pick = np.zeros((4, 256), f32)
    for h in range(4):
        pick[h, (h // 2) * P + 64 * (h % 2):(h // 2) * P + 64 * (h % 2) + 64] = 1.0
    out["k_pick"] = pick
    out["k_upto"] = np.triu(np.ones((P, P), f32))
    out["k_slot_no"] = np.tile(np.arange(1, P + 1, dtype=f32), (P, 1))
    a = np.arange(P)
    same = (a[:, None] // 64) == (a[None, :] // 64)
    out["k_causal"] = np.stack([same & (a[:, None] <= a[None, :]), same & (a[:, None] >= a[None, :])]).astype(f32)
    return out


WEIGHTS = ["w_mod", "w_in", "gla_wa2", "hy_pos_w1", "hy_pos_w2", "hy_pos_w3", "w_br_hy", "w_br_gla", "w_br_att",
           "w_out", "router_w", "moe_w_gate", "moe_w_up", "moe_w_down", "w_in_2", "w_rg_a_2", "w_rg_x_2",
           "w_lru_out_2", "rel_bias_2", "w_dil_out_2", "w_mem_kv_2", "w_mem_out_2", "w_out_2", "w_mlp_in_2",
           "w_mlp_out_2"]
ROWS = ["gla_norm_g", "hy_decay", "hy_skip", "router_b"]


def layout(inputs):
    out = {k: np.ascontiguousarray(v) for k, v in host_constants().items()}
    for name in WEIGHTS:
        a = np.asarray(inputs[name])
        out[name] = np.ascontiguousarray(a[0] if a.shape[0] == 1 else a)
    for name in ROWS:
        out[name] = np.ascontiguousarray(np.asarray(inputs[name]).reshape(1, -1))
    out["xT"] = np.ascontiguousarray(np.asarray(inputs["x"])[0].T)
    out["ctxT"] = np.ascontiguousarray(np.asarray(inputs["ctx"])[0].T)
    out["memT"] = np.ascontiguousarray(np.asarray(inputs["mem_2"])[0].T)
    out["hy_cols"] = np.ascontiguousarray(
        np.stack([np.asarray(inputs[n]).reshape(-1) for n in ("hy_pos_b1", "hy_pos_b2", "hy_sin_freq")], axis=1))
    out["vecs"] = np.ascontiguousarray(
        np.concatenate([np.asarray(inputs[n]).reshape(-1, P).T for n, _ in VECS], axis=1))
    return out


def build(nc, T, out, upto=99, debug=None):
    with ExitStack() as ctx:
        K = Core(nc, ctx, T)
        K.out = out
        K.sc = ctx.enter_context(nc.sbuf_tensor("silu_c", [P, KD, 2], F32))
        g = ctx.enter_context(nc.sbuf_tensor("gains", [P, 24], F32))
        K.gain1, K.gain1c, K.gain2 = g[:, 0:8], g[:, 8:16], g[:, 16:24]
        K.xT, K.hT = K.at(0, KD, S), K.at(16, KD, S)
        K.tot = ctx.enter_context(nc.sbuf_tensor("chunk_decay", [P, 4, 9], F32))
        K.over_list = ctx.enter_context(nc.sbuf_tensor("overflow_list", [1, NEXP + 1], mybir.dt.int32))
        K.gate_rows = nc.dram_tensor("gate_rows", (NEXP, S), F32).ap()
        plan_block1(K)
        K.bias_rows = nc.dram_tensor("bias_rows", (3, 4, NU), F32).ap()
        plan_block2(K)
        done = 0
        for rounded_kb, stages in ((0, block1_stages), (80, expert_stages), (0, block2_stages),
                                   (112, lambda K: [lambda: mlp_stage(K)]), (0, final_stages)):
            with K.phase(rounded_kb):
                for st in stages(K):
                    if done < upto:
                        st()
                        done += 1
                        if debug and done == upto:
                            dump(K, debug)


def dump(K, debug):
    (done,) = K.signals(1)
    with K.nc.Block() as block:
        @block.sync
        def _(sp):
            K.start(sp)
            n = 0
            for ap, src in debug(K):
                sp.dma_start(ap, src).then_inc(done, 16)
                n += 16
            sp.wait_ge(done, n)


def plan_block1(K):
    r, T = K.ring, K.T
    w = T["w_mod"].rearrange("(h t p) c -> h p t c", h=2, p=P)
    for g in range(12):
        for h in range(2):
            r.add("mod", w[h][:, :, g * HALF:(g + 1) * HALF])
    w = T["w_in"]
    r.add_matrix("gk", w, C_GK, C_GK + 256)
    r.add_matrix("gv", w, C_GV, C_GV + 512)
    r.add_matrix("ga", w, C_GA, C_GA + 32)
    r.add_matrix("gq", w, C_GQ, C_GQ + 256)
    r.add_matrix("og", w, C_OG, C_OG + 512)
    r.add_matrix("kv", w, C_KV, C_KV + 512)
    r.add_matrix("q", w, C_Q, C_Q + 1024)
    r.add_matrix("hy", w, C_HY, C_HY + 1536)
    for o in range(2):
        for m in ("k_dft_cos", "k_dft_sin", "k_dft_edge", "k_idft_cos", "k_idft_sin"):
            r.add_matrix(f"dft{o}", T[m], 0, T[m].shape[1])
    for half in range(2):
        for b, y in enumerate(("w_br_hy", "w_br_gla", "w_br_att")):
            a = half * HALF
            r.add_matrix("merge1", w, C_BR + b * D + a, C_BR + b * D + a + HALF)
            r.add_matrix("merge1", T[y], a, a + HALF)
    r.add_matrix("out1", T["w_out"], 0, D)
    for g in range(NEXP // GE):
        for j, m, h in moe_order():
            w = T[("moe_w_gate", "moe_w_up", "moe_w_down")[m]][g * GE + j]
            s = slice(h * HALF, (h + 1) * HALF)
            r.add("moe", (w[:, s] if m == 2 else w[s, :]).rearrange("(t p) c -> p t c", p=P))


def plan_block2(K):
    r, T = K.ring, K.T
    w = T["w_in_2"]
    r.add_matrix("mem", T["w_mem_kv_2"], 0, D)
    r.add_matrix("lru", w, C2_X, C2_X + 512)
    r.add_matrix("lru", w, C2_G, C2_G + 512)
    r.add_matrix("lru", w, C2_X + 512, C2_X + 768)
    r.add_matrix("lru", w, C2_G + 512, C2_G + 768)
    r.add_matrix("qkv", w, C2_QKV, C2_QKV + 2304)
    r.add_matrix("qm", w, C2_QM, C2_QM + 512)
    for half in range(2):
        for b, y in enumerate(("w_lru_out_2", "w_dil_out_2", "w_mem_out_2")):
            a = half * HALF
            r.add_matrix("merge2", w, C2_BR + b * D + a, C2_BR + b * D + a + HALF)
            r.add_matrix("merge2", T[y], a, a + HALF)
    r.add_matrix("out2", T["w_out_2"], 0, D)
    for u in range(8):
        r.add_matrix("mlp", T["w_mlp_in_2"], u * HALF, (u + 1) * HALF)
        r.add_matrix("mlp", T["w_mlp_out_2"][u * HALF:(u + 1) * HALF, :], 0, D)


def gain_of(K, name):
    return lambda t: K.vec(name, t)


def block2_stages(K):
    K.ylruT, K.odT, K.omT = K.at(32, 6, S), K.at(44, 2, S), K.at(48, 4, S)
    K.rg = K.at(92, 2, 6, P)
    K.qd, K.kd, K.vd, K.qm = K.at(56, 6, S), K.at(68, 6, S), K.at(80, 12, 256), K.at(92, 4, S)
    K.kmT, K.vm = K.at(100, 4, NCTX), K.at(104, 2, 512)
    K.hank0, K.hank1, K.hank2 = K.at(108, 4, 256), K.at(112, 4, P), K.at(114, 4, P)
    K.memT = K.at(56, KD, NCTX)
    K.lru_rate, K.flip, K.pick = K.at(151.5, 6), K.at(151, P), K.at(150, 256)[0:4]
    m2 = K.at(56, KD, S)
    return [
        lambda: moe_overflow_stage(K),
        lambda: load_memory_stage(K),
        lambda: norm_stage(K, [(K.memT, NCTX, K.memT, gain_of(K, "g_mem_2"), None),
                               (K.xT, S, K.hT, gain_of(K, "g_mix_2"), None)], 72),
        lambda: memory_project_stage(K),
        lambda: lru_weights_stage(K),
        lambda: lru_stage(K),
        lambda: dilated_project_stage(K),
        lambda: bias_stage(K),
        lambda: dilated_attention_stage(K),
        lambda: memory_attention_stage(K),
        lambda: merge_stage(K, "merge2", K.hT, [(K.ylruT, 6), (K.odT, 2), (K.omT, 4)], m2, "b_gate_2"),
        lambda: residual_stage(K, "out2", m2, None),
        lambda: norm_stage(K, [(K.xT, S, K.hT, gain_of(K, "g_mlp_2"), None)], 72),
    ]


def final_stages(K):
    return [
        lambda: norm_stage(K, [(K.xT, S, K.hT, gain_of(K, "g_final_2"), None)], 72),
        lambda: store_stage(K),
    ]


def block1_stages(K):
    K.hcT = K.at(32, KD, NCTX)
    K.yattT, K.yglaT = K.at(40, 8, S), K.at(56, 4, S)
    K.gv, K.gq, K.gk, K.ga, K.og = K.at(64, 6, 512), K.at(76, 2, S), K.at(80, 2, 768), K.at(86, 2, 768), K.at(92, 4, 512)
    K.qdec, K.kinv, K.kend, K.states = K.at(100, 4, S), K.at(108, 4, S), K.at(116, 6, 4, P), K.at(128, 4, 9, P)
    K.kT, K.v, K.qT = K.at(72, 2, S + NCTX), K.at(78, 6, 256), K.at(84, 8, S)
    K.yhyT, K.x2T, K.x1, K.z = (K.at(64 + 8 * i, 4, S) for i in range(4))
    K.Rf, K.If, K.edge, K.hid = K.at(128, 4, S), K.at(136, 4, S), K.at(144, S), K.at(146, S)[0:64]
    K.mT = K.at(72, 8, S)
    return [
        lambda: mod_stage(K),
        lambda: norm_stage(K, [
            (K.xT, S, K.hT, lambda t: K.gain1[:, t:t + 1], lambda t: mod_col(K, 0, t)),
            (K.at(40, KD, NCTX), NCTX, K.hcT, lambda t: K.gain1c[:, t:t + 1], lambda t: mod_col(K, 0, t, 1))], 72),
        lambda: gla_project_stage(K),
        lambda: gla_decay_stage(K),
        lambda: gla_chunk_stage(K),
        lambda: qk_stage(K),
        lambda: latent_attention_stage(K),
        lambda: hyena_project_stage(K),
        lambda: hyena_hidden_stage(K),
        lambda: hyena_filter_stage(K, 0),
        lambda: hyena_conv_stage(K, 0),
        lambda: hyena_filter_stage(K, 1),
        lambda: hyena_conv_stage(K, 1),
        lambda: merge_stage(K, "merge1", K.hT, [(K.yhyT, 4), (K.yglaT, 4), (K.yattT, 8)], K.mT),
        lambda: residual_stage(K, "out1", K.mT, lambda t: mod_col(K, 2, t)),
        lambda: norm_stage(K, [(K.xT, S, K.hT, lambda t: K.gain2[:, t:t + 1], lambda t: mod_col(K, 3, t))], 72),
    ]


def expert_stages(K):
    K.h_hi, K.h_lo = K.rounded_at(32, ST, D), K.rounded_at(48, ST, D)
    K.gates, K.place, K.slot_no = K.at(150, 64), K.at(150.25, 64 + GE), K.at(151, P)
    return [
        lambda: router_stage(K),
        lambda: moe_stage(K),
    ]


def kernel(**inputs):
    import concourse.bacc as bacc
    from concourse.bass_utils import run_bass_kernel_spmd

    nc = bacc.Bacc("TRN2", target_bir_lowering=False, num_devices=1)
    arrays = layout(inputs)
    T = {k: nc.dram_tensor(k, v.shape, mybir.dt.from_np(v.dtype), kind="ExternalInput").ap() for k, v in arrays.items()}
    out = nc.dram_tensor("out", (D, S), F32, kind="ExternalOutput").ap()
    build(nc, T, out)
    r = run_bass_kernel_spmd(nc, [arrays], core_ids=[0])
    return np.ascontiguousarray(np.asarray(r.results[0]["out"]).T).reshape(1, S, D)
```

```python
from contextlib import ExitStack, contextmanager

import numpy as np

import concourse.bass as bass
from concourse import mybir
from concourse.alu_op_type import AluOpType as ALU

F32 = mybir.dt.float32
F32R = mybir.dt.float32r
ACT = mybir.ActivationFunctionType
AX = mybir.AxisListType

P = 128
D = 1024
KD = D // P
S = 512
NCTX = 256
ST = S // P
CT = NCTX // P
EPS = 1e-6
HALF = 512
RING = 6
NMARKS = 16
NSIG = 20

VECS = [("c", 8), ("c_ctx", 8), ("b_mod", 48), ("norm1_g", 8), ("norm2_g", 8), ("q_norm_g", 1), ("k_norm_g", 1),
        ("gla_ba", 4), ("hy_conv_w", 36), ("hy_conv_b", 12),
        ("g_mix_2", 8), ("b_gate_2", 24), ("conv_w_2", 24), ("conv_b_2", 6), ("b_rg_a_2", 6), ("b_rg_x_2", 6),
        ("lru_lambda_2", 6), ("g_mem_2", 8), ("g_mlp_2", 8), ("g_final_2", 8)]
VEC_AT = {}
NVEC = 0
for _name, _n in VECS:
    VEC_AT[_name] = NVEC
    NVEC += _n

C_KV, C_GK, C_GV, C_GA = 0, 512, 768, 1280
C_Q, C_GQ, C_OG, C_HY, C_BR = 1312, 2336, 2592, 3104, 4640
C2_X, C2_G, C2_QKV, C2_QM, C2_BR = 0, 768, 1536, 3840, 4352
NEG = -1e30
ARENA_KB = 152
NEXP = 16
GE = 4
SLOTS = P


class Ring:

    def __init__(self, nc, ctx):
        self.slots = [ctx.enter_context(nc.sbuf_tensor(f"weights{i}", [P, 4 * HALF], F32)) for i in range(RING)]
        self.arrived = [ctx.enter_context(nc.semaphore(f"arrived{i}")) for i in range(RING)]
        self.used = ctx.enter_context(nc.semaphore("used"))
        self.plan = []
        self.issued = 0

    def add(self, name, ap):
        self.plan.append((name, ap))

    def add_matrix(self, name, w, c0, c1):
        rows = w.shape[0]
        for a in range(c0, c1, HALF):
            b = min(a + HALF, c1)
            for r in range(0, rows, HALF):
                q = min(HALF, rows - r)
                self.add(name, w[r:r + q, a:b].rearrange("(t p) c -> p t c", p=P))

    def first(self, name):
        return [n for n, _ in self.plan].index(name)

    def view(self, n):
        _, ap = self.plan[n]
        t, c = ap.shape[1], ap.shape[2]
        return self.slots[n % RING][:, 0:t * c].rearrange("p (t c) -> p t c", c=c)

    def arrival(self, n):
        return 16 * (n // RING + 1)

    def issue_until(self, sp, n):
        for k in range(self.issued, min(n, len(self.plan))):
            if k >= RING:
                sp.wait_ge(self.used, k - RING + 1)
            sp.dma_start(self.view(k), self.plan[k][1]).then_inc(self.arrived[k % RING], 16)
        self.issued = max(self.issued, min(n, len(self.plan)))


class Core:

    def __init__(self, nc, ctx, T):
        self.nc, self.T = nc, T
        self.ring = Ring(nc, ctx)
        self.regions, self.plain, self.rounded = 0, [], []
        self.marks = ctx.enter_context(nc.sbuf_tensor("marks", [P, NMARKS], F32))
        self.vecs = ctx.enter_context(nc.sbuf_tensor("vec_cols", [P, NVEC], F32))
        self.ident = ctx.enter_context(nc.sbuf_tensor("ident", [P, P], F32))
        self.ones = ctx.enter_context(nc.sbuf_tensor("ones", [P, P], F32))
        self.mods = ctx.enter_context(nc.sbuf_tensor("mods", [P, 96], F32))
        self.ps = ctx.enter_context(nc.psum_tensor("ps", [P, 8, 512], F32))
        self.router = ctx.enter_context(nc.sbuf_tensor("router", [P, (KD + 1) * NEXP + 2 * P], F32))
        self.banks = [[ctx.enter_context(nc.semaphore(f"sig{b}_{i}")) for i in range(NSIG)] for b in range(2)]
        self.loaded = ctx.enter_context(nc.semaphore("loaded"))
        self.load_base = 0
        self.stage = 0

    def loads(self, k):
        return self.load_base + 16 * k

    def signals(self, n):
        self.stage += 1
        self.idle = self.banks[(self.stage + 1) % 2]
        return self.banks[self.stage % 2][:n]

    def start(self, eng):
        if self.stage > 1:
            lo = min(s.num for s in self.idle)
            eng.sem_clear(range(lo, lo + NSIG))

    @contextmanager
    def region(self, low, high, dtype=F32):
        self.regions += 1
        kind = self.rounded if dtype == F32R else self.plain
        with self.nc.sbuf_tensor(f"region{self.regions}", [P, (high - low) * 256], dtype) as mem:
            kind.append((low, high, mem))
            yield
            kind.pop()

    @staticmethod
    def shaped(v, dims):
        if len(dims) == 2:
            v = v.rearrange("p (a b) -> p a b", b=dims[1])
        if len(dims) == 3:
            v = v.rearrange("p (a b c) -> p a b c", b=dims[1], c=dims[2])
        return v

    def at(self, kb, *dims):
        return self.find(self.plain, kb, dims)

    def rounded_at(self, kb, *dims):
        return self.find(self.rounded, kb, dims)

    def find(self, regions, kb, dims):
        n = int(np.prod(dims))
        for low, high, mem in regions:
            if low <= kb and kb * 256 + n <= high * 256:
                o = int((kb - low) * 256)
                return self.shaped(mem[:, o:o + n], dims)
        raise AssertionError(f"no region holds {dims} at {kb}")

    def vec(self, name, t=0):
        o = VEC_AT[name] + t
        return self.vecs[:, o:o + 1]




def accumulate(pe, out, pairs):
    for n, (l, r) in enumerate(pairs):
        last = pe.matmul(out, l, r, start=(n == 0), stop=(n == len(pairs) - 1))
    return last


def project(K, pe, n, col, m, x, tokens, out):
    for k in range(KD):
        w = K.ring.view(n + k // 4)
        ins = pe.matmul(out, w[:, k % 4, col:col + m], x[:, k, tokens], start=(k == 0), stop=(k == KD - 1))
    return ins


def split_products(pe, out, triples, before=None):
    for n, (w_hi, w_lo, x_hi, x_lo) in enumerate(triples):
        if before:
            before(n)
        pe.matmul(out, w_hi, x_hi, start=(n == 0), stop=False)
        pe.matmul(out, w_hi, x_lo, start=False, stop=False)
        last = pe.matmul(out, w_lo, x_hi, start=False, stop=(n == len(triples) - 1))
    return last


def arrived(K, pe, n, count=2):
    for k in range(n, n + count):
        pe.wait_ge(K.ring.arrived[k % RING], K.ring.arrival(k))


def release(K, pe, count=2):
    pe.matmul(K.ps[:, 7, 511:512], K.ones[:, :], K.ones[:, 0:1], start=True, stop=True).then_inc(K.ring.used, count)


def router_loads(K):
    w, b, upto, slot_no = router_views(K)
    T = K.T
    return [(w, T["router_w"].rearrange("(t p) e -> p t e", p=P)), (b, T["router_b"].broadcast_to([P, NEXP])),
            (upto, T["k_upto"]), (slot_no, T["k_slot_no"])]


def router_views(K):
    n = KD * NEXP
    v = K.router
    return (v[:, 0:n].rearrange("p (t e) -> p t e", e=NEXP), v[:, n:n + NEXP], v[:, n + NEXP:n + NEXP + P],
            v[:, n + NEXP + P:n + NEXP + 2 * P])


def mod_stage(K):
    r, T = K.ring, K.T
    act_ready, rows_copied, turned, modded, loaded, ident_in, inputs_in = K.signals(7)
    n0 = r.first("mod")
    GROUPS, BODY = 12, 3
    sc, rows = K.sc, K.at(64, BODY, HALF)[0:2]
    cols = K.ps[:, 0, 0:96]
    w = T["w_mod"].rearrange("(h t p) c -> h p t c", h=2, p=P)
    with K.nc.Block() as block:
        @block.sync
        def _(sp):
            sp.dma_start(K.vecs[:, :], T["vecs"]).then_inc(loaded, 16)
            r.issue_until(sp, 1)
            sp.dma_start(K.ident[:, :], T["k_ident"]).then_inc(ident_in, 16)
            r.issue_until(sp, RING)
            with sp.Fori(1, GROUPS // BODY) as i:
                for s in range(RING):
                    sp.wait_ge(r.used, i * RING + (n0 + s + 1 - RING))
                    sp.dma_start(r.slots[s][:, :].rearrange("p (t c) -> p t c", c=HALF),
                                 w[s % 2][:, :, bass.ds(i * BODY * HALF + (s // 2) * HALF, HALF)])\
                        .then_inc(r.arrived[s], 16)
            r.issued = n0 + 2 * GROUPS
            sp.dma_start(K.xT, T["xT"].rearrange("(t p) n -> p t n", p=P)).then_inc(inputs_in, 16)
            sp.dma_start(K.at(40, 8, NCTX), T["ctxT"].rearrange("(t p) n -> p t n", p=P)).then_inc(inputs_in, 16)
            for dst, src in router_loads(K):
                sp.dma_start(dst, src).then_inc(inputs_in, 16)
            r.issue_until(sp, n0 + 2 * GROUPS + RING)
            sp.wait_ge(inputs_in, 96)

        @block.scalar
        def _(act):
            act.wait_ge(loaded, 16)
            act.activation(sc[:, :, 0], K.vecs[:, VEC_AT["c"]:VEC_AT["c"] + 8], ACT.Silu).then_inc(act_ready, 1)
            act.activation(sc[:, :, 1], K.vecs[:, VEC_AT["c_ctx"]:VEC_AT["c_ctx"] + 8], ACT.Silu)\
                .then_inc(act_ready, 1)
            with act.Fori(0, GROUPS // BODY) as i:
                for g in range(BODY):
                    act.wait_ge(r.used, i * RING + (n0 + 2 * g + 2))
                    act.activation(rows[:, g, :], K.ps[0:2, 1 + g, :], ACT.Copy).then_inc(rows_copied, 1)

        @block.tensor
        def _(pe):
            pe.wait_ge(act_ready, 2)
            pe.wait_ge(ident_in, 16)
            with pe.Fori(0, GROUPS // BODY) as i:
                def turn(g):
                    pe.wait_ge(rows_copied, i * BODY + g + 1)
                    for c in range(4):
                        ins = pe.matmul(K.ps[:, 0, bass.ds((i * BODY + g) * 8 + 2 * c, 2)],
                                        rows[:, g, c * P:(c + 1) * P], K.ident[0:2, 0:2], start=True, stop=True)
                    ins.then_inc(turned, 1)

                for g in range(BODY):
                    for k in range(KD):
                        if k % 4 == 0:
                            pe.wait_ge(r.arrived[2 * g + k // 4], i * 16 + 16)
                        ins = pe.matmul(K.ps[0:2, 1 + g, :], sc[:, k, :],
                                        r.slots[2 * g + k // 4][:, (k % 4) * HALF:(k % 4 + 1) * HALF],
                                        start=(k == 0), stop=(k == KD - 1))
                        if k % 4 == 3:
                            ins.then_inc(r.used, 1)
                    if g == 1:
                        turn(0)
                turn(1)
                turn(2)

        @block.vector
        def _(dve):
            dve.memset(K.ones[:, :], 1.0).then_inc(modded, 1)
            dve.wait_ge(modded, 1)
            dve.wait_ge(loaded, 16)
            dve.wait_ge(turned, GROUPS)
            m = K.mods[:, :].rearrange("p (j b) -> p j b", b=2)
            pv = cols.rearrange("p (j b) -> p j b", b=2)
            bm = K.vecs[:, VEC_AT["b_mod"]:VEC_AT["b_mod"] + 48]
            for b in range(2):
                dve.tensor_tensor(m[:, :, b], pv[:, :, b], bm, ALU.add).then_inc(modded, 1)
            dve.wait_ge(modded, 3)
            g1 = K.vecs[:, VEC_AT["norm1_g"]:VEC_AT["norm1_g"] + 8]
            g2 = K.vecs[:, VEC_AT["norm2_g"]:VEC_AT["norm2_g"] + 8]
            dve.scalar_tensor_tensor(K.gain1, m[:, 8:16, 0], 1.0, g1, ALU.add, ALU.mult).then_inc(modded, 1)
            dve.scalar_tensor_tensor(K.gain1c, m[:, 8:16, 1], 1.0, g1, ALU.add, ALU.mult).then_inc(modded, 1)
            dve.scalar_tensor_tensor(K.gain2, m[:, 32:40, 0], 1.0, g2, ALU.add, ALU.mult).then_inc(modded, 1)
            dve.wait_ge(modded, 6)


def mod_col(K, part, t, b=0):
    o = 2 * (part * KD + t) + b
    return K.mods[:, o:o + 1]


def norm_stage(K, items, tmp, store=None):
    sq_done, stored, mean_done, rec_done, rstd_done, scaled, shifted, sq_used = K.signals(8)
    sq = K.at(tmp, 4, S)
    rec, rstd = K.at(tmp + 8, S), K.at(tmp + 10, S)
    with K.nc.Block() as block:
        @block.sync
        def _(sp):
            K.start(sp)
            if store is not None:
                for t in range(KD):
                    sp.wait_ge(scaled, t + 1)
                    sp.dma_start(store[t * P:(t + 1) * P, :], items[0][2][:, t, :]).then_inc(stored, 16)
                sp.wait_ge(stored, 16 * KD)

        @block.scalar
        def _(act):
            for j, (x, n, out, gain, shift) in enumerate(items):
                for t in range(KD):
                    a = j * KD + t
                    if a >= 4:
                        act.wait_ge(sq_used, a - 3)
                    act.activation(sq[:, a % 4, 0:n], x[:, t, :], ACT.Square).then_inc(sq_done, 1)
                act.wait_ge(rec_done, j + 1)
                act.activation(rstd[:, 0:n], rec[:, 0:n], ACT.Sqrt).then_inc(rstd_done, 1)
                if shift is not None:
                    for t in range(KD):
                        act.wait_ge(scaled, j * KD + t + 1)
                        act.activation(out[:, t, :], out[:, t, :], ACT.Identity, bias=shift(t)).then_inc(shifted, 1)
            if shift is not None:
                act.wait_ge(shifted, 1)

        @block.tensor
        def _(pe):
            for j, (x, n, out, gain, shift) in enumerate(items):
                if j >= 1:
                    pe.wait_ge(mean_done, j)
                for t in range(KD):
                    a = j * KD + t
                    pe.wait_ge(sq_done, a + 1)
                    pe.matmul(K.ps[:, 0, 0:n], K.ones[:, :], sq[:, a % 4, 0:n], start=(t == 0), stop=(t == KD - 1))\
                        .then_inc(sq_used, 1)

        @block.vector
        def _(dve):
            for j, (x, n, out, gain, shift) in enumerate(items):
                dve.wait_ge(sq_used, (j + 1) * KD)
                if j >= 1:
                    dve.wait_ge(scaled, j * KD)
                dve.tensor_scalar(rec[:, 0:n], K.ps[:, 0, 0:n], 1.0 / D, EPS, ALU.mult, ALU.add).then_inc(mean_done, 1)
                dve.wait_ge(mean_done, j + 1)
                dve.reciprocal(rec[:, 0:n], rec[:, 0:n]).then_inc(rec_done, 1)
                dve.wait_ge(rstd_done, j + 1)
                for t in range(KD):
                    dve.scalar_tensor_tensor(out[:, t, :], x[:, t, :], gain(t), rstd[:, 0:n], ALU.mult, ALU.mult)\
                        .then_inc(scaled, 1)
            dve.wait_ge(scaled, len(items) * KD)


def qk_stage(K):
    r, T = K.ring, K.T
    (raw_done, sq_done, ss_done, mean_done, rec_done, rstd_done, qn_done, swap_done, t1_done, t2_done, out_done,
     v_done, v_copied) = K.signals(13)
    sq, rec, rstd, qn, t1, t2 = (K.at(100 + 4 * i, 2, S) for i in range(6))
    cos, sin, swap = K.at(124, S), K.at(126, S), K.at(128, P)
    n0 = r.first("kv")
    items = []
    for h in range(2):
        items.append((n0, h * P, K.hT, S, "k_norm_g", True, K.kT[:, h, 0:S]))
        items.append((n0, h * P, K.hcT, NCTX, "k_norm_g", False, K.kT[:, h, S:S + NCTX]))
    for h in range(8):
        items.append((n0 + 2 + 2 * (h // 4), (h % 4) * P, K.hT, S, "q_norm_g", True, K.qT[:, h, :]))
    NI = len(items)
    rope_no = [sum(1 for it in items[:j] if it[5]) for j in range(NI + 1)]
    with K.nc.Block() as block:
        @block.gpsimd
        def _(pool):
            pool.dma_start(cos, T["k_cos"]).then_inc(K.loaded, 16)
            pool.dma_start(sin, T["k_sin"]).then_inc(K.loaded, 16)
            pool.dma_start(swap, T["k_swap"]).then_inc(K.loaded, 16)

        @block.sync
        def _(sp):
            K.start(sp)
            r.issue_until(sp, n0 + 6 + RING)

        @block.tensor
        def _(pe):
            def raw(j):
                n, col, x, ntok, *_ = items[j]
                if j == 0 or items[j - 1][0] != n:
                    arrived(K, pe, n)
                if j >= 3:
                    pe.wait_ge(qn_done, j - 2)
                project(K, pe, n, col, P, x, slice(0, ntok), K.ps[:, j % 3, 0:ntok]).then_inc(raw_done, 1)
                if n != n0 and col == 3 * P:
                    release(K, pe)

            def values():
                for t in range(ST + CT):
                    x, o = (K.hT, t * P) if t < ST else (K.hcT, (t - ST) * P)
                    if t >= 2:
                        pe.wait_ge(v_copied, t - 1)
                    accumulate(pe, K.ps[:, 5 + t % 2, 0:256],
                               [(x[:, k, o:o + P], r.view(n0 + k // 4)[:, k % 4, 256:512]) for k in range(KD)])\
                        .then_inc(v_done, 1)
                release(K, pe)

            def square_sum(j):
                ntok = items[j][3]
                pe.wait_ge(sq_done, j + 1)
                if j >= 1:
                    pe.wait_ge(mean_done, j)
                pe.matmul(K.ps[:, 3, 0:ntok], K.ones[:, :], sq[:, j % 2, 0:ntok], start=True, stop=True)\
                    .then_inc(ss_done, 1)

            def swapped(j):
                if items[j][5]:
                    pe.wait_ge(qn_done, j + 1)
                    if rope_no[j] >= 1:
                        pe.wait_ge(t2_done, rope_no[j])
                    else:
                        pe.wait_ge(K.loaded, K.loads(3))
                    pe.matmul(K.ps[:, 4, :], swap, qn[:, j % 2, :], start=True, stop=True).then_inc(swap_done, 1)

            for j in range(NI + 2):
                if j < NI:
                    raw(j)
                if j == 3:
                    values()
                if 1 <= j <= NI:
                    square_sum(j - 1)
                if j >= 2:
                    swapped(j - 2)

        @block.scalar
        def _(act):
            def copy_v(t):
                act.wait_ge(v_done, t + 1)
                act.activation(K.v[:, t, :], K.ps[:, 5 + t % 2, 0:256], ACT.Copy).then_inc(v_copied, 1)

            for j in range(NI + 1):
                if j < NI:
                    ntok = items[j][3]
                    act.wait_ge(raw_done, j + 1)
                    if j >= 2:
                        act.wait_ge(ss_done, j - 1)
                    act.activation(sq[:, j % 2, 0:ntok], K.ps[:, j % 3, 0:ntok], ACT.Square).then_inc(sq_done, 1)
                if j == 3:
                    for t in range(ST + CT):
                        copy_v(t)
                if j >= 1:
                    ntok = items[j - 1][3]
                    act.wait_ge(rec_done, j)
                    if j >= 3:
                        act.wait_ge(qn_done, j - 2)
                    act.activation(rstd[:, (j - 1) % 2, 0:ntok], rec[:, (j - 1) % 2, 0:ntok], ACT.Sqrt)\
                        .then_inc(rstd_done, 1)

        @block.vector
        def _(dve):
            def invert(j):
                ntok = items[j][3]
                m = rec[:, j % 2, 0:ntok]
                dve.wait_ge(ss_done, j + 1)
                if j >= 2:
                    dve.wait_ge(rstd_done, j - 1)
                dve.tensor_scalar(m, K.ps[:, 3, 0:ntok], 1.0 / P, EPS, ALU.mult, ALU.add).then_inc(mean_done, 1)
                dve.wait_ge(mean_done, j + 1)
                dve.reciprocal(m, m).then_inc(rec_done, 1)

            def norm(j):
                _, _, _, ntok, gain, rotary, dest = items[j]
                out = qn[:, j % 2, :] if rotary else dest
                dve.wait_ge(rstd_done, j + 1)
                if j >= 2:
                    dve.wait_ge(swap_done, rope_no[j - 1])
                dve.scalar_tensor_tensor(out, K.ps[:, j % 3, 0:ntok], K.vec(gain), rstd[:, j % 2, 0:ntok],
                                         ALU.mult, ALU.mult).then_inc(qn_done, 1)

            def rotate(j):
                rotary, dest = items[j][5:7]
                if rotary:
                    q = rope_no[j]
                    dve.wait_ge(qn_done, j + 1)
                    dve.wait_ge(K.loaded, K.loads(3))
                    dve.tensor_tensor(t1[:, q % 2, :], qn[:, j % 2, :], cos, ALU.mult).then_inc(t1_done, 1)
                    dve.wait_ge(swap_done, q + 1)
                    dve.tensor_tensor(t2[:, q % 2, :], K.ps[:, 4, :], sin, ALU.mult).then_inc(t2_done, 1)
                    dve.wait_ge(t1_done, q + 1)
                    dve.wait_ge(t2_done, q + 1)
                    dve.tensor_tensor(dest, t1[:, q % 2, :], t2[:, q % 2, :], ALU.add).then_inc(out_done, 1)

            for j in range(NI + 1):
                if j < NI:
                    invert(j)
                    norm(j)
                if j >= 1:
                    rotate(j - 1)
            dve.wait_ge(out_done, rope_no[NI])
    K.load_base = K.loads(3)


def items_stage(K, items, issue=None, beside=None, banks=(0, 1, 2, 3)):
    r = K.ring
    mm_done, act_out, dve_out, *others = K.signals(9)
    count = {"act": 0, "dve": 0}
    emptied = []
    for it in items:
        count[it["eng"]] += 1
        emptied.append((act_out if it["eng"] == "act" else dve_out, count[it["eng"]]))
    NB = len(banks)
    beside = beside(K, others, emptied) if beside else {"loads": 0}

    def work(name, eng, j):
        step = beside.get(name, {}).get(j)
        if step:
            step(eng)

    with K.nc.Block() as block:
        if "pool" in beside:
            @block.gpsimd
            def _(pool):
                beside["pool"](pool)

        @block.sync
        def _(sp):
            K.start(sp)
            if issue is not None:
                r.issue_until(sp, issue + RING)
            if "sp" in beside:
                beside["sp"](sp)

        @block.tensor
        def _(pe):
            for j, it in enumerate(items):
                for n in it.get("first", ()):
                    arrived(K, pe, n, 1)
                if j >= NB:
                    pe.wait_ge(*emptied[j - NB])
                it["mm"](pe, K.ps[:, banks[j % NB], :]).then_inc(mm_done, 1)
                if it.get("rel"):
                    release(K, pe, it["rel"])
                work("pe", pe, j)

        @block.scalar
        def _(act):
            for j, it in enumerate(items):
                if it["eng"] == "act":
                    act.wait_ge(mm_done, j + 1)
                    it["out"](act, K.ps[:, banks[j % NB], :]).then_inc(act_out, 1)
                work("act", act, j)

        @block.vector
        def _(dve):
            for j, it in enumerate(items):
                if it["eng"] == "dve":
                    dve.wait_ge(mm_done, j + 1)
                    it["out"](dve, K.ps[:, banks[j % NB], :]).then_inc(dve_out, 1)
                work("dve", dve, j)
    K.load_base = K.loads(beside["loads"])


def channel_item(K, n, col, m, x, ntok, dest, eng="act", func=ACT.Copy, first=(), rel=0, pairs=None, **kw):
    def mm(pe, bank):
        if pairs is not None:
            return accumulate(pe, bank[0:m, 0:ntok], pairs)
        return project(K, pe, n, col, m, x, slice(0, ntok), bank[0:m, 0:ntok])

    def out(e, bank):
        if eng == "act":
            return e.activation(dest, bank[0:m, 0:ntok], func, **kw)
        return e.tensor_copy(dest, bank[0:m, 0:ntok])
    return {"first": first, "mm": mm, "rel": rel, "eng": eng, "out": out}


def token_item(K, n, c0, c1, x, tok, dest, eng="act", func=ACT.Copy, first=(), rel=0, **kw):
    def mm(pe, bank):
        return accumulate(pe, bank[:, 0:c1 - c0],
                          [(x[:, k, tok], K.ring.view(n + k // 4)[:, k % 4, c0:c1]) for k in range(KD)])

    def out(e, bank):
        if eng == "act":
            return e.activation(dest, bank[:, 0:c1 - c0], func, **kw)
        return e.tensor_copy(dest, bank[:, 0:c1 - c0])
    return {"first": first, "mm": mm, "rel": rel, "eng": eng, "out": out}


def gla_project_stage(K):
    r = K.ring
    n = r.first("gk")
    items = []
    for t in range(2):
        items.append(channel_item(K, n, t * P, P, K.hT, S, K.gk[:, t, 0:S], first=(n, n + 1) if t == 0 else ()))
        items.append(channel_item(K, n, t * P, P, K.hcT, NCTX, K.gk[:, t, S:S + NCTX], eng="dve",
                                  rel=2 if t == 1 else 0))
    n += 2
    for d in range(2):
        items.append(channel_item(K, n, 16 * d, 16, K.hT, S, K.ga[d][0:16, 0:S], first=(n, n + 1) if d == 0 else ()))
        items.append(channel_item(K, n, 16 * d, 16, K.hcT, NCTX, K.ga[d][0:16, S:S + NCTX], eng="dve",
                                  rel=2 if d == 1 else 0))
    n += 2
    for t in range(2):
        items.append(channel_item(K, n, t * P, P, K.hT, S, K.gq[:, t, :], func=ACT.Copy, scale=0.125,
                                  first=(n, n + 1) if t == 0 else (), rel=2 if t == 1 else 0))
    n += 2
    for t in range(6):
        x, o = (K.hT, t * P) if t < ST else (K.hcT, (t - ST) * P)
        items.append(token_item(K, n, 0, 512, x, slice(o, o + P), K.gv[:, t, :], eng=("act", "dve")[t % 2],
                                first=(n, n + 1) if t == 0 else (), rel=2 if t == 5 else 0))
    n += 2
    for t in range(ST):
        items.append(token_item(K, n, 0, 512, K.hT, slice(t * P, t * P + P), K.og[:, t, :], func=ACT.Silu,
                                first=(n, n + 1) if t == 0 else (), rel=2 if t == 3 else 0))
    items_stage(K, items, issue=n + 2, beside=gla_decay_work, banks=(0, 1, 2))


def gla_decay_work(K, signals, emptied):
    T = K.T
    L = S + NCTX
    *chains, z_done, kend_done, turned, copied = signals
    scratch = [[K.at(kb + 3 * i, L) for i in range(5)] + [K.at(x, L)] for kb, x in ((40, 146), (131, 56))]
    wa2, mask = K.at(149, 2, 256)[0:16], K.at(128, L)
    STEPS = 13
    kd = [0]

    def pool(pool):
        pool.dma_start(wa2, T["gla_wa2"].rearrange("d r c -> r d c")).then_inc(K.loaded, 16)
        pool.dma_start(mask, T["k_scan"]).then_inc(K.loaded, 16)

    def z_of(u):
        return K.ps[:, 3 + 2 * (u % 2):5 + 2 * (u % 2), :].rearrange("p b n -> p (b n)")[:, 0:L]

    def decays(pe, pair):
        if pair == 0:
            pe.wait_ge(K.loaded, K.loads(2))
            for j in (6, 7):
                pe.wait_ge(*emptied[j])
        else:
            pe.wait_ge(copied, 2)
        for u in (pair, pair + 1):
            w = wa2[:, u // 2, u % 2 * P:(u % 2 + 1) * P]
            bank = 3 + 2 * (u % 2)
            pe.matmul(K.ps[:, bank, :], w, K.ga[u // 2][0:16, 0:S], start=True, stop=True)
            pe.matmul(K.ps[:, bank + 1, 0:NCTX], w, K.ga[u // 2][0:16, S:L], start=True, stop=True).then_inc(z_done, 1)

    def turn(pe, pair):
        for u in (pair, pair + 1):
            pe.wait_ge(chains[u % 2], (u // 2 + 1) * STEPS)
            for t in range(6):
                ins = pe.transpose(z_of(u)[:, t * P:(t + 1) * P], scratch[u % 2][5][:, t * P:(t + 1) * P],
                                   K.ident[:, :])
            ins.then_inc(turned, 1)

    def act_step(act, u, j, out, in_, func, **kw):
        act.wait_ge(chains[u % 2], u // 2 * STEPS + j)
        act.activation(out, in_, func, **kw).then_inc(chains[u % 2], 1)

    A, B, C, E, F, X = zip(*scratch)

    def logs(act, pair):
        act.wait_ge(z_done, pair + 2)
        for u in (pair, pair + 1):
            act_step(act, u, 0, A[u % 2], z_of(u), ACT.Abs, bias=K.vec("gla_ba", u))
        for u in (pair, pair + 1):
            act_step(act, u, 1, A[u % 2], A[u % 2], ACT.Exp, scale=-1.0)
        for u in (pair, pair + 1):
            act_step(act, u, 2, A[u % 2], A[u % 2], ACT.Ln, bias=1.0)

    def exps(act, pair):
        for u in (pair, pair + 1):
            act_step(act, u, 7, A[u % 2][:, 0:S], E[u % 2][:, 0:S], ACT.Exp, scale=1 / 16)
            act_step(act, u, 8, B[u % 2][:, 0:S], E[u % 2][:, 0:S], ACT.Exp, scale=-1 / 16)
            act_step(act, u, 9, F[u % 2], F[u % 2], ACT.Exp, scale=1 / 16)

    def copy(act, pair):
        for u in (pair, pair + 1):
            act.wait_ge(turned, u + 1)
            act.activation(K.kend[:, :, u, :], z_of(u).rearrange("p (t c) -> p t c", c=P), ACT.Copy)\
                .then_inc(copied, 1)

    def last(act):
        copy(act, 2)
        for c in chains:
            act.wait_ge(c, 2 * STEPS)
        act.activation(K.tot[:, :, :], K.tot[:, :, :], ACT.Exp, scale=1 / 16).then_inc(copied, 1)
        act.wait_ge(copied, 5)

    def step(dve, u, j, f):
        dve.wait_ge(chains[u % 2], u // 2 * STEPS + j)
        f().then_inc(chains[u % 2], 1)

    def sums(dve, u):
        d, (A, B, C, E, F, X) = u // 2, scratch[u % 2]
        step(dve, u, 3, lambda: dve.tensor_scalar(B, z_of(u), K.vec("gla_ba", u), 0.0, ALU.add, ALU.min))
        step(dve, u, 4, lambda: dve.tensor_tensor(C, B, A, ALU.subtract))
        step(dve, u, 5, lambda: dve.tensor_tensor_scan(E, mask, C, 0.0, ALU.mult, ALU.add))
        dve.wait_ge(chains[u % 2], u // 2 * STEPS + 6)
        dve.tensor_copy(K.tot[:, u, 0:8], E[:, 0:S].rearrange("p (c t) -> p c t", t=64)[:, :, 63])\
            .then_inc(kend_done, 1)
        dve.tensor_copy(K.tot[:, u, 8:9], E[:, L - 1:L]).then_inc(kend_done, 1)
        n = kd[0] = kd[0] + 2
        dve.wait_ge(kend_done, n)
        tl, tc = K.tot[:, u, 0:8].unsqueeze(2).broadcast_to([P, 8, 64]), K.tot[:, u, 8:9].broadcast_to([P, NCTX])
        if d == 1:
            dve.tensor_tensor(E, C, E, ALU.subtract).then_inc(kend_done, 1)
            dve.wait_ge(kend_done, n + 1)
            dve.tensor_tensor(c64(E), c64(E), tl, ALU.add).then_inc(kend_done, 1)
            dve.tensor_tensor(E[:, S:L], E[:, S:L], tc, ALU.add).then_inc(kend_done, 1)
            dve.wait_ge(kend_done, n + 3)
            kd[0] = n + 3
        dve.tensor_tensor(c64(F), tl, c64(E), ALU.subtract).then_inc(kend_done, 1)
        kd[0] += 1
        dve.wait_ge(kend_done, kd[0])
        step(dve, u, 6, lambda: dve.tensor_tensor(F[:, S:L], tc, E[:, S:L], ALU.subtract))

    def scale(dve, u):
        p, (A, B, C, E, F, X) = u % 2, scratch[u % 2]
        step(dve, u, 10, lambda: dve.tensor_tensor(K.qdec[:, u, :], K.gq[:, p, :], A[:, 0:S], ALU.mult))
        step(dve, u, 11, lambda: dve.tensor_tensor(K.kinv[:, u, :], K.gk[:, p, 0:S], B[:, 0:S], ALU.mult))
        if u >= 2:
            dve.wait_ge(turned, u - 1)
        step(dve, u, 12, lambda: dve.tensor_tensor(X, K.gk[:, p, :], F, ALU.mult))

    def both(f, pair):
        def run(dve):
            if f is sums and pair == 0:
                dve.wait_ge(K.loaded, K.loads(2))
            if f is scale and pair == 0:
                for j in (2, 3, 8, 9):
                    dve.wait_ge(*emptied[j])
            for u in (pair, pair + 1):
                f(dve, u)
        return run

    def turn_and_decays(pe):
        turn(pe, 0)
        decays(pe, 2)

    return {"loads": 2, "pool": pool,
            "pe": {8: lambda pe: decays(pe, 0), 12: turn_and_decays, 18: lambda pe: turn(pe, 2)},
            "act": {8: lambda act: logs(act, 0), 10: lambda act: exps(act, 0), 12: lambda act: copy(act, 0),
                    13: lambda act: logs(act, 2), 15: lambda act: exps(act, 2), 19: last},
            "dve": {8: both(sums, 0), 10: both(scale, 0), 13: both(sums, 2), 15: both(scale, 2)}}


def c64(v):
    return v[:, 0:S].rearrange("p (c t) -> p c t", t=64)


def gla_chunk_stage(K):
    T = K.T
    (cs_done, st_done, att_done, masked, o_done, sq_done, mean_done, rec_done, rstd_done, y_done, turned,
     copied, init_done) = K.signals(13)
    NC = S // 64
    masks = K.at(40, 2, P)
    gain = K.at(41, P)
    att = K.at(42, 2, 2, P)
    ysq = K.at(44, 2, P)
    o_sb = K.at(45, 2, 512)
    stats = K.at(49, 3, 16)
    states = K.states
    with K.nc.Block() as block:
        @block.gpsimd
        def _(pool):
            pool.dma_start(masks, T["k_causal"].rearrange("d s q -> s d q")).then_inc(K.loaded, 16)
            pool.dma_start(gain, T["gla_norm_g"].broadcast_to([P, P])).then_inc(K.loaded, 16)

        @block.sync
        def _(sp):
            K.start(sp)

        def order(d, c):
            return c if d == 0 else NC - 1 - c

        @block.tensor
        def _(pe):
            for u in range(4):
                d, p = u // 2, u % 2
                b = 3 * (u % 2)
                if u >= 2:
                    pe.wait_ge(st_done, (u - 1) * NC)
                for h in range(2):
                    rows = slice(64 * h, 64 * h + 64)
                    hv = slice((2 * p + h) * P, (2 * p + h + 1) * P)
                    accumulate(pe, K.ps[rows, b + 2, 0:P],
                               [(K.kend[:, 4 + t, u, rows], K.gv[:, 4 + t, hv]) for t in range(2)])
                    for c in range(NC):
                        toks = slice(64 * (c % 2), 64 * (c % 2) + 64)
                        ins = pe.matmul(K.ps[rows, b + c % 2, (c // 2) * P:(c // 2 + 1) * P],
                                        K.kend[toks, c // 2, u, rows], K.gv[toks, c // 2, hv], start=True, stop=True)
                ins.then_inc(cs_done, 1)

            def scores(a):
                t, h = a // 4, a % 4
                rows, toks = slice(64 * (h % 2), 64 * (h % 2) + 64), slice(t * P, (t + 1) * P)
                if a >= 2:
                    pe.wait_ge(masked, a - 1)
                else:
                    pe.wait_ge(st_done, 4 * NC)
                for d in range(2):
                    u = 2 * d + h // 2
                    ins = pe.matmul(K.ps[:, a % 2, d * P:(d + 1) * P], K.kinv[rows, u, toks], K.qdec[rows, u, toks],
                                    start=True, stop=True)
                ins.then_inc(att_done, 1)

            def outputs(a):
                t, h = a // 4, a % 4
                rows, toks = slice(64 * (h % 2), 64 * (h % 2) + 64), slice(t * P, (t + 1) * P)
                hv = slice(h * P, (h + 1) * P)
                pe.wait_ge(masked, a + 1)
                if a >= 2:
                    pe.wait_ge(y_done, a - 1)
                out = K.ps[:, 2 + a % 2, 0:P]
                for d in range(2):
                    pe.matmul(out, att[:, a % 2, d, :], K.gv[:, t, hv], start=(d == 0), stop=False)
                for d in range(2):
                    u = 2 * d + h // 2
                    for j in range(2):
                        c = 2 * t + j
                        before = c if d == 0 else NC - 1 - c
                        ins = pe.matmul(K.ps[64 * j:64 * j + 64, 2 + a % 2, 0:P], K.qdec[rows, u, 64 * c:64 * c + 64],
                                        states[rows, u, before, :], start=False, stop=(d == 1))
                ins.then_inc(o_done, 1)

            for a in range(17):
                if a < 16:
                    scores(a)
                if a >= 1:
                    outputs(a - 1)
            for a in range(16):
                t, h = a // 4, a % 4
                if h == 0:
                    pe.wait_ge(y_done, a + 4)
                    if t >= 2:
                        pe.wait_ge(copied, t - 1)
                ins = pe.transpose(K.ps[:, 4 + t % 2, h * P:(h + 1) * P], K.og[:, t, h * P:(h + 1) * P], K.ident[:, :])
                if h == 3:
                    ins.then_inc(turned, 1)

        @block.scalar
        def _(act):
            for a in range(16):
                act.wait_ge(o_done, a + 1)
                act.activation(ysq[:, a % 2, :], K.ps[:, 2 + a % 2, 0:P], ACT.Square, accum_out=stats[:, 0, a:a + 1])\
                    .then_inc(sq_done, 1)
                act.wait_ge(rec_done, a + 1)
                act.activation(stats[:, 2, a:a + 1], stats[:, 1, a:a + 1], ACT.Sqrt).then_inc(rstd_done, 1)
            for t in range(ST):
                act.wait_ge(turned, t + 1)
                act.activation(K.yglaT[:, :, t * P:(t + 1) * P],
                               K.ps[:, 4 + t % 2, :].rearrange("p (h c) -> p h c", c=P), ACT.Copy).then_inc(copied, 1)
            act.wait_ge(copied, ST)

        @block.vector
        def _(dve):
            for u in range(4):
                d = u // 2
                b = 3 * (u % 2)
                dve.wait_ge(cs_done, u + 1)
                dve.tensor_copy(states[:, u, 0, :], K.ps[:, b + 2, 0:P]).then_inc(init_done, 1)
                dve.wait_ge(init_done, u + 1)
                for s in range(NC):
                    c = order(d, s)
                    if s < NC - 1:
                        dve.scalar_tensor_tensor(states[:, u, s + 1, :], states[:, u, s, :], K.tot[:, u, c:c + 1],
                                                 K.ps[:, b + c % 2, (c // 2) * P:(c // 2 + 1) * P], ALU.mult, ALU.add)\
                            .then_inc(st_done, 1)
                        dve.wait_ge(st_done, u * NC + s + 1)
                    else:
                        dve.tensor_copy(stats[:, 0, 0:1], K.tot[:, u, 0:1]).then_inc(st_done, 1)
            dve.wait_ge(K.loaded, K.loads(2))

            def mask(a):
                dve.wait_ge(att_done, a + 1)
                if a >= 2:
                    dve.wait_ge(o_done, a - 1)
                dve.tensor_tensor(att[:, a % 2, :, :], K.ps[:, a % 2, 0:2 * P].rearrange("p (d q) -> p d q", q=P),
                                  masks, ALU.mult).then_inc(masked, 1)

            mask(0)
            for a in range(16):
                t, h = a // 4, a % 4
                if a + 1 < 16:
                    mask(a + 1)
                dve.wait_ge(sq_done, a + 1)
                dve.tensor_scalar(stats[:, 1, a:a + 1], stats[:, 0, a:a + 1], 1.0 / P, EPS, ALU.mult, ALU.add)\
                    .then_inc(mean_done, 1)
                dve.wait_ge(mean_done, 2 * a + 1)
                dve.reciprocal(stats[:, 1, a:a + 1], stats[:, 1, a:a + 1]).then_inc(rec_done, 1)
                dve.wait_ge(rstd_done, a + 1)
                o = o_sb[:, a % 2, 0:P]
                dve.scalar_tensor_tensor(o, K.ps[:, 2 + a % 2, 0:P], stats[:, 2, a:a + 1], gain, ALU.mult, ALU.mult)\
                    .then_inc(mean_done, 1)
                dve.wait_ge(mean_done, 2 * a + 2)
                og = K.og[:, t, h * P:(h + 1) * P]
                dve.tensor_tensor(og, o, og, ALU.mult).then_inc(y_done, 1)
    K.load_base = K.loads(2)


def attention_stage(K, heads, nk, scores, values, dest, scale, tmp):
    s_done, max_done, bias_done, exp_done, rec_done, normed, turned, copied, o_done, o_copied = K.signals(10)
    NB, NJ = heads * ST, nk // P
    Pb = K.at(tmp, 3, nk)
    PT = K.at(tmp + 3 * nk / 256, 2, NJ, S)
    st = K.at(tmp + 3 * nk / 256 + 2 * NJ * 2, 4, NB)
    with K.nc.Block() as block:
        @block.sync
        def _(sp):
            K.start(sp)

        def sbank(a):
            return K.ps[:, 2 * (a % 2):2 * (a % 2) + 2, :].rearrange("p b n -> p (b n)")[:, 0:nk]

        def tbank():
            return K.ps[:, 4:6, :].rearrange("p b n -> p (b n)")[:, 0:nk].rearrange("p (j q) -> p j q", q=P)

        @block.tensor
        def _(pe):
            for a in range(NB + 3):
                if a < NB:
                    if a >= 2:
                        pe.wait_ge(exp_done, a - 1)
                    for cols, l, r in scores(a // ST, a % ST):
                        ins = pe.matmul(sbank(a)[:, cols], l, r, start=True, stop=True)
                    ins.then_inc(s_done, 1)
                b = a - 2
                if 0 <= b < NB:
                    pe.wait_ge(normed, b + 1)
                    if b >= 1:
                        pe.wait_ge(copied, b)
                    for j in range(NJ):
                        ins = pe.transpose(tbank()[:, j, :], Pb[:, b % 3, j * P:(j + 1) * P], K.ident[:, :])
                    ins.then_inc(turned, 1)
                b = a - 3
                if b >= 0 and b % ST == ST - 1:
                    h = b // ST
                    pe.wait_ge(copied, b + 1)
                    if h >= 1:
                        pe.wait_ge(o_copied, h)
                    accumulate(pe, K.ps[:, 6, :], [(values(h, j), PT[:, h % 2, j, :]) for j in range(NJ)])\
                        .then_inc(o_done, 1)

        @block.scalar
        def _(act):
            for a in range(NB + 3):
                if a < NB:
                    act.wait_ge(bias_done, a + 1)
                    if a >= 3:
                        act.wait_ge(turned, a - 2)
                    act.activation(Pb[:, a % 3, :], sbank(a), ACT.Exp, bias=st[:, 1, a:a + 1], scale=scale,
                                   accum_out=st[:, 2, a:a + 1]).then_inc(exp_done, 1)
                b = a - 3
                if b >= 0 and b % ST == ST - 1:
                    h = b // ST
                    act.wait_ge(o_done, h + 1)
                    act.activation(dest(h), K.ps[:, 6, :], ACT.Copy).then_inc(o_copied, 1)
            act.wait_ge(o_copied, heads)

        @block.vector
        def _(dve):
            for a in range(NB + 2):
                if a < NB:
                    dve.wait_ge(s_done, a + 1)
                    dve.tensor_reduce(st[:, 0, a:a + 1], sbank(a), AX.X, ALU.max).then_inc(max_done, 1)
                    dve.wait_ge(max_done, a + 1)
                    dve.tensor_scalar(st[:, 1, a:a + 1], st[:, 0, a:a + 1], -scale, None, ALU.mult)\
                        .then_inc(bias_done, 1)
                b = a - 1
                if 0 <= b < NB:
                    dve.wait_ge(exp_done, b + 1)
                    dve.reciprocal(st[:, 3, b:b + 1], st[:, 2, b:b + 1]).then_inc(rec_done, 1)
                    dve.wait_ge(rec_done, b + 1)
                    dve.tensor_scalar(Pb[:, b % 3, :], Pb[:, b % 3, :], st[:, 3, b:b + 1], None, ALU.mult)\
                        .then_inc(normed, 1)
                b = a - 2
                if b >= 0:
                    dve.wait_ge(turned, b + 1)
                    h = b // ST
                    if h >= 2:
                        dve.wait_ge(o_done, h - 1)
                    dve.tensor_copy(PT[:, h % 2, :, (b % ST) * P:(b % ST + 1) * P], tbank()).then_inc(copied, 1)


def latent_attention_stage(K):
    def scores(h, i):
        q = K.qT[:, h, i * P:(i + 1) * P]
        return [(slice(0, S), q, K.kT[:, h // 4, 0:S]), (slice(S, S + NCTX), q, K.kT[:, h // 4, S:S + NCTX])]

    attention_stage(K, 8, S + NCTX, scores, lambda h, j: K.v[:, j, (h // 4) * P:(h // 4 + 1) * P],
                    lambda h: K.yattT[:, h, :], P ** -0.5, 100)


TWO_PI = 2.0 * np.pi
ROUND = 1.5 * 2.0 ** 23
PI_HI = 6.28125
PI_LO = TWO_PI - PI_HI
SIN_MAX = 3.1415925


def hyena_project_stage(K):
    r = K.ring
    mm_done, mid_done, left_done, conv_done, turned, copied, *others = K.signals(9)
    hidden = HiddenLayers(K, others)
    HIDDEN = (3, 7)
    n0 = r.first("hy")
    NT = 12
    ys = K.at(96, 4, S)
    turn_no = [t if t < 4 else t - 4 for t in range(NT)]

    def y_of(t):
        return K.x2T[:, t - 4, :] if 4 <= t < 8 else ys[:, turn_no[t] % 4, :]

    with K.nc.Block() as block:
        @block.gpsimd
        def _(pool):
            hidden.pool(pool)

        @block.sync
        def _(sp):
            K.start(sp)
            r.issue_until(sp, n0 + 6 + RING)

        @block.tensor
        def _(pe):
            def turn(t):
                if 4 <= t < 8:
                    return
                q = turn_no[t]
                pe.wait_ge(conv_done, t + 1)
                if q >= 2:
                    pe.wait_ge(copied, q - 1)
                for tt in range(ST):
                    ins = pe.transpose(K.ps[:, 4 + q % 2, tt * P:(tt + 1) * P], y_of(t)[:, tt * P:(tt + 1) * P],
                                       K.ident[:, :])
                ins.then_inc(turned, 1)

            for t in range(NT):
                n = n0 + 2 * (t // 4)
                if t % 4 == 0:
                    arrived(K, pe, n)
                if t >= 4:
                    pe.wait_ge(conv_done, t - 3)
                project(K, pe, n, (t % 4) * P, P, K.hT, slice(0, S), K.ps[:, t % 4, :]).then_inc(mm_done, 1)
                if t % 4 == 3:
                    release(K, pe)
                if t >= 2:
                    turn(t - 2)
                if t in HIDDEN:
                    hidden.pe(pe, HIDDEN.index(t))
            turn(NT - 2)
            turn(NT - 1)

        @block.scalar
        def _(act):
            def copy(t):
                if 4 <= t < 8:
                    return
                q = turn_no[t]
                dest = K.x1 if t < 4 else K.z
                act.wait_ge(turned, q + 1)
                act.activation(dest[:, :, (t % 4) * P:(t % 4 + 1) * P],
                               K.ps[:, 4 + q % 2, :].rearrange("p (t c) -> p t c", c=P), ACT.Copy).then_inc(copied, 1)

            for t in range(NT):
                act.wait_ge(mm_done, t + 1)
                q = turn_no[t]
                if not 4 <= t < 8 and q >= 4:
                    act.wait_ge(turned, q - 3)
                act.activation(y_of(t), K.ps[:, t % 4, :], ACT.Identity, bias=K.vec("hy_conv_b", t),
                               scale=K.vec("hy_conv_w", NT + t)).then_inc(mid_done, 1)
                if t >= 3:
                    copy(t - 3)
                if t - 1 in HIDDEN:
                    hidden.act(act, HIDDEN.index(t - 1))
            for t in range(NT - 3, NT):
                copy(t)
            act.wait_ge(copied, 8)

        @block.vector
        def _(dve):
            for t in range(NT):
                y, u = y_of(t), K.ps[:, t % 4, :]
                dve.wait_ge(mid_done, t + 1)
                dve.scalar_tensor_tensor(y[:, 1:S], u[:, 0:S - 1], K.vec("hy_conv_w", t), y[:, 1:S], ALU.mult, ALU.add)\
                    .then_inc(left_done, 1)
                dve.wait_ge(left_done, t + 1)
                dve.scalar_tensor_tensor(y[:, 0:S - 1], u[:, 1:S], K.vec("hy_conv_w", 2 * NT + t), y[:, 0:S - 1],
                                         ALU.mult, ALU.add).then_inc(conv_done, 1)
                if t in HIDDEN:
                    hidden.dve(dve, HIDDEN.index(t))
    K.load_base = K.loads(4)


class HiddenLayers:
    F = 64

    def __init__(self, K, signals):
        self.K, F = K, self.F
        self.mm_done, self.chain, self.sin_done = signals
        self.pos, self.w1, self.w2, self.cols = (K.at(110, S)[0:33], K.at(112, F)[0:33], K.at(112.25, F)[0:F],
                                                 K.at(112.5, 3)[0:F])
        self.a, self.b, self.c, self.h1 = (K.at(114 + 2 * i, S)[0:F] for i in range(4))

    def pool(self, pool):
        T = self.K.T
        for dst, src in ((self.pos, T["k_pos"]), (self.w1, T["hy_pos_w1"]), (self.w2, T["hy_pos_w2"]),
                         (self.cols, T["hy_cols"])):
            pool.dma_start(dst, src).then_inc(self.K.loaded, 16)

    def pe(self, pe, layer):
        K = self.K
        if layer == 0:
            pe.wait_ge(K.loaded, K.loads(4))
        else:
            pe.wait_ge(self.sin_done, 1)
        w, x = ((self.w1, self.pos), (self.w2, self.h1))[layer]
        pe.matmul(K.ps[0:self.F, 6, :], w, x, start=True, stop=True).then_inc(self.mm_done, 1)

    def dve(self, dve, layer):
        K, a, b, c, cols, chain = self.K, self.a, self.b, self.c, self.cols, self.chain
        n = 6 * layer
        if layer:
            dve.wait_ge(self.sin_done, 1)
        else:
            dve.wait_ge(K.loaded, K.loads(4))
        dve.wait_ge(self.mm_done, layer + 1)
        dve.tensor_scalar(a, K.ps[0:self.F, 6, :], cols[:, layer:layer + 1], cols[:, 2:3], ALU.add, ALU.mult)\
            .then_inc(chain, 1)
        dve.wait_ge(chain, n + 1)
        dve.tensor_scalar(b, a, 1.0 / TWO_PI, ROUND, ALU.mult, ALU.add).then_inc(chain, 1)
        dve.wait_ge(chain, n + 2)
        dve.tensor_scalar(b, b, ROUND, None, ALU.subtract).then_inc(chain, 1)
        dve.wait_ge(chain, n + 3)
        dve.scalar_tensor_tensor(c, b, -PI_HI, a, ALU.mult, ALU.add).then_inc(chain, 1)
        dve.wait_ge(chain, n + 4)
        dve.scalar_tensor_tensor(c, b, -PI_LO, c, ALU.mult, ALU.add).then_inc(chain, 1)
        dve.wait_ge(chain, n + 5)
        dve.tensor_scalar(c, c, SIN_MAX, -SIN_MAX, ALU.min, ALU.max).then_inc(chain, 1)

    def act(self, act, layer):
        act.wait_ge(self.chain, 6 * layer + 6)
        act.activation((self.h1, self.K.hid)[layer], self.c, ACT.Sin).then_inc(self.sin_done, 1)


def hyena_stage(K, o):
    r, T = K.ring, K.T
    (dec_done, filt_done, win_done, g_done, abs_done, sum_done, chain, ft_done, ft_out, abs_dec, z_done,
     z_out, part_done, prod, inv_done, out_done) = K.signals(16)
    n0 = r.first(f"dft{o}")
    nC, nS, nE, nCi, nSi = range(n0, n0 + 5)
    Zr, Zi = K.at(32, 4, S), K.at(64 if o == 0 else 80, 4, S)
    tmp = K.at(120, 4, S)
    outs = [(0, "re"), (0, "im"), (0, "edge")] + [(m, p) for m in range(1, 4) for p in ("re", "im")]
    outs_of = [3, 5, 7, 9]
    g = K.at(96, 8, S)
    total = K.at(112, 4, S)
    absb, win, dec, inv = K.at(112, 2, S), K.at(124, 2, S), K.at(120, 2, S), K.at(144, S)
    w3, row, skip, cols = K.at(148, 1024)[0:64], K.at(72 + 64, 1024)[0:1], K.at(140, S)[0:1], K.at(142, 5)
    with K.nc.Block() as block:
        @block.gpsimd
        def _(pool):
            for dst, src in ((w3, T["hy_pos_w3"][:, o * 1024:(o + 1) * 1024]),
                             (row, T["hy_decay"][:, o * 1024:(o + 1) * 1024]),
                             (skip, T["hy_skip"][:, o * S:(o + 1) * S]), (cols, T["k_time"])):
                pool.dma_start(dst, src).then_inc(K.loaded, 16)

        @block.sync
        def _(sp):
            K.start(sp)
            r.issue_until(sp, n0 + 5 + RING)

        @block.tensor
        def _(pe):
            C, Sm, Ed, Ci, Si = (r.view(n) for n in range(n0, n0 + 5))

            def transform(j):
                if j >= 2:
                    pe.wait_ge(z_out, j - 1)
                else:
                    pe.wait_ge(abs_dec, 2)
                w, m = (C, Sm)[j // 4], j % 4
                accumulate(pe, K.ps[:, 5 + j % 2, :], [(w[:, t, m * P:(m + 1) * P], K.z[:, t, :]) for t in range(4)])\
                    .then_inc(z_done, 1)

            arrived(K, pe, n0)
            pe.wait_ge(K.loaded, K.loads(4))
            for d in range(2):
                pe.matmul(K.ps[:, 5 + d, :], K.ones[0:1, :], row[:, d * S:(d + 1) * S], start=True, stop=True)\
                    .then_inc(dec_done, 1)
            for e in range(9):
                if e < 8:
                    if e >= 2:
                        pe.wait_ge(g_done, e - 1)
                    pe.matmul(K.ps[:, e % 2, :], K.hid[:, (e % 4) * P:(e % 4 + 1) * P],
                              w3[:, (e // 4) * S:(e // 4 + 1) * S], start=True, stop=True).then_inc(filt_done, 1)
                if e >= 1:
                    pe.wait_ge(abs_done, e)
                    pe.matmul(K.ps[:, 2, :], K.ones[:, :], absb[:, (e - 1) % 2, :], start=(e == 1), stop=(e == 8))\
                        .then_inc(sum_done, 1)
                if e % 2 == 0 and e < 8:
                    transform(e // 2)
            for j in range(4, 8):
                transform(j)
            pe.wait_ge(chain, 19)
            arrived(K, pe, nE, 1)
            for j, (m, p) in enumerate(outs):
                if j >= 2:
                    pe.wait_ge(ft_out, j - 1)
                cols = slice(m * P, (m + 1) * P)
                pairs = {"re": lambda: [(C[:, t, cols], total[:, t, :]) for t in range(4)],
                         "im": lambda: [((Ed[:, t, P:2 * P] if m == 0 else Sm[:, t, cols]), g[:, t, :])
                                        for t in range(4)],
                         "edge": lambda: [(Ed[:, t, 0:P], total[:, t, :]) for t in range(4)]}[p]()
                accumulate(pe, K.ps[:, 3 + j % 2, :], pairs).then_inc(ft_done, 1)
            release(K, pe, 3)
            arrived(K, pe, nCi)
            for m in range(4):
                pe.wait_ge(out_done, m - 1) if m >= 2 else pe.wait_ge(ft_out, 9)
                cols = slice(m * P, (m + 1) * P)
                for n in range(8):
                    k, w, x = n // 2, (Ci, Si)[n % 2], (Zr, Zi)[n % 2]
                    if m == 0 and n % 2 == 0:
                        pe.wait_ge(prod, 2 * (k + 1))
                    l, rhs = (w[:, k, cols], x[:, k, :]) if o == 0 else (x[:, k, cols], w[:, k, :])
                    ins = pe.matmul(K.ps[:, 3 + m % 2, :], l, rhs, start=(n == 0), stop=(n == 7))
                ins.then_inc(inv_done, 1)
            release(K, pe, 2)

        @block.scalar
        def _(act):
            def copy_z(j):
                act.wait_ge(z_done, j + 1)
                act.activation((Zr, Zi)[j // 4][:, j % 4, :], K.ps[:, 5 + j % 2, :], ACT.Copy).then_inc(z_out, 1)

            for d in range(2):
                act.wait_ge(dec_done, d + 1)
                act.activation(dec[:, d, :], K.ps[:, 5 + d, :], ACT.Abs).then_inc(abs_dec, 1)
            act.wait_ge(K.loaded, K.loads(4))
            for e in range(9):
                if e < 8:
                    act.wait_ge(abs_dec, e // 4 + 1)
                    if e >= 2:
                        act.wait_ge(g_done, e - 1)
                    act.activation(win[:, e % 2, :], dec[:, e // 4, :], ACT.Exp, scale=cols[:, e % 4:e % 4 + 1])\
                        .then_inc(win_done, 1)
                if e >= 1:
                    act.wait_ge(g_done, e)
                    if e >= 3:
                        act.wait_ge(sum_done, e - 2)
                    act.activation(absb[:, (e - 1) % 2, :], g[:, e - 1, :], ACT.Abs).then_inc(abs_done, 1)
                if e % 2 == 0 and e < 8:
                    copy_z(e // 2)
            for j in range(4, 8):
                copy_z(j)
            for j, (m, p) in enumerate(outs):
                dest = {"re": K.Rf[:, m, :], "im": K.If[:, m, :], "edge": K.edge}[p]
                act.wait_ge(ft_done, j + 1)
                act.activation(dest, K.ps[:, 3 + j % 2, :], ACT.Copy).then_inc(ft_out, 1)
            act.wait_ge(ft_out, 9)

        @block.vector
        def _(dve):
            dve.wait_ge(K.loaded, K.loads(4))
            for e in range(8):
                dve.wait_ge(filt_done, e + 1)
                dve.wait_ge(win_done, e + 1)
                if e == 4:
                    dve.scalar_tensor_tensor(g[:, e, :], K.ps[:, e % 2, :], cols[:, 4:5], win[:, e % 2, :],
                                             ALU.mult, ALU.mult).then_inc(g_done, 1)
                else:
                    dve.tensor_tensor(g[:, e, :], K.ps[:, e % 2, :], win[:, e % 2, :], ALU.mult).then_inc(g_done, 1)
            dve.wait_ge(sum_done, 8)
            dve.tensor_scalar(inv, K.ps[:, 2, :], EPS, None, ALU.add).then_inc(chain, 1)
            dve.wait_ge(chain, 1)
            dve.reciprocal(inv, inv).then_inc(chain, 1)
            dve.wait_ge(chain, 2)
            for e in range(8):
                dve.tensor_tensor(g[:, e, :], g[:, e, :], inv, ALU.mult).then_inc(chain, 1)
            dve.wait_ge(chain, 10)
            dve.tensor_tensor(g[0:1, 0, :], g[0:1, 0, :], skip, ALU.add).then_inc(chain, 1)
            dve.wait_ge(chain, 11)
            for t in range(4):
                dve.tensor_tensor(total[:, t, :], g[:, t, :], g[:, 4 + t, :], ALU.add).then_inc(chain, 1)
                dve.wait_ge(chain, 12 + 2 * t)
                dve.tensor_tensor(g[:, t, :], g[:, t, :], g[:, 4 + t, :], ALU.subtract).then_inc(chain, 1)
            dve.wait_ge(z_out, 8)
            for m in range(4):
                zr, zi = Zr[:, m, :], Zi[:, m, :]
                dve.wait_ge(ft_out, outs_of[m])
                if m >= 1:
                    dve.wait_ge(prod, 2 * m)
                dve.tensor_tensor(tmp[:, 0, :], zr, K.Rf[:, m, :], ALU.mult).then_inc(part_done, 1)
                dve.tensor_tensor(tmp[:, 1, :], zi, K.If[:, m, :], ALU.mult).then_inc(part_done, 1)
                dve.tensor_tensor(tmp[:, 2, :], zr, K.If[:, m, :], ALU.mult).then_inc(part_done, 1)
                dve.tensor_tensor(tmp[:, 3, :], zi, K.edge if m == 0 else K.Rf[:, m, :], ALU.mult)\
                    .then_inc(part_done, 1)
                dve.wait_ge(part_done, 4 * m + 4)
                dve.tensor_tensor(zr, tmp[:, 0, :], tmp[:, 1, :], ALU.subtract).then_inc(prod, 1)
                dve.tensor_tensor(zi, tmp[:, 2, :], tmp[:, 3, :], ALU.add).then_inc(prod, 1)
            for m in range(4):
                gate, dest = (K.x1, K.z) if o == 0 else (K.x2T, K.yhyT)
                dve.wait_ge(inv_done, m + 1)
                dve.tensor_tensor(dest[:, m, :], K.ps[:, 3 + m % 2, :], gate[:, m, :], ALU.mult).then_inc(out_done, 1)
            dve.wait_ge(out_done, 4)
    K.load_base = K.loads(4)


def merge_chunks(K, name, w, c0, ys, out):
    def quarter(m, a):
        return m[:, a:a + 256].rearrange("(t p) c -> p t c", p=P)
    gates = [quarter(w, c0 + b * D + q * 256) for q in range(4) for b in range(3)]
    outs = [quarter(ys[b], q * 256) for q in range(4) for b in range(3)]
    order = gates[:1]
    for i in range(1, 12):
        order += [gates[i], outs[i - 1]]
    for ap in order + [outs[11]] + [quarter(out, q * 256) for q in range(4)]:
        K.ring.add(name, ap)


def merge_stage(K, name, branches, parts, mT, tmp, bias=None, gate=None):
    r = K.ring
    (x_hi_done, x_lo_done, w_hi_done, spent, y_spent, gate_done, y_done, sig_done, prod_done, sum_done, m_hi_done,
     m_lo_done, out_done, x_added) = K.signals(14)
    n0 = r.first(name)
    NI, NW = 12, 16
    sig, tm = K.at(tmp, 2, S), K.at(tmp + 4, 2, S)
    x_hi, x_lo = K.rounded_at(parts, KD, S), K.rounded_at(parts + 16, KD, S)

    def split_at(i):
        return n0 + (i and 2 * i - 1) if i < NI else n0 + 24 + i - NI

    def y_at(i):
        return n0 + min(2 * i + 2, 23)

    def part(i, lo):
        return K.rounded_at(parts + 32 + 16 * (i % 2) + 8 * lo, KD, 256)

    def flat(v):
        return v.rearrange("p t c -> p (t c)")

    def triples(i, c):
        return [(part(i, 0)[:, k, c * P:(c + 1) * P], part(i, 1)[:, k, c * P:(c + 1) * P], x_hi[:, k, :], x_lo[:, k, :])
                for k in range(KD)]

    def m_of(i, c):
        return mT[:, i // 3 * 2 + c, :]

    with K.nc.Block() as block:
        @block.sync
        def _(sp):
            K.start(sp)
            r.issue_until(sp, n0 + 28 + RING)

        @block.gpsimd
        def _(pool):
            def rest(i):
                n = split_at(i)
                pool.wait_ge(w_hi_done, i + 1)
                pool.tensor_tensor(flat(part(i, 1)), r.slots[n % RING][:, :], flat(part(i, 0)).bitcast(F32),
                                   ALU.subtract).then_inc(r.used, 1)

            rest(0)
            rest(1)
            for i in range(NI):
                if i == NI - 1:
                    pool.wait_ge(y_spent, i + 1)
                    pool.memset(K.marks[:, i:i + 1], 0.0).then_inc(r.used, 1)
                    rest(NI)
                    rest(NI + 1)
                else:
                    pool.wait_ge(y_spent, i + 1)
                    pool.memset(K.marks[:, i:i + 1], 0.0).then_inc(r.used, 1)
                    if i + 2 < NI:
                        rest(i + 2)
            rest(NI + 2)
            rest(NI + 3)

        @block.tensor
        def _(pe):
            def count(sem):
                pe.matmul(K.ps[:, 7, 511:512], K.ones[:, :], K.ones[:, 0:1], start=True, stop=True).then_inc(sem, 1)

            for i in range(NI):
                y, kt = branches[i % 3]
                for c in range(2):
                    a = 2 * i + c
                    if c == 0:
                        pe.wait_ge(r.used, split_at(i) + 1)
                    if a >= 2:
                        pe.wait_ge(sig_done, a - 1)
                    split_products(pe, K.ps[:, c, :], triples(i, c),
                                   before=(lambda k: pe.wait_ge(x_lo_done, k + 1)) if a == 0 else None)\
                        .then_inc(gate_done, 1)
                count(spent)
                arrived(K, pe, y_at(i), 1)
                w = r.view(y_at(i))
                for c in range(2):
                    a = 2 * i + c
                    if a >= 2:
                        pe.wait_ge(prod_done, a - 1)
                    accumulate(pe, K.ps[:, 2 + c, :],
                               [(w[:, k, c * P:(c + 1) * P], y[:, k, :]) for k in range(kt)]).then_inc(y_done, 1)
                count(y_spent)
            for t in range(KD):
                i = NI + t // 2
                if t % 2 == 0:
                    pe.wait_ge(r.used, split_at(i) + 1)
                if t >= 2:
                    pe.wait_ge(x_added, t - 1)
                split_products(pe, K.ps[:, 4 + t % 2, :], triples(i, t % 2),
                               before=(lambda k: pe.wait_ge(m_lo_done, k + 1)) if t == 0 else None)\
                    .then_inc(out_done, 1)
                if t % 2 == 1:
                    count(spent)

        @block.scalar
        def _(act):
            def high(i):
                n = split_at(i)
                act.wait_ge(r.arrived[n % RING], r.arrival(n))
                if i >= 2:
                    act.wait_ge(spent, i - 1)
                act.activation(flat(part(i, 0)), r.slots[n % RING][:, :], ACT.Copy).then_inc(w_hi_done, 1)

            high(0)
            for k in range(KD):
                act.activation(x_hi[:, k, :], K.hT[:, k, :], ACT.Copy).then_inc(x_hi_done, 1)
            high(1)
            for i in range(NI):
                for c in range(2):
                    a = 2 * i + c
                    act.wait_ge(gate_done, a + 1)
                    if a >= 2:
                        act.wait_ge(prod_done, a - 1)
                    kw = {} if bias is None else {"bias": K.vec(bias, i % 3 * KD + i // 3 * 2 + c)}
                    act.activation(sig[:, c, :], K.ps[:, c, :], ACT.Sigmoid, **kw).then_inc(sig_done, 1)
                high(i + 2)
            for k in range(KD):
                act.wait_ge(sum_done, min(2 * (k // 2 + 1) * 2 - 1 + k % 2, 16))
                act.activation(x_hi[:, k, :], mT[:, k, :], ACT.Copy).then_inc(m_hi_done, 1)
            high(NI + 2)
            high(NI + 3)

        @block.vector
        def _(dve):
            for k in range(KD):
                dve.wait_ge(x_hi_done, k + 1)
                dve.tensor_tensor(x_lo[:, k, :], K.hT[:, k, :], x_hi[:, k, :].bitcast(F32), ALU.subtract)\
                    .then_inc(x_lo_done, 1)
            sums = 0
            for i in range(NI):
                b = i % 3
                for c in range(2):
                    a, m = 2 * i + c, m_of(i, c)
                    dve.wait_ge(sig_done, a + 1)
                    dve.wait_ge(y_done, a + 1)
                    dve.tensor_tensor(tm[:, c, :] if b else m, K.ps[:, 2 + c, :], sig[:, c, :], ALU.mult)\
                        .then_inc(prod_done, 1)
                    if b:
                        dve.wait_ge(prod_done, a + 1)
                        if b == 2:
                            dve.wait_ge(sum_done, sums - 1)
                        dve.tensor_tensor(m, m, tm[:, c, :], ALU.add).then_inc(sum_done, 1)
                        sums += 1
            for k in range(KD):
                dve.wait_ge(m_hi_done, k + 1)
                dve.tensor_tensor(x_lo[:, k, :], mT[:, k, :], x_hi[:, k, :].bitcast(F32), ALU.subtract)\
                    .then_inc(m_lo_done, 1)
            for t in range(KD):
                x = K.xT[:, t, :]
                dve.wait_ge(out_done, t + 1)
                if gate is None:
                    ins = dve.tensor_tensor(x, K.ps[:, 4 + t % 2, :], x, ALU.add)
                else:
                    ins = dve.scalar_tensor_tensor(x, K.ps[:, 4 + t % 2, :], gate(t), x, ALU.mult, ALU.add)
                ins.then_inc(x_added, 1)
            dve.wait_ge(x_added, KD)


def router_stage(K):
    s_done, sig_done, chain, masked, copied, stored, place_done, over_done, turned, hi_done, lo_done, placed, \
        full_done = K.signals(13)
    full = K.at(112, 2 * ST, 512)
    rw, rb, upto, slot_no = router_views(K)
    sc, sel, mask = K.at(130, 64), K.at(130.25, 64), K.at(130.5, 64)
    hi, lo, top, gs = (K.at(131 + 0.25 * i, 4 * 4 * 2) for i in range(4))
    rank, lose, gt, over = K.at(132, 64), K.at(132.25, 16), K.at(132.5, 16), K.at(132.75, 64)
    flags, frank, eq, listed = (K.at(133 + 0.25 * i, 16)[0:1] for i in range(4))
    match = K.at(137, NEXP, NEXP)[0:1]
    oT = K.at(135, S)[0:NEXP]
    gates = K.gates

    def e4(v):
        return v.rearrange("p (g e) -> p g e", e=4)

    with K.nc.Block() as block:
        @block.gpsimd
        def _(pool):
            for j in range(2 * ST):
                pool.wait_ge(hi_done, j + 1)
                pool.wait_ge(full_done, j + 1)
                pool.tensor_tensor(K.h_lo[:, j // 2, (j % 2) * 512:(j % 2 + 1) * 512], full[:, j, :],
                                   K.h_hi[:, j // 2, (j % 2) * 512:(j % 2 + 1) * 512].bitcast(F32), ALU.subtract)\
                    .then_inc(lo_done, 1)

        @block.sync
        def _(sp):
            K.start(sp)
            sp.wait_ge(copied, 1)
            sp.dma_start(K.gate_rows, oT).then_inc(stored, 16)
            sp.wait_ge(stored, 16)

        @block.tensor
        def _(pe):
            for t in range(ST):
                ins = accumulate(pe, K.ps[:, 0, t * NEXP:(t + 1) * NEXP],
                                 [(K.hT[:, k, t * P:(t + 1) * P], rw[:, k, :]) for k in range(KD)])
            ins.then_inc(s_done, 1)
            for j in range(2 * ST):
                t, half = j // 2, j % 2
                if j >= 4:
                    pe.wait_ge(full_done, j - 3)
                for c in range(4):
                    ins = pe.transpose(K.ps[:, 2 + j % 4, c * P:(c + 1) * P],
                                       K.hT[:, half * 4 + c, t * P:(t + 1) * P], K.ident[:, :])
                ins.then_inc(turned, 1)
            pe.wait_ge(masked, 1)
            for t in range(ST):
                accumulate(pe, K.ps[:, 1, t * NEXP:(t + 1) * NEXP],
                           [(upto, mask[:, t * NEXP:(t + 1) * NEXP])] +
                           [(K.ones[:, :], mask[:, b * NEXP:(b + 1) * NEXP]) for b in range(t)])
            accumulate(pe, K.ps[:, 1, 64:64 + NEXP],
                       [(K.ones[:, :], mask[:, b * NEXP:(b + 1) * NEXP]) for b in range(ST)]).then_inc(place_done, 1)
            pe.wait_ge(over_done, 1)
            for t in range(ST):
                ins = pe.transpose(K.ps[0:NEXP, 6, t * P:(t + 1) * P], over[:, t * NEXP:(t + 1) * NEXP], K.ident[:, :])
            ins.then_inc(s_done, 1)

        @block.scalar
        def _(act):
            act.wait_ge(s_done, 1)
            act.activation(sc, K.ps[:, 0, 0:64], ACT.Sigmoid).then_inc(sig_done, 1)
            for j in range(2 * ST):
                act.wait_ge(turned, j + 1)
                act.activation(K.h_hi[:, j // 2, (j % 2) * 512:(j % 2 + 1) * 512], K.ps[:, 2 + j % 4, :], ACT.Copy)\
                    .then_inc(hi_done, 1)
                act.activation(full[:, j, :], K.ps[:, 2 + j % 4, :], ACT.Copy).then_inc(full_done, 1)
            act.wait_ge(s_done, 2)
            act.activation(oT, K.ps[0:NEXP, 6, :], ACT.Copy).then_inc(copied, 1)

        @block.vector
        def _(dve):
            n = [0]

            def then(ins):
                n[0] += 1
                ins.then_inc(chain, 1)
                dve.wait_ge(chain, n[0])

            def tt(out, a, b, op):
                then(dve.tensor_tensor(out, a, b, op))

            dve.wait_ge(sig_done, 1)
            tt(sel.rearrange("p (t e) -> p t e", e=NEXP), sc.rearrange("p (t e) -> p t e", e=NEXP),
               rb.unsqueeze(1).broadcast_to([P, ST, NEXP]), ALU.add)
            s4 = e4(sel)
            pair = sel.rearrange("p (g h e) -> p g h e", h=2, e=2)
            h2, l2 = hi.rearrange("p (g h) -> p g h", h=2), lo.rearrange("p (g h) -> p g h", h=2)
            tt(h2, pair[:, :, :, 0], pair[:, :, :, 1], ALU.max)
            tt(l2, pair[:, :, :, 0], pair[:, :, :, 1], ALU.min)
            t1, t2 = top[:, 0:16], top[:, 16:32]
            tt(t1, h2[:, :, 0], h2[:, :, 1], ALU.min)
            tt(t2, l2[:, :, 0], l2[:, :, 1], ALU.max)
            tt(t2, t1, t2, ALU.max)
            tt(t1, h2[:, :, 0], h2[:, :, 1], ALU.max)
            g = gs[:, 0:16]
            tt(g, t1, t2, ALU.add)
            then(dve.memset(lose, 0.0))
            then(dve.memset(rank, 0.0))
            then(dve.memset(K.place[:, 64:64 + GE], 0.0))
            gg, ll, r4 = g.rearrange("p (t g) -> p t g", g=4), lose.rearrange("p (t g) -> p t g", g=4), e4(rank)
            gt4 = gt[:, 0:4]
            for i in range(4):
                for j in range(i + 1, 4):
                    tt(gt4, gg[:, :, j], gg[:, :, i], ALU.is_gt)
                    tt(ll[:, :, i], ll[:, :, i], gt4, ALU.add)
                    then(dve.scalar_tensor_tensor(ll[:, :, j], ll[:, :, j], 1.0, gt4, ALU.add, ALU.subtract))
                    tt(gt, s4[:, :, j], s4[:, :, i], ALU.is_gt)
                    tt(r4[:, :, i], r4[:, :, i], gt, ALU.add)
                    then(dve.scalar_tensor_tensor(r4[:, :, j], r4[:, :, j], 1.0, gt, ALU.add, ALU.subtract))
            then(dve.tensor_scalar(lose, lose, 0.5, None, ALU.is_lt))
            n[0] += 1
            dve.scalar_tensor_tensor(e4(mask), e4(rank), 1.5, lose.unsqueeze(2).broadcast_to([P, 16, 4]), ALU.is_lt,
                                     ALU.mult).then_inc(chain, 1)
            dve.wait_ge(chain, n[0])
            dve.memset(flags, 0.0).then_inc(masked, 1)
            tt(gates, mask, sc, ALU.mult)
            g16 = gates.rearrange("p (t e) -> p t e", e=NEXP)
            then(dve.tensor_reduce(gt4, g16, AX.X, ALU.add))
            then(dve.reciprocal(gt4, gt4))
            tt(g16, g16, gt4.unsqueeze(2).broadcast_to([P, ST, NEXP]), ALU.mult)
            dve.wait_ge(place_done, 1)
            tt(K.place[:, 0:64], K.ps[:, 1, 0:64], mask, ALU.mult)
            dve.scalar_tensor_tensor(over, K.place[:, 0:64], SLOTS + 0.5, gates, ALU.is_gt, ALU.mult).then_inc(over_done, 1)
            dve.wait_ge(masked, 1)
            then(dve.tensor_scalar(flags, K.ps[0:1, 1, 64:64 + NEXP], SLOTS + 0.5, None, ALU.is_gt))
            then(dve.tensor_tensor_scan(frank, K.ones[0:1, 0:NEXP], flags, 0.0, ALU.mult, ALU.add))
            dve.tensor_copy(K.over_list[0:1, NEXP:NEXP + 1], frank[:, NEXP - 1:NEXP]).then_inc(placed, 1)
            tt(eq, frank, flags, ALU.mult)
            no = slot_no[0:1, 0:NEXP]
            tt(match, eq.unsqueeze(1).broadcast_to([1, NEXP, NEXP]), no.unsqueeze(2).broadcast_to([1, NEXP, NEXP]),
               ALU.is_equal)
            tt(match, match, no.unsqueeze(1).broadcast_to([1, NEXP, NEXP]), ALU.mult)
            then(dve.tensor_reduce(listed, match, AX.X, ALU.add))
            then(dve.tensor_scalar(listed, listed, -1.0, 0.0, ALU.add, ALU.max))
            dve.tensor_copy(K.over_list[0:1, 0:NEXP], listed).then_inc(placed, 1)
            dve.wait_ge(placed, 2)
            dve.wait_ge(over_done, 1)


def moe_stage(K):
    r, T = K.ring, K.T
    (sel_done, sel_free, gat_done, gat_copied, gate_done, up_done, silu_done, slot_gates, slot_gates_in, hid_done,
     turn_done, turn_copied, back_done, back_copied, y_done, hi_done, lo_done, scat_done, x_added) = K.signals(19)
    n0 = r.first("moe")
    GROUPS, CH = NEXP // GE, 6 * GE
    hg, sel_r, back = K.at(112, KD, S), K.rounded_at(64, ST, GE, SLOTS), K.rounded_at(72, GE, S)
    y_hi, y_lo = K.rounded_at(80, GE, D), K.rounded_at(96, GE, D)
    silu, hid, hidT, gcol = K.at(128, 512), K.at(130, 512), K.at(132, 512), K.at(134, GE)
    gates = K.gates.rearrange("p (t e) -> p t e", e=NEXP)
    sel = sel_r.bitcast(F32)

    def view(c):
        return r.slots[(n0 + c) % RING][:, :].rearrange("p (t c) -> p t c", c=HALF)

    order = moe_order()
    at = {key: c for c, key in enumerate(order)}

    def source(g, c):
        j, m, h = order[c]
        s = slice(h * HALF, (h + 1) * HALF)
        w = T[("moe_w_gate", "moe_w_up", "moe_w_down")[m]]
        return w[bass.ds(g * GE + j, 1), :, s] if m == 2 else w[bass.ds(g * GE + j, 1), s, :]

    with K.nc.Block() as block:
        @block.sync
        def _(sp):
            K.start(sp)
            with sp.Fori(0, GROUPS - 1) as g:
                for k in range(CH):
                    c = k + RING
                    sp.wait_ge(r.used, g * CH + (n0 + c - RING + 1))
                    sp.dma_start(view(c), source(g + c // CH, c % CH).rearrange("o (t p) c -> p (o t) c", p=P))\
                        .then_inc(r.arrived[(n0 + c) % RING], 16)
            r.issued = n0 + RING + (GROUPS - 1) * CH
            r.issue_until(sp, n0 + GROUPS * CH + RING)

        @block.tensor
        def _(pe):
            def arrive(g, c):
                pe.wait_ge(r.arrived[(n0 + c) % RING], g * (16 * CH // RING) + r.arrival(n0 + c))

            def hidden(g, j):
                for m, done in ((0, gate_done), (1, up_done)):
                    for h in range(2):
                        arrive(g, at[j, m, h])
                    if m == 0 and j == 0:
                        pe.wait_ge(gat_copied, g * KD + KD)
                    for k in range(KD):
                        ins = pe.matmul(K.ps[:, m, :], hg[:, k, j * P:(j + 1) * P], view(at[j, m, k // 4])[:, k % 4, :],
                                        start=(k == 0), stop=(k == KD - 1))
                    ins.then_inc(done, 1)
                    release(K, pe, 2)

            def down(g, j):
                pe.wait_ge(turn_copied, g * GE + j + 1)
                for h in range(2):
                    arrive(g, at[j, 2, h])
                    pe.wait_ge(lo_done, g * (2 * GE) + 2 * j + h + 1)
                    for k in range(4):
                        ins = pe.matmul(K.ps[:, 3 + h, :], hidT[:, k * P:(k + 1) * P], view(at[j, 2, h])[:, k, :],
                                        start=(k == 0), stop=(k == 3))
                    ins.then_inc(y_done, 1)
                release(K, pe, 2)

            with pe.Fori(0, GROUPS) as g:
                pe.wait_ge(sel_done, g * ST + ST)
                for c in range(KD):
                    if c < 2:
                        pe.wait_ge(x_added, g * KD + 1)
                    else:
                        pe.wait_ge(gat_copied, g * KD + c - 1)
                    accumulate(pe, K.ps[:, 5 + c % 2, :],
                               [(part[:, t, c * P:(c + 1) * P], sel_r[:, t, :, :])
                                for t in range(ST) for part in (K.h_hi, K.h_lo)]).then_inc(gat_done, 1)
                for j in range(GE):
                    ins = accumulate(pe, K.ps[:, 2, j:j + 1],
                                     [(sel[:, t, j, :], gates[:, t, bass.ds(g * GE + j, 1)]) for t in range(ST)])
                ins.then_inc(slot_gates, 1)
                for j in range(GE):
                    hidden(g, j)
                    if j == 0:
                        for i in range(GE):
                            if i >= 2:
                                pe.wait_ge(back_copied, g * GE + i - 1)
                            for t in range(ST):
                                ins = pe.transpose(K.ps[:, 5 + i % 2, t * P:(t + 1) * P], sel[:, t, i, :],
                                                   K.ident[:, :])
                            ins.then_inc(back_done, 1)
                        pe.transpose(K.ps[:, 7, 0:P], sel[:, 0, 0, :], K.ident[:, :]).then_inc(sel_free, 1)
                    else:
                        down(g, j - 1)
                    pe.wait_ge(hid_done, g * GE + j + 1)
                    for k in range(4):
                        ins = pe.transpose(K.ps[:, 2, k * P:(k + 1) * P], hid[:, k * P:(k + 1) * P], K.ident[:, :])
                    ins.then_inc(turn_done, 1)
                down(g, GE - 1)
                pe.wait_ge(back_copied, g * GE + GE)
                pe.wait_ge(lo_done, g * (2 * GE) + 2 * GE + 2)
                for c in range(KD):
                    if c >= 2:
                        pe.wait_ge(x_added, g * KD + c)
                    accumulate(pe, K.ps[:, 5 + c % 2, :],
                               [(part[:, j, c * P:(c + 1) * P], back[:, j, :])
                                for j in range(GE) for part in (y_hi, y_lo)]).then_inc(scat_done, 1)

        @block.scalar
        def _(act):
            with act.Fori(0, GROUPS) as g:
                act.wait_ge(x_added, g * KD + 1)
                for c in range(KD):
                    act.wait_ge(gat_done, g * KD + c + 1)
                    act.activation(hg[:, c, :], K.ps[:, 5 + c % 2, :], ACT.Copy).then_inc(gat_copied, 1)

                def split(j):
                    for h in range(2):
                        act.wait_ge(y_done, g * (2 * GE) + 2 * j + h + 1)
                        act.activation(y_hi[:, j, h * 512:(h + 1) * 512], K.ps[:, 3 + h, :], ACT.Copy)\
                            .then_inc(hi_done, 1)

                for j in range(GE):
                    act.wait_ge(gate_done, g * GE + j + 1)
                    act.activation(silu, K.ps[:, 0, :], ACT.Silu).then_inc(silu_done, 1)
                    if j == 0:
                        for i in range(GE):
                            act.wait_ge(back_done, g * GE + i + 1)
                            act.activation(back[:, i, :], K.ps[:, 5 + i % 2, :], ACT.Copy).then_inc(back_copied, 1)
                    else:
                        split(j - 1)
                    act.wait_ge(turn_done, g * GE + j + 1)
                    act.activation(hidT, K.ps[:, 2, :], ACT.Copy).then_inc(turn_copied, 1)
                split(GE - 1)

        @block.vector
        def _(dve):
            dve.memset(silu[:, 0:1], 0.0).then_inc(lo_done, 1)
            dve.memset(silu[:, 1:2], 0.0).then_inc(lo_done, 1)
            dve.wait_ge(lo_done, 2)
            dve.memset(silu[:, 2:3], 0.0).then_inc(x_added, 1)

            def select(g):
                for t in range(ST):
                    dve.tensor_tensor(sel_r[:, t, :, :], K.slot_no.unsqueeze(1).broadcast_to([P, GE, SLOTS]),
                                      K.place[:, bass.ds(g * GE + t * NEXP, GE)].unsqueeze(2)
                                      .broadcast_to([P, GE, SLOTS]), ALU.is_equal).then_inc(sel_done, 1)

            select(0)
            with dve.Fori(0, GROUPS) as g:
                def split(j):
                    for h in range(2):
                        s = slice(h * 512, (h + 1) * 512)
                        dve.wait_ge(hi_done, g * (2 * GE) + 2 * j + h + 1)
                        dve.tensor_tensor(y_lo[:, j, s], K.ps[:, 3 + h, :], y_hi[:, j, s].bitcast(F32), ALU.subtract)\
                            .then_inc(lo_done, 1)

                dve.wait_ge(slot_gates, g + 1)
                dve.tensor_copy(gcol, K.ps[:, 2, 0:GE]).then_inc(slot_gates_in, 1)
                dve.wait_ge(slot_gates_in, g + 1)
                for j in range(GE):
                    dve.wait_ge(up_done, g * GE + j + 1)
                    dve.wait_ge(silu_done, g * GE + j + 1)
                    if j >= 1:
                        dve.wait_ge(turn_done, g * GE + j)
                    dve.scalar_tensor_tensor(hid, K.ps[:, 1, :], gcol[:, j:j + 1], silu, ALU.mult, ALU.mult)\
                        .then_inc(hid_done, 1)
                    if j >= 1:
                        split(j - 1)
                    if j == 2:
                        dve.wait_ge(sel_free, g + 1)
                        select(g + 1)
                split(GE - 1)
                for c in range(KD):
                    dve.wait_ge(scat_done, g * KD + c + 1)
                    dve.scalar_tensor_tensor(K.xT[:, c, :], K.ps[:, 5 + c % 2, :], mod_col(K, 5, c), K.xT[:, c, :],
                                             ALU.mult, ALU.add).then_inc(x_added, 1)
            dve.wait_ge(x_added, GROUPS * KD + 1)
            dve.wait_ge(sel_done, (GROUPS + 1) * ST)


def moe_order():
    out = []
    for j in range(GE):
        out += [(j, m, h) for m in range(2) for h in range(2)]
        if j >= 1:
            out += [(j - 1, 2, h) for h in range(2)]
    return out + [(GE - 1, 2, h) for h in range(2)]


def moe_overflow_stage(K):
    T = K.T
    came, freed, gu_done, silu_done, up_done, hid_done, down_done, x_added = K.signals(8)
    FT = 4
    w = K.at(32, 6, 2048)
    silu, prod, hid, row = K.at(80, 2, S), K.at(84, 2, S), K.at(88, FT, S), K.at(96, S)
    wg, wu, wd = T["moe_w_gate"], T["moe_w_up"], T["moe_w_down"]
    LOADS = 7

    def part(s):
        return w[:, s, :].rearrange("p (t c) -> p t c", c=HALF)

    def experts(eng, body):
        count = eng.value_load(K.over_list[0:1, NEXP:NEXP + 1], min_val=0, max_val=NEXP)
        with eng.If(count > 0):
            with eng.Fori(0, count) as i:
                body(i)

    with K.nc.Block() as block:
        @block.sync
        def _(sp):
            K.start(sp)

            def body(i):
                e = sp.value_load(K.over_list[0:1, bass.ds(i, 1)], min_val=0, max_val=NEXP - 1)
                sp.wait_ge(freed, i + 1)
                for s in range(6):
                    h = slice((s % 2) * HALF, (s % 2 + 1) * HALF)
                    src = (wg, wg, wu, wu)[s][bass.ds(e, 1), h, :] if s < 4 else wd[bass.ds(e, 1), :, h]
                    sp.dma_start(part(s), src.rearrange("o (t p) c -> p (o t) c", p=P)).then_inc(came, 16)
                sp.dma_start(row, K.gate_rows[bass.ds(e, 1), :].broadcast_to([P, S])).then_inc(came, 16)
            experts(sp, body)

        @block.tensor
        def _(pe):
            def body(i):
                pe.wait_ge(came, i * (16 * LOADS) + 16 * LOADS)
                for f in range(FT):
                    pe.wait_ge(up_done, i * FT + f + 1)
                    for m in range(2):
                        for k in range(KD):
                            ins = pe.matmul(K.ps[:, 2 * m + f % 2, :], part(2 * m + k // 4)[:, k % 4, f * P:(f + 1) * P],
                                            K.hT[:, k, :], start=(k == 0), stop=(k == KD - 1))
                    ins.then_inc(gu_done, 1)
                pe.wait_ge(hid_done, i * FT + FT)
                for t in range(KD):
                    pe.wait_ge(x_added, i * KD + t + 1)
                    accumulate(pe, K.ps[:, 4 + t % 2, :],
                               [(part(4 + t // 4)[:, k, (t % 4) * P:(t % 4 + 1) * P], hid[:, k, :])
                                for k in range(FT)]).then_inc(down_done, 1)
            experts(pe, body)

        @block.scalar
        def _(act):
            def body(i):
                for f in range(FT):
                    act.wait_ge(gu_done, i * FT + f + 1)
                    act.wait_ge(up_done, i * FT + f + 1)
                    act.activation(silu[:, f % 2, :], K.ps[:, f % 2, :], ACT.Silu).then_inc(silu_done, 1)
            experts(act, body)

        @block.vector
        def _(dve):
            for b in range(2):
                dve.memset(prod[:, b, 0:1], 0.0).then_inc(up_done, 1)
                dve.memset(prod[:, b, 1:2], 0.0).then_inc(x_added, 1)
            dve.wait_ge(up_done, 2)
            dve.wait_ge(x_added, 2)
            dve.memset(prod[:, 0, 2:3], 0.0).then_inc(freed, 1)
            dve.wait_ge(freed, 1)

            def body(i):
                for f in range(FT):
                    dve.wait_ge(silu_done, i * FT + f + 1)
                    dve.tensor_tensor(prod[:, f % 2, :], K.ps[:, 2 + f % 2, :], silu[:, f % 2, :], ALU.mult)\
                        .then_inc(up_done, 1)
                    dve.wait_ge(up_done, i * FT + f + 3)
                    dve.tensor_tensor(hid[:, f, :], prod[:, f % 2, :], row, ALU.mult).then_inc(hid_done, 1)
                for t in range(KD):
                    dve.wait_ge(down_done, i * KD + t + 1)
                    dve.scalar_tensor_tensor(K.xT[:, t, :], K.ps[:, 4 + t % 2, :], mod_col(K, 5, t), K.xT[:, t, :],
                                             ALU.mult, ALU.add).then_inc(x_added, 1)
                dve.wait_ge(x_added, i * KD + KD + 2)
                dve.memset(prod[:, 0, 2:3], 0.0).then_inc(freed, 1)
            experts(dve, body)


def lru_weights_stage(K):
    T = K.T
    zeroed, chain, exp_done, stored = K.signals(4)
    LT = 6
    lam = K.vecs[:, VEC_AT["lru_lambda_2"]:VEC_AT["lru_lambda_2"] + LT]
    e, w, s, p, y = (K.at(150 + 0.25 * i, LT) for i in range(5))
    with K.nc.Block() as block:
        @block.sync
        def _(sp):
            K.start(sp)
            sp.wait_ge(zeroed, 1)
            for m, name in enumerate(("w_rg_a_2", "w_rg_x_2")):
                for h in range(2):
                    blocks = T[name].rearrange("(t h) i j -> h i t j", h=2)[h]
                    sp.dma_start(K.rg[64 * h:64 * h + 64, m, :, 64 * h:64 * h + 64], blocks).then_inc(stored, 16)
            sp.wait_ge(stored, 64)

        @block.scalar
        def _(act):
            act.wait_ge(chain, 1)
            act.activation(e, e, ACT.Exp).then_inc(exp_done, 1)

        @block.vector
        def _(dve):
            dve.memset(K.rg, 0.0).then_inc(zeroed, 1)
            n = [0]

            def then(ins):
                n[0] += 1
                ins.then_inc(chain, 1)
                dve.wait_ge(chain, n[0])

            then(dve.scalar_tensor_tensor(e, lam, -1.0, lam, ALU.mult, ALU.min))
            then(dve.tensor_scalar(y, lam, -1.0, 0.0, ALU.mult, ALU.max))
            dve.wait_ge(exp_done, 1)
            then(dve.tensor_scalar(w, e, 2.0, None, ALU.add))
            then(dve.reciprocal(w, w))
            then(dve.tensor_tensor(w, w, e, ALU.mult))
            then(dve.tensor_tensor(s, w, w, ALU.mult))
            then(dve.tensor_scalar(p, s, 1.0 / 15, 1.0 / 13, ALU.mult, ALU.add))
            for d in (11, 9, 7, 5, 3, 1):
                then(dve.tensor_tensor(p, p, s, ALU.mult))
                then(dve.tensor_scalar(p, p, 1.0 / d, None, ALU.add))
            then(dve.tensor_tensor(p, p, w, ALU.mult))
            then(dve.scalar_tensor_tensor(p, p, 2.0, y, ALU.mult, ALU.add))
            then(dve.tensor_scalar(K.lru_rate, p, -8.0, None, ALU.mult))


def lru_stage(K):
    r = K.ring
    (x_done, mid_done, conv_done, rg_done, sig_done, exp_done, tanh_done, chain, sqrt_done, g_done, gelu_done,
     y_done, h_chain, qm_done, qm_out) = K.signals(15)
    n0, nq, qm_banks = r.first("lru"), r.first("qm"), (6, 4, 0, 1)
    LT = 6
    xc, rr, ii, aa, th, bb, ge = (K.at(56 + 4 * j, 2, S) for j in range(7))
    with K.nc.Block() as block:
        @block.sync
        def _(sp):
            K.start(sp)
            r.issue_until(sp, n0 + 10 + RING)

        @block.tensor
        def _(pe):
            for t in range(LT + 1):
                if t < LT:
                    n = n0 + 4 * (t // 4)
                    if t % 4 == 0:
                        arrived(K, pe, n, 4)
                    if t >= 2:
                        pe.wait_ge(conv_done, 3 * (t - 1))
                    project(K, pe, n, (t % 4) * P, P, K.hT, slice(0, S), K.ps[:, t % 2, :]).then_inc(x_done, 1)
                    if t >= 2:
                        pe.wait_ge(gelu_done, t - 1)
                    project(K, pe, n + 2, (t % 4) * P, P, K.hT, slice(0, S), K.ps[:, 4 + t % 2, :]).then_inc(g_done, 1)
                    if t in (3, LT - 1):
                        release(K, pe, 4)
                if t >= 1:
                    u = t - 1
                    pe.wait_ge(conv_done, 3 * (u + 1))
                    if u >= 1:
                        pe.wait_ge(sig_done, 2 * u)
                    for m in range(2):
                        pe.matmul(K.ps[:, 2 + m, :], K.rg[:, m, u, :], xc[:, u % 2, :], start=True, stop=True)\
                            .then_inc(rg_done, 1)
            arrived(K, pe, nq)
            for c in range(4):
                if c == 1:
                    pe.wait_ge(gelu_done, LT - 1)
                if c == 2:
                    pe.wait_ge(conv_done, 3 * LT)
                project(K, pe, nq, c * P, P, K.hT, slice(0, S), K.ps[:, qm_banks[c], :]).then_inc(qm_done, 1)
            release(K, pe)

        @block.scalar
        def _(act):
            for t in range(LT + 1):
                if t < LT:
                    act.wait_ge(x_done, t + 1)
                    if t >= 2:
                        act.wait_ge(y_done, t - 1)
                    act.activation(xc[:, t % 2, :], K.ps[:, t % 2, :], ACT.Identity, bias=K.vec("conv_b_2", t),
                                   scale=K.vec("conv_w_2", 3 * LT + t)).then_inc(mid_done, 1)
                if t >= 1:
                    u = t - 1
                    b = u % 2
                    act.wait_ge(rg_done, 2 * t)
                    act.activation(rr[:, b, :], K.ps[:, 2, :], ACT.Sigmoid, bias=K.vec("b_rg_a_2", u))\
                        .then_inc(sig_done, 1)
                    act.activation(ii[:, b, :], K.ps[:, 3, :], ACT.Sigmoid, bias=K.vec("b_rg_x_2", u))\
                        .then_inc(sig_done, 1)
                    act.wait_ge(sig_done, 2 * u + 1)
                    act.activation(th[:, b, :], rr[:, b, :], ACT.Tanh, scale=K.lru_rate[:, u:u + 1])\
                        .then_inc(tanh_done, 1)
                    act.activation(aa[:, b, :], rr[:, b, :], ACT.Exp, scale=K.lru_rate[:, u:u + 1])\
                        .then_inc(exp_done, 1)
                    act.wait_ge(g_done, u + 1)
                    act.activation(ge[:, b, :], K.ps[:, 4 + b, :], ACT.Gelu_apprx_tanh).then_inc(gelu_done, 1)
                    act.wait_ge(chain, 4 * u + 3)
                    act.activation(bb[:, b, :], bb[:, b, :], ACT.Sqrt).then_inc(sqrt_done, 1)
            for c in range(4):
                act.wait_ge(qm_done, c + 1)
                act.activation(K.qm[:, c, :], K.ps[:, qm_banks[c], :], ACT.Copy).then_inc(qm_out, 1)
            act.wait_ge(qm_out, 4)

        @block.vector
        def _(dve):
            for t in range(LT + 1):
                if t < LT:
                    x, u = xc[:, t % 2, :], K.ps[:, t % 2, :]
                    dve.wait_ge(mid_done, t + 1)
                    for k in range(1, 4):
                        dve.scalar_tensor_tensor(x[:, k:S], u[:, 0:S - k], K.vec("conv_w_2", (3 - k) * LT + t),
                                                 x[:, k:S], ALU.mult, ALU.add).then_inc(conv_done, 1)
                        dve.wait_ge(conv_done, 3 * t + k)
                if t >= 1:
                    u = t - 1
                    b = u % 2
                    dve.wait_ge(tanh_done, u + 1)
                    dve.tensor_scalar(bb[:, b, :], th[:, b, :], -1.0, 1.0, ALU.mult, ALU.add).then_inc(chain, 1)
                    dve.wait_ge(chain, 4 * u + 1)
                    dve.reciprocal(bb[:, b, :], bb[:, b, :]).then_inc(chain, 1)
                    dve.wait_ge(chain, 4 * u + 2)
                    dve.scalar_tensor_tensor(bb[:, b, :], th[:, b, :], -2.0, bb[:, b, :], ALU.mult, ALU.mult)\
                        .then_inc(chain, 1)
                    dve.wait_ge(sig_done, 2 * u + 2)
                    dve.tensor_tensor(ii[:, b, :], ii[:, b, :], xc[:, b, :], ALU.mult).then_inc(chain, 1)
                    dve.wait_ge(chain, 4 * u + 4)
                    dve.wait_ge(sqrt_done, u + 1)
                    dve.wait_ge(exp_done, u + 1)
                    dve.wait_ge(gelu_done, u + 1)
                    dve.tensor_tensor(bb[:, b, :], bb[:, b, :], ii[:, b, :], ALU.mult).then_inc(h_chain, 1)
                    dve.wait_ge(h_chain, 2 * u + 1)
                    dve.tensor_tensor_scan(th[:, b, :], aa[:, b, :], bb[:, b, :], 0.0, ALU.mult, ALU.add)\
                        .then_inc(h_chain, 1)
                    dve.wait_ge(h_chain, 2 * u + 2)
                    dve.tensor_tensor(K.ylruT[:, u, :], th[:, b, :], ge[:, b, :], ALU.mult).then_inc(y_done, 1)
            dve.wait_ge(y_done, LT)


def memory_project_stage(K):
    n = K.ring.first("mem")
    items = [channel_item(K, n, t * P, P, K.memT, NCTX, K.kmT[:, t, :], eng=("act", "dve")[t % 2],
                          first=(n, n + 1) if t == 0 else (), rel=2 if t == 3 else 0) for t in range(4)]
    n += 2
    items += [token_item(K, n, 0, 512, K.memT, slice(t * P, t * P + P), K.vm[:, t, :], eng=("act", "dve")[t],
                         first=(n, n + 1) if t == 0 else (), rel=2 if t == 1 else 0) for t in range(2)]
    items_stage(K, items, issue=n + 2)


def group_tokens(v, g, j):
    return v[:, j * P:(j + 1) * P] if g == 0 else v.rearrange("p (l r) -> p r l", r=4)[:, j, :]


def dilated_project_stage(K):
    n0 = K.ring.first("qkv")
    items = []
    for c in range(12):
        n = n0 + 2 * (c // 4)
        dest = K.qd[:, c, :] if c < 6 else K.kd[:, c - 6, :]
        items.append(channel_item(K, n, (c % 4) * P, P, K.hT, S, dest, eng="act" if c < 6 else "dve",
                                  first=(n, n + 1) if c % 4 == 0 else (), rel=2 if c % 4 == 3 else 0,
                                  **({"scale": 0.125} if c < 6 else {})))
    for g in range(3):
        n = n0 + 6 + 2 * (g // 2)
        for j in range(4):
            c0 = 256 * (g % 2)

            def mm(pe, bank, g=g, j=j, n=n, c0=c0):
                return accumulate(pe, bank[:, 0:256],
                                  [(group_tokens(K.hT[:, k, :], g, j), K.ring.view(n + k // 4)[:, k % 4, c0:c0 + 256])
                                   for k in range(KD)])
            dest = K.vd[:, g * 4 + j, :]
            items.append({"first": (n, n + 1) if (g != 1 and j == 0) else (), "mm": mm,
                          "rel": 2 if (g > 0 and j == 3) else 0, "eng": "act" if j % 2 else "dve",
                          "out": (lambda e, bank, dest=dest: e.activation(dest, bank[:, 0:256], ACT.Copy)) if j % 2 else
                                 (lambda e, bank, dest=dest: e.tensor_copy(dest, bank[:, 0:256]))})
    items_stage(K, items, issue=n0 + 10, beside=bias_work)


NU = 384


def bias_work(K, signals, emptied):
    T = K.T
    table, hot, neg, u = K.at(116, 12)[0:32], K.at(117, 3, NU)[0:32], K.at(122, 3, NU)[0:4], K.at(127, 3, NU)[0:4]
    mm_done, added, stored, read = signals[:4]
    rows = K.bias_rows

    def pool(pool):
        for dst, src in ((table, T["rel_bias_2"]), (hot, T["k_bucket"]), (neg, T["k_neg"]),
                         (K.flip, T["k_flip"]), (K.pick, T["k_pick"])):
            pool.dma_start(dst, src).then_inc(K.loaded, 16)
        pool.wait_ge(K.loaded, K.loads(5))

    def sp(sp):
        sp.wait_ge(added, 3)
        sp.dma_start(rows.rearrange("g h n -> h g n"), u).then_inc(stored, 16)
        sp.wait_ge(stored, 16)
        n = 0
        for h in range(4):
            for dst, off, c in ((K.hank0, 0, 256), (K.hank1, 4 * NU + P, P), (K.hank2, 8 * NU + P, P)):
                sp.dma_start(dst[:, h, :], bass.AP(rows.tensor, off + h * NU, [[1, P], [1, c]])).then_inc(read, 16)
                n += 16
        sp.wait_ge(read, n)

    def pe(pe):
        pe.wait_ge(K.loaded, K.loads(5))
        for g in range(3):
            pe.matmul(K.ps[0:4, 4 + g, 0:NU], table[:, 4 * g:4 * g + 4], hot[:, g, :], start=True, stop=True)\
                .then_inc(mm_done, 1)

    def dve(dve):
        dve.wait_ge(K.loaded, K.loads(5))
        for g in range(3):
            dve.wait_ge(mm_done, g + 1)
            dve.tensor_tensor(u[:, g, :], K.ps[0:4, 4 + g, 0:NU], neg[:, g, :], ALU.add).then_inc(added, 1)

    return {"loads": 5, "pool": pool, "sp": sp, "pe": {4: pe}, "dve": {4: dve}}


def dilated_attention_stage(K):
    (s_done, max_done, neg_done, exp_done, turned, copied, o_done, o_copied, st_turned, st_copied, chain, e_done,
     bc_done, part, summed) = K.signals(15)
    units = [(g, j, h) for g in range(3) for j in range(4) for h in range(4)]
    NUNIT = len(units)
    Pb, PT = K.at(116, 3, 256), K.at(119, 2, 2, P)
    stats = K.at(121, 3, NUNIT)
    num = K.at(122, 6, S)
    mrow, drow = K.at(134, 3, S)[0:4], K.at(140, 3, S)[0:4]
    m, tmp = K.at(146, S)[0:4], K.at(116, 2, S)

    def keys(g, j):
        return ([j - 1, j] if j else [0]) if g == 0 else [j]

    def hank(g, j, h):
        return (K.hank0[:, h, 0:256] if j else K.hank0[:, h, P:256]) if g == 0 else (K.hank1, K.hank2)[g - 1][:, h, :]

    def key_view(g, j, rows, c):
        v = K.kd[rows, c, :]
        return v[:, (j - 1) * P:(j + 1) * P] if g == 0 and j else group_tokens(v, g, j)

    def spread(v, g, j):
        return group_tokens(v, g, j)

    with K.nc.Block() as block:
        @block.sync
        def _(sp):
            K.start(sp)

        @block.tensor
        def _(pe):
            def scores(b):
                g, j, h = units[b]
                c, rows = g * 2 + h // 2, slice(64 * (h % 2), 64 * (h % 2) + 64)
                nk = P * len(keys(g, j))
                if b >= 2:
                    pe.wait_ge(exp_done, b - 1)
                out = K.ps[:, b % 2, 0:nk]
                pe.matmul(out, K.flip, hank(g, j, h), start=True, stop=False)
                pe.matmul(out, group_tokens(K.qd[rows, c, :], g, j), key_view(g, j, rows, c), start=False, stop=True)\
                    .then_inc(s_done, 1)

            def turn(b):
                g, j, h = units[b]
                pe.wait_ge(exp_done, b + 1)
                if b >= 2:
                    pe.wait_ge(copied, b - 1)
                ks = keys(g, j)
                for i in range(len(ks)):
                    ins = pe.transpose(K.ps[:, 2 + b % 2, i * P:(i + 1) * P], Pb[:, b % 3, i * P:(i + 1) * P],
                                       K.ident[:, :])
                ins.then_inc(turned, 1)

            def values(b):
                g, j, h = units[b]
                ks = keys(g, j)
                if h == 3:
                    q = b // 4
                    if q >= 1:
                        pe.wait_ge(st_copied, 2 * q)
                    for i in (0, 2):
                        ins = pe.transpose(K.ps[0:4, 6, (i // 2) * P:(i // 2 + 1) * P], stats[:, i, b - 3:b + 1],
                                           K.ident[:, :])
                    ins.then_inc(st_turned, 1)
                if h == 0 and b >= 8:
                    pe.wait_ge(o_copied, b // 4 - 1)
                pe.wait_ge(copied, b + 1)
                out = K.ps[64 * (h % 2):64 * (h % 2) + 64, 4 + (b // 4) % 2, (h // 2) * P:(h // 2 + 1) * P]
                accumulate(pe, out, [(K.vd[:, g * 4 + kt, 64 * h:64 * h + 64], PT[:, b % 2, i, :])
                                     for i, kt in enumerate(ks)]).then_inc(o_done, 1)

            for a in range(NUNIT + 3):
                if a < NUNIT:
                    scores(a)
                if 0 <= a - 2 < NUNIT:
                    turn(a - 2)
                if a >= 3:
                    values(a - 3)
            pe.wait_ge(chain, 11)
            for i in range(6):
                if i >= 2:
                    pe.wait_ge(part, i - 1)
                pe.matmul(K.ps[:, i % 2, :], K.pick[:, (i % 2) * P:(i % 2 + 1) * P], drow[:, i // 2, :], start=True,
                          stop=True).then_inc(bc_done, 1)

        @block.scalar
        def _(act):
            def empty(b):
                g, j, h = units[b]
                if h == 3:
                    q = b // 4
                    act.wait_ge(st_turned, q + 1)
                    for dst, c in ((mrow, 0), (drow, 1)):
                        act.activation(spread(dst[:, g, :], g, j), K.ps[0:4, 6, c * P:(c + 1) * P],
                                       ACT.Copy).then_inc(st_copied, 1)
                    act.wait_ge(o_done, b + 1)
                    for pr in range(2):
                        ins = act.activation(spread(num[:, 2 * g + pr, :], g, j),
                                             K.ps[:, 4 + q % 2, pr * P:(pr + 1) * P], ACT.Copy)
                    ins.then_inc(o_copied, 1)

            for b in range(NUNIT + 3):
                if b < NUNIT:
                    g, j, h = units[b]
                    nk = P * len(keys(g, j))
                    act.wait_ge(neg_done, b + 1)
                    if b >= 3:
                        act.wait_ge(turned, b - 2)
                    act.activation(Pb[:, b % 3, 0:nk], K.ps[:, b % 2, 0:nk], ACT.Exp, bias=stats[:, 1, b:b + 1],
                                   accum_out=stats[:, 2, b:b + 1]).then_inc(exp_done, 1)
                if b >= 3:
                    empty(b - 3)
            for g in range(3):
                act.wait_ge(chain, 2 + g + 1)
                act.activation(mrow[:, g, :], mrow[:, g, :], ACT.Exp).then_inc(e_done, 1)

        @block.vector
        def _(dve):
            def maximum(b):
                g, j, h = units[b]
                dve.wait_ge(s_done, b + 1)
                dve.tensor_reduce(stats[:, 0, b:b + 1], K.ps[:, b % 2, 0:P * len(keys(g, j))], AX.X, ALU.max)\
                    .then_inc(max_done, 1)
                dve.wait_ge(max_done, b + 1)
                dve.tensor_scalar(stats[:, 1, b:b + 1], stats[:, 0, b:b + 1], -1.0, None, ALU.mult)\
                    .then_inc(neg_done, 1)

            for a in range(NUNIT + 2):
                if a < NUNIT:
                    maximum(a)
                if a < 2:
                    continue
                b = a - 2
                g, j, h = units[b]
                n = len(keys(g, j))
                dve.wait_ge(turned, b + 1)
                if b >= 2:
                    dve.wait_ge(o_done, b - 1)
                dve.tensor_copy(PT[:, b % 2, 0:n, :], K.ps[:, 2 + b % 2, 0:n * P].rearrange("p (i q) -> p i q", q=P))\
                    .then_inc(copied, 1)
            dve.wait_ge(st_copied, 24)
            dve.tensor_tensor(m, mrow[:, 0, :], mrow[:, 1, :], ALU.max).then_inc(chain, 1)
            dve.wait_ge(chain, 1)
            dve.tensor_tensor(m, m, mrow[:, 2, :], ALU.max).then_inc(chain, 1)
            dve.wait_ge(chain, 2)
            for g in range(3):
                dve.tensor_tensor(mrow[:, g, :], mrow[:, g, :], m, ALU.subtract).then_inc(chain, 1)
            t0 = tmp[0:4, 0, :]
            for g in range(3):
                dve.wait_ge(e_done, g + 1)
                dve.wait_ge(chain, 5 if g == 0 else 5 + g)
                if g == 0:
                    dve.tensor_tensor(m, drow[:, 0, :], mrow[:, 0, :], ALU.mult).then_inc(chain, 1)
                else:
                    dve.tensor_tensor(drow[:, g, :], drow[:, g, :], mrow[:, g, :], ALU.mult).then_inc(chain, 1)
            dve.wait_ge(chain, 8)
            dve.tensor_tensor(t0, drow[:, 1, :], drow[:, 2, :], ALU.add).then_inc(summed, 1)
            dve.wait_ge(summed, 1)
            dve.tensor_tensor(m, m, t0, ALU.add).then_inc(summed, 1)
            dve.wait_ge(summed, 2)
            dve.reciprocal(m, m).then_inc(summed, 1)
            dve.wait_ge(summed, 3)
            for g in range(3):
                dve.tensor_tensor(drow[:, g, :], mrow[:, g, :], m, ALU.mult).then_inc(chain, 1)
            dve.wait_ge(o_copied, 12)
            for i in range(6):
                g, pr = i // 2, i % 2
                dve.wait_ge(bc_done, i + 1)
                dest = K.odT[:, pr, :]
                dve.tensor_tensor(dest if g == 0 else tmp[:, pr, :], K.ps[:, i % 2, :], num[:, i, :], ALU.mult)\
                    .then_inc(part, 1)
                dve.wait_ge(part, i + 1)
                if g:
                    dve.tensor_tensor(dest, dest, tmp[:, pr, :], ALU.add).then_inc(summed, 1)
                    dve.wait_ge(summed, 3 + i - 1)


def memory_attention_stage(K):
    attention_stage(K, 4, NCTX, lambda h, i: [(slice(0, NCTX), K.qm[:, h, i * P:(i + 1) * P], K.kmT[:, h, :])],
                    lambda h, j: K.vm[:, j, h * P:(h + 1) * P], lambda h: K.omT[:, h, :], P ** -0.5, 116)


def mlp_stage(K):
    r, T = K.ring, K.T
    (h_hi_done, h_lo_done, w_hi_done, spent, up_done, relu_done, prod_done, hid_hi_done, hid_done, down_done,
     x_added) = K.signals(11)
    n0 = r.first("mlp")
    UNITS, CH, FT = 8, 4, 4
    BODY = 3
    LOOPS = UNITS // BODY
    BC = BODY * CH
    h_hi, h_lo = K.rounded_at(32, KD, S), K.rounded_at(48, KD, S)
    hid_hi, hid_lo = K.rounded_at(64, FT, S), K.rounded_at(72, FT, S)
    relu, prod = K.at(144, 2, S), K.at(148, 2, S)
    win, wout = T["w_mlp_in_2"], T["w_mlp_out_2"]

    def raw(c):
        return r.slots[(n0 + c) % RING]

    def part(c, lo):
        return K.rounded_at(80 + 16 * (c % CH) + 8 * lo, 4, HALF)

    def flat(v):
        return v.rearrange("p t c -> p (t c)")

    with K.nc.Block() as block:
        @block.sync
        def _(sp):
            K.start(sp)
            with sp.Fori(0, LOOPS) as i:
                for k in range(BC):
                    c = k + RING
                    u, s = i * BODY + c // CH, c % CH
                    sp.wait_ge(r.used, i * BC + (n0 + c - RING + 1))
                    src = (win[s * HALF:(s + 1) * HALF, bass.ds(u * HALF, HALF)] if s < 2 else
                           wout[bass.ds(u * HALF, HALF), (s - 2) * HALF:(s - 1) * HALF])
                    sp.dma_start(raw(c).rearrange("p (t c) -> p t c", c=HALF), src.rearrange("(t p) c -> p t c", p=P))\
                        .then_inc(r.arrived[(n0 + c) % RING], 16)
            r.issued = n0 + RING + LOOPS * BC
            r.issue_until(sp, n0 + UNITS * CH + RING)

        @block.gpsimd
        def _(pool):
            def rest(c, i):
                pool.wait_ge(w_hi_done, i * BC + c + 1)
                pool.tensor_tensor(flat(part(c, 1)), raw(c)[:, :], flat(part(c, 0)).bitcast(F32), ALU.subtract)\
                    .then_inc(r.used, 1)

            with pool.Fori(0, LOOPS) as i:
                for c in range(BC):
                    rest(c, i)
            for c in range(LOOPS * BC, UNITS * CH):
                rest(c, 0)

        @block.tensor
        def _(pe):
            def unit(v, i):
                u = i * BODY + v
                for f in range(FT):
                    pe.wait_ge(prod_done, u * FT + f + 1)
                    ins = split_products(pe, K.ps[:, f % 2, :],
                                         [(part(k // 4, 0)[:, k % 4, f * P:(f + 1) * P],
                                           part(k // 4, 1)[:, k % 4, f * P:(f + 1) * P], h_hi[:, k, :], h_lo[:, k, :])
                                          for k in range(KD)],
                                         before=(lambda k: first_reads(v, i, k)) if f == 0 else None)
                    ins.then_inc(up_done, 1)
                spend(2)
                for t in range(KD):
                    pe.wait_ge(x_added, u * KD + t + 1)
                    if t % 4 == 0:
                        pe.wait_ge(r.used, i * BC + (n0 + v * CH + 3 + t // 4))
                    c = 2 + t // 4
                    cols = slice((t % 4) * P, (t % 4 + 1) * P)
                    split_products(pe, K.ps[:, 4 + t % 2, :],
                                   [(part(c, 0)[:, k, cols], part(c, 1)[:, k, cols], hid_hi[:, k, :], hid_lo[:, k, :])
                                    for k in range(FT)],
                                   before=(lambda k: pe.wait_ge(hid_done, u * FT + k + 1)) if t == 0 else None)\
                        .then_inc(down_done, 1)
                    if t % 4 == 3:
                        spend(1)

            def spend(count):
                pe.matmul(K.ps[:, 7, 511:512], K.ones[:, :], K.ones[:, 0:1], start=True, stop=True)\
                    .then_inc(spent, count)

            def first_reads(v, i, k):
                if k % 4 == 0:
                    pe.wait_ge(r.used, i * BC + (n0 + v * CH + 1 + k // 4))
                if v == 0:
                    pe.wait_ge(h_lo_done, k + 1)

            with pe.Fori(0, LOOPS) as i:
                for v in range(BODY):
                    unit(v, i)
            for v in range(LOOPS * BODY, UNITS):
                unit(v, 0)

        @block.scalar
        def _(act):
            def high(c, i):
                n = n0 + c
                act.wait_ge(r.arrived[n % RING], i * 32 + r.arrival(n))
                if c >= CH:
                    act.wait_ge(spent, i * BC + c - CH + 1)
                act.activation(flat(part(c, 0)), raw(c)[:, :], ACT.Copy).then_inc(w_hi_done, 1)

            def unit(v, i):
                u = i * BODY + v
                for f in range(FT):
                    act.wait_ge(up_done, u * FT + f + 1)
                    act.wait_ge(prod_done, u * FT + f + 1)
                    act.activation(relu[:, f % 2, :], K.ps[:, f % 2, :], ACT.Relu).then_inc(relu_done, 1)

            high(0, 0)
            for k in range(KD):
                if k == 4:
                    high(1, 0)
                act.activation(h_hi[:, k, :], K.hT[:, k, :], ACT.Copy).then_inc(h_hi_done, 1)
            high(2, 0)
            high(3, 0)
            with act.Fori(0, LOOPS) as i:
                for v in range(BODY):
                    unit(v, i)
                    for s in range(CH):
                        high((v + 1) * CH + s, i)
            for v in range(LOOPS * BODY, UNITS):
                unit(v, 0)
                if v + 1 < UNITS:
                    for s in range(CH):
                        high((v + 1) * CH + s, 0)

        @block.vector
        def _(dve):
            for k in range(KD):
                dve.wait_ge(h_hi_done, k + 1)
                dve.tensor_tensor(h_lo[:, k, :], K.hT[:, k, :], h_hi[:, k, :].bitcast(F32), ALU.subtract)\
                    .then_inc(h_lo_done, 1)
            for b in range(2):
                dve.memset(prod[:, b, 0:1], 0.0).then_inc(prod_done, 1)
                dve.memset(prod[:, b, 1:2], 0.0).then_inc(x_added, 1)
            dve.wait_ge(prod_done, 2)
            dve.wait_ge(x_added, 2)
            with dve.Fori(0, UNITS) as u:
                for f in range(FT):
                    m = prod[:, f % 2, :]
                    dve.wait_ge(relu_done, u * FT + f + 1)
                    dve.tensor_tensor(m, K.ps[:, f % 2, :], relu[:, f % 2, :], ALU.mult).then_inc(prod_done, 1)
                    dve.wait_ge(prod_done, u * FT + f + 3)
                    dve.tensor_copy(hid_hi[:, f, :], m).then_inc(hid_hi_done, 1)
                    dve.wait_ge(hid_hi_done, u * FT + f + 1)
                    dve.tensor_tensor(hid_lo[:, f, :], m, hid_hi[:, f, :].bitcast(F32), ALU.subtract)\
                        .then_inc(hid_done, 1)
                for t in range(KD):
                    dve.wait_ge(down_done, u * KD + t + 1)
                    dve.tensor_tensor(K.xT[:, t, :], K.ps[:, 4 + t % 2, :], K.xT[:, t, :], ALU.add)\
                        .then_inc(x_added, 1)
            dve.wait_ge(x_added, UNITS * KD + 2)


def load_memory_stage(K):
    (came,) = K.signals(1)
    with K.nc.Block() as block:
        @block.sync
        def _(sp):
            K.start(sp)
            sp.dma_start(K.memT, K.T["memT"].rearrange("(t p) n -> p t n", p=P)).then_inc(came, 16)
            sp.wait_ge(came, 16)


def host_constants():
    f32 = np.float32
    out = {"k_ident": np.eye(P, dtype=f32)}
    pos = np.arange(S)
    inv = f32(10000.0) ** (-np.arange(32, dtype=f32) / f32(32))
    ang = np.concatenate([(pos // 64).astype(f32)[:, None] * inv, (pos % 64).astype(f32)[:, None] * inv], axis=1)
    out["k_cos"] = np.repeat(np.cos(ang.astype(f32)), 2, axis=1).T.astype(f32)
    out["k_sin"] = np.repeat(np.sin(ang.astype(f32)), 2, axis=1).T.astype(f32)
    swap = np.zeros((P, P), f32)
    for i in range(0, P, 2):
        swap[i + 1, i] = -1.0
        swap[i, i + 1] = 1.0
    out["k_swap"] = swap
    scan = np.ones((P, S + NCTX), f32)
    scan[:, 0:S:64] = 0.0
    scan[:, S] = 0.0
    out["k_scan"] = scan
    t = np.arange(S, dtype=f32)
    tn = (t / f32(S)).astype(f32)
    bands = np.linspace(1e-4, 15, 16, dtype=f32)
    phase = (f32(2 * np.pi / S) * t[:, None] * bands[None, :]).astype(f32)
    out["k_pos"] = np.concatenate([tn[:, None], np.cos(phase), -np.sin(phase)], axis=1).T.astype(f32)
    first = np.ones(P, f32)
    first[0] = 0.0
    out["k_time"] = np.concatenate([-tn.reshape(ST, P).T, first[:, None]], axis=1)
    nn = 2 * S
    ang2 = 2 * np.pi * ((np.arange(S)[:, None] * np.arange(S)[None, :]) % nn) / nn
    alt = 1.0 - 2.0 * (np.arange(S) % 2)
    cosm, sinm = np.cos(ang2), -np.sin(ang2)
    out["k_dft_cos"] = cosm.astype(f32)
    s1 = sinm.copy()
    s1[:, 0] = alt
    out["k_dft_sin"] = s1.astype(f32)
    c1 = cosm[:, 0:P].copy()
    c1[:, 0] = alt
    out["k_dft_edge"] = np.concatenate([c1, sinm[:, 0:P]], axis=1).astype(f32)
    ic, isn = 2.0 * cosm / nn, 2.0 * sinm / nn
    ic[0] = 1.0 / nn
    isn[0] = alt / nn
    out["k_idft_cos"] = ic.astype(f32)
    out["k_idft_sin"] = isn.astype(f32)
    hot, neg = np.zeros((32, 3, NU), f32), np.zeros((4, 3, NU), f32)
    for g, (dil, each) in enumerate(((1, 1), (4, 1), (4, 4))):
        for j in range(NU):
            off = 255 - j
            if not (0 <= off <= P and off % each == 0):
                neg[:, g, j] = NEG
                continue
            dist = off * dil
            b = dist
            if dist >= 16:
                large = f32(np.log(f32(dist) / f32(16))) / f32(np.log(128.0)) * f32(16)
                b = min(16 + int(large), 31)
            hot[b, g, j] = 1.0
    out["k_bucket"], out["k_neg"] = hot, neg
    out["k_flip"] = np.eye(P, dtype=f32)[::-1]
    pick = np.zeros((4, 256), f32)
    for h in range(4):
        pick[h, (h // 2) * P + 64 * (h % 2):(h // 2) * P + 64 * (h % 2) + 64] = 1.0
    out["k_pick"] = pick
    out["k_upto"] = np.triu(np.ones((P, P), f32))
    out["k_slot_no"] = np.tile(np.arange(1, P + 1, dtype=f32), (P, 1))
    a = np.arange(P)
    same = (a[:, None] // 64) == (a[None, :] // 64)
    out["k_causal"] = np.stack([same & (a[:, None] <= a[None, :]), same & (a[:, None] >= a[None, :])]).astype(f32)
    return out


WEIGHTS = ["w_mod", "w_in", "gla_wa2", "hy_pos_w1", "hy_pos_w2", "hy_pos_w3", "w_br_hy", "w_br_gla", "w_br_att",
           "w_out", "router_w", "moe_w_gate", "moe_w_up", "moe_w_down", "w_in_2", "w_rg_a_2", "w_rg_x_2",
           "w_lru_out_2", "rel_bias_2", "w_dil_out_2", "w_mem_kv_2", "w_mem_out_2", "w_out_2", "w_mlp_in_2",
           "w_mlp_out_2"]
ROWS = ["gla_norm_g", "hy_decay", "hy_skip", "router_b"]


def layout(inputs):
    out = {k: np.ascontiguousarray(v) for k, v in host_constants().items()}
    for name in WEIGHTS:
        a = np.asarray(inputs[name])
        out[name] = np.ascontiguousarray(a[0] if a.shape[0] == 1 else a)
    for name in ROWS:
        out[name] = np.ascontiguousarray(np.asarray(inputs[name]).reshape(1, -1))
    out["xT"] = np.ascontiguousarray(np.asarray(inputs["x"])[0].T)
    out["ctxT"] = np.ascontiguousarray(np.asarray(inputs["ctx"])[0].T)
    out["memT"] = np.ascontiguousarray(np.asarray(inputs["mem_2"])[0].T)
    out["hy_cols"] = np.ascontiguousarray(
        np.stack([np.asarray(inputs[n]).reshape(-1) for n in ("hy_pos_b1", "hy_pos_b2", "hy_sin_freq")], axis=1))
    out["vecs"] = np.ascontiguousarray(
        np.concatenate([np.asarray(inputs[n]).reshape(-1, P).T for n, _ in VECS], axis=1))
    return out


def build(nc, T, out, upto=99, debug=None):
    with ExitStack() as ctx:
        K = Core(nc, ctx, T)
        K.out = out
        K.sc = ctx.enter_context(nc.sbuf_tensor("silu_c", [P, KD, 2], F32))
        g = ctx.enter_context(nc.sbuf_tensor("gains", [P, 24], F32))
        K.gain1, K.gain1c, K.gain2 = g[:, 0:8], g[:, 8:16], g[:, 16:24]
        K.tot = ctx.enter_context(nc.sbuf_tensor("chunk_decay", [P, 4, 9], F32))
        K.over_list = ctx.enter_context(nc.sbuf_tensor("overflow_list", [1, NEXP + 1], mybir.dt.int32))
        K.gate_rows = nc.dram_tensor("gate_rows", (NEXP, S), F32).ap()
        plan_block1(K)
        K.bias_rows = nc.dram_tensor("bias_rows", (3, 4, NU), F32).ap()
        plan_block2(K)
        done = 0
        with K.region(0, 32):
            K.xT, K.hT = K.at(0, KD, S), K.at(16, KD, S)
            for kept, phases in (
                    ([(32, 72, F32)], [([(72, ARENA_KB, F32)], block1_stages),
                                       ([(72, 136, F32R), (136, ARENA_KB, F32)], merge1_stages)]),
                    ([], [([(32, 112, F32R), (112, ARENA_KB, F32)], expert_stages),
                          ([(32, ARENA_KB, F32)], lambda K: [lambda: moe_overflow_stage(K)])]),
                    ([(32, 56, F32)], [([(56, ARENA_KB, F32)], block2_stages),
                                       ([(56, 120, F32R), (120, ARENA_KB, F32)], merge2_stages)]),
                    ([], [([(32, 144, F32R), (144, ARENA_KB, F32)], lambda K: [lambda: mlp_stage(K)]),
                          ([(32, ARENA_KB, F32)], final_stages)])):
                with ExitStack() as block_memory:
                    for low, high, dtype in kept:
                        block_memory.enter_context(K.region(low, high, dtype))
                    for regions, stages in phases:
                        with ExitStack() as memory:
                            for low, high, dtype in regions:
                                memory.enter_context(K.region(low, high, dtype))
                            for stage in stages(K):
                                if done < upto:
                                    stage()
                                    done += 1
                                    if debug and done == upto:
                                        dump(K, debug)


def dump(K, debug):
    (done,) = K.signals(1)
    with K.nc.Block() as block:
        @block.sync
        def _(sp):
            K.start(sp)
            n = 0
            for ap, src in debug(K):
                sp.dma_start(ap, src).then_inc(done, 16)
                n += 16
            sp.wait_ge(done, n)


def plan_block1(K):
    r, T = K.ring, K.T
    w = T["w_mod"].rearrange("(h t p) c -> h p t c", h=2, p=P)
    for g in range(12):
        for h in range(2):
            r.add("mod", w[h][:, :, g * HALF:(g + 1) * HALF])
    w = T["w_in"]
    r.add_matrix("gk", w, C_GK, C_GK + 256)
    r.add_matrix("ga", w, C_GA, C_GA + 32)
    r.add_matrix("gq", w, C_GQ, C_GQ + 256)
    r.add_matrix("gv", w, C_GV, C_GV + 512)
    r.add_matrix("og", w, C_OG, C_OG + 512)
    r.add_matrix("kv", w, C_KV, C_KV + 512)
    r.add_matrix("q", w, C_Q, C_Q + 1024)
    r.add_matrix("hy", w, C_HY, C_HY + 1536)
    for o in range(2):
        for m in ("k_dft_cos", "k_dft_sin", "k_dft_edge", "k_idft_cos", "k_idft_sin"):
            r.add_matrix(f"dft{o}", T[m], 0, T[m].shape[1])
    merge_chunks(K, "merge1", w, C_BR, [T["w_br_hy"], T["w_br_gla"], T["w_br_att"]], T["w_out"])
    for g in range(NEXP // GE):
        for j, m, h in moe_order():
            w = T[("moe_w_gate", "moe_w_up", "moe_w_down")[m]][g * GE + j]
            s = slice(h * HALF, (h + 1) * HALF)
            r.add("moe", (w[:, s] if m == 2 else w[s, :]).rearrange("(t p) c -> p t c", p=P))


def plan_block2(K):
    r, T = K.ring, K.T
    w = T["w_in_2"]
    r.add_matrix("mem", T["w_mem_kv_2"], 0, D)
    r.add_matrix("lru", w, C2_X, C2_X + 512)
    r.add_matrix("lru", w, C2_G, C2_G + 512)
    r.add_matrix("lru", w, C2_X + 512, C2_X + 768)
    r.add_matrix("lru", w, C2_G + 512, C2_G + 768)
    r.add_matrix("qm", w, C2_QM, C2_QM + 512)
    r.add_matrix("qkv", w, C2_QKV, C2_QKV + 2304)
    merge_chunks(K, "merge2", w, C2_BR, [T["w_lru_out_2"], T["w_dil_out_2"], T["w_mem_out_2"]], T["w_out_2"])
    for u in range(8):
        r.add_matrix("mlp", T["w_mlp_in_2"], u * HALF, (u + 1) * HALF)
        r.add_matrix("mlp", T["w_mlp_out_2"][u * HALF:(u + 1) * HALF, :], 0, D)


def gain_of(K, name):
    return lambda t: K.vec(name, t)


def block2_stages(K):
    K.ylruT, K.odT, K.omT = K.at(32, 6, S), K.at(44, 2, S), K.at(48, 4, S)
    K.rg = K.at(120, 2, 6, P)
    K.qd, K.kd, K.vd, K.qm = K.at(56, 6, S), K.at(68, 6, S), K.at(80, 12, 256), K.at(92, 4, S)
    K.kmT, K.vm = K.at(100, 4, NCTX), K.at(104, 2, 512)
    K.hank0, K.hank1, K.hank2 = K.at(108, 4, 256), K.at(112, 4, P), K.at(114, 4, P)
    K.memT = K.at(56, KD, NCTX)
    K.lru_rate, K.flip, K.pick = K.at(151.5, 6), K.at(151, P), K.at(150, 256)[0:4]
    return [
        lambda: load_memory_stage(K),
        lambda: norm_stage(K, [(K.memT, NCTX, K.memT, gain_of(K, "g_mem_2"), None),
                               (K.xT, S, K.hT, gain_of(K, "g_mix_2"), None)], 72),
        lambda: memory_project_stage(K),
        lambda: lru_weights_stage(K),
        lambda: lru_stage(K),
        lambda: dilated_project_stage(K),
        lambda: dilated_attention_stage(K),
        lambda: memory_attention_stage(K),
    ]


def merge2_stages(K):
    return [
        lambda: merge_stage(K, "merge2", [(K.ylruT, 6), (K.odT, 2), (K.omT, 4)], 56, K.at(120, KD, S), 136,
                            bias="b_gate_2"),
        lambda: norm_stage(K, [(K.xT, S, K.hT, gain_of(K, "g_mlp_2"), None)], 32),
    ]


def final_stages(K):
    return [
        lambda: norm_stage(K, [(K.xT, S, K.hT, gain_of(K, "g_final_2"), None)], 72, store=K.out),
    ]


def block1_stages(K):
    K.hcT = K.at(32, KD, NCTX)
    K.yattT, K.yglaT = K.at(40, 8, S), K.at(56, 4, S)
    K.gq, K.gv, K.gk, K.og = K.at(64, 2, S), K.at(72, 6, 512), K.at(84, 2, 768), K.at(90, 4, 512)
    K.ga = [K.at(60, 768), K.at(68, 768)]
    K.qdec, K.kinv, K.kend, K.states = K.at(100, 4, S), K.at(108, 4, S), K.at(116, 6, 4, P), K.at(128, 4, 9, P)
    K.kT, K.v, K.qT = K.at(72, 2, S + NCTX), K.at(78, 6, 256), K.at(84, 8, S)
    K.yhyT, K.x2T, K.x1, K.z = (K.at(64 + 8 * i, 4, S) for i in range(4))
    K.Rf, K.If, K.edge, K.hid = K.at(128, 4, S), K.at(136, 4, S), K.at(144, S), K.at(146, S)[0:64]
    return [
        lambda: mod_stage(K),
        lambda: norm_stage(K, [
            (K.xT, S, K.hT, lambda t: K.gain1[:, t:t + 1], lambda t: mod_col(K, 0, t)),
            (K.at(40, KD, NCTX), NCTX, K.hcT, lambda t: K.gain1c[:, t:t + 1], lambda t: mod_col(K, 0, t, 1))], 72),
        lambda: gla_project_stage(K),
        lambda: gla_chunk_stage(K),
        lambda: qk_stage(K),
        lambda: latent_attention_stage(K),
        lambda: hyena_project_stage(K),
        lambda: hyena_stage(K, 0),
        lambda: hyena_stage(K, 1),
    ]


def merge1_stages(K):
    return [
        lambda: merge_stage(K, "merge1", [(K.yhyT, 4), (K.yglaT, 4), (K.yattT, 8)], 72, K.at(136, KD, S), 32,
                            gate=lambda t: mod_col(K, 2, t)),
        lambda: norm_stage(K, [(K.xT, S, K.hT, lambda t: K.gain2[:, t:t + 1], lambda t: mod_col(K, 3, t))], 32),
    ]


def expert_stages(K):
    K.h_hi, K.h_lo = K.rounded_at(32, ST, D), K.rounded_at(48, ST, D)
    K.gates, K.place, K.slot_no = K.at(150, 64), K.at(150.25, 64 + GE), router_views(K)[3]
    return [
        lambda: router_stage(K),
        lambda: moe_stage(K),
    ]


def kernel(**inputs):
    import concourse.bacc as bacc
    from concourse.bass_utils import run_bass_kernel_spmd

    nc = bacc.Bacc("TRN2", target_bir_lowering=False, num_devices=1)
    arrays = layout(inputs)
    T = {k: nc.dram_tensor(k, v.shape, mybir.dt.from_np(v.dtype), kind="ExternalInput").ap() for k, v in arrays.items()}
    out = nc.dram_tensor("out", (D, S), F32, kind="ExternalOutput").ap()
    build(nc, T, out)
    r = run_bass_kernel_spmd(nc, [arrays], core_ids=[0])
    return np.ascontiguousarray(np.asarray(r.results[0]["out"]).T).reshape(1, S, D)
```
